# Optimizing a Trainium2 kernel written in Bass

```python
import math
import jax
import jax.numpy as jnp
from jax import lax

D_MODEL = 1024
BATCH = 1
SEQ = 1024
DEPTH = 1
DEC_BATCH = 8
DEC_SEQ = 4
PAST_LEN = 256
PAGE_SIZE = 128

W_MIX = D_MODEL
W_A = W_MIX // 4
H_A = 4
DH_A = W_A // H_A
SB_QBLOCK = 128
SB_BIAS_INIT = -6.0
W_B = W_MIX // 4
G_B = 4
DG_B = W_B // G_B
GMLP_CHUNK = 128
W_C = W_MIX // 4
G_C = 4
DG_C = W_C // G_C
POOL_WINDOWS = (2, 4, 8, 16)
POOL_BUF = max(POOL_WINDOWS) - 1
W_D = W_MIX - W_A - W_B - W_C
H_D = 4
DK_D = W_D // H_D
DV_D = W_D // H_D
CONV_K = 4
DELTA_CHUNK = 64
N_MEM = 256
XA_HEADS = 4
XA_DH = D_MODEL // XA_HEADS
N_EXPERTS = 16
N_GROUPS = 4
EXPERTS_PER_GROUP = N_EXPERTS // N_GROUPS
TOP_K = 2
D_EXPERT = 256
ALPHA = (2 * DEPTH) ** 0.25
INIT_BETA = (8 * DEPTH) ** -0.25
LN_EPS = 1e-5
IN_SPLITS = (W_A, W_A, W_A, W_B, W_B, W_C, 3 * W_D, W_D, H_D, H_D)
N_IN = sum(IN_SPLITS)

kernel_name = 'hybrid_sb_gmlp_pool_gdn_moe_step'

def layer_norm(x, g, b):
    xf = x.astype(jnp.float32)
    mu = jnp.mean(xf, -1, keepdims=True)
    var = jnp.mean(jnp.square(xf - mu), -1, keepdims=True)
    y = (xf - mu) * lax.rsqrt(var + LN_EPS) * g.astype(jnp.float32) + b.astype(jnp.float32)
    return y.astype(x.dtype)

def rms_norm(x, g):
    xf = x.astype(jnp.float32)
    y = xf * lax.rsqrt(jnp.mean(xf * xf, -1, keepdims=True) + 1e-6) * g.astype(jnp.float32)
    return y.astype(x.dtype)

def l2_normalize(x):
    xf = x.astype(jnp.float32)
    return xf * lax.rsqrt(jnp.sum(xf * xf, -1, keepdims=True) + 1e-6)

def gather_pages(pool, page_table):
    rows = pool[page_table]
    b, n, p = rows.shape[:3]
    return rows.reshape((b, n * p) + rows.shape[3:])

def stick_breaking(q, k, v, q_pos, k_pos, bias):
    z = jnp.einsum('bqhd,bkhd->bhqk', q, k).astype(jnp.float32) * (q.shape[-1] ** -0.5)
    z = z + bias.astype(jnp.float32)[None, :, None, None]
    mask = k_pos[None, :] < q_pos[:, None]
    log_beta = jax.nn.log_sigmoid(z)
    log_keep = jnp.where(mask, jax.nn.log_sigmoid(-z), 0.0)
    suffix = lax.cumsum(log_keep, axis=3, reverse=True)
    after = jnp.concatenate([suffix[..., 1:], jnp.zeros_like(suffix[..., :1])], axis=-1)
    att = jnp.where(mask, jnp.exp(log_beta + after), 0.0)
    return jnp.einsum('bhqk,bkhd->bqhd', att.astype(v.dtype), v)

def stick_breaking_prompt(q, k, v, bias):
    b, t, h, dh = q.shape
    nb = t // SB_QBLOCK
    qb = jnp.moveaxis(q.reshape(b, nb, SB_QBLOCK, h, dh), 1, 0)
    k_pos = jnp.arange(t)

    def block(args):
        q_blk, i = args
        return stick_breaking(q_blk, k, v, i * SB_QBLOCK + jnp.arange(SB_QBLOCK), k_pos, bias)

    out = lax.map(block, (qb, jnp.arange(nb)))
    return jnp.moveaxis(out, 0, 1).reshape(b, t, h, dh)

def gmlp_gate(u, v, ws, bs, ln_g, ln_b):
    b, t, _ = u.shape
    c = min(t, GMLP_CHUNK)
    nc = t // c
    u = jax.nn.gelu(u)
    vn = layer_norm(jax.nn.gelu(v).reshape(b, t, G_B, DG_B), ln_g, ln_b)
    w = jnp.where(jnp.tril(jnp.ones((c, c), bool)), ws[:, :c, :c], 0.0).astype(vn.dtype)
    mixed = jnp.einsum('gts,bnsgd->bntgd', w, vn.reshape(b, nc, c, G_B, DG_B))
    mixed = mixed + jnp.swapaxes(bs[:, :c], 0, 1)[:, :, None].astype(vn.dtype)
    return u * mixed.reshape(b, t, W_B), vn.reshape(b, t, W_B)

def pool_mix(xc, prev, start, w_pool, gamma):
    b, t, _ = xc.shape
    xx = jnp.concatenate([prev.astype(xc.dtype), xc], axis=1)
    xf = xx.astype(jnp.float32)
    cs = jnp.concatenate([jnp.zeros_like(xf[:, :1]), jnp.cumsum(xf, axis=1)], axis=1)
    pos = start + jnp.arange(t)
    means = []
    for gi, w in enumerate(POOL_WINDOWS):
        ch = slice(gi * DG_C, (gi + 1) * DG_C)
        win = cs[:, POOL_BUF + 1:POOL_BUF + 1 + t, ch] - cs[:, POOL_BUF + 1 - w:POOL_BUF + 1 - w + t, ch]
        cnt = jnp.minimum(pos + 1, w).astype(jnp.float32)
        means.append(win / cnt[None, :, None])
    d = (jnp.concatenate(means, -1) - xc.astype(jnp.float32)).reshape(b, t, G_C, DG_C)
    y = jnp.einsum('btgc,gcd->btgd', d, w_pool.astype(jnp.float32)).reshape(b, t, W_C) * gamma.astype(jnp.float32)
    return y.astype(xc.dtype), xx[:, t:]

def short_conv(x, prev, w):
    t = x.shape[1]
    xx = jnp.concatenate([prev.astype(x.dtype), x], axis=1)
    y = xx[:, 0:t] * w[0]
    for i in range(1, CONV_K):
        y = y + xx[:, i:i + t] * w[i]
    return jax.nn.silu(y), xx[:, t:]

def gated_delta_rule(q, k, v, g, beta, s0):
    b, t, h, dk = q.shape
    dv = v.shape[-1]
    c = DELTA_CHUNK
    pad = (-t) % c
    n = (t + pad) // c

    def chunks(a):
        a = a.astype(jnp.float32)
        a = jnp.pad(a, [(0, 0), (0, pad)] + [(0, 0)] * (a.ndim - 2))
        a = a.reshape((b, n, c) + a.shape[2:])
        return jnp.moveaxis(a, 3, 1)

    qc = chunks(q) * (dk ** -0.5)
    kc = chunks(k)
    vc = chunks(v)
    gc = jnp.cumsum(chunks(g), axis=-1)
    bc = chunks(beta)
    incl = jnp.tril(jnp.ones((c, c), bool))
    strict = jnp.tril(jnp.ones((c, c), bool), -1)
    diff = gc[..., :, None] - gc[..., None, :]
    decay = jnp.where(incl, jnp.exp(jnp.where(incl, diff, 0.0)), 0.0)
    kb = kc * bc[..., None]
    vb = vc * bc[..., None]
    lower = jnp.where(strict, jnp.einsum('bhnid,bhnjd->bhnij', kb, kc) * decay, 0.0)
    eye = jnp.eye(c, dtype=jnp.float32)
    t_inv = lax.linalg.triangular_solve(eye + lower, jnp.broadcast_to(eye, lower.shape),
                                        left_side=True, lower=True, unit_diagonal=True)
    u = t_inv @ vb
    w = t_inv @ (kb * jnp.exp(gc)[..., None])
    intra = jnp.where(incl, jnp.einsum('bhnid,bhnjd->bhnij', qc, kc) * decay, 0.0)
    qg = qc * jnp.exp(gc)[..., None]
    kg = kc * jnp.exp(gc[..., -1:] - gc)[..., None]
    g_last = jnp.exp(gc[..., -1])
    xs = tuple(jnp.moveaxis(a, 2, 0) for a in (u, w, intra, qg, kg, g_last))

    def step(s, xs_i):
        u_i, w_i, a_i, qg_i, kg_i, gl_i = xs_i
        v_new = u_i - w_i @ s
        o_i = qg_i @ s + a_i @ v_new
        s = s * gl_i[..., None, None] + jnp.swapaxes(kg_i, -1, -2) @ v_new
        return s, o_i

    s_final, o = lax.scan(step, s0.astype(jnp.float32), xs)
    o = jnp.moveaxis(o, 0, 2).reshape(b, h, n * c, dv)
    return jnp.moveaxis(o, 1, 2)[:, :t], s_final

def mixer_sublayer(h, P, l, sb_past, pool_prev, conv_prev, s0, start):
    b, t, _ = h.shape
    z = h @ P['w_in'][l]
    idx = []
    acc = 0
    for s in IN_SPLITS[:-1]:
        acc += s
        idx.append(acc)
    qa, ka, va, ub, vb, xc, qkv, zg, bd, ad = jnp.split(z, idx, axis=-1)
    qa = qa.reshape(b, t, H_A, DH_A)
    ka = ka.reshape(b, t, H_A, DH_A)
    va = va.reshape(b, t, H_A, DH_A)
    if sb_past is None:
        oa = stick_breaking_prompt(qa, ka, va, P['sb_bias'][l])
    else:
        past_k, past_v = sb_past
        p_len = past_k.shape[1]
        k_all = jnp.concatenate([past_k.astype(ka.dtype), ka], axis=1)
        v_all = jnp.concatenate([past_v.astype(va.dtype), va], axis=1)
        oa = stick_breaking(qa, k_all, v_all, p_len + jnp.arange(t), jnp.arange(p_len + t), P['sb_bias'][l])
    ob, v_rows = gmlp_gate(ub, vb, P['gmlp_ws'][l], P['gmlp_bs'][l], P['gmlp_ln_g'][l], P['gmlp_ln_b'][l])
    oc, pool_new = pool_mix(xc, pool_prev, start, P['pool_w'][l], P['pool_gamma'][l])
    qkv, conv_new = short_conv(qkv, conv_prev, P['conv_w'][l])
    qd, kd, vd = jnp.split(qkv, 3, axis=-1)
    qd = l2_normalize(qd.reshape(b, t, H_D, DK_D))
    kd = l2_normalize(kd.reshape(b, t, H_D, DK_D))
    vd = vd.reshape(b, t, H_D, DV_D)
    beta = jax.nn.sigmoid(bd.astype(jnp.float32))
    g = -jnp.exp(P['dn_a_log'][l].astype(jnp.float32)) * jax.nn.softplus(
        ad.astype(jnp.float32) + P['dn_dt_bias'][l].astype(jnp.float32))
    od, s_new = gated_delta_rule(qd, kd, vd, g, beta, s0)
    od = rms_norm(od, P['dn_norm_g'][l]) * jax.nn.silu(zg.reshape(b, t, H_D, DV_D).astype(jnp.float32))
    od = od.reshape(b, t, W_D).astype(h.dtype)
    o = jnp.concatenate([oa.reshape(b, t, W_A), ob, oc, od], axis=-1) @ P['w_out'][l]
    return o, (ka, va, v_rows, pool_new, conv_new, s_new)

def cross_attention(h, mem_k, mem_v, wq, wo):
    b, t, _ = h.shape
    q = (h @ wq).reshape(b, t, XA_HEADS, XA_DH)
    s = jnp.einsum('bthd,bmhd->bhtm', q, mem_k.astype(q.dtype)).astype(jnp.float32) * (XA_DH ** -0.5)
    p = jax.nn.softmax(s, axis=-1).astype(h.dtype)
    o = jnp.einsum('bhtm,bmhd->bthd', p, mem_v.astype(h.dtype)).reshape(b, t, D_MODEL)
    return o @ wo

def moe_ffn(h, w_router, router_bias, wg, wu, wd):
    b, t, d = h.shape
    x = h.reshape(b * t, d)
    s = jax.nn.sigmoid((x @ w_router).astype(jnp.float32))
    sel = (s + router_bias.astype(jnp.float32)).reshape(-1, N_GROUPS, EXPERTS_PER_GROUP)
    group_score = jnp.sum(lax.top_k(sel, TOP_K)[0], axis=-1)
    gidx = jnp.argmax(group_score, axis=-1)
    in_group = jnp.take_along_axis(sel, gidx[:, None, None], axis=1)[:, 0]
    _, local = lax.top_k(in_group, TOP_K)
    eidx = gidx[:, None] * EXPERTS_PER_GROUP + local
    gate = jnp.take_along_axis(s, eidx, axis=-1)
    gate = gate / jnp.sum(gate, -1, keepdims=True)
    combine = jnp.sum(jax.nn.one_hot(eidx, N_EXPERTS, dtype=jnp.float32) * gate[..., None], axis=1)
    hg = jnp.einsum('nd,edf->nef', x, wg)
    hu = jnp.einsum('nd,edf->nef', x, wu)
    act = jax.nn.silu(hg) * hu * combine[:, :, None].astype(x.dtype)
    y = jnp.einsum('nef,efd->nd', act, wd)
    return y.reshape(b, t, d)

def trunk(x, P, sb_past, pool_prev, conv_prev, s0, start, mem_k, mem_v):
    h = layer_norm(x, P['ln0_g'], P['ln0_b'])
    states = []
    for l in range(DEPTH):
        past = None if sb_past is None else sb_past[l]
        m, st = mixer_sublayer(h, P, l, past, pool_prev[l], conv_prev[l], s0[l], start)
        h = layer_norm(ALPHA * h + m, P['ln1_g'][l], P['ln1_b'][l])
        c = cross_attention(h, mem_k[l], mem_v[l], P['xa_wq'][l], P['xa_wo'][l])
        h = layer_norm(ALPHA * h + c, P['ln2_g'][l], P['ln2_b'][l])
        f = moe_ffn(h, P['w_router'], P['router_bias'], P['ex_wg'][l], P['ex_wu'][l], P['ex_wd'][l])
        h = layer_norm(ALPHA * h + f, P['ln3_g'][l], P['ln3_b'][l])
        states.append(st)
    return h, states

def setup_inputs(seed: int = 0) -> dict:
    key = jax.random.key(seed)
    ks = jax.random.split(key, 64)
    cnt = [0]

    def nk():
        cnt[0] += 1
        return ks[cnt[0] - 1]

    def nrm(shape, scale=1.0):
        return jax.random.normal(nk(), shape, jnp.float32) * scale

    def gain(shape):
        return 1.0 + nrm(shape, 0.02)

    n_pages = PAST_LEN // PAGE_SIZE
    n_used = DEC_BATCH * n_pages
    n_phys = n_used + n_used // 4
    page_table = jax.random.permutation(nk(), n_phys)[:n_used].reshape(DEC_BATCH, n_pages).astype(jnp.int32)
    dt = jnp.exp(jax.random.uniform(nk(), (DEPTH, H_D), jnp.float32, math.log(1e-3), math.log(1e-1)))
    dn_dt_bias = dt + jnp.log(-jnp.expm1(-dt))
    dn_a_log = jnp.log(jax.random.uniform(nk(), (DEPTH, H_D), jnp.float32, 1.0, 16.0))
    return {
        'x_prompt': nrm((BATCH, SEQ, D_MODEL)),
        'x_sample': nrm((DEC_BATCH, DEC_SEQ, D_MODEL)),
        'cache_sb_k': nrm((DEPTH, n_phys, PAGE_SIZE, H_A, DH_A)),
        'cache_sb_v': nrm((DEPTH, n_phys, PAGE_SIZE, H_A, DH_A)),
        'state_pool': nrm((DEPTH, DEC_BATCH, POOL_BUF, W_C)),
        'state_conv': nrm((DEPTH, DEC_BATCH, CONV_K - 1, 3 * W_D)),
        'state_delta': nrm((DEPTH, DEC_BATCH, H_D, DK_D, DV_D), 0.1),
        'cache_mem_k': nrm((DEPTH, DEC_BATCH, N_MEM, XA_HEADS, XA_DH)),
        'cache_mem_v': nrm((DEPTH, DEC_BATCH, N_MEM, XA_HEADS, XA_DH)),
        'page_table': page_table,
        'mem_prompt': nrm((BATCH, N_MEM, D_MODEL)),
        'ln0_g': gain((D_MODEL,)),
        'ln0_b': nrm((D_MODEL,), 0.02),
        'w_in': nrm((DEPTH, D_MODEL, N_IN), D_MODEL ** -0.5),
        'sb_bias': SB_BIAS_INIT + nrm((DEPTH, H_A), 0.1),
        'gmlp_ln_g': gain((DEPTH, G_B, DG_B)),
        'gmlp_ln_b': nrm((DEPTH, G_B, DG_B), 0.02),
        'gmlp_ws': nrm((DEPTH, G_B, GMLP_CHUNK, GMLP_CHUNK), GMLP_CHUNK ** -0.5),
        'gmlp_bs': 1.0 + nrm((DEPTH, G_B, GMLP_CHUNK), 0.1),
        'pool_w': nrm((DEPTH, G_C, DG_C, DG_C), DG_C ** -0.5),
        'pool_gamma': 1.0 + nrm((DEPTH, W_C), 0.1),
        'conv_w': nrm((DEPTH, CONV_K, 3 * W_D), CONV_K ** -0.5),
        'dn_a_log': dn_a_log,
        'dn_dt_bias': dn_dt_bias,
        'dn_norm_g': gain((DEPTH, DV_D)),
        'w_out': nrm((DEPTH, W_MIX, D_MODEL), INIT_BETA * W_MIX ** -0.5),
        'ln1_g': gain((DEPTH, D_MODEL)),
        'ln1_b': nrm((DEPTH, D_MODEL), 0.02),
        'xa_wq': nrm((DEPTH, D_MODEL, D_MODEL), D_MODEL ** -0.5),
        'xa_wk': nrm((DEPTH, D_MODEL, D_MODEL), D_MODEL ** -0.5),
        'xa_wv': nrm((DEPTH, D_MODEL, D_MODEL), D_MODEL ** -0.5),
        'xa_wo': nrm((DEPTH, D_MODEL, D_MODEL), INIT_BETA * D_MODEL ** -0.5),
        'ln2_g': gain((DEPTH, D_MODEL)),
        'ln2_b': nrm((DEPTH, D_MODEL), 0.02),
        'w_router': nrm((D_MODEL, N_EXPERTS), D_MODEL ** -0.5),
        'router_bias': nrm((N_EXPERTS,), 0.01),
        'ex_wg': nrm((DEPTH, N_EXPERTS, D_MODEL, D_EXPERT), D_MODEL ** -0.5),
        'ex_wu': nrm((DEPTH, N_EXPERTS, D_MODEL, D_EXPERT), D_MODEL ** -0.5),
        'ex_wd': nrm((DEPTH, N_EXPERTS, D_EXPERT, D_MODEL), INIT_BETA * D_EXPERT ** -0.5),
        'ln3_g': gain((DEPTH, D_MODEL)),
        'ln3_b': nrm((DEPTH, D_MODEL), 0.02),
    }

def reference(x_prompt, x_sample, cache_sb_k, cache_sb_v, state_pool, state_conv, state_delta,
              cache_mem_k, cache_mem_v, page_table, mem_prompt,
              ln0_g, ln0_b, w_in, sb_bias, gmlp_ln_g, gmlp_ln_b, gmlp_ws, gmlp_bs, pool_w, pool_gamma,
              conv_w, dn_a_log, dn_dt_bias, dn_norm_g, w_out, ln1_g, ln1_b,
              xa_wq, xa_wk, xa_wv, xa_wo, ln2_g, ln2_b, w_router, router_bias,
              ex_wg, ex_wu, ex_wd, ln3_g, ln3_b):
    P = {'ln0_g': ln0_g, 'ln0_b': ln0_b, 'w_in': w_in, 'sb_bias': sb_bias,
         'gmlp_ln_g': gmlp_ln_g, 'gmlp_ln_b': gmlp_ln_b,
         'gmlp_ws': gmlp_ws, 'gmlp_bs': gmlp_bs, 'pool_w': pool_w, 'pool_gamma': pool_gamma,
         'conv_w': conv_w, 'dn_a_log': dn_a_log, 'dn_dt_bias': dn_dt_bias, 'dn_norm_g': dn_norm_g,
         'w_out': w_out, 'ln1_g': ln1_g, 'ln1_b': ln1_b, 'xa_wq': xa_wq, 'xa_wo': xa_wo,
         'ln2_g': ln2_g, 'ln2_b': ln2_b, 'w_router': w_router, 'router_bias': router_bias,
         'ex_wg': ex_wg, 'ex_wu': ex_wu, 'ex_wd': ex_wd, 'ln3_g': ln3_g, 'ln3_b': ln3_b}
    bp = x_prompt.shape[0]
    mem_k_p = jnp.stack([(mem_prompt @ xa_wk[l]).reshape(bp, -1, XA_HEADS, XA_DH) for l in range(DEPTH)])
    mem_v_p = jnp.stack([(mem_prompt @ xa_wv[l]).reshape(bp, -1, XA_HEADS, XA_DH) for l in range(DEPTH)])
    pool0 = [jnp.zeros((bp, POOL_BUF, W_C), x_prompt.dtype)] * DEPTH
    conv0 = [jnp.zeros((bp, CONV_K - 1, 3 * W_D), x_prompt.dtype)] * DEPTH
    s00 = [jnp.zeros((bp, H_D, DK_D, DV_D), jnp.float32)] * DEPTH
    y_prompt, st_p = trunk(x_prompt, P, None, pool0, conv0, s00, 0, mem_k_p, mem_v_p)
    past_len = page_table.shape[1] * PAGE_SIZE
    sb_past = [(gather_pages(cache_sb_k[l], page_table), gather_pages(cache_sb_v[l], page_table))
               for l in range(DEPTH)]
    y_sample, st_s = trunk(x_sample, P, sb_past, state_pool, state_conv, state_delta, past_len,
                           cache_mem_k, cache_mem_v)

    def stk(sts, i):
        return jnp.stack([s[i] for s in sts])

    return (y_prompt, y_sample,
            stk(st_p, 0), stk(st_p, 1), stk(st_s, 0), stk(st_s, 1),
            stk(st_s, 2),
            stk(st_p, 3), stk(st_s, 3),
            stk(st_p, 4), stk(st_s, 4),
            stk(st_p, 5), stk(st_s, 5),
            mem_k_p, mem_v_p)


_drawn_inputs = setup_inputs


def setup_inputs(seed=0):
    import zlib

    import numpy as np

    out = dict(_drawn_inputs(seed))
    spreads = {}
    factors = {'sb_bias': 8.0,
     'gmlp_ln_g': 8.661,
     'gmlp_ln_b': 8.568,
     'dn_norm_g': 5.064,
     'ln3_g': 7.416,
     'ln3_b': 7.037}
    for name, (base, spread) in spreads.items():
        noise = np.random.default_rng([zlib.crc32(name.encode()), seed]).standard_normal(out[name].shape)
        drawn = base * np.exp(spread * noise) if base else spread * noise
        out[name] = jnp.asarray(drawn.astype(out[name].dtype))
    for name, factor in factors.items():
        out[name] = (out[name] * factor).astype(out[name].dtype)
    return out
```

```python
from contextlib import ExitStack

import numpy as np
import concourse.bass as bass
from concourse import mybir

F32 = mybir.dt.float32
I32 = mybir.dt.int32
ALU = mybir.AluOpType
ACT = mybir.ActivationFunctionType
AX = mybir.AxisListType.X

P = 128
D = 1024
KC = D // P
SEQ = 1024
NT = SEQ // P
DB, DS = 8, 4
NS = DB * DS
TOK = SEQ + NS
TILES = NT + 1
GRP = 3
GT = TOK // GRP
PAGE = 128
NPG = 2
HEADS = 4
DH = 64
CH = 64
POOLB = 15
WINDOWS = (2, 4, 8, 16)
NMEM = 256
XDH = 256
NE = 16
DE = 256
ALPHA = float(2 ** 0.25)
LN_EPS = 1e-5
QA, KA, VA, UB, VB, XC, QKV, ZG, BD = 0, 256, 512, 768, 1024, 1280, 1536, 2304, 2560

EXPLN = "natural_log_exp_and_others"


def rows(i):
    return P if i < NT else NS


def const_blocks():
    p = np.arange(P)[:, None]
    f = np.arange(P)[None, :]
    one = np.ones((P, P))
    chunk = p // CH == f // CH
    blk4 = p // DS == f // DS
    c = {
        "ident": p == f,
        "ones": one,
        "cum64": (p <= f) & chunk,
        "low64": (p > f) & chunk,
        "blk64": chunk,
        "negsuf": -1.0 * (p >= f),
        "negone": -one,
        "before": p < f,
        "upto": p <= f,
        "cum4": (p <= f) & blk4,
        "low4": (p > f) & blk4,
        "blk4": blk4,
        "before4": (p < f) & blk4,
        "rep4": np.where((p < DS) & (f % DS == p), 1.0, 0.0),
        "up1": (f % 2 == 1) & (p == f - 1),
    }
    for b in (1, 2, 4, 8, 16, 32):
        c[f"lvl{b}"] = (p // (2 * b) == f // (2 * b)) & ((p // b) % 2 == 1) & ((f // b) % 2 == 0)
    return {k: np.asarray(v, np.float32) for k, v in c.items()}


def pool_blocks():
    p = np.arange(P)[:, None]
    f = np.arange(P)[None, :]
    blk4 = p // DS == f // DS
    c = {}
    for g, w in enumerate(WINDOWS):
        c[f"band{g}"] = ((p <= f) & (p > f - w)) / w - 1.0 * (p == f)
        c[f"bandprev{g}"] = (p > f - w + P) / w
        c[f"bandfirst{g}"] = ((p <= f) & (p > f - w)) / np.minimum(f + 1, w) - 1.0 * (p == f)
        b_, q_ = p // POOLB, p % POOLB
        c[f"spool{g}"] = ((b_ == f // DS) & (q_ >= POOLB + 1 + f % DS - w) & (p < DB * POOLB) & (f < NS)) / w
        c[f"scur{g}"] = (blk4 & (p <= f) & (p > f - w)) / w - 1.0 * (p == f)
    return {k: np.asarray(v, np.float32) for k, v in c.items()}


CONSTS = const_blocks()
POOL_CONSTS = pool_blocks()
CONST_AT = {k: n * P for n, k in enumerate(CONSTS)}
POOL_AT = {k: n * P for n, k in enumerate(POOL_CONSTS)}
NCONST = len(CONSTS) * P

_INS = ['x_prompt', 'x_sample', 'cache_sb_k', 'cache_sb_v', 'state_pool', 'state_conv', 'state_delta',
        'cache_mem_k', 'cache_mem_v', 'page_table', 'mem_prompt', 'ln0_g', 'ln0_b', 'w_in', 'sb_bias',
        'gmlp_ln_g', 'gmlp_ln_b', 'gmlp_ws', 'gmlp_bs', 'pool_w', 'pool_gamma', 'conv_w', 'dn_a_log',
        'dn_dt_bias', 'dn_norm_g', 'w_out', 'ln1_g', 'ln1_b', 'xa_wq', 'xa_wk', 'xa_wv', 'xa_wo', 'ln2_g',
        'ln2_b', 'w_router', 'router_bias', 'ex_wg', 'ex_wu', 'ex_wd', 'ln3_g', 'ln3_b']
_OUTS = [('y_prompt', (1, SEQ, D)), ('y_sample', (DB, DS, D)),
         ('sb_k_prompt', (1, 1, SEQ, HEADS, DH)), ('sb_v_prompt', (1, 1, SEQ, HEADS, DH)),
         ('sb_k_sample', (1, DB, DS, HEADS, DH)), ('sb_v_sample', (1, DB, DS, HEADS, DH)),
         ('gmlp_v_sample', (1, DB, DS, 256)),
         ('pool_prompt', (1, 1, POOLB, 256)), ('pool_sample', (1, DB, POOLB, 256)),
         ('conv_prompt', (1, 1, 3, 768)), ('conv_sample', (1, DB, 3, 768)),
         ('delta_prompt', (1, 1, HEADS, DH, DH)), ('delta_sample', (1, DB, HEADS, DH, DH)),
         ('mem_k_prompt', (1, 1, NMEM, HEADS, XDH)), ('mem_v_prompt', (1, 1, NMEM, HEADS, XDH))]


class Chain:

    def __init__(self, eng, sem):
        self.eng, self.sem, self.n = eng, sem, 0

    def __call__(self, ins):
        self.n += 1
        ins.then_inc(self.sem, 1)
        self.eng.wait_ge(self.sem, self.n)


class Ctx:
    pass


def setup(nc, ctx, T, O):
    c = Ctx()
    c.nc, c.T, c.O = nc, T, O

    held, stack = [], [ctx.enter_context(ExitStack())]

    def sem(name):
        held.append(stack[0].enter_context(nc.semaphore(name)))
        return held[-1]

    def renew_semaphores():
        with nc.Block() as block:
            @block.sync
            def _(sp):
                for x in held:
                    sp.sem_clear(x)
        held.clear()
        stack[0].close()
        stack[0] = ctx.enter_context(ExitStack())

    c.sem, c.renew_semaphores = sem, renew_semaphores
    c.ps = [ctx.enter_context(nc.psum_tensor(f"bank{b}", [P, 512], F32)) for b in range(8)]
    c.const = ctx.enter_context(nc.sbuf_tensor("const", [P, NCONST], F32))
    c.h = ctx.enter_context(nc.sbuf_tensor("h", [P, TILES, D], F32))
    c.hT = ctx.enter_context(nc.sbuf_tensor("hT", [P, KC, TOK], F32))
    c.small = ctx.enter_context(nc.sbuf_tensor("small", [P, 1024], F32))
    AR = 29200
    c.arena = ctx.enter_context(nc.sbuf_tensor("arena", [P, AR], F32))
    c.at = {}
    c.small_used = 0

    def K(name, r=P, w=P):
        a = CONST_AT[name]
        return c.const[0:r, a:a + w]

    c.K = K

    def place(**sizes):
        at = sizes.pop("start", 0)
        for k, n in sizes.items():
            assert at + n <= AR, (k, at, n)
            c.at[k] = (at, n)
            at += n
        return at

    def A(k):
        a, n = c.at[k]
        return c.arena[:, a:a + n]

    c.place, c.A = place, A

    def small(n):
        a = c.small_used
        c.small_used += n
        assert c.small_used <= 1024
        return c.small[:, a:a + n]

    c.new_small = small
    c.ids = ctx.enter_context(nc.sbuf_tensor("page_ids", [1, DB * NPG], I32))
    return c


def row_bc(ap, n=P):
    return ap.partition_broadcast(n)


def x_tile(T, i):
    if i < NT:
        return T['x_prompt'][0, i * P:(i + 1) * P, :]
    return T['x_sample'].rearrange("b t d -> (b t) d")


def ln_stats(nc, link, h, i, st, mv):
    r = rows(i)
    nc.vector.bn_stats(st[0:r, 0:6], h[0:r, i, 0:512])
    link(nc.vector.bn_stats(st[0:r, 6:12], h[0:r, i, 512:1024]))
    return nc.vector.bn_aggr(mv[0:r, :], st[0:r, :])


def ln_rstd(nc, link, i, mv, rstd, eps):
    r = rows(i)
    link(nc.scalar.activation(rstd[0:r, :], mv[0:r, 1:2], ACT.Ln, bias=eps[0:r, :]))
    return nc.scalar.activation(rstd[0:r, :], rstd[0:r, :], ACT.Exp, scale=-0.5)


def ln_apply(nc, link, h, i, mv, rstd, g, b):
    r = rows(i)
    link(nc.vector.tensor_scalar(h[0:r, i, :], h[0:r, i, :], mv[0:r, 0:1], rstd[0:r, :],
                                 ALU.subtract, ALU.mult))
    link(nc.vector.tensor_tensor(h[0:r, i, :], h[0:r, i, :], g[0:r, :], ALU.mult))
    return nc.vector.tensor_tensor(h[0:r, i, :], h[0:r, i, :], b[0:r, :], ALU.add)


def stage_entry(c):
    nc, T, O, K = c.nc, c.T, c.O, c.K
    c.free_at = c.place(kT=2 * TOK, vtok=TILES * 256, zT=2 * TOK)
    c.after_q = c.place(start=c.free_at, qkvT=6 * TOK, qT=2 * TOK)
    at = c.place(start=c.after_q, vg=TILES * 256, xc=TILES * 256, uT=2 * TOK)
    c.place(start=c.free_at, wtok=KC * 1032)
    c.place(start=at, lng=D, lnb=D, ktok=2 * 256)
    c.scratch = at
    kT = c.A("kT").rearrange("p (c t) -> p c t", c=2)
    vtok = c.A("vtok").rearrange("p (i n) -> p i n", i=TILES)
    vg = c.A("vg").rearrange("p (i n) -> p i n", i=TILES)
    xc = c.A("xc").rearrange("p (i n) -> p i n", i=TILES)
    wt = c.A("wtok").rearrange("p (k n) -> p k n", k=KC)
    ktok = c.A("ktok").rearrange("p (s n) -> p s n", s=2)
    g, b = c.A("lng"), c.A("lnb")
    c.kT, c.vtok, c.vg, c.xc = kT, vtok, vg, xc
    c.ba = c.new_small(TILES * 8).rearrange("p (i n) -> p i n", i=TILES)
    c.st = c.new_small(2 * 12).rearrange("p (s n) -> p s n", s=2)
    c.mv = c.new_small(2 * 2).rearrange("p (s n) -> p s n", s=2)
    c.rstd = c.new_small(2).rearrange("p (s n) -> p s n", s=2)
    c.eps = c.new_small(1)
    h, hT, ps = c.h, c.hT, c.ps

    s = c.sem
    x_in, w_in, const_in, ln_in = s("e_x"), s("e_w"), s("e_const"), s("e_ln")
    eps_set, stats, rstd_ok, normed = s("e_eps"), s("e_stats"), s("e_rstd"), s("e_normed")
    turned, hT_ok, proj_kv, proj_vx, proj_ba = s("e_turned"), s("e_hT"), s("e_kv"), s("e_vx"), s("e_ba")
    kv_out, vx_out, ba_out, k_turned, kT_ok = s("e_kvo"), s("e_vxo"), s("e_bao"), s("e_kt"), s("e_kTo")
    stored = [s("e_stored0"), s("e_stored1")]
    dve_chain, act_chain, zeroed = s("e_dve"), s("e_act"), s("e_zero")
    w_view = T['w_in'][0].rearrange("(k p) n -> p k n", p=P)

    with nc.Block() as block:
        @block.sync
        def _(sp):
            for i in range(TILES):
                sp.dma_start(h[0:rows(i), i, :], x_tile(T, i)).then_inc(x_in, 16)
                if i == 0:
                    sp.dma_start(g, row_bc(T['ln0_g'])).then_inc(ln_in, 16)
                    sp.dma_start(b, row_bc(T['ln0_b'])).then_inc(ln_in, 16)
                if i == 1:
                    sp.dma_start(wt[:, :, 0:512], w_view[:, :, KA:KA + 512]).then_inc(w_in, 16)
                    sp.dma_start(wt[:, :, 512:1024], w_view[:, :, VB:VB + 512]).then_inc(w_in, 16)
                    sp.dma_start(wt[:, :, 1024:1032], w_view[:, :, BD:BD + 8]).then_inc(w_in, 16)
            for i in range(TILES):
                sp.wait_ge(kv_out, 2 * i + 2)
                if i < NT:
                    ko = O['sb_k_prompt'][0, 0, i * P:(i + 1) * P].rearrange("t h d -> t (h d)")
                    vo = O['sb_v_prompt'][0, 0, i * P:(i + 1) * P].rearrange("t h d -> t (h d)")
                else:
                    ko = O['sb_k_sample'][0].rearrange("b t h d -> (b t) (h d)")
                    vo = O['sb_v_sample'][0].rearrange("b t h d -> (b t) (h d)")
                sp.dma_start(ko, ktok[0:rows(i), i % 2, :]).then_inc(stored[i % 2], 16)
                sp.dma_start(vo, vtok[0:rows(i), i, :]).then_inc(stored[i % 2], 16)
            sp.wait_ge(stored[0], 32 * 5)
            sp.wait_ge(stored[1], 32 * 4)

        @block.vector
        def _(dve):
            link = Chain(dve, dve_chain)
            nc.vector.memset(c.eps, LN_EPS).then_inc(eps_set, 1)
            nc.vector.memset(vg[:, NT, :], 0.0).then_inc(zeroed, 1)
            nc.vector.memset(c.ba[:, NT, :], 0.0).then_inc(zeroed, 1)
            dve.wait_ge(zeroed, 2)

            def evac_ba(i):
                dve.wait_ge(proj_ba, i + 1)
                nc.vector.tensor_copy(c.ba[0:rows(i), i, :], ps[4][0:rows(i), 0:8]).then_inc(ba_out, 1)

            for i in range(TILES):
                dve.wait_ge(x_in, 16 * TILES)
                if i >= 2:
                    dve.wait_ge(rstd_ok, i - 1)
                ln_stats(nc, link, h, i, c.st[:, i % 2, :], c.mv[:, i % 2, :]).then_inc(stats, 1)
                if i == 0:
                    dve.wait_ge(ln_in, 32)
                dve.wait_ge(stats, i + 1)
                dve.wait_ge(rstd_ok, i + 1)
                ln_apply(nc, link, h, i, c.mv[:, i % 2, :], c.rstd[:, i % 2, :], g, b).then_inc(normed, 1)
                if i >= 1:
                    evac_ba(i - 1)
            evac_ba(TILES - 1)

        @block.scalar
        def _(act):
            link = Chain(act, act_chain)
            act.dma_start(c.const[:, :], T['const_tables']).then_inc(const_in, 16)
            act.wait_ge(eps_set, 1)
            act.wait_ge(zeroed, 2)

            def evac(i):
                r = rows(i)
                act.wait_ge(proj_kv, i + 1)
                if i >= 2:
                    act.wait_ge(k_turned, i - 1)
                    act.wait_ge(stored[i % 2], 32 * (i // 2))
                nc.scalar.copy(ktok[0:r, i % 2, :], ps[2 + 4 * (i % 2)][0:r, 0:256]).then_inc(kv_out, 1)
                nc.scalar.copy(vtok[0:r, i, :], ps[2 + 4 * (i % 2)][0:r, 256:512]).then_inc(kv_out, 1)
                act.wait_ge(proj_vx, i + 1)
                nc.scalar.activation(vg[0:r, i, :], ps[3 + 4 * (i % 2)][0:r, 0:256],
                                     ACT.Gelu_apprx_tanh).then_inc(vx_out, 1)
                nc.scalar.copy(xc[0:r, i, :], ps[3 + 4 * (i % 2)][0:r, 256:512]).then_inc(vx_out, 1)

            def evac_kT(i):
                r = rows(i)
                act.wait_ge(k_turned, i + 1)
                nc.scalar.copy(kT[:, :, i * P:i * P + r],
                               ps[5][:, 0:2 * r].rearrange("p (c t) -> p c t", c=2)).then_inc(kT_ok, 1)

            for i in range(TILES + 2):
                if i < TILES:
                    r = rows(i)
                    act.wait_ge(stats, i + 1)
                    if i >= 2:
                        act.wait_ge(normed, i - 1)
                    nc.scalar.preload_act_table_set(EXPLN)
                    ln_rstd(nc, link, i, c.mv[:, i % 2, :], c.rstd[:, i % 2, :], c.eps).then_inc(rstd_ok, 1)
                    for q in range(2):
                        act.wait_ge(turned, 2 * i + q + 1)
                        nc.scalar.copy(hT[:, 4 * q:4 * q + 4, i * P:i * P + r],
                                       ps[q][:, 0:4 * r].rearrange("p (k t) -> p k t", k=4)).then_inc(hT_ok, 1)
                if 1 <= i <= TILES:
                    evac(i - 1)
                if i >= 2:
                    evac_kT(i - 2)

        @block.tensor
        def _(pe):
            pe.wait_ge(const_in, 16)

            def turn(i):
                r = rows(i)
                pe.wait_ge(normed, i + 1)
                for q in range(2):
                    if i >= 1:
                        pe.wait_ge(hT_ok, 2 * (i - 1) + q + 1)
                    for k in range(4):
                        last = nc.tensor.transpose(ps[q][:, k * r:(k + 1) * r],
                                                   h[0:r, i, (4 * q + k) * P:(4 * q + k + 1) * P], K("ident", r, r))
                    last.then_inc(turned, 1)

            def project(i):
                r = rows(i)
                pe.wait_ge(hT_ok, 2 * i + 2)
                for bank, col, n, out_sem, free in ((2 + 4 * (i % 2), 0, 512, proj_kv, kv_out),
                                                    (3 + 4 * (i % 2), 512, 512, proj_vx, vx_out),
                                                    (4, 1024, 8, proj_ba, ba_out)):
                    if bank == 4:
                        if i >= 1:
                            pe.wait_ge(free, i)
                    elif i >= 2:
                        pe.wait_ge(free, 2 * (i - 1))
                    for k in range(KC):
                        last = nc.tensor.matmul(ps[bank][0:r, 0:n], hT[:, k, i * P:i * P + r],
                                                wt[:, k, col:col + n], start=(k == 0), stop=(k == KC - 1))
                    last.then_inc(out_sem, 1)

            def turn_k(i):
                r = rows(i)
                pe.wait_ge(kv_out, 2 * i + 1)
                if i >= 1:
                    pe.wait_ge(kT_ok, i)
                for q in range(2):
                    last = nc.tensor.transpose(ps[5][:, q * r:(q + 1) * r], ktok[0:r, i % 2, q * P:(q + 1) * P],
                                               K("ident", r, r))
                last.then_inc(k_turned, 1)

            turn(0)
            pe.wait_ge(w_in, 48)
            for i in range(TILES):
                if i + 1 < TILES:
                    turn(i + 1)
                project(i)
                if i >= 1:
                    turn_k(i - 1)
            turn_k(TILES - 1)


def stage_features(c):
    nc, T, O, K = c.nc, c.T, c.O, c.K
    c.place(start=c.scratch, ring=4 * KC * P, vsq=TILES * 256, glng=256, glnb=256)
    ring = c.A("ring").rearrange("p (s k n) -> p s k n", s=4, k=KC)
    qT = c.A("qT").rearrange("p (c t) -> p c t", c=2)
    uT = c.A("uT").rearrange("p (c t) -> p c t", c=2)
    zT = c.A("zT").rearrange("p (c t) -> p c t", c=2)
    qkvT = c.A("qkvT").rearrange("p (c t) -> p c t", c=6)
    c.qT, c.uT, c.zT, c.qkvT = qT, uT, zT, qkvT
    hT, ps = c.hT, c.ps
    plan = ([(UB + P * n, uT[:, n], "gelu") for n in range(2)] + [(ZG + P * n, zT[:, n], "silu") for n in range(2)]
            + [(QA + P * n, qT[:, n], "scale") for n in range(2)] + [(QKV + P * n, qkvT[:, n], "copy") for n in range(6)])
    s = c.sem
    w_in = [s(f"f_w{n}") for n in range(4)]
    ln_in, product, evacuated = s("f_ln"), s("f_prod"), s("f_evac")
    stats, rstd_ok, normed, stored = s("f_stats"), s("f_rstd"), s("f_normed"), s("f_stored")
    dve_chain, act_chain = s("f_dve"), s("f_act")
    w_view = T['w_in'][0].rearrange("(k p) n -> p k n", p=P)
    vg = c.vg.rearrange("p i (g d) -> p (i g) d", g=HEADS)
    vsq = c.A("vsq").rearrange("p (m d) -> p m d", d=DH)
    mom = c.new_small(2 * TILES * HEADS).rearrange("p (s n) -> p s n", s=2)
    NG = TILES * HEADS

    with nc.Block() as block:
        @block.sync
        def _(sp):
            for n, (col, _, _) in enumerate(plan):
                if n >= 4:
                    sp.wait_ge(product, GRP * (n - 3))
                sp.dma_start(ring[:, n % 4], w_view[:, :, col:col + P]).then_inc(w_in[n % 4], 16)
                if n == 0:
                    sp.dma_start(c.A("glng"), row_bc(T['gmlp_ln_g'][0].rearrange("g d -> (g d)"))).then_inc(ln_in, 16)
                    sp.dma_start(c.A("glnb"), row_bc(T['gmlp_ln_b'][0].rearrange("g d -> (g d)"))).then_inc(ln_in, 16)
            sp.wait_ge(normed, 1)
            sp.dma_start(O['gmlp_v_sample'][0].rearrange("b t n -> (b t) n"), c.vg[0:NS, NT, :]).then_inc(stored, 16)
            sp.wait_ge(stored, 16)

        @block.tensor
        def _(pe):
            for n in range(len(plan)):
                pe.wait_ge(w_in[n % 4], 16 * (n // 4 + 1))
                for g in range(GRP):
                    u = GRP * n + g
                    if u >= 8:
                        pe.wait_ge(evacuated, u - 7)
                    for k in range(KC):
                        last = nc.tensor.matmul(ps[u % 8][:, 0:GT], ring[:, n % 4, k, :], hT[:, k, g * GT:(g + 1) * GT],
                                                start=(k == 0), stop=(k == KC - 1))
                    last.then_inc(product, 1)

        @block.scalar
        def _(act):
            link = Chain(act, act_chain)
            for n, (_, dst, how) in enumerate(plan):
                for g in range(GRP):
                    u = GRP * n + g
                    act.wait_ge(product, u + 1)
                    o, i = dst[:, g * GT:(g + 1) * GT], ps[u % 8][:, 0:GT]
                    if how == "gelu":
                        ins = nc.scalar.activation(o, i, ACT.Gelu_apprx_tanh)
                    elif how == "silu":
                        ins = nc.scalar.activation(o, i, ACT.Silu)
                    elif how == "scale":
                        ins = nc.scalar.mul(o, i, DH ** -0.5)
                    else:
                        ins = nc.scalar.copy(o, i)
                    ins.then_inc(evacuated, 1)
            nc.scalar.preload_act_table_set(EXPLN)
            act.wait_ge(stats, 1)
            link(nc.scalar.activation(mom[:, 1, :], mom[:, 1, :], ACT.Ln, bias=c.eps, scale=1.0 / DH))
            nc.scalar.activation(mom[:, 1, :], mom[:, 1, :], ACT.Exp, scale=-0.5).then_inc(rstd_ok, 1)

        @block.vector
        def _(dve):
            link = Chain(dve, dve_chain)

            def bc(row):
                return row.unsqueeze(2).to_broadcast([P, NG, DH])

            link(nc.vector.tensor_reduce(mom[:, 0, :], vg, AX, ALU.add))
            link(nc.vector.tensor_scalar(mom[:, 0, :], mom[:, 0, :], 1.0 / DH, None, ALU.mult))
            link(nc.vector.tensor_tensor(vg, vg, bc(mom[:, 0, :]), ALU.subtract))
            link(nc.vector.tensor_tensor(vsq, vg, vg, ALU.mult))
            nc.vector.tensor_reduce(mom[:, 1, :], vsq, AX, ALU.add).then_inc(stats, 1)
            dve.wait_ge(rstd_ok, 1)
            link(nc.vector.tensor_tensor(vg, vg, bc(mom[:, 1, :]), ALU.mult))
            dve.wait_ge(ln_in, 32)
            link(nc.vector.tensor_tensor(c.vg, c.vg, c.A("glng").unsqueeze(1).to_broadcast([P, TILES, 256]), ALU.mult))
            nc.vector.tensor_tensor(c.vg, c.vg, c.A("glnb").unsqueeze(1).to_broadcast([P, TILES, 256]),
                                    ALU.add).then_inc(normed, 1)


def stage_gate_and_pool(c):
    nc, T, O, K = c.nc, c.T, c.O, c.K
    c.place(start=c.scratch, ws=HEADS * P, wsT=HEADS * P, wsS=HEADS * NS, bs=512, bsb=2 * P, bsbS=2 * NS,
            bands=len(POOL_CONSTS) * P, prev=256, pw=2 * P, gam=2, dT=2 * 256, mix=256, ws4=128)
    ws = c.A("ws").rearrange("p (g s) -> p g s", g=HEADS)
    wsT = c.A("wsT").rearrange("p (g s) -> p g s", g=HEADS)
    wsS = c.A("wsS").rearrange("p (g s) -> p g s", g=HEADS)
    ws4 = c.A("ws4").rearrange("p (g s) -> p g s", g=HEADS)
    bsb = c.A("bsb").rearrange("p (c s) -> p c s", c=2)
    bsbS = c.A("bsbS").rearrange("p (c s) -> p c s", c=2)
    pw = c.A("pw").rearrange("p (c s) -> p c s", c=2)
    dT = c.A("dT").rearrange("p (s n) -> p s n", s=2)
    mix = c.A("mix")
    bands, prev, gam = c.A("bands"), c.A("prev"), c.A("gam")
    ps, oT, xc, vg, uT = c.ps, c.hT, c.xc, c.vg, c.uT

    def band(name, r=P, w=P):
        return bands[0:r, POOL_AT[name]:POOL_AT[name] + w]

    s = c.sem
    loaded, zeroed, stored = s("g_load"), s("g_zero"), s("g_stored")
    small_mm, small_ev, mixed, mixed_used = s("g_smm"), s("g_sev"), s("g_mixed"), s("g_mixused")
    diff, diff_ok, pooled, pooled_used, dve_chain = s("g_diff"), s("g_diffok"), s("g_pooled"), s("g_poolused"), s("g_dve")
    LOADS = 8 + HEADS

    with nc.Block() as block:
        @block.gpsimd
        def _(pool):
            nc.gpsimd.memset(pw, 0.0).then_inc(zeroed, 1)

        @block.sync
        def _(sp):
            sp.dma_start(ws, T['gmlp_ws'][0].rearrange("g t s -> t g s")).then_inc(loaded, 16)
            sp.dma_start(c.A("bs")[0:1, :], T['gmlp_bs'].rearrange("a g s -> a (g s)")).then_inc(loaded, 16)
            sp.dma_start(bands, T['pool_tables']).then_inc(loaded, 16)
            sp.dma_start(prev[0:DB * POOLB, :], T['state_pool'][0].rearrange("b q n -> (b q) n")).then_inc(loaded, 16)
            for n in range(2):
                sp.dma_start(gam[:, n:n + 1], T['pool_gamma'][0, n * P:(n + 1) * P].unsqueeze(1)).then_inc(loaded, 16)
            sp.wait_ge(zeroed, 1)
            for g in range(HEADS):
                q = (g % 2) * DH
                sp.dma_start(pw[q:q + DH, g // 2, q:q + DH], T['pool_w'][0, g]).then_inc(loaded, 16)
            sp.dma_start(O['pool_prompt'][0, 0], xc[P - POOLB:P, NT - 1, :]).then_inc(stored, 16)
            sp.dma_start(O['pool_sample'][0, :, 0:POOLB - DS, :], T['state_pool'][0, :, DS:POOLB, :]).then_inc(stored, 16)
            for b in range(DB):
                sp.dma_start(O['pool_sample'][0, b, POOLB - DS:POOLB, :], xc[b * DS:(b + 1) * DS, NT, :]).then_inc(stored, 16)
            sp.wait_ge(stored, 16 * (2 + DB))

        @block.tensor
        def _(pe):
            pe.wait_ge(loaded, 16 * 10)
            for g in range(HEADS):
                last = nc.tensor.transpose(ps[0][:, g * P:(g + 1) * P], ws[:, g, :], K("ident"))
            last.then_inc(small_mm, 1)
            for g in range(HEADS):
                q = (g % 2) * DH
                last = nc.tensor.matmul(ps[1][q:q + DH, (g // 2) * P:(g // 2 + 1) * P], K("ones", 1, DH),
                                        c.A("bs")[0:1, g * P:(g + 1) * P], start=True, stop=True)
            last.then_inc(small_mm, 1)
            for g in range(HEADS):
                last = nc.tensor.matmul(ps[2][0:DS, g * NS:(g + 1) * NS], ws[0:DS, g, 0:DS], K("rep4", DS, NS),
                                        start=True, stop=True)
            last.then_inc(small_mm, 1)
            pe.wait_ge(small_ev, 3)
            last = nc.tensor.matmul(ps[3][0:NS, 0:4 * NS], K("rep4", DS, NS), ws4[0:DS].rearrange("p g s -> p (g s)"),
                                    start=True, stop=True)
            last.then_inc(small_mm, 1)
            pe.wait_ge(small_ev, 5)

            def mixes(i):
                r = rows(i)
                if i >= 2:
                    pe.wait_ge(mixed_used, i - 1)
                for g in range(HEADS):
                    q = (g % 2) * DH
                    w = wsT[:, g, :] if i < NT else wsS[0:NS, g, :]
                    last = nc.tensor.matmul(ps[4 + i % 2][q:q + DH, (g // 2) * P:(g // 2) * P + r],
                                            vg[0:r, i, g * DH:(g + 1) * DH], w, start=True, stop=True)
                last.then_inc(mixed, 1)

            def diffs(i):
                r = rows(i)
                if i >= 1:
                    pe.wait_ge(diff_ok, i)
                for g in range(HEADS):
                    q = (g % 2) * DH
                    out = ps[6][q:q + DH, (g // 2) * P:(g // 2) * P + r]
                    x = xc[0:r, i, g * DH:(g + 1) * DH]
                    if i == 0:
                        last = nc.tensor.matmul(out, x, band(f"bandfirst{g}"), start=True, stop=True)
                    elif i < NT:
                        nc.tensor.matmul(out, x, band(f"band{g}"), start=True, stop=False)
                        last = nc.tensor.matmul(out, xc[:, i - 1, g * DH:(g + 1) * DH], band(f"bandprev{g}"),
                                                start=False, stop=True)
                    else:
                        nc.tensor.matmul(out, x, band(f"scur{g}", NS, NS), start=True, stop=False)
                        n = DB * POOLB
                        last = nc.tensor.matmul(out, prev[0:n, g * DH:(g + 1) * DH], band(f"spool{g}", n, NS),
                                                start=False, stop=True)
                last.then_inc(diff, 1)

            def pools(i):
                r = rows(i)
                pe.wait_ge(diff_ok, i + 1)
                if i >= 1:
                    pe.wait_ge(pooled_used, i)
                for n in range(2):
                    last = nc.tensor.matmul(ps[7][:, n * P:n * P + r], pw[:, n, :], dT[:, i % 2, n * P:n * P + r],
                                            start=True, stop=True)
                last.then_inc(pooled, 1)

            for i in range(TILES):
                mixes(i)
                diffs(i)
                pools(i)

        @block.vector
        def _(dve):
            link = Chain(dve, dve_chain)
            dve.wait_ge(small_mm, 1)
            nc.vector.tensor_tensor(wsT, ps[0][:, :].rearrange("p (g s) -> p g s", g=HEADS),
                                    K("upto").unsqueeze(1).to_broadcast([P, HEADS, P]), ALU.mult).then_inc(small_ev, 1)
            dve.wait_ge(small_mm, 2)
            nc.vector.tensor_copy(bsb, ps[1][:, 0:2 * P].rearrange("p (c s) -> p c s", c=2)).then_inc(small_ev, 1)
            dve.wait_ge(small_mm, 3)
            nc.vector.tensor_copy(ws4[0:DS], ps[2][0:DS, 0:4 * NS].rearrange("p (g s) -> p g s", g=HEADS)).then_inc(small_ev, 1)
            dve.wait_ge(small_mm, 4)
            nc.vector.tensor_tensor(wsS[0:NS], ps[3][0:NS, 0:4 * NS].rearrange("p (g s) -> p g s", g=HEADS),
                                    K("cum4", NS, NS).unsqueeze(1).to_broadcast([NS, HEADS, NS]), ALU.mult).then_inc(small_ev, 1)
            for n in range(2):
                last = nc.vector.tensor_copy(bsbS[:, n, :].rearrange("p (b t) -> p b t", b=DB),
                                             bsb[:, n, 0:DS].unsqueeze(1).to_broadcast([P, DB, DS]))
                if n == 0:
                    link(last)
            last.then_inc(small_ev, 1)
            dve.wait_ge(small_ev, 5)
            for i in range(TILES):
                r = rows(i)
                dve.wait_ge(mixed, i + 1)
                m = mix.rearrange("p (c s) -> p c s", c=2)[:, :, 0:r]
                p = ps[4 + i % 2][:, 0:2 * P].rearrange("p (c s) -> p c s", c=2)[:, :, 0:r]
                if i >= 1:
                    dve.wait_ge(mixed_used, i)
                link(nc.vector.tensor_tensor(m, p, bsb if i < NT else bsbS, ALU.add))
                nc.vector.tensor_tensor(oT[:, 2:4, i * P:i * P + r], m, uT[:, :, i * P:i * P + r],
                                        ALU.mult).then_inc(mixed_used, 1)

        @block.scalar
        def _(act):
            act.wait_ge(loaded, 16 * 10)
            for i in range(TILES):
                r = rows(i)
                act.wait_ge(diff, i + 1)
                if i >= 2:
                    act.wait_ge(pooled, i - 1)
                nc.scalar.copy(dT[:, i % 2, :].rearrange("p (c s) -> p c s", c=2)[:, :, 0:r],
                               ps[6][:, 0:2 * P].rearrange("p (c s) -> p c s", c=2)[:, :, 0:r]).then_inc(diff_ok, 1)
                act.wait_ge(pooled, i + 1)
                for n in range(2):
                    last = nc.scalar.activation(oT[:, 4 + n, i * P:i * P + r], ps[7][:, n * P:n * P + r], ACT.Copy,
                                                scale=gam[:, n:n + 1])
                last.then_inc(pooled_used, 1)


def stage_stick_prompt(c):
    nc, K = c.nc, c.K
    c.place(start=c.after_q, qz=2 * 512, bias=512, zb=3 * 512, tmp=2 * 512, sp=3 * 512, att=2 * 512, ssum=3 * 512,
            sb=HEADS)

    def ring(name, n):
        return c.A(name).rearrange("p (s h q) -> p s h q", s=n, h=HEADS)

    qz, zb, tmp, sp_, att, ssum = ring("qz", 2), ring("zb", 3), ring("tmp", 2), ring("sp", 3), ring("att", 2), ring("ssum", 3)
    bias = c.A("bias").rearrange("p (h q) -> p h q", h=HEADS)
    c.bias = bias
    ps, oT, qT, kT, vtok = c.ps, c.hT, c.qT, c.kT, c.vtok
    steps = [(qb, kb) for qb in range(NT) for kb in range(qb, -1, -1)]
    N = len(steps)
    s = c.sem
    zeroed, q_ready, bias_in, bias_ok = s("a_zero"), s("a_q"), s("a_bin"), s("a_bias")
    score, zb_ok, soft, sp_ok, sum_ok, sums = s("a_score"), s("a_zb"), s("a_soft"), s("a_sp"), s("a_sumok"), s("a_sums")
    arg_ok, exp_ok, att_ok, pv, out_ok = s("a_arg"), s("a_exp"), s("a_att"), s("a_pv"), s("a_out")
    dve_chain, act_chain = s("a_dve"), s("a_act")
    last_of = [max(n for n, x in enumerate(steps) if x[0] == qb) for qb in range(NT)]

    def head4(bank):
        return ps[bank][:, :].rearrange("p (h q) -> p h q", h=HEADS)

    with nc.Block() as block:
        @block.sync
        def _(sp):
            sp.dma_start(c.A("sb"), row_bc(c.T['sb_bias'][0])).then_inc(bias_in, 16)

        @block.gpsimd
        def _(pool):
            nc.gpsimd.memset(c.A("qz"), 0.0).then_inc(zeroed, 1)
            pool.wait_ge(zeroed, 1)
            n = 0

            def stage_queries(qb):
                if qb >= 2:
                    pool.wait_ge(score, last_of[qb - 2] + 1)
                t = slice(qb * P, (qb + 1) * P)
                nc.gpsimd.tensor_copy(qz[0:DH, qb % 2, 0:4:2, :], qT[0:DH, :, t]).then_inc(q_ready, 1)
                pool.wait_ge(q_ready, 2 * qb + 1)
                nc.gpsimd.tensor_copy(qz[DH:P, qb % 2, 1:4:2, :], qT[DH:P, :, t]).then_inc(q_ready, 1)
                pool.wait_ge(q_ready, 2 * qb + 2)

            stage_queries(0)
            for qb in range(NT):
                if qb + 1 < NT:
                    stage_queries(qb + 1)
                for j in range(qb + 1):
                    pool.wait_ge(sp_ok, n + 1)
                    if n >= 2:
                        pool.wait_ge(sums, n - 1)
                    if j == 0:
                        nc.gpsimd.tensor_copy(ssum[:, n % 3], sp_[:, n % 3]).then_inc(sum_ok, 1)
                    else:
                        nc.gpsimd.tensor_tensor(ssum[:, n % 3], ssum[:, (n - 1) % 3], sp_[:, n % 3],
                                                ALU.add).then_inc(sum_ok, 1)
                    n += 1
                    pool.wait_ge(sum_ok, n)

        @block.tensor
        def _(pe):
            def scores(n):
                qb, kb = steps[n]
                pe.wait_ge(q_ready, 2 * qb + 2)
                if n >= 2:
                    pe.wait_ge(zb_ok, n - 1)
                for pair in range(2):
                    last = nc.tensor.matmul(ps[n % 2][:, pair * 256:(pair + 1) * 256], kT[:, pair, kb * P:(kb + 1) * P],
                                            qz[:, qb % 2, 2 * pair:2 * pair + 2, :].rearrange("p h q -> p (h q)"),
                                            start=True, stop=True)
                last.then_inc(score, 1)

            def suffix(n):
                qb, kb = steps[n]
                pe.wait_ge(sp_ok, n + 1)
                if n >= 2:
                    pe.wait_ge(arg_ok, n - 1)
                flat = "p h q -> p (h q)"
                last = nc.tensor.matmul(ps[2 + n % 2][:, :], K("negsuf"), sp_[:, n % 3].rearrange(flat),
                                        start=True, stop=(kb == qb))
                if kb < qb:
                    pe.wait_ge(sum_ok, n)
                    last = nc.tensor.matmul(ps[2 + n % 2][:, :], K("negone"), ssum[:, (n - 1) % 3].rearrange(flat),
                                            start=False, stop=True)
                last.then_inc(sums, 1)

            def values(n):
                qb, kb = steps[n]
                if kb == qb:
                    pe.wait_ge(att_ok, qb + 1)
                else:
                    pe.wait_ge(exp_ok, n + 1)
                if kb == qb and qb >= 2:
                    pe.wait_ge(out_ok, 2 * (qb - 1))
                for pair in range(2):
                    last = nc.tensor.matmul(ps[4 + qb % 2][:, pair * 256:(pair + 1) * 256],
                                            vtok[:, kb, pair * P:(pair + 1) * P],
                                            att[:, n % 2, 2 * pair:2 * pair + 2, :].rearrange("p h q -> p (h q)"),
                                            start=(kb == qb and pair == 0), stop=(kb == 0), skip_group_check=True)
                last.then_inc(pv, 1)

            for n in range(N + 2):
                if n < N:
                    scores(n)
                if 1 <= n <= N:
                    suffix(n - 1)
                if n >= 2:
                    values(n - 2)

        @block.scalar
        def _(act):
            link = Chain(act, act_chain)
            nc.scalar.preload_act_table_set(EXPLN)

            def softplus(n):
                act.wait_ge(zb_ok, n + 1)
                if n >= 2:
                    act.wait_ge(sp_ok, n - 1)
                t = tmp[:, n % 2]
                link(nc.scalar.activation(t, zb[:, n % 3], ACT.Abs))
                link(nc.scalar.activation(t, t, ACT.Exp, scale=-1.0))
                nc.scalar.activation(t, t, ACT.Ln, bias=1.0).then_inc(soft, 1)

            def weights(n):
                act.wait_ge(arg_ok, n + 1)
                if n >= 2:
                    act.wait_ge(pv, n - 1)
                nc.scalar.activation(att[:, n % 2], zb[:, n % 3], ACT.Exp).then_inc(exp_ok, 1)

            for n in range(N + 2):
                if n >= 2:
                    weights(n - 2)
                if n < N:
                    softplus(n)

        @block.vector
        def _(dve):
            link = Chain(dve, dve_chain)
            dve.wait_ge(bias_in, 16)
            for h in range(HEADS):
                ins = nc.vector.tensor_scalar(bias[:, h, :], K("ones"), c.A("sb")[:, h:h + 1], None, ALU.mult)
                ins.then_inc(bias_ok, 1)
            dve.wait_ge(bias_ok, HEADS)
            mask = K("before").unsqueeze(1).to_broadcast([P, HEADS, P])

            def add_bias(n):
                dve.wait_ge(score, n + 1)
                if n >= 3:
                    dve.wait_ge(exp_ok, n - 2)
                nc.vector.tensor_tensor(zb[:, n % 3], head4(n % 2), bias, ALU.add).then_inc(zb_ok, 1)

            def soft_sum(n):
                qb, kb = steps[n]
                dve.wait_ge(soft, n + 1)
                if n >= 3:
                    dve.wait_ge(sums, n - 2)
                    dve.wait_ge(sum_ok, n - 2)
                ins = nc.vector.scalar_tensor_tensor(sp_[:, n % 3], zb[:, n % 3], 0.0, tmp[:, n % 2], ALU.max, ALU.add)
                if kb == qb:
                    link(ins)
                    ins = nc.vector.tensor_tensor(sp_[:, n % 3], sp_[:, n % 3], mask, ALU.mult)
                ins.then_inc(sp_ok, 1)

            def argument(n):
                dve.wait_ge(sums, n + 1)
                dve.wait_ge(sp_ok, n + 1)
                nc.vector.tensor_tensor(zb[:, n % 3], head4(2 + n % 2), zb[:, n % 3], ALU.add).then_inc(arg_ok, 1)

            def mask_weights(n):
                dve.wait_ge(exp_ok, n + 1)
                a = att[:, n % 2]
                nc.vector.tensor_tensor(a, a, mask, ALU.mult).then_inc(att_ok, 1)

            def outputs(qb):
                dve.wait_ge(pv, last_of[qb] + 1)
                for half in range(2):
                    q = slice(half * DH, (half + 1) * DH)
                    nc.vector.tensor_copy(oT[q, 0:2, qb * P:(qb + 1) * P],
                                          head4(4 + qb % 2)[q, half:4:2, :]).then_inc(out_ok, 1)

            for n in range(N + 3):
                if n >= 3 and steps[n - 3][0] == steps[n - 3][1]:
                    mask_weights(n - 3)
                if n < N:
                    add_bias(n)
                if 1 <= n <= N:
                    soft_sum(n - 1)
                if 2 <= n <= N + 1:
                    argument(n - 2)
                if n >= 3 and n - 3 in last_of:
                    outputs(last_of.index(n - 3))


def stage_stick_sample(c):
    nc, T, K = c.nc, c.T, c.K
    HQ = HEADS * NS
    c.place(start=c.after_q, Kp=DB * NPG * 256, Vp=DB * NPG * 256, kTs=DB * NPG * 256, qzs=HQ, biasS=HQ, sb=HEADS,
            zS=3 * HQ, tS=3 * HQ, spS=3 * HQ)
    Kp = c.A("Kp").rearrange("p (g n) -> p g n", n=256)
    Vp = c.A("Vp").rearrange("p (g n) -> p g n", n=256)
    kTs = c.A("kTs").rearrange("p (g n) -> p g n", n=256)
    qzs = c.A("qzs").rearrange("p (h q) -> p h q", h=HEADS)
    z, t, sp_ = c.A("zS"), c.A("tS"), c.A("spS")
    ids = c.ids
    ps, oT, qT, kT, vtok = c.ps, c.hT, c.qT, c.kT, c.vtok
    NPAGES = DB * NPG
    s = c.sem
    ids_in, bias_in = s("s_ids"), s("s_bias")
    page_in = [s(f"s_page{n}") for n in range(4)]
    q_ok, turned, kT_ok, score, zb_ok = s("s_q"), s("s_turned"), s("s_kT"), s("s_score"), s("s_zb")
    soft, sp_ok, sums, arg_ok, exp_ok, att_ok, pv = (s("s_soft"), s("s_sp"), s("s_sums"), s("s_arg"), s("s_exp"),
                                                     s("s_att"), s("s_pv"))
    out_ok, dve_chain, act_chain, v_in = s("s_out"), s("s_dve"), s("s_act"), s("s_v")
    N2, N3 = 2 * HQ, 3 * HQ
    new = slice(N2, N3)

    with nc.Block() as block:
        @block.sync
        def _(sp):
            sp.dma_start(ids[0:1, :], T['page_table'].rearrange("b g -> (b g)").unsqueeze(0)).then_inc(ids_in, 16)
            sp.dma_start(c.A("sb"), row_bc(T['sb_bias'][0])).then_inc(bias_in, 16)
            sp.wait_ge(ids_in, 16)
            n_phys = T['cache_sb_k'].shape[1]
            for g in range(NPAGES):
                page = sp.value_load(ids[0:1, g:g + 1], min_val=0, max_val=n_phys - 1)
                for src, dst, done in (('cache_sb_k', Kp, page_in[g // 4]), ('cache_sb_v', Vp, v_in)):
                    pages = T[src][0].rearrange("n t h d -> n t (h d)")
                    sp.dma_start(dst[:, g, :], pages[bass.ds(page, 1)].rearrange("a t n -> (a t) n")).then_inc(done, 16)

        @block.tensor
        def _(pe):
            def turn(g):
                pe.wait_ge(page_in[g // 4], 64)
                u = g // 2
                if u >= 4 and g % 2 == 0:
                    pe.wait_ge(kT_ok, u - 3)
                for pair in range(2):
                    last = nc.tensor.transpose(ps[u % 4][:, (g % 2) * 256 + pair * P:(g % 2) * 256 + (pair + 1) * P],
                                               Kp[:, g, pair * P:(pair + 1) * P], K("ident"))
                if g % 2 == 1:
                    last.then_inc(turned, 1)

            for g in range(NPAGES):
                turn(g)
            pe.wait_ge(q_ok, 3)
            pages = ps[4][:, 0:N2].rearrange("p (g h b q) -> p g h b q", g=NPG, h=HEADS, b=DB)
            qv = qzs.rearrange("p h (b q) -> p h b q", b=DB)
            for g in range(NPAGES):
                b, page = g // NPG, g % NPG
                pe.wait_ge(kT_ok, g // 2 + 1)
                for pair in range(2):
                    hh = slice(2 * pair, 2 * pair + 2)
                    last = nc.tensor.matmul(pages[:, page, hh, b, :], kTs[:, g, pair * P:(pair + 1) * P], qv[:, hh, b, :],
                                            start=True, stop=True)
            last.then_inc(score, 1)
            for pair in range(2):
                last = nc.tensor.matmul(ps[5][0:NS, pair * 64:(pair + 1) * 64], kT[:, pair, SEQ:TOK],
                                        qzs[:, 2 * pair:2 * pair + 2, :].rearrange("p h q -> p (h q)"), start=True, stop=True)
            last.then_inc(score, 1)
            pe.wait_ge(sp_ok, 3)
            nc.tensor.matmul(ps[6][:, HQ:N2], K("negsuf"), sp_[:, HQ:N2], start=True, stop=False)
            nc.tensor.matmul(ps[6][:, HQ:N2], K("negone", NS), sp_[0:NS, new], start=False, stop=True)
            nc.tensor.matmul(ps[6][:, 0:HQ], K("negsuf"), sp_[:, 0:HQ], start=True, stop=False)
            nc.tensor.matmul(ps[6][:, 0:HQ], K("negone"), sp_[:, HQ:N2], start=False, stop=False)
            nc.tensor.matmul(ps[6][:, 0:HQ], K("negone", NS), sp_[0:NS, new], start=False, stop=True).then_inc(sums, 1)
            nc.tensor.matmul(ps[7][0:NS, 0:HQ], K("negsuf", NS, NS), sp_[0:NS, new], start=True, stop=True).then_inc(sums, 1)
            pe.wait_ge(exp_ok, 2)
            pe.wait_ge(att_ok, 1)
            pe.wait_ge(v_in, 16 * NPAGES)
            att = z[:, 0:N2].rearrange("p (g h b q) -> p g h b q", g=NPG, h=HEADS, b=DB)
            an = z[:, new].rearrange("p (h q) -> p h q", h=HEADS)
            for pair in range(2):
                hh = slice(2 * pair, 2 * pair + 2)
                out = ps[0][:, pair * 64:(pair + 1) * 64]
                nc.tensor.matmul(out, vtok[0:NS, NT, pair * P:(pair + 1) * P], an[0:NS, hh, :].rearrange("p h q -> p (h q)"),
                                 start=(pair == 0), stop=False, skip_group_check=True)
                ov = out.rearrange("p (h b q) -> p h b q", h=2, b=DB)
                for g in range(NPAGES):
                    last = nc.tensor.matmul(ov[:, :, g // NPG, :], Vp[:, g, pair * P:(pair + 1) * P],
                                            att[:, g % NPG, hh, g // NPG, :], start=False, stop=(g == NPAGES - 1),
                                            skip_group_check=True)
            last.then_inc(pv, 1)

        @block.scalar
        def _(act):
            link = Chain(act, act_chain)
            nc.scalar.preload_act_table_set(EXPLN)
            for u in range(NPAGES // 2):
                act.wait_ge(turned, u + 1)
                nc.scalar.copy(kTs[:, 2 * u:2 * u + 2, :], ps[u % 4][:, :].rearrange("p (g n) -> p g n", g=2)).then_inc(kT_ok, 1)
            act.wait_ge(zb_ok, 2)
            for r, sl in ((P, slice(0, N2)), (NS, new)):
                link(nc.scalar.activation(t[0:r, sl], z[0:r, sl], ACT.Abs))
                link(nc.scalar.activation(t[0:r, sl], t[0:r, sl], ACT.Exp, scale=-1.0))
                nc.scalar.activation(t[0:r, sl], t[0:r, sl], ACT.Ln, bias=1.0).then_inc(soft, 1)
            act.wait_ge(arg_ok, 2)
            nc.scalar.activation(z[:, 0:N2], z[:, 0:N2], ACT.Exp).then_inc(exp_ok, 1)
            nc.scalar.activation(z[0:NS, new], z[0:NS, new], ACT.Exp).then_inc(exp_ok, 1)

        @block.vector
        def _(dve):
            link = Chain(dve, dve_chain)
            nc.vector.memset(c.A("qzs"), 0.0).then_inc(q_ok, 1)
            dve.wait_ge(q_ok, 1)
            nc.vector.tensor_copy(qzs[0:DH, 0:4:2, :], qT[0:DH, :, SEQ:TOK]).then_inc(q_ok, 1)
            nc.vector.tensor_copy(qzs[DH:P, 1:4:2, :], qT[DH:P, :, SEQ:TOK]).then_inc(q_ok, 1)
            dve.wait_ge(bias_in, 16)
            bias = c.A("biasS")
            for h in range(HEADS):
                ins = nc.vector.tensor_scalar(bias[:, h * NS:(h + 1) * NS], K("ones", P, NS), c.A("sb")[:, h:h + 1], None, ALU.mult)
                link(ins)
            dve.wait_ge(score, 1)
            nc.vector.tensor_tensor(z[:, 0:N2].rearrange("p (g n) -> p g n", g=2), ps[4][:, 0:N2].rearrange("p (g n) -> p g n", g=2),
                                    bias.unsqueeze(1).to_broadcast([P, 2, HQ]), ALU.add).then_inc(zb_ok, 1)
            dve.wait_ge(score, 2)
            nc.vector.tensor_tensor(z[0:NS, new], ps[5][0:NS, 0:HQ], bias[0:NS, :], ALU.add).then_inc(zb_ok, 1)
            dve.wait_ge(zb_ok, 2)
            dve.wait_ge(soft, 1)
            nc.vector.scalar_tensor_tensor(sp_[:, 0:N2], z[:, 0:N2], 0.0, t[:, 0:N2], ALU.max, ALU.add).then_inc(sp_ok, 1)
            dve.wait_ge(soft, 2)
            nc.vector.scalar_tensor_tensor(sp_[0:NS, new], z[0:NS, new], 0.0, t[0:NS, new], ALU.max, ALU.add).then_inc(sp_ok, 1)
            dve.wait_ge(sp_ok, 2)
            mask = K("before4", NS, NS).unsqueeze(1).to_broadcast([NS, HEADS, NS])
            sn = sp_[0:NS, new].rearrange("p (h q) -> p h q", h=HEADS)
            zn = z[0:NS, new].rearrange("p (h q) -> p h q", h=HEADS)
            nc.vector.tensor_tensor(sn, sn, mask, ALU.mult).then_inc(sp_ok, 1)
            dve.wait_ge(sums, 1)
            nc.vector.tensor_tensor(z[:, 0:N2], ps[6][:, 0:N2], z[:, 0:N2], ALU.add).then_inc(arg_ok, 1)
            dve.wait_ge(sums, 2)
            nc.vector.tensor_tensor(z[0:NS, new], ps[7][0:NS, 0:HQ], z[0:NS, new], ALU.add).then_inc(arg_ok, 1)
            dve.wait_ge(exp_ok, 2)
            nc.vector.tensor_tensor(zn, zn, mask, ALU.mult).then_inc(att_ok, 1)
            dve.wait_ge(pv, 1)
            ov = ps[0][:, 0:P].rearrange("p (c h q) -> p c h q", c=2, h=2)
            for half in range(2):
                q = slice(half * DH, (half + 1) * DH)
                nc.vector.tensor_copy(oT[q, 0:2, SEQ:TOK], ov[q, :, half, :]).then_inc(out_ok, 1)


def stage_delta_inputs(c):
    nc, T, O, K = c.nc, c.T, c.O, c.K
    c.place(start=0, dnorm=1, SQ=2 * TOK)
    c.place(start=c.free_at + 6 * TOK, cs=768, cw=6 * 28, xs=6 * DB * 7, y=2 * SEQ, ys=6 * NS, stp=768, sts=768, rn=3 * GT,
            rows4=8)
    qkvT = c.qkvT
    cs, stp, sts, rn = c.A("cs"), c.A("stp"), c.A("sts"), c.A("rn")
    cw = c.A("cw").rearrange("p (c n) -> p c n", c=6)
    xs = c.A("xs").rearrange("p (c b t) -> p c b t", c=6, b=DB)
    ys = c.A("ys").rearrange("p (c b t) -> p c b t", c=6, b=DB)
    y = c.A("y").rearrange("p (s t) -> p s t", s=2)
    sq = c.A("SQ").rearrange("p (s t) -> p s t", s=2)
    NC = TILES * HEADS

    def col():
        return c.new_small(NC).rearrange("p (i h) -> p i h", i=TILES)

    c.beta, c.g, c.log_decay, c.be, c.kgf = col(), col(), col(), col(), col()
    tx, tl = col(), col()
    eps6 = c.new_small(1)
    c.eps6 = eps6
    bd, ad = c.ba[:, :, 0:HEADS], c.ba[:, :, HEADS:2 * HEADS]
    ps = c.ps
    s = c.sem
    loaded, cw_mm, cw_ok, st_mm, st_ok, stored = s("c_load"), s("c_cwmm"), s("c_cwok"), s("c_stmm"), s("c_stok"), s("c_stored")
    gd, ga, gpe, conv_ok, silu_ok, staged = s("c_gd"), s("c_ga"), s("c_gpe"), s("c_conv"), s("c_silu"), s("c_staged")
    sq_ok, ss, rn_ok, unit, dve_chain, act_chain, eps_ok = (s("c_sq"), s("c_ss"), s("c_rn"), s("c_unit"), s("c_dve"),
                                                            s("c_act"), s("c_eps"))
    rows4 = c.A("rows4")

    with nc.Block() as block:
        @block.sync
        def _(sp):
            sp.dma_start(cs[0:24, :], T['state_conv'][0].rearrange("b t n -> (b t) n")).then_inc(loaded, 16)
            sp.dma_start(cs[24:28, :], T['conv_w'][0]).then_inc(loaded, 16)
            sp.dma_start(rows4[:, 0:4], row_bc(T['dn_dt_bias'][0])).then_inc(loaded, 16)
            sp.dma_start(rows4[:, 4:8], row_bc(T['dn_a_log'][0])).then_inc(loaded, 16)
            for half in range(2):
                sp.dma_start(c.A("dnorm")[half * DH:(half + 1) * DH, :], T['dn_norm_g'][0].unsqueeze(1)).then_inc(loaded, 16)
            sp.wait_ge(st_ok, 4)
            sp.dma_start(O['conv_prompt'][0, 0], stp[0:3, :]).then_inc(stored, 16)
            for b in range(DB):
                sp.dma_start(O['conv_sample'][0, b], sts[b * DS + 1:(b + 1) * DS, :]).then_inc(stored, 16)
            sp.wait_ge(stored, 16 * (DB + 1))

        @block.tensor
        def _(pe):
            pe.wait_ge(loaded, 96)
            for n in range(6):
                last = nc.tensor.transpose(ps[0][:, n * 28:(n + 1) * 28], cs[0:28, n * P:(n + 1) * P], K("ident", 28, 28))
            last.then_inc(cw_mm, 1)
            for bank, r, t0, chunks in ((1, 3, SEQ - 3, range(4)), (2, 3, SEQ - 3, range(4, 6)),
                                        (3, NS, SEQ, range(4)), (4, NS, SEQ, range(4, 6))):
                for n in chunks:
                    last = nc.tensor.transpose(ps[bank][0:r, (n % 4) * P:(n % 4 + 1) * P], qkvT[:, n, t0:t0 + r], K("ident"))
                last.then_inc(st_mm, 1)
            pe.wait_ge(gd, 5)
            for q, (a, b) in enumerate((("cum64", "cum4"), ("blk64", "blk4"))):
                nc.tensor.matmul(ps[5][:, q * NC:q * NC + NT * HEADS], K(a), c.g[:, 0:NT, :].rearrange("p i h -> p (i h)"),
                                 start=True, stop=True)
                last = nc.tensor.matmul(ps[5][0:NS, q * NC + NT * HEADS:(q + 1) * NC], K(b, NS, NS), c.g[0:NS, NT, :],
                                        start=True, stop=True)
            last.then_inc(gpe, 1)
            for n in range(4):
                pe.wait_ge(sq_ok, n + 1)
                for g in range(GRP):
                    if n >= 1:
                        pe.wait_ge(rn_ok, GRP * (n - 1) + g + 1)
                    elif g == 0:
                        pe.wait_ge(gd, 6)
                    bank = (5, 6, 7)[g]
                    nc.tensor.matmul(ps[bank][:, 0:GT], K("blk64"), sq[:, n % 2, g * GT:(g + 1) * GT],
                                     start=True, stop=True).then_inc(ss, 1)

        @block.scalar
        def _(act):
            link = Chain(act, act_chain)
            nc.scalar.preload_act_table_set(EXPLN)
            act.wait_ge(cw_mm, 1)
            nc.scalar.copy(cw, ps[0][:, 0:168].rearrange("p (c n) -> p c n", c=6)).then_inc(cw_ok, 1)
            for n, (bank, r, dst, w) in enumerate(((1, 3, stp[0:3, 0:512], 512), (2, 3, stp[0:3, 512:768], 256),
                                                   (3, NS, sts[0:NS, 0:512], 512), (4, NS, sts[0:NS, 512:768], 256))):
                act.wait_ge(st_mm, n + 1)
                nc.scalar.copy(dst, ps[bank][0:r, 0:w]).then_inc(st_ok, 1)
            act.wait_ge(gd, 1)
            nc.scalar.activation(c.beta, bd, ACT.Exp, scale=-1.0).then_inc(ga, 1)
            nc.scalar.activation(rows4[:, 4:8], rows4[:, 4:8], ACT.Exp).then_inc(ga, 1)
            link(nc.scalar.activation(tl, tx, ACT.Abs))
            link(nc.scalar.activation(tl, tl, ACT.Exp, scale=-1.0))
            nc.scalar.activation(tl, tl, ACT.Ln, bias=1.0).then_inc(ga, 1)
            act.wait_ge(gd, 6)
            nc.scalar.activation(c.be, c.log_decay, ACT.Exp).then_inc(ga, 1)
            nc.scalar.activation(c.kgf, c.kgf, ACT.Exp).then_inc(ga, 1)
            for n in range(6):
                act.wait_ge(conv_ok, n + 1)
                nc.scalar.activation(qkvT[:, n, 0:SEQ], y[:, n % 2, :], ACT.Silu).then_inc(silu_ok, 1)
                nc.scalar.activation(qkvT[:, n, SEQ:TOK].rearrange("p (b t) -> p b t", b=DB), ys[:, n], ACT.Silu).then_inc(silu_ok, 1)
            act.wait_ge(silu_ok, 12)
            act.wait_ge(eps_ok, 1)
            for n in range(4):
                if n >= 2:
                    act.wait_ge(ss, GRP * (n - 1))
                nc.scalar.activation(sq[:, n % 2, :], qkvT[:, n, :], ACT.Square).then_inc(sq_ok, 1)
                nc.scalar.preload_act_table_set(EXPLN)
                for g in range(GRP):
                    u = GRP * n + g
                    act.wait_ge(ss, u + 1)
                    if n >= 1:
                        act.wait_ge(unit, u - 2)
                    t = rn[:, g * GT:(g + 1) * GT]
                    link(nc.scalar.activation(t, ps[(5, 6, 7)[g]][:, 0:GT], ACT.Ln, bias=eps6))
                    nc.scalar.activation(t, t, ACT.Exp, scale=-0.5).then_inc(rn_ok, 1)

        @block.vector
        def _(dve):
            link = Chain(dve, dve_chain)
            nc.vector.memset(eps6, 1e-6).then_inc(eps_ok, 1)
            nc.vector.memset(c.log_decay[:, NT, :], 0.0).then_inc(staged, 1)
            nc.vector.memset(c.kgf[:, NT, :], 0.0).then_inc(staged, 1)
            dve.wait_ge(loaded, 96)
            bc = rows4[:, 0:4].unsqueeze(1).to_broadcast([P, TILES, HEADS])
            nea = rows4[:, 4:8]
            nc.vector.tensor_tensor(tx, ad, bc, ALU.add).then_inc(gd, 1)
            dve.wait_ge(ga, 3)
            nc.vector.tensor_scalar(c.beta, c.beta, 1.0, None, ALU.add).then_inc(gd, 1)
            dve.wait_ge(gd, 2)
            nc.vector.reciprocal(c.beta, c.beta).then_inc(gd, 1)
            link(nc.vector.scalar_tensor_tensor(tx, tx, 0.0, tl, ALU.max, ALU.add))
            nc.vector.tensor_scalar(nea, nea, -1.0, None, ALU.mult).then_inc(gd, 1)
            dve.wait_ge(gd, 4)
            nc.vector.tensor_tensor(c.g, tx, nea.unsqueeze(1).to_broadcast([P, TILES, HEADS]), ALU.mult).then_inc(gd, 1)
            dve.wait_ge(gpe, 1)
            dve.wait_ge(staged, 2)
            gp = ps[5][:, 0:2 * NC].rearrange("p (q i h) -> p q i h", q=2, i=TILES)
            link(nc.vector.tensor_copy(c.log_decay[:, 0:NT, :], gp[:, 0, 0:NT, :]))
            link(nc.vector.tensor_copy(c.log_decay[0:NS, NT, :], gp[0:NS, 0, NT, :]))
            link(nc.vector.tensor_tensor(c.kgf[:, 0:NT, :], gp[:, 1, 0:NT, :], c.log_decay[:, 0:NT, :], ALU.subtract))
            nc.vector.tensor_tensor(c.kgf[0:NS, NT, :], gp[0:NS, 1, NT, :], c.log_decay[0:NS, NT, :], ALU.subtract).then_inc(gd, 1)
            dve.wait_ge(ga, 4)
            link(nc.vector.tensor_tensor(c.be, c.be, c.beta, ALU.mult))
            dve.wait_ge(cw_ok, 1)
            nc.vector.tensor_copy(xs[:, :, :, 0:3], cw[:, :, 0:24].rearrange("p c (b t) -> p c b t", b=DB)).then_inc(staged, 1)
            nc.vector.tensor_copy(xs[:, :, :, 3:7], qkvT[:, :, SEQ:TOK].rearrange("p c (b t) -> p c b t", b=DB)).then_inc(staged, 1)
            dve.wait_ge(staged, 4)
            dve.wait_ge(st_mm, 4)
            for n in range(6):
                if n >= 2:
                    dve.wait_ge(silu_ok, 2 * (n - 1))
                yy = y[:, n % 2, :]
                w = lambda i: cw[:, n, 24 + i:25 + i]
                link(nc.vector.tensor_scalar(yy, qkvT[:, n, 0:SEQ], w(3), None, ALU.mult))
                for sh in (3, 2, 1):
                    link(nc.vector.scalar_tensor_tensor(yy[:, sh:], qkvT[:, n, 0:SEQ - sh], w(3 - sh), yy[:, sh:],
                                                        ALU.mult, ALU.add))
                link(nc.vector.tensor_scalar(ys[:, n], xs[:, n, :, 3:7], w(3), None, ALU.mult))
                for sh in (3, 2, 1):
                    ins = nc.vector.scalar_tensor_tensor(ys[:, n], xs[:, n, :, 3 - sh:7 - sh], w(3 - sh), ys[:, n],
                                                         ALU.mult, ALU.add)
                    if sh > 1:
                        link(ins)
                ins.then_inc(conv_ok, 1)
            for n in range(4):
                for g in range(GRP):
                    u = GRP * n + g
                    dve.wait_ge(rn_ok, u + 1)
                    t = qkvT[:, n, g * GT:(g + 1) * GT]
                    nc.vector.scalar_tensor_tensor(t, t, DH ** -0.5 if n < 2 else 1.0, rn[:, g * GT:(g + 1) * GT],
                                                   ALU.mult, ALU.mult).then_inc(unit, 1)


def stage_delta(c):
    nc, T, O, K = c.nc, c.T, c.O, c.K
    kept = dict(u=256, wT=256, eg=256)
    c.place(start=0, dnorm=1, SQ=2 * TOK, S=2 * P, dS=2 * P, **{f"{k}{u}": n for u in range(2) for k, n in kept.items()})
    lane_sizes = dict(kvt=512, gcum=512, DL=512, DT=512, kz=512, qz=512, L=512, Lb=1024, X=512, Y=512, Pm=512,
                      vb=256, kbe=256, kg=512, qg=256, vz=512)
    sizes = {f"{k}{u}": n for u in range(2) for k, n in lane_sizes.items()}
    c.place(start=c.free_at + 6 * TOK, **sizes)
    h4 = "p (h t) -> p h t"
    B = {k: [c.A(f"{k}{u}") for u in range(2)] for k in {**lane_sizes, **kept}}

    def V(k, u, h=HEADS):
        return B[k][u].rearrange(h4, h=h)

    odT = c.A("SQ").rearrange("p (c t) -> p c t", c=2)
    S = c.A("S").rearrange("p (c n) -> p c n", c=2)
    dS = c.A("dS").rearrange("p (c n) -> p c n", c=2)
    c.place(start=c.at["kvt0"][0], rsq=2 * TOK, rrn=2 * TOK)
    c.rsq = c.A("rsq").rearrange("p (n t) -> p n t", n=2)
    c.rrn = c.A("rrn").rearrange("p (n t) -> p n t", n=2)
    a1 = c.at["kvt1"][0]
    c.place(start=a1, SS=DB * 2 * P, wSs=2 * NS, Vx=HEADS * 512, Sn=HEADS * 512)
    SS = c.A("SS").rearrange("p (b c n) -> p b c n", b=DB, c=2)
    wSs = c.A("wSs").rearrange("p (c t) -> p c t", c=2)
    Vx = c.A("Vx").rearrange("p (h b n) -> p h b n", h=HEADS, b=DB)
    Sn = c.A("Sn").rearrange("p (h b n) -> p h b n", h=HEADS, b=DB)
    qkvT, zT, oT = c.qkvT, c.zT, c.hT
    ps = c.ps
    LV = {i: ((2, 4, 8, 16, 32) if i < NT else (2,)) for i in range(TILES)}
    groups = [(0, 1), (2, 3), (4, 5), (6, 7), (8,)]
    number, n = {}, 0
    for grp in groups:
        for l in range(len(LV[grp[0]])):
            for i in grp:
                n += 1
                number[(i, l)] = n
    total_levels = n
    s = c.sem
    sx = {k: s("d_" + k) for k in ("zero", "kvt", "kvc", "gcum", "G", "dif", "ddve", "eg", "dexp", "dmask", "kz", "kk", "L",
                                   "intra", "X1", "Xt", "Y1", "Lb", "P", "Pc", "YX", "Y", "scaled", "uw", "uc", "qg",
                                   "vW", "vn", "o", "oc", "S", "dve", "act", "init", "sload", "swS", "swc", "swt",
                                   "svn", "svx", "so", "soc", "sdS", "sSn", "ost", "rs", "rss", "rrn", "rout", "zq")}
    dims = lambda i: (rows(i), (K("cum64"), K("low64")) if i < NT else (K("cum4", NS, NS), K("low4", NS, NS)))

    def bk(i, n):
        return ps[4 * (i % 2 if i < NT else 0) + n]

    def lane(i):
        return i % 2

    def v4(ap, i):
        r = rows(i)
        return ap[:, 0:4 * r].rearrange("p (h t) -> p h t", h=HEADS)

    def v2(ap, i):
        r = rows(i)
        return ap[:, 0:2 * r].rearrange("p (c t) -> p c t", c=2)

    def tok(i):
        return slice(i * P, i * P + rows(i))

    with nc.Block() as block:
        @block.gpsimd
        def _(pool):
            for nm in ("kz", "qz", "kg", "vz"):
                for u in range(2):
                    nc.gpsimd.memset(B[nm][u], 0.0).then_inc(sx["zero"], 1)
            nc.gpsimd.memset(c.A("S"), 0.0).then_inc(sx["zero"], 1)
            pool.wait_ge(sx["zero"], 9)
            for grp in groups:
                for i in grp:
                    r, (cum, low) = dims(i)
                    u = lane(i)
                    pool.wait_ge(sx["dexp"], 2 * i + 2)
                    for q, (nm, m) in enumerate((("DL", low), ("DT", cum))):
                        a = v4(B[nm][u], i)[0:r]
                        nc.gpsimd.tensor_tensor(a, a, m.unsqueeze(1).to_broadcast([r, HEADS, r]), ALU.mult).then_inc(sx["dmask"], 1)
                        pool.wait_ge(sx["dmask"], 2 * i + q + 1)
                for l in range(len(LV[grp[0]])):
                    for i in grp:
                        r = rows(i)
                        pool.wait_ge(sx["L"], i + 1)
                        m = K(f"lvl{LV[i][l]}", r, r).unsqueeze(1).to_broadcast([r, HEADS, r])
                        if l >= 2:
                            pool.wait_ge(sx["P"], number[(i, l - 2)])
                        elif i >= 2:
                            pool.wait_ge(sx["P"], number[(i - 2, len(LV[i - 2]) - 1)])
                        dst = B["Lb"][lane(i)].rearrange("p (s n) -> p s n", s=2)[:, l % 2, :]
                        nc.gpsimd.tensor_tensor(v4(dst, i)[0:r], v4(B["L"][lane(i)], i)[0:r], m, ALU.mult).then_inc(sx["Lb"], 1)
                        pool.wait_ge(sx["Lb"], number[(i, l)])

        @block.tensor
        def _(pe):
            pe.wait_ge(sx["zero"], 9)
            for gi, grp in enumerate(groups):
                for i in grp:
                    r = rows(i)
                    if gi >= 1:
                        pe.wait_ge(sx["uc"], 2 * (grp[0] - 1))
                        pe.wait_ge(sx["S"], 2 * grp[0])
                        pe.wait_ge(sx["oc"], 2 * grp[0])
                    for n in range(4):
                        last = nc.tensor.transpose(bk(i, 3)[0:r, n * P:(n + 1) * P], qkvT[:, 2 + n, tok(i)], K("ident"))
                    last.then_inc(sx["kvt"], 1)
                for i in grp:
                    r = rows(i)
                    pe.wait_ge(sx["gcum"], i + 1)
                    nc.tensor.matmul(bk(i, 0)[:, 0:4 * r], K("ones", r, P), B["gcum"][lane(i)][0:r, 0:4 * r],
                                     start=True, stop=True).then_inc(sx["G"], 1)
                for i in grp:
                    r = rows(i)
                    pe.wait_ge(sx["kz"], 4 * i + 4)
                    for n, nm in ((1, "kz"), (2, "qz")):
                        z = v4(B[nm][lane(i)], i)
                        for pair in range(2):
                            last = nc.tensor.matmul(bk(i, n)[0:r, pair * 2 * r:(pair + 1) * 2 * r], qkvT[:, 2 + pair, tok(i)],
                                                    z[:, 2 * pair:2 * pair + 2, :].rearrange("p h t -> p (h t)"),
                                                    start=True, stop=True)
                    last.then_inc(sx["kk"], 1)
                for i in grp:
                    r = rows(i)
                    pe.wait_ge(sx["X1"], i + 1)
                    pe.wait_ge(sx["eg"], 2 * i + 2)
                    X = v4(B["X"][lane(i)], i)
                    for hd in range(HEADS):
                        last = nc.tensor.transpose(bk(i, 0)[0:r, hd * r:(hd + 1) * r], X[0:r, hd, :], K("ident", r, r))
                    last.then_inc(sx["Xt"], 1)
                for l in range(len(LV[grp[0]])):
                    for i in grp:
                        r = rows(i)
                        pe.wait_ge(sx["Lb"], number[(i, l)])
                        if l == 0:
                            pe.wait_ge(sx["Y1"], i + 1)
                        else:
                            pe.wait_ge(sx["Y"], 2 * number[(i, l - 1)])
                        Lb = v4(B["Lb"][lane(i)].rearrange("p (s n) -> p s n", s=2)[:, l % 2, :], i)
                        Y = v4(B["Y"][lane(i)], i)
                        for hd in range(HEADS):
                            last = nc.tensor.matmul(bk(i, 0)[0:r, hd * r:(hd + 1) * r], Lb[0:r, hd, :], Y[0:r, hd, :],
                                                    start=True, stop=True)
                        last.then_inc(sx["P"], 1)
                    for i in grp:
                        r = rows(i)
                        pe.wait_ge(sx["Pc"], number[(i, l)])
                        X, Pm = v4(B["X"][lane(i)], i), v4(B["Pm"][lane(i)], i)
                        for hd in range(HEADS):
                            nc.tensor.matmul(bk(i, 1)[0:r, hd * r:(hd + 1) * r], X[0:r, hd, :], Pm[0:r, hd, :],
                                             start=True, stop=True)
                        for hd in range(HEADS):
                            last = nc.tensor.matmul(bk(i, 2)[0:r, hd * r:(hd + 1) * r], Pm[0:r, hd, :], X[0:r, hd, :],
                                                    start=True, stop=True)
                        last.then_inc(sx["YX"], 1)
                for i in grp:
                    r = rows(i)
                    pe.wait_ge(sx["scaled"], 4 * i + 4)
                    pe.wait_ge(sx["Y"], 2 * number[(i, len(LV[i]) - 1)])
                    Y = v4(B["Y"][lane(i)], i)
                    for hd in range(HEADS):
                        nc.tensor.matmul(bk(i, 3)[0:r, hd * DH:(hd + 1) * DH], Y[0:r, hd, :],
                                         B["vb"][lane(i)][0:r, hd * DH:(hd + 1) * DH], start=True, stop=True)
                    for hd in range(HEADS):
                        q = (hd % 2) * DH
                        last = nc.tensor.matmul(bk(i, 0)[q:q + DH, (hd // 2) * r:(hd // 2 + 1) * r],
                                                B["kbe"][lane(i)][0:r, hd * DH:(hd + 1) * DH], Y[0:r, hd, :],
                                                start=True, stop=True)
                    last.then_inc(sx["uw"], 1)
                if grp[0] < NT:
                    for i in grp:
                        u = lane(i)
                        pe.wait_ge(sx["uc"], 2 * i + 2)
                        pe.wait_ge(sx["qg"], i + 1)
                        wT, qg = v2(B["wT"][u], i), v2(B["qg"][u], i)
                        vz = V("vz", u)
                        dT = V("DT", u)
                        kg = B["kg"][u].rearrange("p (s n) -> p s n", s=2)
                        for cc in range(2):
                            e = 2 * i + cc
                            if e >= 1:
                                pe.wait_ge(sx["S"], e)
                            for pair in range(2):
                                last = nc.tensor.matmul(bk(i, 0)[:, pair * P:(pair + 1) * P], wT[:, pair, :], S[:, pair, :],
                                                        start=True, stop=True)
                            last.then_inc(sx["vW"], 1)
                            t = slice(cc * CH, (cc + 1) * CH)
                            if e >= 1:
                                pe.wait_ge(sx["oc"], e)
                            pe.wait_ge(sx["vn"], e + 1)
                            for pair in range(2):
                                out = bk(i, 1)[:, pair * CH:(pair + 1) * CH]
                                nc.tensor.matmul(out, S[:, pair, :], qg[:, pair, t], start=True, stop=False)
                                for hh in range(2):
                                    hd = 2 * pair + hh
                                    last = nc.tensor.matmul(out, vz[:, hd, :], dT[:, hd, t], start=False, stop=(hh == 1))
                            last.then_inc(sx["o"], 1)
                            for pair in range(2):
                                vp = B["vz"][u][:, pair * 256:(pair + 1) * 256].rearrange("p (h n) -> p h n", h=2)
                                for hh in range(2):
                                    last = nc.tensor.matmul(bk(i, 2)[:, pair * P + hh * DH:pair * P + (hh + 1) * DH],
                                                            kg[:, cc, pair * P:(pair + 1) * P], vp[:, hh, hh * DH:(hh + 1) * DH],
                                                            start=True, stop=True)
                            last.then_inc(sx["vW"], 1)
                else:
                    i = NT
                    pe.wait_ge(sx["uc"], 2 * i + 2)
                    pe.wait_ge(sx["qg"], i + 1)
                    pe.wait_ge(sx["sload"], 16 * DB * HEADS)
                    wT, qg = v2(B["wT"][0], i), v2(B["qg"][0], i)
                    for pair in range(2):
                        for b in range(DB):
                            t = slice(b * DS, (b + 1) * DS)
                            last = nc.tensor.matmul(ps[4][:, pair * NS + b * DS:pair * NS + (b + 1) * DS], SS[:, b, pair, :],
                                                    wT[:, pair, t], start=True, stop=True)
                    last.then_inc(sx["swS"], 1)
                    pe.wait_ge(sx["swc"], 1)
                    for pair in range(2):
                        last = nc.tensor.transpose(ps[5][0:NS, pair * P:(pair + 1) * P], wSs[:, pair, :], K("ident"))
                    last.then_inc(sx["swt"], 1)
                    pe.wait_ge(sx["svn"], 1)
                    vz, dT = V("vz", 0), v4(B["DT"][0], i)
                    for pair in range(2):
                        for hh in range(2):
                            hd = 2 * pair + hh
                            nc.tensor.matmul(ps[6][:, pair * NS:(pair + 1) * NS], vz[0:NS, hd, :], dT[0:NS, hd, :],
                                             start=(pair == 0 and hh == 0), stop=False, skip_group_check=True)
                        for b in range(DB):
                            t = slice(b * DS, (b + 1) * DS)
                            last = nc.tensor.matmul(ps[6][:, pair * NS + b * DS:pair * NS + (b + 1) * DS], SS[:, b, pair, :],
                                                    qg[:, pair, t], start=False, stop=(b == DB - 1), skip_group_check=True)
                    last.then_inc(sx["so"], 1)
                    for hd in range(HEADS):
                        bank = (7, 1, 2, 5)[hd]
                        pe.wait_ge(sx["svx"], hd + 1)
                        nc.tensor.matmul(ps[bank][:, :], B["kg"][0][0:NS, (hd // 2) * P:(hd // 2 + 1) * P],
                                         Vx[0:NS, hd].rearrange("p b n -> p (b n)"), start=True, stop=True).then_inc(sx["sdS"], 1)
            for n in range(2):
                pe.wait_ge(sx["rs"], n + 1)
                for g in range(GRP):
                    bank = ps[(0, 3, 4)[g]]
                    if n:
                        pe.wait_ge(sx["rrn"], g + 1)
                    nc.tensor.matmul(bank[:, 0:GT], K("blk64"), c.rsq[:, n, g * GT:(g + 1) * GT], start=True,
                                     stop=True).then_inc(sx["rss"], 1)

        @block.scalar
        def _(act):
            link = Chain(act, sx["act"])
            nc.scalar.preload_act_table_set(EXPLN)
            for gi, grp in enumerate(groups):
                for i in grp:
                    r = rows(i)
                    act.wait_ge(sx["kvt"], i + 1)
                    nc.scalar.copy(B["kvt"][lane(i)][0:r, :], bk(i, 3)[0:r, :]).then_inc(sx["kvc"], 1)
                for i in grp:
                    r, _ = dims(i)
                    act.wait_ge(sx["ddve"], 2 * i + 2)
                    G = v4(bk(i, 0), i)
                    eg = v2(B["eg"][lane(i)], i)
                    for half in range(2):
                        q = slice(half * DH, (half + 1) * DH)
                        nc.scalar.activation(eg[q], G[q, half:4:2, :], ACT.Exp).then_inc(sx["eg"], 1)
                    for nm, sc in (("DL", -1.0), ("DT", 1.0)):
                        a = v4(B[nm][lane(i)], i)[0:r]
                        nc.scalar.activation(a, a, ACT.Exp, scale=sc).then_inc(sx["dexp"], 1)
                for i in grp:
                    r = rows(i)
                    act.wait_ge(sx["Xt"], i + 1)
                    nc.scalar.copy(B["Y"][lane(i)][0:r, 0:4 * r], bk(i, 0)[0:r, 0:4 * r]).then_inc(sx["Y1"], 1)
                for l in range(len(LV[grp[0]])):
                    for i in grp:
                        r = rows(i)
                        act.wait_ge(sx["P"], number[(i, l)])
                        nc.scalar.copy(B["Pm"][lane(i)][0:r, 0:4 * r], bk(i, 0)[0:r, 0:4 * r]).then_inc(sx["Pc"], 1)
                for i in grp:
                    r = rows(i)
                    act.wait_ge(sx["uw"], i + 1)
                    nc.scalar.copy(B["u"][lane(i)][0:r, :], bk(i, 3)[0:r, 0:256]).then_inc(sx["uc"], 1)
                    nc.scalar.copy(B["wT"][lane(i)][:, 0:2 * r], bk(i, 0)[:, 0:2 * r]).then_inc(sx["uc"], 1)
                if grp[0] < NT:
                    for i in grp:
                        for cc in range(2):
                            act.wait_ge(sx["o"], 2 * i + cc + 1)
                            nc.scalar.copy(odT[:, :, i * P + cc * CH:i * P + (cc + 1) * CH],
                                           bk(i, 1)[:, 0:P].rearrange("p (c t) -> p c t", c=2)).then_inc(sx["oc"], 1)
                else:
                    act.wait_ge(sx["swS"], 1)
                    nc.scalar.copy(wSs, ps[4][:, 0:2 * NS].rearrange("p (c t) -> p c t", c=2)).then_inc(sx["swc"], 1)
                    act.wait_ge(sx["so"], 1)
                    nc.scalar.copy(odT[:, :, SEQ:TOK], ps[6][:, 0:2 * NS].rearrange("p (c t) -> p c t", c=2)).then_inc(sx["oc"], 1)
            act.wait_ge(sx["oc"], 2 * NT + 1)
            for n in range(2):
                nc.scalar.activation(c.rsq[:, n, :], odT[:, n, :], ACT.Square).then_inc(sx["rs"], 1)
            for n in range(2):
                for g in range(GRP):
                    act.wait_ge(sx["rss"], GRP * n + g + 1)
                    t = c.rrn[:, n, g * GT:(g + 1) * GT]
                    link(nc.scalar.activation(t, ps[(0, 3, 4)[g]][:, 0:GT], ACT.Ln, bias=c.eps6, scale=1.0 / DH))
                    nc.scalar.activation(t, t, ACT.Exp, scale=-0.5).then_inc(sx["rrn"], 1)

        @block.vector
        def _(dve):
            link = Chain(dve, sx["dve"])
            dve.wait_ge(sx["zero"], 9)
            for gi, grp in enumerate(groups):
                for i in grp:
                    r, (cum, low) = dims(i)
                    u = lane(i)
                    if gi >= 1:
                        dve.wait_ge(sx["vW"], 4 * grp[0])
                    gb = c.g[0:r, i, :].unsqueeze(2).to_broadcast([r, HEADS, r])
                    nc.vector.tensor_tensor(v4(B["gcum"][u], i)[0:r], cum.unsqueeze(1).to_broadcast([r, HEADS, r]), gb,
                                            ALU.mult).then_inc(sx["gcum"], 1)
                    if i == NT:
                        for nm in ("kz", "qz"):
                            nc.vector.memset(B[nm][0], 0.0).then_inc(sx["zq"], 1)
                        dve.wait_ge(sx["zq"], 2)
                    for nm, ch in (("kz", 2), ("qz", 0)):
                        z = v4(B[nm][u], i)
                        for half in range(2):
                            q = slice(half * DH, (half + 1) * DH)
                            nc.vector.tensor_copy(z[q, half:4:2, :], qkvT[q, ch:ch + 2, tok(i)]).then_inc(sx["kz"], 1)
                for i in grp:
                    r = rows(i)
                    u = lane(i)
                    dve.wait_ge(sx["G"], i + 1)
                    gcb = c.log_decay[0:r, i, :].unsqueeze(2).to_broadcast([r, HEADS, r])
                    d = v4(B["gcum"][u], i)[0:r]
                    nc.vector.tensor_tensor(d, v4(bk(i, 0), i)[0:r], gcb, ALU.subtract).then_inc(sx["dif"], 1)
                    dve.wait_ge(sx["dif"], i + 1)
                    nc.vector.tensor_scalar(v4(B["DL"][u], i)[0:r], d, 0.0, None, ALU.max).then_inc(sx["ddve"], 1)
                    nc.vector.tensor_scalar(v4(B["DT"][u], i)[0:r], d, 0.0, None, ALU.min).then_inc(sx["ddve"], 1)
                for i in grp:
                    r = rows(i)
                    u = lane(i)
                    dve.wait_ge(sx["kvc"], i + 1)
                    kv = B["kvt"][u].rearrange("p (q h d) -> p q h d", q=2, h=HEADS)

                    def by(col):
                        return col[0:r, i, :].unsqueeze(2).to_broadcast([r, HEADS, DH])

                    hd_view = lambda ap: ap.rearrange("p (h d) -> p h d", h=HEADS)
                    nc.vector.tensor_tensor(hd_view(B["vb"][u])[0:r], kv[0:r, 1], by(c.beta), ALU.mult).then_inc(sx["scaled"], 1)
                    nc.vector.tensor_tensor(hd_view(B["kbe"][u])[0:r], kv[0:r, 0], by(c.be), ALU.mult).then_inc(sx["scaled"], 1)
                    kg = B["kg"][u].rearrange("p (s h d) -> p s h d", s=2, h=HEADS)
                    if i < NT:
                        for cc in range(2):
                            q = slice(cc * CH, (cc + 1) * CH)
                            nc.vector.tensor_tensor(kg[q, cc], kv[q, 0], c.kgf[q, i, :].unsqueeze(2).to_broadcast([CH, HEADS, DH]),
                                                    ALU.mult).then_inc(sx["scaled"], 1)
                    else:
                        nc.vector.tensor_tensor(kg[0:r, 0], kv[0:r, 0], by(c.kgf), ALU.mult).then_inc(sx["scaled"], 2)
                    dve.wait_ge(sx["eg"], 2 * i + 2)
                    nc.vector.tensor_tensor(v2(B["qg"][u], i), qkvT[:, 0:2, tok(i)], v2(B["eg"][u], i), ALU.mult).then_inc(sx["qg"], 1)
                for i in grp:
                    r = rows(i)
                    u = lane(i)
                    dve.wait_ge(sx["kk"], i + 1)
                    dve.wait_ge(sx["dmask"], 2 * i + 2)
                    L, DL, X = (v4(B[nm][u], i)[0:r] for nm in ("L", "DL", "X"))
                    for hd in range(HEADS):
                        ins = nc.vector.scalar_tensor_tensor(L[:, hd, :], v4(bk(i, 1), i)[0:r, hd, :], c.beta[0:r, i, hd:hd + 1],
                                                             DL[:, hd, :], ALU.mult, ALU.mult)
                        link(ins) if hd < HEADS - 1 else ins.then_inc(sx["L"], 1)
                    dt = v4(B["DT"][u], i)[0:r]
                    nc.vector.tensor_tensor(dt, v4(bk(i, 2), i)[0:r], dt, ALU.mult).then_inc(sx["intra"], 1)
                    dve.wait_ge(sx["L"], i + 1)
                    link(nc.vector.tensor_tensor(X, L, K("lvl1", r, r).unsqueeze(1).to_broadcast([r, HEADS, r]), ALU.mult))
                    nc.vector.scalar_tensor_tensor(X, X, -1.0, K("ident", r, r).unsqueeze(1).to_broadcast([r, HEADS, r]),
                                                   ALU.mult, ALU.add).then_inc(sx["X1"], 1)
                for l in range(len(LV[grp[0]])):
                    for i in grp:
                        r = rows(i)
                        u = lane(i)
                        dve.wait_ge(sx["YX"], number[(i, l)])
                        Y, X = B["Y"][u][0:r, 0:4 * r], B["X"][u][0:r, 0:4 * r]
                        if l == 0:
                            dve.wait_ge(sx["Y1"], i + 1)
                            dve.wait_ge(sx["X1"], i + 1)
                        nc.vector.tensor_tensor(Y, Y, bk(i, 1)[0:r, 0:4 * r], ALU.subtract).then_inc(sx["Y"], 1)
                        nc.vector.tensor_tensor(X, X, bk(i, 2)[0:r, 0:4 * r], ALU.subtract).then_inc(sx["Y"], 1)
                        if l + 1 < len(LV[i]):
                            dve.wait_ge(sx["Y"], 2 * number[(i, l)])
                if grp[0] < NT:
                    for i in grp:
                        u = lane(i)
                        r = P
                        eg = v2(B["eg"][u], i)
                        dve.wait_ge(sx["uc"], 2 * i + 2)
                        for cc in range(2):
                            e = 2 * i + cc
                            q = slice(cc * CH, (cc + 1) * CH)
                            dve.wait_ge(sx["vW"], 2 * e + 1)
                            for pair in range(2):
                                for hh in range(2):
                                    hd = 2 * pair + hh
                                    nc.vector.tensor_tensor(V("vz", u)[q, hd, hh * DH:(hh + 1) * DH],
                                                            B["u"][u][q, hd * DH:(hd + 1) * DH],
                                                            bk(i, 0)[q, hd * DH:(hd + 1) * DH], ALU.subtract)\
                                        .then_inc(sx["vn"] if hd == 3 else sx["init"], 1)
                            dve.wait_ge(sx["vW"], 2 * e + 2)
                            link(nc.vector.tensor_tensor(dS, bk(i, 2)[:, 0:256].rearrange("p (c n) -> p c n", c=2),
                                                         K("blk64").unsqueeze(1).to_broadcast([P, 2, P]), ALU.mult))
                            for pair in range(2):
                                ins = nc.vector.scalar_tensor_tensor(S[:, pair, :], S[:, pair, :],
                                                                     eg[:, pair, cc * CH + CH - 1:cc * CH + CH], dS[:, pair, :],
                                                                     ALU.mult, ALU.add)
                                link(ins) if pair == 0 else ins.then_inc(sx["S"], 1)
                            dve.wait_ge(sx["S"], e + 1)
                    if grp[0] == NT - 2:
                        nc.vector.memset(c.A("SS"), 0.0).then_inc(sx["sSn"], 1)
                else:
                    i = NT
                    dve.wait_ge(sx["swt"], 1)
                    dve.wait_ge(sx["uc"], 2 * i + 2)
                    for hd in range(HEADS):
                        hh = hd % 2
                        ins = nc.vector.tensor_tensor(V("vz", 0)[0:NS, hd, hh * DH:(hh + 1) * DH],
                                                      B["u"][0][0:NS, hd * DH:(hd + 1) * DH],
                                                      ps[5][0:NS, hd * DH:(hd + 1) * DH], ALU.subtract)
                        link(ins) if hd < 3 else ins.then_inc(sx["svn"], 1)
                    dve.wait_ge(sx["svn"], 1)
                    sel = K("blk4", NS, NS)[:, 0:NS:DS]
                    for hd in range(HEADS):
                        hh = hd % 2
                        vn = V("vz", 0)[0:NS, hd, hh * DH:(hh + 1) * DH].unsqueeze(1).to_broadcast([NS, DB, DH])
                        nc.vector.tensor_tensor(Vx[0:NS, hd], vn, sel.unsqueeze(2).to_broadcast([NS, DB, DH]),
                                                ALU.mult).then_inc(sx["svx"], 1)
                    eg = v2(B["eg"][0], i)
                    for hd in range(HEADS):
                        pair, hh = hd // 2, hd % 2
                        q = slice(hh * DH, (hh + 1) * DH)
                        gl = eg[q, pair, DS - 1:NS:DS].unsqueeze(2).to_broadcast([DH, DB, DH])
                        link(nc.vector.tensor_tensor(Sn[q, hd], SS[q, :, pair, q], gl, ALU.mult))
                        dve.wait_ge(sx["sdS"], hd + 1)
                        bank = (7, 1, 2, 5)[hd]
                        nc.vector.tensor_tensor(Sn[q, hd], ps[bank][q, :].rearrange("p (b n) -> p b n", b=DB), Sn[q, hd],
                                                ALU.add).then_inc(sx["ost"], 1)
            for n in range(2):
                for g in range(GRP):
                    t = slice(g * GT, (g + 1) * GT)
                    dve.wait_ge(sx["rrn"], GRP * n + g + 1)
                    link(nc.vector.scalar_tensor_tensor(odT[:, n, t], odT[:, n, t], c.A("dnorm")[:, 0:1], c.rrn[:, n, t],
                                                        ALU.mult, ALU.mult))
                    nc.vector.tensor_tensor(oT[:, 6 + n, t], odT[:, n, t], zT[:, n, t], ALU.mult).then_inc(sx["rout"], 1)

        @block.sync
        def _(sp):
            sp.wait_ge(sx["sSn"], 1)
            for hd in range(HEADS):
                q = slice((hd % 2) * DH, (hd % 2 + 1) * DH)
                for b in range(DB):
                    sp.dma_start(SS[q, b, hd // 2, q], T['state_delta'][0, b, hd]).then_inc(sx["sload"], 16)
            for hd in range(HEADS):
                q = slice((hd % 2) * DH, (hd % 2 + 1) * DH)
                sp.dma_start(O['delta_prompt'][0, 0, hd], S[q, hd // 2, q]).then_inc(sx["soc"], 16)
            for hd in range(HEADS):
                q = slice((hd % 2) * DH, (hd % 2 + 1) * DH)
                sp.wait_ge(sx["ost"], hd + 1)
                sp.dma_start(O['delta_sample'][0, :, hd].rearrange("b k v -> k b v"), Sn[q, hd]).then_inc(sx["soc"], 16)
            sp.wait_ge(sx["soc"], 16 * 2 * HEADS)


def stage_residual(c, tag, src, weight, gain, shift, turn):
    nc, T, O, K = c.nc, c.T, c.O, c.K
    c.place(start=c.res_at, rw=KC * D, rg=D, rb=D)
    w = c.A("rw").rearrange("p (k n) -> p k n", k=KC)
    g, b = c.A("rg"), c.A("rb")
    h, hT, ps = c.h, c.hT, c.ps
    s = lambda n: c.sem(f"{tag}_{n}")
    w_in = [s(f"w{n}") for n in range(2)]
    ln_in, prod, added, stats, rstd_ok, normed, turned, hT_ok = (s("ln"), s("prod"), s("added"), s("stats"), s("rstd"),
                                                                 s("normed"), s("turned"), s("hT"))
    dve_chain, act_chain = s("dve"), s("act")
    wv = T[weight][0].rearrange("(k p) n -> p k n", p=P)

    with nc.Block() as block:
        @block.sync
        def _(sp):
            for q in range(2):
                sp.dma_start(w[:, :, q * 512:(q + 1) * 512], wv[:, :, q * 512:(q + 1) * 512]).then_inc(w_in[q], 16)
            sp.dma_start(g, row_bc(T[gain][0])).then_inc(ln_in, 16)
            sp.dma_start(b, row_bc(T[shift][0])).then_inc(ln_in, 16)

        @block.tensor
        def _(pe):
            def product(i):
                r = rows(i)
                for q in range(2):
                    if i == 0:
                        pe.wait_ge(w_in[q], 16)
                    if i >= 2:
                        pe.wait_ge(added, 2 * (i - 2) + q + 1)
                    for k in range(KC):
                        last = nc.tensor.matmul(ps[2 * (i % 2) + q][0:r, :], src[:, k, i * P:i * P + r],
                                                w[:, k, q * 512:(q + 1) * 512], start=(k == 0), stop=(k == KC - 1))
                    last.then_inc(prod, 1)

            def transposes(i):
                r = rows(i)
                pe.wait_ge(normed, i + 1)
                for q in range(2):
                    if i >= 1:
                        pe.wait_ge(hT_ok, 2 * (i - 1) + q + 1)
                    for k in range(4):
                        last = nc.tensor.transpose(ps[4 + q][:, k * r:(k + 1) * r],
                                                   h[0:r, i, (4 * q + k) * P:(4 * q + k + 1) * P], K("ident", r, r))
                    last.then_inc(turned, 1)

            for i in range(TILES + 1):
                if i < TILES:
                    product(i)
                if turn and i >= 1:
                    transposes(i - 1)

        @block.vector
        def _(dve):
            link = Chain(dve, dve_chain)

            def add(i):
                r = rows(i)
                for q in range(2):
                    dve.wait_ge(prod, 2 * i + q + 1)
                    x = h[0:r, i, q * 512:(q + 1) * 512]
                    nc.vector.scalar_tensor_tensor(x, x, ALPHA, ps[2 * (i % 2) + q][0:r, :], ALU.mult, ALU.add).then_inc(added, 1)
                dve.wait_ge(added, 2 * i + 2)
                if i >= 2:
                    dve.wait_ge(rstd_ok, i - 1)
                ln_stats(nc, link, h, i, c.st[:, i % 2, :], c.mv[:, i % 2, :]).then_inc(stats, 1)
                dve.wait_ge(stats, i + 1)

            def apply(i):
                dve.wait_ge(rstd_ok, i + 1)
                ln_apply(nc, link, h, i, c.mv[:, i % 2, :], c.rstd[:, i % 2, :], g, b).then_inc(normed, 1)

            dve.wait_ge(ln_in, 32)
            for i in range(TILES):
                add(i)
                apply(i)

        @block.scalar
        def _(act):
            link = Chain(act, act_chain)
            nc.scalar.preload_act_table_set(EXPLN)
            for i in range(TILES + 1):
                if i < TILES:
                    act.wait_ge(stats, i + 1)
                    if i >= 2:
                        act.wait_ge(normed, i - 1)
                    ln_rstd(nc, link, i, c.mv[:, i % 2, :], c.rstd[:, i % 2, :], c.eps).then_inc(rstd_ok, 1)
                if turn and i >= 1:
                    r = rows(i - 1)
                    for q in range(2):
                        act.wait_ge(turned, 2 * (i - 1) + q + 1)
                        act.wait_ge(prod, 2 * i)
                        nc.scalar.copy(hT[:, 4 * q:4 * q + 4, (i - 1) * P:(i - 1) * P + r],
                                       ps[4 + q][:, 0:4 * r].rearrange("p (k t) -> p k t", k=4)).then_inc(hT_ok, 1)


def stage_memory(c):
    nc, T, O, K = c.nc, c.T, c.O, c.K
    c.place(start=0, KT=KC * NMEM, Vm=2 * D, qXT=KC * TOK)
    c.place(start=4096, Km=2 * D, mem=2 * D, memT=KC * NMEM, wk=KC * D, wv=KC * D)
    KT = c.A("KT").rearrange("p (k m) -> p k m", k=KC)
    Vm, Km, mem = (c.A(n).rearrange("p (m n) -> p m n", m=2) for n in ("Vm", "Km", "mem"))
    memT = c.A("memT").rearrange("p (k m) -> p k m", k=KC)
    w = {n: c.A(n).rearrange("p (k n) -> p k n", k=KC) for n in ("wk", "wv")}
    c.KT, c.Vm = KT, Vm
    ps = c.ps
    s = lambda n: c.sem(f"m_{n}")
    mem_in, wk_in, wv_in, turned, mT_ok, prod, out_ok, kturned, kT_ok, stored = (
        s("mem"), s("wk"), s("wv"), s("turned"), s("mT"), s("prod"), s("out"), s("kturned"), s("kT"), s("stored"))

    with nc.Block() as block:
        @block.sync
        def _(sp):
            sp.dma_start(mem, T['mem_prompt'][0].rearrange("(m p) n -> p m n", p=P)).then_inc(mem_in, 16)
            sp.dma_start(w["wk"], T['xa_wk'][0].rearrange("(k p) n -> p k n", p=P)).then_inc(wk_in, 16)
            sp.dma_start(w["wv"], T['xa_wv'][0].rearrange("(k p) n -> p k n", p=P)).then_inc(wv_in, 16)
            for n, (name, t) in enumerate((('mem_k_prompt', Km), ('mem_v_prompt', Vm))):
                sp.wait_ge(out_ok, 4 * (n + 1))
                sp.dma_start(O[name][0, 0].rearrange("(m p) h d -> p m (h d)", p=P), t).then_inc(stored, 16)
            sp.wait_ge(stored, 32)

        @block.tensor
        def _(pe):
            def turns(src, f, base, sem_t, freed):
                for k in (2 * f, 2 * f + 1):
                    for m in range(2):
                        last = nc.tensor.transpose(ps[base + f % 4][:, (k % 2) * NMEM + m * P:(k % 2) * NMEM + (m + 1) * P],
                                                   src[:, m, k * P:(k + 1) * P], K("ident"))
                last.then_inc(sem_t, 1)

            pe.wait_ge(mem_in, 16)
            for f in range(4):
                turns(mem, f, 0, turned, None)
            pe.wait_ge(mT_ok, 4)
            u = 0
            for name, arrived in (("wk", wk_in), ("wv", wv_in)):
                pe.wait_ge(arrived, 16)
                for m in range(2):
                    for q in range(2):
                        if u >= 4:
                            pe.wait_ge(out_ok, u - 3)
                        for k in range(KC):
                            last = nc.tensor.matmul(ps[4 + u % 4][:, :], memT[:, k, m * P:(m + 1) * P],
                                                    w[name][:, k, q * 512:(q + 1) * 512], start=(k == 0), stop=(k == KC - 1))
                        last.then_inc(prod, 1)
                        u += 1
                if name == "wk":
                    pe.wait_ge(out_ok, 4)
                    for f in range(4):
                        turns(Km, f, 0, kturned, None)

        @block.scalar
        def _(act):
            for f in range(4):
                act.wait_ge(turned, f + 1)
                nc.scalar.copy(memT[:, 2 * f:2 * f + 2, :], ps[f][:, :].rearrange("p (k m) -> p k m", k=2)).then_inc(mT_ok, 1)
            for f in range(4):
                act.wait_ge(kturned, f + 1)
                nc.scalar.copy(KT[:, 2 * f:2 * f + 2, :], ps[f][:, :].rearrange("p (k m) -> p k m", k=2)).then_inc(kT_ok, 1)

        @block.vector
        def _(dve):
            for u in range(8):
                dst = (Km, Vm)[u // 4][:, (u // 2) % 2, (u % 2) * 512:(u % 2 + 1) * 512]
                dve.wait_ge(prod, u + 1)
                nc.vector.tensor_copy(dst, ps[4 + u % 4][:, :]).then_inc(out_ok, 1)


def stage_queries(c):
    nc, T = c.nc, c.T
    c.place(start=4096 + KC * TOK, qring=4 * KC * P)
    ring = c.A("qring").rearrange("p (s k n) -> p s k n", s=4, k=KC)
    qXT = c.A("qXT").rearrange("p (k t) -> p k t", k=KC)
    c.qXT = qXT
    ps, hT = c.ps, c.hT
    s = lambda n: c.sem(f"q_{n}")
    w_in, prod, evac = [s(f"w{n}") for n in range(4)], s("prod"), s("evac")
    wv = T['xa_wq'][0].rearrange("(k p) n -> p k n", p=P)
    with nc.Block() as block:
        @block.sync
        def _(sp):
            for n in range(KC):
                if n >= 4:
                    sp.wait_ge(prod, GRP * (n - 3))
                sp.dma_start(ring[:, n % 4], wv[:, :, n * P:(n + 1) * P]).then_inc(w_in[n % 4], 16)

        @block.tensor
        def _(pe):
            for n in range(KC):
                pe.wait_ge(w_in[n % 4], 16 * (n // 4 + 1))
                for g in range(GRP):
                    u = GRP * n + g
                    if u >= 8:
                        pe.wait_ge(evac, u - 7)
                    for k in range(KC):
                        last = nc.tensor.matmul(ps[u % 8][:, 0:GT], ring[:, n % 4, k, :], hT[:, k, g * GT:(g + 1) * GT],
                                                start=(k == 0), stop=(k == KC - 1))
                    last.then_inc(prod, 1)

        @block.scalar
        def _(act):
            for u in range(GRP * KC):
                act.wait_ge(prod, u + 1)
                nc.scalar.copy(qXT[:, u // GRP, (u % GRP) * GT:(u % GRP + 1) * GT], ps[u % 8][:, 0:GT]).then_inc(evac, 1)


def stage_cross(c):
    nc, T, O, K = c.nc, c.T, c.O, c.K
    c.place(start=4096 + KC * TOK, xp=2 * D, xpT=D, Kb=2 * 2 * D, KTb=2 * D, Vb=3 * 2 * D, sS=256, xps=256, xpTs=256)
    KT, Vm, qXT = c.KT, c.Vm, c.qXT
    xp = c.A("xp").rearrange("p (s h m) -> p s h m", s=2, h=HEADS)
    xpT = c.A("xpT").rearrange("p (m h q) -> p m h q", m=2, h=HEADS)
    Kb = c.A("Kb").rearrange("p (s m n) -> p s m n", s=2, m=2)
    Vb = c.A("Vb").rearrange("p (s m n) -> p s m n", s=3, m=2)
    KTb = c.A("KTb").rearrange("p (k m) -> p k m", k=KC)
    sS, xps, xpTs = c.A("sS"), c.A("xps"), c.A("xpTs")
    mx = c.new_small(2 * HEADS).rearrange("p (s h) -> p s h", s=2)
    sm = c.new_small(2 * HEADS).rearrange("p (s h) -> p s h", s=2)
    mxs, sms = c.new_small(1), c.new_small(1)
    ps = c.ps
    s = lambda n: c.sem(f"x_{n}")
    k_in, v_in = [s("k0"), s("k1")], [s(f"v{n}") for n in range(3)]
    score, neg, exp_ok, p_ok, pturned, pT_ok, val, val_ok = (s("score"), s("neg"), s("exp"), s("p"), s("pturned"),
                                                             s("pT"), s("val"), s("valok"))
    kturned, kT_ok, sscore, s_ok, s_back, s_neg, s_exp, s_p, s_pt, s_pT, v_done, x_ok = (
        s("kturned"), s("kT"), s("sscore"), s("sok"), s("sback"), s("sneg"), s("sexp"), s("sp"), s("spt"), s("spT"),
        s("vdone"), s("xok"))
    dve_chain, act_chain = s("dve"), s("act")
    SC = XDH ** -0.5

    with nc.Block() as block:
        @block.sync
        def _(sp):
            def load(name, dst, b, done):
                sp.dma_start(dst, T[name][0, b].rearrange("(m p) h d -> p m (h d)", p=P)).then_inc(done, 16)

            for b in range(DB):
                if b >= 2:
                    sp.wait_ge(kturned, 4 * (b - 1))
                load('cache_mem_k', Kb[:, b % 2], b, k_in[b % 2])
            for b in range(DB):
                if b >= 3:
                    sp.wait_ge(v_done, b - 2)
                load('cache_mem_v', Vb[:, b % 3], b, v_in[b % 3])

        @block.tensor
        def _(pe):
            def turn_keys(b, f):
                if f == 0:
                    pe.wait_ge(k_in[b % 2], 16 * (b // 2 + 1))
                if 4 * b + f >= 1:
                    pe.wait_ge(kT_ok, 4 * b + f)
                for k in (2 * f, 2 * f + 1):
                    for m in range(2):
                        last = nc.tensor.transpose(ps[6][:, (k % 2) * NMEM + m * P:(k % 2) * NMEM + (m + 1) * P],
                                                   Kb[:, b % 2, m, k * P:(k + 1) * P], K("ident"))
                last.then_inc(kturned, 1)

            def sample_scores(b):
                pe.wait_ge(kT_ok, 4 * b + 4)
                for m in range(2):
                    for hd in range(HEADS):
                        at = m * P + b * HEADS * DS + hd * DS
                        for dc in range(2):
                            last = nc.tensor.matmul(ps[7][:, at:at + DS], KTb[:, 2 * hd + dc, m * P:(m + 1) * P],
                                                    qXT[:, 2 * hd + dc, SEQ + b * DS:SEQ + (b + 1) * DS],
                                                    start=(dc == 0), stop=(dc == 1))
                last.then_inc(sscore, 1)

            def scores(i):
                if i >= 1:
                    pe.wait_ge(exp_ok, HEADS * i)
                    pe.wait_ge(neg, i)
                for hd in range(HEADS):
                    for dc in range(2):
                        last = nc.tensor.matmul(ps[hd // 2][:, (hd % 2) * NMEM:(hd % 2 + 1) * NMEM],
                                                qXT[:, 2 * hd + dc, i * P:(i + 1) * P], KT[:, 2 * hd + dc, :],
                                                start=(dc == 0), stop=(dc == 1))
                last.then_inc(score, 1)

            def turn_p(i):
                pe.wait_ge(p_ok, i + 1)
                if i >= 1:
                    pe.wait_ge(pT_ok, 2 * i)
                for m in range(2):
                    for hd in range(HEADS):
                        last = nc.tensor.transpose(ps[2 + m][:, hd * P:(hd + 1) * P], xp[:, i % 2, hd, m * P:(m + 1) * P],
                                                   K("ident"))
                    last.then_inc(pturned, 1)

            def values(i):
                pe.wait_ge(pT_ok, 2 * i + 2)
                if i >= 1:
                    pe.wait_ge(val_ok, 2 * i)
                for k in range(KC):
                    for m in range(2):
                        last = nc.tensor.matmul(ps[4 + k // 4][:, (k % 4) * P:(k % 4 + 1) * P], Vm[:, m, k * P:(k + 1) * P],
                                                xpT[:, m, k // 2, :], start=(m == 0), stop=(m == 1))
                    if k % 4 == 3:
                        last.then_inc(val, 1)

            for i in range(NT + 1):
                if i < NT:
                    turn_keys(i, 0)
                    scores(i)
                    turn_keys(i, 1)
                if i >= 1:
                    turn_p(i - 1)
                if i < NT:
                    turn_keys(i, 2)
                if i >= 1:
                    values(i - 1)
                if i < NT:
                    turn_keys(i, 3)
                    sample_scores(i)
            pe.wait_ge(s_ok, 1)
            pe.wait_ge(exp_ok, HEADS * NT)
            for m in range(2):
                last = nc.tensor.transpose(ps[0][:, m * P:(m + 1) * P], sS[:, m * P:(m + 1) * P], K("ident"))
            last.then_inc(s_back, 1)
            pe.wait_ge(s_p, 1)
            for m in range(2):
                last = nc.tensor.transpose(ps[1][:, m * P:(m + 1) * P], xps[:, m * P:(m + 1) * P], K("ident"))
            last.then_inc(s_pt, 1)
            pe.wait_ge(s_pT, 1)
            for b in range(DB):
                pe.wait_ge(v_in[b % 3], 16 * (b // 3 + 1))
                for k in range(KC):
                    at = b * HEADS * DS + (k // 2) * DS
                    for m in range(2):
                        last = nc.tensor.matmul(ps[6][:, k * NS + b * DS:k * NS + (b + 1) * DS],
                                                Vb[:, b % 3, m, k * P:(k + 1) * P], xpTs[:, m * P + at:m * P + at + DS],
                                                start=(m == 0), stop=(m == 1))
                last.then_inc(v_done, 1)

        @block.scalar
        def _(act):
            link = Chain(act, act_chain)
            nc.scalar.preload_act_table_set(EXPLN)

            def exps(i):
                act.wait_ge(neg, i + 1)
                if i >= 2:
                    act.wait_ge(pturned, 2 * (i - 1))
                for hd in range(HEADS):
                    nc.scalar.activation(xp[:, i % 2, hd, :], ps[hd // 2][:, (hd % 2) * NMEM:(hd % 2 + 1) * NMEM], ACT.Exp,
                                         bias=mx[:, i % 2, hd:hd + 1], scale=SC,
                                         accum_out=sm[:, i % 2, hd:hd + 1]).then_inc(exp_ok, 1)

            def pT(i):
                for m in range(2):
                    act.wait_ge(pturned, 2 * i + m + 1)
                    if i >= 1:
                        act.wait_ge(val, 2 * i)
                    nc.scalar.copy(xpT[:, m], ps[2 + m][:, :].rearrange("p (h q) -> p h q", h=HEADS)).then_inc(pT_ok, 1)

            def keyT(b, f):
                act.wait_ge(kturned, 4 * b + f + 1)
                if b >= 1 and f == 0:
                    act.wait_ge(sscore, b)
                nc.scalar.copy(KTb[:, 2 * f:2 * f + 2, :], ps[6][:, :].rearrange("p (k m) -> p k m", k=2)).then_inc(kT_ok, 1)

            for i in range(NT + 1):
                if i < NT:
                    keyT(i, 0)
                    keyT(i, 1)
                if i >= 1:
                    pT(i - 1)
                if i < NT:
                    keyT(i, 2)
                    exps(i)
                    keyT(i, 3)
            act.wait_ge(s_neg, 1)
            nc.scalar.activation(xps, ps[0][:, 0:256], ACT.Exp, bias=mxs, scale=SC, accum_out=sms).then_inc(s_exp, 1)

        @block.vector
        def _(dve):
            link = Chain(dve, dve_chain)

            def maxima(i):
                dve.wait_ge(score, i + 1)
                if i >= 2:
                    dve.wait_ge(exp_ok, HEADS * (i - 1))
                m = mx[:, i % 2, :]
                for q in range(2):
                    link(nc.vector.tensor_reduce(m[:, 2 * q:2 * q + 2], ps[q][:, :].rearrange("p (h m) -> p h m", h=2), AX, ALU.max))
                nc.vector.tensor_scalar(m, m, -SC, None, ALU.mult).then_inc(neg, 1)

            def normalise(i):
                dve.wait_ge(exp_ok, HEADS * (i + 1))
                link(nc.vector.reciprocal(sm[:, i % 2, :], sm[:, i % 2, :]))
                p = xp[:, i % 2]
                nc.vector.tensor_tensor(p, p, sm[:, i % 2, :].unsqueeze(2).to_broadcast([P, HEADS, NMEM]), ALU.mult)\
                    .then_inc(p_ok, 1)

            def outs(i):
                for q in range(2):
                    dve.wait_ge(val, 2 * i + q + 1)
                    nc.vector.tensor_copy(qXT[:, 4 * q:4 * q + 4, i * P:(i + 1) * P],
                                          ps[4 + q][:, :].rearrange("p (k t) -> p k t", k=4)).then_inc(val_ok, 1)

            for i in range(NT + 1):
                if i < NT:
                    maxima(i)
                if i >= 1:
                    outs(i - 1)
                if i < NT:
                    normalise(i)
            dve.wait_ge(sscore, DB)
            nc.vector.tensor_copy(sS, ps[7][:, 0:256]).then_inc(s_ok, 1)
            dve.wait_ge(s_back, 1)
            link(nc.vector.tensor_reduce(mxs, ps[0][:, 0:256], AX, ALU.max))
            nc.vector.tensor_scalar(mxs, mxs, -SC, None, ALU.mult).then_inc(s_neg, 1)
            dve.wait_ge(s_exp, 1)
            link(nc.vector.reciprocal(sms, sms))
            nc.vector.tensor_scalar(xps, xps, sms, None, ALU.mult).then_inc(s_p, 1)
            dve.wait_ge(s_pt, 1)
            nc.vector.tensor_copy(xpTs, ps[1][:, 0:256]).then_inc(s_pT, 1)
            dve.wait_ge(v_done, DB)
            nc.vector.tensor_copy(qXT[:, :, SEQ:TOK], ps[6][:, 0:KC * NS].rearrange("p (k t) -> p k t", k=KC)).then_inc(x_ok, 1)


def stage_route(c):
    nc, T, K = c.nc, c.T, c.K
    G4, NE_ = 4, NE
    c.place(start=0, wr=KC * NE, rbias=NE, sel=TILES * NE, sc=TILES * NE, cmpa=TILES * NE * 4, cmpb=TILES * NE * 4,
            rank=TILES * NE, gs=TILES * G4, grank=TILES * G4, den=TILES, comb=TILES * NE, combT=TOK, tri=16)
    v = lambda n, pat, **k: c.A(n).rearrange(pat, **k)
    wr = v("wr", "p (k e) -> p k e", k=KC)
    sc, sel, comb = c.A("sc"), c.A("sel"), c.A("comb")
    rank, gs, grank, den = c.A("rank"), c.A("gs"), c.A("grank"), c.A("den")
    ca, cb = c.A("cmpa"), c.A("cmpb")
    ps, hT = c.ps, c.hT
    s = lambda n: c.sem(f"r_{n}")
    loaded, logit, e_ok, chain, comb_ok, turned, cT_ok, stored, zeroed = (
        s("load"), s("logit"), s("e"), s("dve"), s("comb"), s("turned"), s("cT"), s("stored"), s("zero"))
    M = TILES * G4

    with nc.Block() as block:
        @block.sync
        def _(sp):
            sp.dma_start(wr, T['w_router'].rearrange("(k p) e -> p k e", p=P)).then_inc(loaded, 16)
            sp.dma_start(c.A("rbias"), row_bc(T['router_bias'])).then_inc(loaded, 16)
            sp.dma_start(c.A("tri"), T['tie_table']).then_inc(loaded, 16)
            sp.wait_ge(cT_ok, 3)
            sp.dma_start(c.combine_dram, c.A("combT")[0:NE, :]).then_inc(stored, 16)
            sp.wait_ge(stored, 16)

        @block.tensor
        def _(pe):
            pe.wait_ge(loaded, 48)
            for i in range(TILES):
                r = rows(i)
                for k in range(KC):
                    last = nc.tensor.matmul(ps[0][0:r, i * NE:(i + 1) * NE], hT[:, k, i * P:i * P + r], wr[:, k, :],
                                            start=(k == 0), stop=(k == KC - 1))
            last.then_inc(logit, 1)
            pe.wait_ge(comb_ok, 1)
            for i in range(TILES):
                r = rows(i)
                last = nc.tensor.transpose(ps[1 + i // 4][0:NE, (i % 4) * P:(i % 4) * P + r], comb[0:r, i * NE:(i + 1) * NE],
                                           K("ident", r, r))
            last.then_inc(turned, 1)

        @block.scalar
        def _(act):
            act.wait_ge(zeroed, 1)
            act.wait_ge(logit, 1)
            nc.scalar.preload_act_table_set(EXPLN)
            nc.scalar.activation(sc[:, 0:NT * NE], ps[0][:, 0:NT * NE], ACT.Exp, scale=-1.0).then_inc(e_ok, 1)
            nc.scalar.activation(sc[0:NS, NT * NE:], ps[0][0:NS, NT * NE:TILES * NE], ACT.Exp, scale=-1.0).then_inc(e_ok, 1)
            act.wait_ge(turned, 1)
            for q, n in enumerate((512, 512, NS)):
                nc.scalar.copy(c.A("combT")[0:NE, q * 512:q * 512 + n], ps[1 + q][0:NE, 0:n]).then_inc(cT_ok, 1)

        @block.vector
        def _(dve):
            link = Chain(dve, chain)
            vt = nc.vector
            vt.memset(sc, 0.0).then_inc(zeroed, 1)
            dve.wait_ge(e_ok, 2)
            dve.wait_ge(loaded, 48)
            link(vt.tensor_scalar(sc, sc, 1.0, None, ALU.add))
            link(vt.reciprocal(sc, sc))
            link(vt.tensor_tensor(sel.rearrange("p (i e) -> p i e", e=NE), sc.rearrange("p (i e) -> p i e", e=NE),
                                  c.A("rbias").unsqueeze(1).to_broadcast([P, TILES, NE]), ALU.add))

            def ranks(x, m, out):
                xi = x.rearrange("p (m i) -> p m i", i=4).unsqueeze(2).to_broadcast([P, m, 4, 4])
                xj = x.rearrange("p (m j) -> p m j", j=4).unsqueeze(3).to_broadcast([P, m, 4, 4])
                a = ca[:, 0:16 * m].rearrange("p (m j i) -> p m j i", j=4, i=4)
                b = cb[:, 0:16 * m].rearrange("p (m j i) -> p m j i", j=4, i=4)
                tri = c.A("tri").rearrange("p (j i) -> p j i", j=4).unsqueeze(1).to_broadcast([P, m, 4, 4])
                link(vt.tensor_tensor(a, xi, xj, ALU.is_equal))
                link(vt.tensor_tensor(a, a, tri, ALU.mult))
                link(vt.tensor_tensor(b, xi, xj, ALU.is_gt))
                link(vt.tensor_tensor(a, a, b, ALU.add))
                link(vt.tensor_reduce(out.rearrange("p (m j) -> p m j", j=4), a, AX, ALU.add))

            ranks(sel, M, rank)
            link(vt.tensor_scalar(rank, rank, 1.5, None, ALU.is_lt))
            link(vt.tensor_tensor(comb, rank, sel, ALU.mult))
            link(vt.tensor_reduce(gs, comb.rearrange("p (m e) -> p m e", e=4), AX, ALU.add))
            ranks(gs, TILES, grank)
            link(vt.tensor_scalar(grank, grank, 0.5, None, ALU.is_lt))
            link(vt.tensor_tensor(rank.rearrange("p (m e) -> p m e", e=4), rank.rearrange("p (m e) -> p m e", e=4),
                                  grank.unsqueeze(2).to_broadcast([P, M, 4]), ALU.mult))
            link(vt.tensor_tensor(comb, rank, sc, ALU.mult))
            link(vt.tensor_reduce(den, comb.rearrange("p (i e) -> p i e", e=NE), AX, ALU.add))
            link(vt.reciprocal(den, den))
            c3 = comb.rearrange("p (i e) -> p i e", e=NE)
            vt.tensor_tensor(c3, c3, den.unsqueeze(2).to_broadcast([P, TILES, NE]), ALU.mult).then_inc(comb_ok, 1)


def stage_experts(c):
    nc, T, O, K = c.nc, c.T, c.O, c.K
    EW = KC * DE
    c.place(start=0, xw=2 * 3 * EW, cb=2 * TOK, act=2 * 2 * TOK, sg=2 * GT, rg=D, rb=D)
    xw = c.A("xw").rearrange("p (s n) -> p s n", s=2)
    wgv = [xw[:, u, 0:EW].rearrange("p (k f) -> p k f", k=KC) for u in range(2)]
    wuv = [xw[:, u, EW:2 * EW].rearrange("p (k f) -> p k f", k=KC) for u in range(2)]
    wdv = [xw[:, u, 2 * EW:].rearrange("p (f n) -> p f n", f=2) for u in range(2)]
    cb = c.A("cb").rearrange("p (s t) -> p s t", s=2)
    actT = c.A("act").rearrange("p (s f t) -> p s f t", s=2, f=2)
    sg = c.A("sg").rearrange("p (s t) -> p s t", s=2)
    g, b = c.A("rg"), c.A("rb")
    h, hT, ps = c.h, c.hT, c.ps
    s = lambda n: c.sem(f"x{n}")
    loaded = [s("l0"), s("l1")]
    ln_in, scaled, up, sig, acts, down, added, used = (s("ln"), s("scaled"), s("up"), s("sig"), s("acts"), s("down"),
                                                       s("added"), s("used"))
    half, dve_chain, act_chain, rstd_ok, stats, normed, stored = (s("half"), s("dve"), s("act"), s("rstd"), s("stats"),
                                                                  s("normed"), s("stored"))
    UP, DN = 2 * GRP, 2 * TILES
    LN2 = 2

    def unit_up(n):
        return n // GRP, n % GRP

    with nc.Block() as block:
        @block.sync
        def _(sp):
            sp.dma_start(g, row_bc(T['ln3_g'][0])).then_inc(ln_in, 16)
            sp.dma_start(b, row_bc(T['ln3_b'][0])).then_inc(ln_in, 16)

            for i in range(TILES):
                sp.wait_ge(normed, i + 1)
                dst = O['y_prompt'][0, i * P:(i + 1) * P, :] if i < NT else O['y_sample'].rearrange("b t d -> (b t) d")
                sp.dma_start(dst, h[0:rows(i), i, :]).then_inc(stored, 16)
            sp.wait_ge(stored, 16 * TILES)

        @block.gpsimd
        def _(gp):
            def load(e, u):
                gp.dma_start(wgv[u], T['ex_wg'][0][bass.ds(e, 1)].rearrange("a (k p) f -> p (a k) f", p=P)).then_inc(loaded[u], 16)
                gp.dma_start(wuv[u], T['ex_wu'][0][bass.ds(e, 1)].rearrange("a (k p) f -> p (a k) f", p=P)).then_inc(loaded[u], 16)
                gp.dma_start(wdv[u], T['ex_wd'][0][bass.ds(e, 1)].rearrange("a (f p) n -> p (a f) n", p=P)).then_inc(loaded[u], 16)
                gp.dma_start(cb[:, u, :], c.combine_dram[bass.ds(e, 1), :].rearrange("a t -> (a t)").partition_broadcast(P))\
                    .then_inc(loaded[u], 16)

            load(0, 0)
            load(1, 1)
            with gp.Fori(0, NE // 2 - 1) as j:
                for u in range(2):
                    gp.wait_ge(down, (j * 2 + u + 1) * DN)
                    gp.wait_ge(acts, (j * 2 + u + 1) * UP)
                    load(j * 2 + u + 2, u)

        @block.tensor
        def _(pe):
            def body(j, u, first):
                e = j * 2 + u
                pe.wait_ge(loaded[u], (j + 1) * 64)
                for n in range(UP):
                    f, grp = unit_up(n)
                    if first and n < 2:
                        pass
                    else:
                        pe.wait_ge(acts, e * UP + n - 1)
                    for bank, w in ((2 * (n % 2), wgv[u]), (2 * (n % 2) + 1, wuv[u])):
                        for k in range(KC):
                            last = nc.tensor.matmul(ps[bank][:, 0:GT], w[:, k, f * P:(f + 1) * P],
                                                    hT[:, k, grp * GT:(grp + 1) * GT], start=(k == 0), stop=(k == KC - 1))
                    last.then_inc(up, 1)
                pe.wait_ge(acts, (e + 1) * UP)
                for n in range(DN):
                    i, q = n // 2, n % 2
                    r = rows(i)
                    if first and n < 4:
                        pass
                    else:
                        pe.wait_ge(added, e * DN + n - 3)
                    for f in range(2):
                        last = nc.tensor.matmul(ps[4 + n % 4][0:r, :], actT[:, u, f, i * P:i * P + r],
                                                wdv[u][:, f, q * 512:(q + 1) * 512], start=(f == 0), stop=(f == 1))
                    last.then_inc(down, 1)

            body(0, 0, True)
            body(0, 1, False)
            with pe.Fori(1, NE // 2) as j:
                for u in range(2):
                    body(j, u, False)

        @block.scalar
        def _(act):
            link = Chain(act, act_chain)

            def body(j, u, first):
                e = j * 2 + u
                for n in range(UP):
                    act.wait_ge(up, e * UP + n + 1)
                    if not (first and n < 2):
                        act.wait_ge(acts, e * UP + n - 1)
                    nc.scalar.activation(sg[:, n % 2, :], ps[2 * (n % 2)][:, 0:GT], ACT.Silu).then_inc(sig, 1)

            body(0, 0, True)
            body(0, 1, False)
            with act.Fori(1, NE // 2) as j:
                for u in range(2):
                    body(j, u, False)
            nc.scalar.preload_act_table_set(EXPLN)
            for i in range(TILES):
                act.wait_ge(stats, i + 1)
                if i >= 2:
                    act.wait_ge(normed, i - 1)
                ln_rstd(nc, link, i, c.mv[:, i % 2, :], c.rstd[:, i % 2, :], c.eps).then_inc(rstd_ok, 1)

        @block.vector
        def _(dve):
            link = Chain(dve, dve_chain)
            nc.vector.tensor_scalar(h[:, 0:NT, :], h[:, 0:NT, :], ALPHA, None, ALU.mult).then_inc(scaled, 1)
            nc.vector.tensor_scalar(h[0:NS, NT, :], h[0:NS, NT, :], ALPHA, None, ALU.mult).then_inc(scaled, 1)
            dve.wait_ge(scaled, 2)

            def body(j, u, first):
                e = j * 2 + u
                dve.wait_ge(loaded[u], (j + 1) * 64)
                for n in range(UP):
                    f, grp = unit_up(n)
                    t = slice(grp * GT, (grp + 1) * GT)
                    dve.wait_ge(sig, e * UP + n + 1)
                    x = sg[:, n % 2, :]
                    nc.vector.tensor_tensor(x, ps[2 * (n % 2) + 1][:, 0:GT], x, ALU.mult).then_inc(half, 1)
                    dve.wait_ge(half, e * UP + n + 1)
                    nc.vector.tensor_tensor(actT[:, u, f, t], x, cb[:, u, t], ALU.mult).then_inc(acts, 1)
                for n in range(DN):
                    i, q = n // 2, n % 2
                    r = rows(i)
                    dve.wait_ge(down, e * DN + n + 1)
                    if not first:
                        dve.wait_ge(added, e * DN + n + 1 - DN)
                    x = h[0:r, i, q * 512:(q + 1) * 512]
                    nc.vector.tensor_tensor(x, ps[4 + n % 4][0:r, :], x, ALU.add).then_inc(added, 1)

            body(0, 0, True)
            body(0, 1, False)
            with dve.Fori(1, NE // 2) as j:
                for u in range(2):
                    body(j, u, False)
            dve.wait_ge(ln_in, 32)
            for i in range(TILES):
                dve.wait_ge(added, (NE - 1) * DN + 2 * i + 2)
                if i >= 2:
                    dve.wait_ge(rstd_ok, i - 1)
                ln_stats(nc, link, h, i, c.st[:, i % 2, :], c.mv[:, i % 2, :]).then_inc(stats, 1)
                dve.wait_ge(stats, i + 1)
                dve.wait_ge(rstd_ok, i + 1)
                ln_apply(nc, link, h, i, c.mv[:, i % 2, :], c.rstd[:, i % 2, :], g, b).then_inc(normed, 1)


def build(nc, T, O):
    with ExitStack() as ctx:
        c = setup(nc, ctx, T, O)
        c.combine_dram = nc.dram_tensor("combine", (NE, TOK), F32, kind="Internal").ap()
        stage_entry(c)
        stage_features(c)
        stage_gate_and_pool(c)
        stage_stick_prompt(c)
        stage_stick_sample(c)
        stage_delta_inputs(c)
        stage_delta(c)
        c.renew_semaphores()
        c.res_at = 0
        stage_residual(c, "o", c.hT, 'w_out', 'ln1_g', 'ln1_b', True)
        stage_memory(c)
        stage_queries(c)
        stage_cross(c)
        c.res_at = 4096 + KC * TOK
        stage_residual(c, "w", c.qXT, 'xa_wo', 'ln2_g', 'ln2_b', True)
        stage_route(c)
        stage_experts(c)


def kernel(**inputs):
    import numpy as _np
    import concourse.bacc as _bacc
    from concourse import mybir as _mybir
    from concourse.bass_utils import run_bass_kernel_spmd as _run

    nc = _bacc.Bacc("TRN2", target_bir_lowering=False, num_devices=1)
    arrays, T, O = {}, {}, {}
    for name in _INS:
        a = _np.ascontiguousarray(inputs[name])
        arrays[f"in_{name}_dram"] = a
        T[name] = nc.dram_tensor(f"in_{name}_dram", a.shape, _mybir.dt.from_np(a.dtype), kind="ExternalInput").ap()
    for key, blocks in (('const_tables', CONSTS), ('pool_tables', POOL_CONSTS)):
        table = _np.concatenate(list(blocks.values()), axis=1)
        arrays[f"{key}_dram"] = table
        T[key] = nc.dram_tensor(f"{key}_dram", table.shape, F32, kind="ExternalInput").ap()
    ties = _np.tile((_np.arange(4)[None, :] < _np.arange(4)[:, None]).reshape(1, 16), (P, 1)).astype(_np.float32)
    arrays["tie_table_dram"] = ties
    T['tie_table'] = nc.dram_tensor("tie_table_dram", ties.shape, F32, kind="ExternalInput").ap()
    for name, shape in _OUTS:
        O[name] = nc.dram_tensor(f"out_{name}_dram", shape, F32, kind="ExternalOutput").ap()
    build(nc, T, O)
    r = _run(nc, [arrays], core_ids=[0])
    return tuple(r.results[0][f"out_{name}_dram"] for name, _ in _OUTS)
```

```python
from contextlib import ExitStack

import numpy as np
import concourse.bass as bass
from concourse import mybir

F32 = mybir.dt.float32
I32 = mybir.dt.int32
ALU = mybir.AluOpType
ACT = mybir.ActivationFunctionType
AX = mybir.AxisListType.X

P = 128
D = 1024
KC = D // P
SEQ = 1024
NT = SEQ // P
DB, DS = 8, 4
NS = DB * DS
TOK = SEQ + NS
TILES = NT + 1
GRP = 3
GT = TOK // GRP
PAGE = 128
NPG = 2
HEADS = 4
DH = 64
CH = 64
POOLB = 15
WINDOWS = (2, 4, 8, 16)
NMEM = 256
XDH = 256
NE = 16
DE = 256
MOE_TILES = (2 * TOK - NE) // P + NE
ALPHA = float(2 ** 0.25)
LN_EPS = 1e-5
QA, KA, VA, UB, VB, XC, QKV, ZG, BD = 0, 256, 512, 768, 1024, 1280, 1536, 2304, 2560

EXPLN = "natural_log_exp_and_others"


def rows(i):
    return P if i < NT else NS


def const_blocks():
    p = np.arange(P)[:, None]
    f = np.arange(P)[None, :]
    one = np.ones((P, P))
    chunk = p // CH == f // CH
    blk4 = p // DS == f // DS
    c = {
        "ident": p == f,
        "ones": one,
        "cum64": (p <= f) & chunk,
        "low64": (p > f) & chunk,
        "blk64": chunk,
        "negsuf": -1.0 * (p >= f),
        "negone": -one,
        "before": p < f,
        "upto": p <= f,
        "cum4": (p <= f) & blk4,
        "low4": (p > f) & blk4,
        "blk4": blk4,
        "before4": (p < f) & blk4,
        "rep4": np.where((p < DS) & (f % DS == p), 1.0, 0.0),
        "up1": (f % 2 == 1) & (p == f - 1),
    }
    for b in (1, 2, 4, 8, 16, 32):
        c[f"lvl{b}"] = (p // (2 * b) == f // (2 * b)) & ((p // b) % 2 == 1) & ((f // b) % 2 == 0)
    return {k: np.asarray(v, np.float32) for k, v in c.items()}


def pool_blocks():
    p = np.arange(P)[:, None]
    f = np.arange(P)[None, :]
    blk4 = p // DS == f // DS
    c = {}
    for g, w in enumerate(WINDOWS):
        c[f"band{g}"] = ((p <= f) & (p > f - w)) / w - 1.0 * (p == f)
        c[f"bandprev{g}"] = (p > f - w + P) / w
        c[f"bandfirst{g}"] = ((p <= f) & (p > f - w)) / np.minimum(f + 1, w) - 1.0 * (p == f)
        b_, q_ = p // POOLB, p % POOLB
        c[f"spool{g}"] = ((b_ == f // DS) & (q_ >= POOLB + 1 + f % DS - w) & (p < DB * POOLB) & (f < NS)) / w
        c[f"scur{g}"] = (blk4 & (p <= f) & (p > f - w)) / w - 1.0 * (p == f)
    return {k: np.asarray(v, np.float32) for k, v in c.items()}


CONSTS = const_blocks()
POOL_CONSTS = pool_blocks()
CONST_AT = {k: n * P for n, k in enumerate(CONSTS)}
POOL_AT = {k: n * P for n, k in enumerate(POOL_CONSTS)}
NCONST = len(CONSTS) * P


def route_blocks():
    p = np.arange(P)[:, None]
    row = lambda x: np.tile(np.asarray(x).reshape(1, -1), (P, 1))
    token = p + P * np.arange(TILES)[None, :]
    c = {
        "tie": row(np.arange(4)[None, :] < np.arange(4)[:, None]),
        "iota128": row(np.arange(P)),
        "iota32": row(np.arange(MOE_TILES)),
        "thr9": row(P * np.arange(9)),
        "tri16": row(np.arange(NE)[None, :] < np.arange(NE)[:, None]),
        "token": np.where(token < TOK, token, 0),
        "valid": token < TOK,
    }
    return {k: np.asarray(v, np.float32) for k, v in c.items()}


ROUTE_CONSTS = route_blocks()
ROUTE_AT, NROUTE = {}, 0
for _name, _block in ROUTE_CONSTS.items():
    ROUTE_AT[_name] = NROUTE
    NROUTE += _block.shape[1]

_INS = ['x_prompt', 'x_sample', 'cache_sb_k', 'cache_sb_v', 'state_pool', 'state_conv', 'state_delta',
        'cache_mem_k', 'cache_mem_v', 'page_table', 'mem_prompt', 'ln0_g', 'ln0_b', 'w_in', 'sb_bias',
        'gmlp_ln_g', 'gmlp_ln_b', 'gmlp_ws', 'gmlp_bs', 'pool_w', 'pool_gamma', 'conv_w', 'dn_a_log',
        'dn_dt_bias', 'dn_norm_g', 'w_out', 'ln1_g', 'ln1_b', 'xa_wq', 'xa_wk', 'xa_wv', 'xa_wo', 'ln2_g',
        'ln2_b', 'w_router', 'router_bias', 'ex_wg', 'ex_wu', 'ex_wd', 'ln3_g', 'ln3_b']
_OUTS = [('y_prompt', (1, SEQ, D)), ('y_sample', (DB, DS, D)),
         ('sb_k_prompt', (1, 1, SEQ, HEADS, DH)), ('sb_v_prompt', (1, 1, SEQ, HEADS, DH)),
         ('sb_k_sample', (1, DB, DS, HEADS, DH)), ('sb_v_sample', (1, DB, DS, HEADS, DH)),
         ('gmlp_v_sample', (1, DB, DS, 256)),
         ('pool_prompt', (1, 1, POOLB, 256)), ('pool_sample', (1, DB, POOLB, 256)),
         ('conv_prompt', (1, 1, 3, 768)), ('conv_sample', (1, DB, 3, 768)),
         ('delta_prompt', (1, 1, HEADS, DH, DH)), ('delta_sample', (1, DB, HEADS, DH, DH)),
         ('mem_k_prompt', (1, 1, NMEM, HEADS, XDH)), ('mem_v_prompt', (1, 1, NMEM, HEADS, XDH))]


class Chain:

    def __init__(self, eng, sem):
        self.eng, self.sem, self.n = eng, sem, 0

    def __call__(self, ins):
        self.n += 1
        ins.then_inc(self.sem, 1)
        self.eng.wait_ge(self.sem, self.n)


class Ctx:
    pass


def setup(nc, ctx, T, O):
    c = Ctx()
    c.nc, c.T, c.O = nc, T, O

    held, stack = [], [ctx.enter_context(ExitStack())]

    def sem(name):
        held.append(stack[0].enter_context(nc.semaphore(name)))
        return held[-1]

    def renew_semaphores():
        with nc.Block() as block:
            @block.sync
            def _(sp):
                for x in held:
                    sp.sem_clear(x)
        held.clear()
        stack[0].close()
        stack[0] = ctx.enter_context(ExitStack())

    c.sem, c.renew_semaphores = sem, renew_semaphores
    c.ps = [ctx.enter_context(nc.psum_tensor(f"bank{b}", [P, 512], F32)) for b in range(8)]
    c.const = ctx.enter_context(nc.sbuf_tensor("const", [P, NCONST], F32))
    c.h = ctx.enter_context(nc.sbuf_tensor("h", [P, TILES, D], F32))
    c.hT = ctx.enter_context(nc.sbuf_tensor("hT", [P, KC, TOK], F32))
    c.small = ctx.enter_context(nc.sbuf_tensor("small", [P, 1024], F32))
    AR = 29200
    c.arena = ctx.enter_context(nc.sbuf_tensor("arena", [P, AR], F32))
    c.at = {}
    c.small_used = 0

    def K(name, r=P, w=P):
        a = CONST_AT[name]
        return c.const[0:r, a:a + w]

    c.K = K

    def place(**sizes):
        at = sizes.pop("start", 0)
        for k, n in sizes.items():
            assert at + n <= AR, (k, at, n)
            c.at[k] = (at, n)
            at += n
        return at

    def A(k):
        a, n = c.at[k]
        return c.arena[:, a:a + n]

    c.place, c.A = place, A

    def small(n):
        a = c.small_used
        c.small_used += n
        assert c.small_used <= 1024
        return c.small[:, a:a + n]

    c.new_small = small
    c.slot = ctx.enter_context(nc.sbuf_tensor("slot", [P, 2 * TILES], I32))
    c.row_token = ctx.enter_context(nc.sbuf_tensor("row_token", [P, MOE_TILES], I32))
    c.tile_expert = ctx.enter_context(nc.sbuf_tensor("tile_expert", [1, MOE_TILES], I32))
    c.gate, c.off = small(2 * TILES), small(2)
    c.ids = ctx.enter_context(nc.sbuf_tensor("page_ids", [1, DB * NPG], I32))
    return c


def row_bc(ap, n=P):
    return ap.partition_broadcast(n)


def x_tile(T, i):
    if i < NT:
        return T['x_prompt'][0, i * P:(i + 1) * P, :]
    return T['x_sample'].rearrange("b t d -> (b t) d")


def ln_stats(nc, link, h, i, st, mv):
    r = rows(i)
    nc.vector.bn_stats(st[0:r, 0:6], h[0:r, i, 0:512])
    link(nc.vector.bn_stats(st[0:r, 6:12], h[0:r, i, 512:1024]))
    return nc.vector.bn_aggr(mv[0:r, :], st[0:r, :])


def ln_rstd(nc, link, i, mv, rstd, eps):
    r = rows(i)
    link(nc.scalar.activation(rstd[0:r, :], mv[0:r, 1:2], ACT.Ln, bias=eps[0:r, :]))
    return nc.scalar.activation(rstd[0:r, :], rstd[0:r, :], ACT.Exp, scale=-0.5)


def ln_apply(nc, link, h, i, mv, rstd, g, b):
    r = rows(i)
    link(nc.vector.tensor_scalar(h[0:r, i, :], h[0:r, i, :], mv[0:r, 0:1], rstd[0:r, :],
                                 ALU.subtract, ALU.mult))
    link(nc.vector.tensor_tensor(h[0:r, i, :], h[0:r, i, :], g[0:r, :], ALU.mult))
    return nc.vector.tensor_tensor(h[0:r, i, :], h[0:r, i, :], b[0:r, :], ALU.add)


def stage_entry(c):
    nc, T, O, K = c.nc, c.T, c.O, c.K
    c.free_at = c.place(kT=2 * TOK, vtok=TILES * 256, zT=2 * TOK)
    c.after_q = c.place(start=c.free_at, qkvT=6 * TOK, qT=2 * TOK)
    at = c.place(start=c.after_q, vg=TILES * 256, xc=TILES * 256, uT=2 * TOK)
    c.place(start=c.free_at, wtok=KC * 1032)
    c.place(start=at, lng=D, lnb=D, ktok=2 * 256)
    c.scratch = at
    kT = c.A("kT").rearrange("p (c t) -> p c t", c=2)
    vtok = c.A("vtok").rearrange("p (i n) -> p i n", i=TILES)
    vg = c.A("vg").rearrange("p (i n) -> p i n", i=TILES)
    xc = c.A("xc").rearrange("p (i n) -> p i n", i=TILES)
    wt = c.A("wtok").rearrange("p (k n) -> p k n", k=KC)
    ktok = c.A("ktok").rearrange("p (s n) -> p s n", s=2)
    g, b = c.A("lng"), c.A("lnb")
    c.kT, c.vtok, c.vg, c.xc = kT, vtok, vg, xc
    c.ba = c.new_small(TILES * 8).rearrange("p (i n) -> p i n", i=TILES)
    c.st = c.new_small(2 * 12).rearrange("p (s n) -> p s n", s=2)
    c.mv = c.new_small(2 * 2).rearrange("p (s n) -> p s n", s=2)
    c.rstd = c.new_small(2).rearrange("p (s n) -> p s n", s=2)
    c.eps = c.new_small(1)
    h, hT, ps = c.h, c.hT, c.ps

    s = c.sem
    x_in, w_in, const_in, ln_in = s("e_x"), s("e_w"), s("e_const"), s("e_ln")
    eps_set, stats, rstd_ok, normed = s("e_eps"), s("e_stats"), s("e_rstd"), s("e_normed")
    turned, hT_ok, proj_kv, proj_vx, proj_ba = s("e_turned"), s("e_hT"), s("e_kv"), s("e_vx"), s("e_ba")
    kv_out, vx_out, ba_out, k_turned, kT_ok = s("e_kvo"), s("e_vxo"), s("e_bao"), s("e_kt"), s("e_kTo")
    stored = [s("e_stored0"), s("e_stored1")]
    dve_chain, act_chain, zeroed = s("e_dve"), s("e_act"), s("e_zero")
    w_view = T['w_in'][0].rearrange("(k p) n -> p k n", p=P)

    with nc.Block() as block:
        @block.sync
        def _(sp):
            for i in range(TILES):
                sp.dma_start(h[0:rows(i), i, :], x_tile(T, i)).then_inc(x_in, 16)
                if i == 0:
                    sp.dma_start(g, row_bc(T['ln0_g'])).then_inc(ln_in, 16)
                    sp.dma_start(b, row_bc(T['ln0_b'])).then_inc(ln_in, 16)
                if i == 1:
                    sp.dma_start(wt[:, :, 0:512], w_view[:, :, KA:KA + 512]).then_inc(w_in, 16)
                    sp.dma_start(wt[:, :, 512:1024], w_view[:, :, VB:VB + 512]).then_inc(w_in, 16)
                    sp.dma_start(wt[:, :, 1024:1032], w_view[:, :, BD:BD + 8]).then_inc(w_in, 16)
            for i in range(TILES):
                sp.wait_ge(kv_out, 2 * i + 2)
                if i < NT:
                    ko = O['sb_k_prompt'][0, 0, i * P:(i + 1) * P].rearrange("t h d -> t (h d)")
                    vo = O['sb_v_prompt'][0, 0, i * P:(i + 1) * P].rearrange("t h d -> t (h d)")
                else:
                    ko = O['sb_k_sample'][0].rearrange("b t h d -> (b t) (h d)")
                    vo = O['sb_v_sample'][0].rearrange("b t h d -> (b t) (h d)")
                sp.dma_start(ko, ktok[0:rows(i), i % 2, :]).then_inc(stored[i % 2], 16)
                sp.dma_start(vo, vtok[0:rows(i), i, :]).then_inc(stored[i % 2], 16)
            sp.wait_ge(stored[0], 32 * 5)
            sp.wait_ge(stored[1], 32 * 4)

        @block.vector
        def _(dve):
            link = Chain(dve, dve_chain)
            nc.vector.memset(c.eps, LN_EPS).then_inc(eps_set, 1)
            nc.vector.memset(vg[:, NT, :], 0.0).then_inc(zeroed, 1)
            nc.vector.memset(c.ba[:, NT, :], 0.0).then_inc(zeroed, 1)
            dve.wait_ge(zeroed, 2)

            def evac_ba(i):
                dve.wait_ge(proj_ba, i + 1)
                nc.vector.tensor_copy(c.ba[0:rows(i), i, :], ps[4][0:rows(i), 0:8]).then_inc(ba_out, 1)

            for i in range(TILES):
                dve.wait_ge(x_in, 16 * TILES)
                if i >= 2:
                    dve.wait_ge(rstd_ok, i - 1)
                ln_stats(nc, link, h, i, c.st[:, i % 2, :], c.mv[:, i % 2, :]).then_inc(stats, 1)
                if i == 0:
                    dve.wait_ge(ln_in, 32)
                dve.wait_ge(stats, i + 1)
                dve.wait_ge(rstd_ok, i + 1)
                ln_apply(nc, link, h, i, c.mv[:, i % 2, :], c.rstd[:, i % 2, :], g, b).then_inc(normed, 1)
                if i >= 1:
                    evac_ba(i - 1)
            evac_ba(TILES - 1)

        @block.scalar
        def _(act):
            link = Chain(act, act_chain)
            act.dma_start(c.const[:, :], T['const_tables']).then_inc(const_in, 16)
            act.wait_ge(eps_set, 1)
            act.wait_ge(zeroed, 2)

            def evac(i):
                r = rows(i)
                act.wait_ge(proj_kv, i + 1)
                if i >= 2:
                    act.wait_ge(k_turned, i - 1)
                    act.wait_ge(stored[i % 2], 32 * (i // 2))
                nc.scalar.copy(ktok[0:r, i % 2, :], ps[2 + 4 * (i % 2)][0:r, 0:256]).then_inc(kv_out, 1)
                nc.scalar.copy(vtok[0:r, i, :], ps[2 + 4 * (i % 2)][0:r, 256:512]).then_inc(kv_out, 1)
                act.wait_ge(proj_vx, i + 1)
                nc.scalar.activation(vg[0:r, i, :], ps[3 + 4 * (i % 2)][0:r, 0:256],
                                     ACT.Gelu_apprx_tanh).then_inc(vx_out, 1)
                nc.scalar.copy(xc[0:r, i, :], ps[3 + 4 * (i % 2)][0:r, 256:512]).then_inc(vx_out, 1)

            def evac_kT(i):
                r = rows(i)
                act.wait_ge(k_turned, i + 1)
                nc.scalar.copy(kT[:, :, i * P:i * P + r],
                               ps[5][:, 0:2 * r].rearrange("p (c t) -> p c t", c=2)).then_inc(kT_ok, 1)

            for i in range(TILES + 2):
                if i < TILES:
                    r = rows(i)
                    act.wait_ge(stats, i + 1)
                    if i >= 2:
                        act.wait_ge(normed, i - 1)
                    nc.scalar.preload_act_table_set(EXPLN)
                    ln_rstd(nc, link, i, c.mv[:, i % 2, :], c.rstd[:, i % 2, :], c.eps).then_inc(rstd_ok, 1)
                    for q in range(2):
                        act.wait_ge(turned, 2 * i + q + 1)
                        nc.scalar.copy(hT[:, 4 * q:4 * q + 4, i * P:i * P + r],
                                       ps[q][:, 0:4 * r].rearrange("p (k t) -> p k t", k=4)).then_inc(hT_ok, 1)
                if 1 <= i <= TILES:
                    evac(i - 1)
                if i >= 2:
                    evac_kT(i - 2)

        @block.tensor
        def _(pe):
            pe.wait_ge(const_in, 16)

            def turn(i):
                r = rows(i)
                pe.wait_ge(normed, i + 1)
                for q in range(2):
                    if i >= 1:
                        pe.wait_ge(hT_ok, 2 * (i - 1) + q + 1)
                    for k in range(4):
                        last = nc.tensor.transpose(ps[q][:, k * r:(k + 1) * r],
                                                   h[0:r, i, (4 * q + k) * P:(4 * q + k + 1) * P], K("ident", r, r))
                    last.then_inc(turned, 1)

            def project(i):
                r = rows(i)
                pe.wait_ge(hT_ok, 2 * i + 2)
                for bank, col, n, out_sem, free in ((2 + 4 * (i % 2), 0, 512, proj_kv, kv_out),
                                                    (3 + 4 * (i % 2), 512, 512, proj_vx, vx_out),
                                                    (4, 1024, 8, proj_ba, ba_out)):
                    if bank == 4:
                        if i >= 1:
                            pe.wait_ge(free, i)
                    elif i >= 2:
                        pe.wait_ge(free, 2 * (i - 1))
                    for k in range(KC):
                        last = nc.tensor.matmul(ps[bank][0:r, 0:n], hT[:, k, i * P:i * P + r],
                                                wt[:, k, col:col + n], start=(k == 0), stop=(k == KC - 1))
                    last.then_inc(out_sem, 1)

            def turn_k(i):
                r = rows(i)
                pe.wait_ge(kv_out, 2 * i + 1)
                if i >= 1:
                    pe.wait_ge(kT_ok, i)
                for q in range(2):
                    last = nc.tensor.transpose(ps[5][:, q * r:(q + 1) * r], ktok[0:r, i % 2, q * P:(q + 1) * P],
                                               K("ident", r, r))
                last.then_inc(k_turned, 1)

            turn(0)
            pe.wait_ge(w_in, 48)
            for i in range(TILES):
                if i + 1 < TILES:
                    turn(i + 1)
                project(i)
                if i >= 1:
                    turn_k(i - 1)
            turn_k(TILES - 1)


def stage_features(c):
    nc, T, O, K = c.nc, c.T, c.O, c.K
    c.place(start=c.scratch, ring=4 * KC * P, vsq=TILES * 256, glng=256, glnb=256)
    ring = c.A("ring").rearrange("p (s k n) -> p s k n", s=4, k=KC)
    qT = c.A("qT").rearrange("p (c t) -> p c t", c=2)
    uT = c.A("uT").rearrange("p (c t) -> p c t", c=2)
    zT = c.A("zT").rearrange("p (c t) -> p c t", c=2)
    qkvT = c.A("qkvT").rearrange("p (c t) -> p c t", c=6)
    c.qT, c.uT, c.zT, c.qkvT = qT, uT, zT, qkvT
    hT, ps = c.hT, c.ps
    plan = ([(UB + P * n, uT[:, n], "gelu") for n in range(2)] + [(ZG + P * n, zT[:, n], "silu") for n in range(2)]
            + [(QA + P * n, qT[:, n], "scale") for n in range(2)] + [(QKV + P * n, qkvT[:, n], "copy") for n in range(6)])
    s = c.sem
    w_in = [s(f"f_w{n}") for n in range(4)]
    ln_in, product, evacuated = s("f_ln"), s("f_prod"), s("f_evac")
    stats, rstd_ok, normed, stored = s("f_stats"), s("f_rstd"), s("f_normed"), s("f_stored")
    dve_chain, act_chain = s("f_dve"), s("f_act")
    w_view = T['w_in'][0].rearrange("(k p) n -> p k n", p=P)
    vg = c.vg.rearrange("p i (g d) -> p (i g) d", g=HEADS)
    vsq = c.A("vsq").rearrange("p (m d) -> p m d", d=DH)
    mom = c.new_small(2 * TILES * HEADS).rearrange("p (s n) -> p s n", s=2)
    NG = TILES * HEADS

    with nc.Block() as block:
        @block.sync
        def _(sp):
            for n, (col, _, _) in enumerate(plan):
                if n >= 4:
                    sp.wait_ge(product, GRP * (n - 3))
                sp.dma_start(ring[:, n % 4], w_view[:, :, col:col + P]).then_inc(w_in[n % 4], 16)
                if n == 0:
                    sp.dma_start(c.A("glng"), row_bc(T['gmlp_ln_g'][0].rearrange("g d -> (g d)"))).then_inc(ln_in, 16)
                    sp.dma_start(c.A("glnb"), row_bc(T['gmlp_ln_b'][0].rearrange("g d -> (g d)"))).then_inc(ln_in, 16)
            sp.wait_ge(normed, 1)
            sp.dma_start(O['gmlp_v_sample'][0].rearrange("b t n -> (b t) n"), c.vg[0:NS, NT, :]).then_inc(stored, 16)
            sp.wait_ge(stored, 16)

        @block.tensor
        def _(pe):
            for n in range(len(plan)):
                pe.wait_ge(w_in[n % 4], 16 * (n // 4 + 1))
                for g in range(GRP):
                    u = GRP * n + g
                    if u >= 8:
                        pe.wait_ge(evacuated, u - 7)
                    for k in range(KC):
                        last = nc.tensor.matmul(ps[u % 8][:, 0:GT], ring[:, n % 4, k, :], hT[:, k, g * GT:(g + 1) * GT],
                                                start=(k == 0), stop=(k == KC - 1))
                    last.then_inc(product, 1)

        @block.scalar
        def _(act):
            link = Chain(act, act_chain)
            for n, (_, dst, how) in enumerate(plan):
                for g in range(GRP):
                    u = GRP * n + g
                    act.wait_ge(product, u + 1)
                    o, i = dst[:, g * GT:(g + 1) * GT], ps[u % 8][:, 0:GT]
                    if how == "gelu":
                        ins = nc.scalar.activation(o, i, ACT.Gelu_apprx_tanh)
                    elif how == "silu":
                        ins = nc.scalar.activation(o, i, ACT.Silu)
                    elif how == "scale":
                        ins = nc.scalar.mul(o, i, DH ** -0.5)
                    else:
                        ins = nc.scalar.copy(o, i)
                    ins.then_inc(evacuated, 1)
            nc.scalar.preload_act_table_set(EXPLN)
            act.wait_ge(stats, 1)
            link(nc.scalar.activation(mom[:, 1, :], mom[:, 1, :], ACT.Ln, bias=c.eps, scale=1.0 / DH))
            nc.scalar.activation(mom[:, 1, :], mom[:, 1, :], ACT.Exp, scale=-0.5).then_inc(rstd_ok, 1)

        @block.vector
        def _(dve):
            link = Chain(dve, dve_chain)

            def bc(row):
                return row.unsqueeze(2).to_broadcast([P, NG, DH])

            link(nc.vector.tensor_reduce(mom[:, 0, :], vg, AX, ALU.add))
            link(nc.vector.tensor_scalar(mom[:, 0, :], mom[:, 0, :], 1.0 / DH, None, ALU.mult))
            link(nc.vector.tensor_tensor(vg, vg, bc(mom[:, 0, :]), ALU.subtract))
            link(nc.vector.tensor_tensor(vsq, vg, vg, ALU.mult))
            nc.vector.tensor_reduce(mom[:, 1, :], vsq, AX, ALU.add).then_inc(stats, 1)
            dve.wait_ge(rstd_ok, 1)
            link(nc.vector.tensor_tensor(vg, vg, bc(mom[:, 1, :]), ALU.mult))
            dve.wait_ge(ln_in, 32)
            link(nc.vector.tensor_tensor(c.vg, c.vg, c.A("glng").unsqueeze(1).to_broadcast([P, TILES, 256]), ALU.mult))
            nc.vector.tensor_tensor(c.vg, c.vg, c.A("glnb").unsqueeze(1).to_broadcast([P, TILES, 256]),
                                    ALU.add).then_inc(normed, 1)


def stage_gate_and_pool(c):
    nc, T, O, K = c.nc, c.T, c.O, c.K
    c.place(start=c.scratch, ws=HEADS * P, wsT=HEADS * P, wsS=HEADS * NS, bs=512, bsb=2 * P, bsbS=2 * NS,
            bands=len(POOL_CONSTS) * P, prev=256, pw=2 * P, gam=2, dT=2 * 256, mix=256, ws4=128)
    ws = c.A("ws").rearrange("p (g s) -> p g s", g=HEADS)
    wsT = c.A("wsT").rearrange("p (g s) -> p g s", g=HEADS)
    wsS = c.A("wsS").rearrange("p (g s) -> p g s", g=HEADS)
    ws4 = c.A("ws4").rearrange("p (g s) -> p g s", g=HEADS)
    bsb = c.A("bsb").rearrange("p (c s) -> p c s", c=2)
    bsbS = c.A("bsbS").rearrange("p (c s) -> p c s", c=2)
    pw = c.A("pw").rearrange("p (c s) -> p c s", c=2)
    dT = c.A("dT").rearrange("p (s n) -> p s n", s=2)
    mix = c.A("mix")
    bands, prev, gam = c.A("bands"), c.A("prev"), c.A("gam")
    ps, oT, xc, vg, uT = c.ps, c.hT, c.xc, c.vg, c.uT

    def band(name, r=P, w=P):
        return bands[0:r, POOL_AT[name]:POOL_AT[name] + w]

    s = c.sem
    loaded, zeroed, stored = s("g_load"), s("g_zero"), s("g_stored")
    small_mm, small_ev, mixed, mixed_used = s("g_smm"), s("g_sev"), s("g_mixed"), s("g_mixused")
    diff, diff_ok, pooled, pooled_used, dve_chain = s("g_diff"), s("g_diffok"), s("g_pooled"), s("g_poolused"), s("g_dve")
    LOADS = 8 + HEADS

    with nc.Block() as block:
        @block.gpsimd
        def _(pool):
            nc.gpsimd.memset(pw, 0.0).then_inc(zeroed, 1)

        @block.sync
        def _(sp):
            sp.dma_start(ws, T['gmlp_ws'][0].rearrange("g t s -> t g s")).then_inc(loaded, 16)
            sp.dma_start(c.A("bs")[0:1, :], T['gmlp_bs'].rearrange("a g s -> a (g s)")).then_inc(loaded, 16)
            sp.dma_start(bands, T['pool_tables']).then_inc(loaded, 16)
            sp.dma_start(prev[0:DB * POOLB, :], T['state_pool'][0].rearrange("b q n -> (b q) n")).then_inc(loaded, 16)
            for n in range(2):
                sp.dma_start(gam[:, n:n + 1], T['pool_gamma'][0, n * P:(n + 1) * P].unsqueeze(1)).then_inc(loaded, 16)
            sp.wait_ge(zeroed, 1)
            for g in range(HEADS):
                q = (g % 2) * DH
                sp.dma_start(pw[q:q + DH, g // 2, q:q + DH], T['pool_w'][0, g]).then_inc(loaded, 16)
            sp.dma_start(O['pool_prompt'][0, 0], xc[P - POOLB:P, NT - 1, :]).then_inc(stored, 16)
            sp.dma_start(O['pool_sample'][0, :, 0:POOLB - DS, :], T['state_pool'][0, :, DS:POOLB, :]).then_inc(stored, 16)
            for b in range(DB):
                sp.dma_start(O['pool_sample'][0, b, POOLB - DS:POOLB, :], xc[b * DS:(b + 1) * DS, NT, :]).then_inc(stored, 16)
            sp.wait_ge(stored, 16 * (2 + DB))

        @block.tensor
        def _(pe):
            pe.wait_ge(loaded, 16 * 10)
            for g in range(HEADS):
                last = nc.tensor.transpose(ps[0][:, g * P:(g + 1) * P], ws[:, g, :], K("ident"))
            last.then_inc(small_mm, 1)
            for g in range(HEADS):
                q = (g % 2) * DH
                last = nc.tensor.matmul(ps[1][q:q + DH, (g // 2) * P:(g // 2 + 1) * P], K("ones", 1, DH),
                                        c.A("bs")[0:1, g * P:(g + 1) * P], start=True, stop=True)
            last.then_inc(small_mm, 1)
            for g in range(HEADS):
                last = nc.tensor.matmul(ps[2][0:DS, g * NS:(g + 1) * NS], ws[0:DS, g, 0:DS], K("rep4", DS, NS),
                                        start=True, stop=True)
            last.then_inc(small_mm, 1)
            pe.wait_ge(small_ev, 3)
            last = nc.tensor.matmul(ps[3][0:NS, 0:4 * NS], K("rep4", DS, NS), ws4[0:DS].rearrange("p g s -> p (g s)"),
                                    start=True, stop=True)
            last.then_inc(small_mm, 1)
            pe.wait_ge(small_ev, 5)

            def mixes(i):
                r = rows(i)
                if i >= 2:
                    pe.wait_ge(mixed_used, i - 1)
                for g in range(HEADS):
                    q = (g % 2) * DH
                    w = wsT[:, g, :] if i < NT else wsS[0:NS, g, :]
                    last = nc.tensor.matmul(ps[4 + i % 2][q:q + DH, (g // 2) * P:(g // 2) * P + r],
                                            vg[0:r, i, g * DH:(g + 1) * DH], w, start=True, stop=True)
                last.then_inc(mixed, 1)

            def diffs(i):
                r = rows(i)
                if i >= 1:
                    pe.wait_ge(diff_ok, i)
                for g in range(HEADS):
                    q = (g % 2) * DH
                    out = ps[6][q:q + DH, (g // 2) * P:(g // 2) * P + r]
                    x = xc[0:r, i, g * DH:(g + 1) * DH]
                    if i == 0:
                        last = nc.tensor.matmul(out, x, band(f"bandfirst{g}"), start=True, stop=True)
                    elif i < NT:
                        nc.tensor.matmul(out, x, band(f"band{g}"), start=True, stop=False)
                        last = nc.tensor.matmul(out, xc[:, i - 1, g * DH:(g + 1) * DH], band(f"bandprev{g}"),
                                                start=False, stop=True)
                    else:
                        nc.tensor.matmul(out, x, band(f"scur{g}", NS, NS), start=True, stop=False)
                        n = DB * POOLB
                        last = nc.tensor.matmul(out, prev[0:n, g * DH:(g + 1) * DH], band(f"spool{g}", n, NS),
                                                start=False, stop=True)
                last.then_inc(diff, 1)

            def pools(i):
                r = rows(i)
                pe.wait_ge(diff_ok, i + 1)
                if i >= 1:
                    pe.wait_ge(pooled_used, i)
                for n in range(2):
                    last = nc.tensor.matmul(ps[7][:, n * P:n * P + r], pw[:, n, :], dT[:, i % 2, n * P:n * P + r],
                                            start=True, stop=True)
                last.then_inc(pooled, 1)

            for i in range(TILES):
                mixes(i)
                diffs(i)
                pools(i)

        @block.vector
        def _(dve):
            link = Chain(dve, dve_chain)
            dve.wait_ge(small_mm, 1)
            nc.vector.tensor_tensor(wsT, ps[0][:, :].rearrange("p (g s) -> p g s", g=HEADS),
                                    K("upto").unsqueeze(1).to_broadcast([P, HEADS, P]), ALU.mult).then_inc(small_ev, 1)
            dve.wait_ge(small_mm, 2)
            nc.vector.tensor_copy(bsb, ps[1][:, 0:2 * P].rearrange("p (c s) -> p c s", c=2)).then_inc(small_ev, 1)
            dve.wait_ge(small_mm, 3)
            nc.vector.tensor_copy(ws4[0:DS], ps[2][0:DS, 0:4 * NS].rearrange("p (g s) -> p g s", g=HEADS)).then_inc(small_ev, 1)
            dve.wait_ge(small_mm, 4)
            nc.vector.tensor_tensor(wsS[0:NS], ps[3][0:NS, 0:4 * NS].rearrange("p (g s) -> p g s", g=HEADS),
                                    K("cum4", NS, NS).unsqueeze(1).to_broadcast([NS, HEADS, NS]), ALU.mult).then_inc(small_ev, 1)
            for n in range(2):
                last = nc.vector.tensor_copy(bsbS[:, n, :].rearrange("p (b t) -> p b t", b=DB),
                                             bsb[:, n, 0:DS].unsqueeze(1).to_broadcast([P, DB, DS]))
                if n == 0:
                    link(last)
            last.then_inc(small_ev, 1)
            dve.wait_ge(small_ev, 5)
            for i in range(TILES):
                r = rows(i)
                dve.wait_ge(mixed, i + 1)
                m = mix.rearrange("p (c s) -> p c s", c=2)[:, :, 0:r]
                p = ps[4 + i % 2][:, 0:2 * P].rearrange("p (c s) -> p c s", c=2)[:, :, 0:r]
                if i >= 1:
                    dve.wait_ge(mixed_used, i)
                link(nc.vector.tensor_tensor(m, p, bsb if i < NT else bsbS, ALU.add))
                nc.vector.tensor_tensor(oT[:, 2:4, i * P:i * P + r], m, uT[:, :, i * P:i * P + r],
                                        ALU.mult).then_inc(mixed_used, 1)

        @block.scalar
        def _(act):
            act.wait_ge(loaded, 16 * 10)
            for i in range(TILES):
                r = rows(i)
                act.wait_ge(diff, i + 1)
                if i >= 2:
                    act.wait_ge(pooled, i - 1)
                nc.scalar.copy(dT[:, i % 2, :].rearrange("p (c s) -> p c s", c=2)[:, :, 0:r],
                               ps[6][:, 0:2 * P].rearrange("p (c s) -> p c s", c=2)[:, :, 0:r]).then_inc(diff_ok, 1)
                act.wait_ge(pooled, i + 1)
                for n in range(2):
                    last = nc.scalar.activation(oT[:, 4 + n, i * P:i * P + r], ps[7][:, n * P:n * P + r], ACT.Copy,
                                                scale=gam[:, n:n + 1])
                last.then_inc(pooled_used, 1)


def stage_stick_prompt(c):
    nc, K = c.nc, c.K
    c.place(start=c.after_q, qz=2 * 512, bias=512, zb=3 * 512, tmp=2 * 512, sp=3 * 512, att=2 * 512, ssum=3 * 512,
            sb=HEADS)

    def ring(name, n):
        return c.A(name).rearrange("p (s h q) -> p s h q", s=n, h=HEADS)

    qz, zb, tmp, sp_, att, ssum = ring("qz", 2), ring("zb", 3), ring("tmp", 2), ring("sp", 3), ring("att", 2), ring("ssum", 3)
    bias = c.A("bias").rearrange("p (h q) -> p h q", h=HEADS)
    c.bias = bias
    ps, oT, qT, kT, vtok = c.ps, c.hT, c.qT, c.kT, c.vtok
    steps = [(qb, kb) for qb in range(NT) for kb in range(qb, -1, -1)]
    N = len(steps)
    s = c.sem
    zeroed, q_ready, bias_in, bias_ok = s("a_zero"), s("a_q"), s("a_bin"), s("a_bias")
    score, zb_ok, soft, sp_ok, sum_ok, sums = s("a_score"), s("a_zb"), s("a_soft"), s("a_sp"), s("a_sumok"), s("a_sums")
    arg_ok, exp_ok, att_ok, pv, out_ok = s("a_arg"), s("a_exp"), s("a_att"), s("a_pv"), s("a_out")
    dve_chain, act_chain = s("a_dve"), s("a_act")
    last_of = [max(n for n, x in enumerate(steps) if x[0] == qb) for qb in range(NT)]

    def head4(bank):
        return ps[bank][:, :].rearrange("p (h q) -> p h q", h=HEADS)

    with nc.Block() as block:
        @block.sync
        def _(sp):
            sp.dma_start(c.A("sb"), row_bc(c.T['sb_bias'][0])).then_inc(bias_in, 16)

        @block.gpsimd
        def _(pool):
            nc.gpsimd.memset(c.A("qz"), 0.0).then_inc(zeroed, 1)
            pool.wait_ge(zeroed, 1)
            n = 0

            def stage_queries(qb):
                if qb >= 2:
                    pool.wait_ge(score, last_of[qb - 2] + 1)
                t = slice(qb * P, (qb + 1) * P)
                nc.gpsimd.tensor_copy(qz[0:DH, qb % 2, 0:4:2, :], qT[0:DH, :, t]).then_inc(q_ready, 1)
                pool.wait_ge(q_ready, 2 * qb + 1)
                nc.gpsimd.tensor_copy(qz[DH:P, qb % 2, 1:4:2, :], qT[DH:P, :, t]).then_inc(q_ready, 1)
                pool.wait_ge(q_ready, 2 * qb + 2)

            stage_queries(0)
            for qb in range(NT):
                if qb + 1 < NT:
                    stage_queries(qb + 1)
                for j in range(qb + 1):
                    pool.wait_ge(sp_ok, n + 1)
                    if n >= 2:
                        pool.wait_ge(sums, n - 1)
                    if j == 0:
                        nc.gpsimd.tensor_copy(ssum[:, n % 3], sp_[:, n % 3]).then_inc(sum_ok, 1)
                    else:
                        nc.gpsimd.tensor_tensor(ssum[:, n % 3], ssum[:, (n - 1) % 3], sp_[:, n % 3],
                                                ALU.add).then_inc(sum_ok, 1)
                    n += 1
                    pool.wait_ge(sum_ok, n)

        @block.tensor
        def _(pe):
            def scores(n):
                qb, kb = steps[n]
                pe.wait_ge(q_ready, 2 * qb + 2)
                if n >= 2:
                    pe.wait_ge(zb_ok, n - 1)
                for pair in range(2):
                    last = nc.tensor.matmul(ps[n % 2][:, pair * 256:(pair + 1) * 256], kT[:, pair, kb * P:(kb + 1) * P],
                                            qz[:, qb % 2, 2 * pair:2 * pair + 2, :].rearrange("p h q -> p (h q)"),
                                            start=True, stop=True)
                last.then_inc(score, 1)

            def suffix(n):
                qb, kb = steps[n]
                pe.wait_ge(sp_ok, n + 1)
                if n >= 2:
                    pe.wait_ge(arg_ok, n - 1)
                flat = "p h q -> p (h q)"
                last = nc.tensor.matmul(ps[2 + n % 2][:, :], K("negsuf"), sp_[:, n % 3].rearrange(flat),
                                        start=True, stop=(kb == qb))
                if kb < qb:
                    pe.wait_ge(sum_ok, n)
                    last = nc.tensor.matmul(ps[2 + n % 2][:, :], K("negone"), ssum[:, (n - 1) % 3].rearrange(flat),
                                            start=False, stop=True)
                last.then_inc(sums, 1)

            def values(n):
                qb, kb = steps[n]
                if kb == qb:
                    pe.wait_ge(att_ok, qb + 1)
                else:
                    pe.wait_ge(exp_ok, n + 1)
                if kb == qb and qb >= 2:
                    pe.wait_ge(out_ok, 2 * (qb - 1))
                for pair in range(2):
                    last = nc.tensor.matmul(ps[4 + qb % 2][:, pair * 256:(pair + 1) * 256],
                                            vtok[:, kb, pair * P:(pair + 1) * P],
                                            att[:, n % 2, 2 * pair:2 * pair + 2, :].rearrange("p h q -> p (h q)"),
                                            start=(kb == qb and pair == 0), stop=(kb == 0), skip_group_check=True)
                last.then_inc(pv, 1)

            for n in range(N + 2):
                if n < N:
                    scores(n)
                if 1 <= n <= N:
                    suffix(n - 1)
                if n >= 2:
                    values(n - 2)

        @block.scalar
        def _(act):
            link = Chain(act, act_chain)
            nc.scalar.preload_act_table_set(EXPLN)

            def softplus(n):
                act.wait_ge(zb_ok, n + 1)
                if n >= 2:
                    act.wait_ge(sp_ok, n - 1)
                t = tmp[:, n % 2]
                link(nc.scalar.activation(t, zb[:, n % 3], ACT.Abs))
                link(nc.scalar.activation(t, t, ACT.Exp, scale=-1.0))
                nc.scalar.activation(t, t, ACT.Ln, bias=1.0).then_inc(soft, 1)

            def weights(n):
                act.wait_ge(arg_ok, n + 1)
                if n >= 2:
                    act.wait_ge(pv, n - 1)
                nc.scalar.activation(att[:, n % 2], zb[:, n % 3], ACT.Exp).then_inc(exp_ok, 1)

            for n in range(N + 2):
                if n >= 2:
                    weights(n - 2)
                if n < N:
                    softplus(n)

        @block.vector
        def _(dve):
            link = Chain(dve, dve_chain)
            dve.wait_ge(bias_in, 16)
            for h in range(HEADS):
                ins = nc.vector.tensor_scalar(bias[:, h, :], K("ones"), c.A("sb")[:, h:h + 1], None, ALU.mult)
                ins.then_inc(bias_ok, 1)
            dve.wait_ge(bias_ok, HEADS)
            mask = K("before").unsqueeze(1).to_broadcast([P, HEADS, P])

            def add_bias(n):
                dve.wait_ge(score, n + 1)
                if n >= 3:
                    dve.wait_ge(exp_ok, n - 2)
                nc.vector.tensor_tensor(zb[:, n % 3], head4(n % 2), bias, ALU.add).then_inc(zb_ok, 1)

            def soft_sum(n):
                qb, kb = steps[n]
                dve.wait_ge(soft, n + 1)
                if n >= 3:
                    dve.wait_ge(sums, n - 2)
                    dve.wait_ge(sum_ok, n - 2)
                ins = nc.vector.scalar_tensor_tensor(sp_[:, n % 3], zb[:, n % 3], 0.0, tmp[:, n % 2], ALU.max, ALU.add)
                if kb == qb:
                    link(ins)
                    ins = nc.vector.tensor_tensor(sp_[:, n % 3], sp_[:, n % 3], mask, ALU.mult)
                ins.then_inc(sp_ok, 1)

            def argument(n):
                dve.wait_ge(sums, n + 1)
                dve.wait_ge(sp_ok, n + 1)
                nc.vector.tensor_tensor(zb[:, n % 3], head4(2 + n % 2), zb[:, n % 3], ALU.add).then_inc(arg_ok, 1)

            def mask_weights(n):
                dve.wait_ge(exp_ok, n + 1)
                a = att[:, n % 2]
                nc.vector.tensor_tensor(a, a, mask, ALU.mult).then_inc(att_ok, 1)

            def outputs(qb):
                dve.wait_ge(pv, last_of[qb] + 1)
                for half in range(2):
                    q = slice(half * DH, (half + 1) * DH)
                    nc.vector.tensor_copy(oT[q, 0:2, qb * P:(qb + 1) * P],
                                          head4(4 + qb % 2)[q, half:4:2, :]).then_inc(out_ok, 1)

            for n in range(N + 3):
                if n >= 3 and steps[n - 3][0] == steps[n - 3][1]:
                    mask_weights(n - 3)
                if n < N:
                    add_bias(n)
                if 1 <= n <= N:
                    soft_sum(n - 1)
                if 2 <= n <= N + 1:
                    argument(n - 2)
                if n >= 3 and n - 3 in last_of:
                    outputs(last_of.index(n - 3))


def stage_stick_sample(c):
    nc, T, K = c.nc, c.T, c.K
    HQ = HEADS * NS
    c.place(start=c.after_q, Kp=DB * NPG * 256, Vp=DB * NPG * 256, kTs=DB * NPG * 256, qzs=HQ, biasS=HQ, sb=HEADS,
            zS=3 * HQ, tS=3 * HQ, spS=3 * HQ)
    Kp = c.A("Kp").rearrange("p (g n) -> p g n", n=256)
    Vp = c.A("Vp").rearrange("p (g n) -> p g n", n=256)
    kTs = c.A("kTs").rearrange("p (g n) -> p g n", n=256)
    qzs = c.A("qzs").rearrange("p (h q) -> p h q", h=HEADS)
    z, t, sp_ = c.A("zS"), c.A("tS"), c.A("spS")
    ids = c.ids
    ps, oT, qT, kT, vtok = c.ps, c.hT, c.qT, c.kT, c.vtok
    NPAGES = DB * NPG
    s = c.sem
    ids_in, bias_in = s("s_ids"), s("s_bias")
    page_in = [s(f"s_page{n}") for n in range(4)]
    q_ok, turned, kT_ok, score, zb_ok = s("s_q"), s("s_turned"), s("s_kT"), s("s_score"), s("s_zb")
    soft, sp_ok, sums, arg_ok, exp_ok, att_ok, pv = (s("s_soft"), s("s_sp"), s("s_sums"), s("s_arg"), s("s_exp"),
                                                     s("s_att"), s("s_pv"))
    out_ok, dve_chain, act_chain, v_in = s("s_out"), s("s_dve"), s("s_act"), s("s_v")
    N2, N3 = 2 * HQ, 3 * HQ
    new = slice(N2, N3)

    with nc.Block() as block:
        @block.sync
        def _(sp):
            sp.dma_start(ids[0:1, :], T['page_table'].rearrange("b g -> (b g)").unsqueeze(0)).then_inc(ids_in, 16)
            sp.dma_start(c.A("sb"), row_bc(T['sb_bias'][0])).then_inc(bias_in, 16)
            sp.wait_ge(ids_in, 16)
            n_phys = T['cache_sb_k'].shape[1]
            for g in range(NPAGES):
                page = sp.value_load(ids[0:1, g:g + 1], min_val=0, max_val=n_phys - 1)
                for src, dst, done in (('cache_sb_k', Kp, page_in[g // 4]), ('cache_sb_v', Vp, v_in)):
                    pages = T[src][0].rearrange("n t h d -> n t (h d)")
                    sp.dma_start(dst[:, g, :], pages[bass.ds(page, 1)].rearrange("a t n -> (a t) n")).then_inc(done, 16)

        @block.tensor
        def _(pe):
            def turn(g):
                pe.wait_ge(page_in[g // 4], 64)
                u = g // 2
                if u >= 4 and g % 2 == 0:
                    pe.wait_ge(kT_ok, u - 3)
                for pair in range(2):
                    last = nc.tensor.transpose(ps[u % 4][:, (g % 2) * 256 + pair * P:(g % 2) * 256 + (pair + 1) * P],
                                               Kp[:, g, pair * P:(pair + 1) * P], K("ident"))
                if g % 2 == 1:
                    last.then_inc(turned, 1)

            for g in range(NPAGES):
                turn(g)
            pe.wait_ge(q_ok, 3)
            pages = ps[4][:, 0:N2].rearrange("p (g h b q) -> p g h b q", g=NPG, h=HEADS, b=DB)
            qv = qzs.rearrange("p h (b q) -> p h b q", b=DB)
            for g in range(NPAGES):
                b, page = g // NPG, g % NPG
                pe.wait_ge(kT_ok, g // 2 + 1)
                for pair in range(2):
                    hh = slice(2 * pair, 2 * pair + 2)
                    last = nc.tensor.matmul(pages[:, page, hh, b, :], kTs[:, g, pair * P:(pair + 1) * P], qv[:, hh, b, :],
                                            start=True, stop=True)
            last.then_inc(score, 1)
            for pair in range(2):
                last = nc.tensor.matmul(ps[5][0:NS, pair * 64:(pair + 1) * 64], kT[:, pair, SEQ:TOK],
                                        qzs[:, 2 * pair:2 * pair + 2, :].rearrange("p h q -> p (h q)"), start=True, stop=True)
            last.then_inc(score, 1)
            pe.wait_ge(sp_ok, 3)
            nc.tensor.matmul(ps[6][:, HQ:N2], K("negsuf"), sp_[:, HQ:N2], start=True, stop=False)
            nc.tensor.matmul(ps[6][:, HQ:N2], K("negone", NS), sp_[0:NS, new], start=False, stop=True)
            nc.tensor.matmul(ps[6][:, 0:HQ], K("negsuf"), sp_[:, 0:HQ], start=True, stop=False)
            nc.tensor.matmul(ps[6][:, 0:HQ], K("negone"), sp_[:, HQ:N2], start=False, stop=False)
            nc.tensor.matmul(ps[6][:, 0:HQ], K("negone", NS), sp_[0:NS, new], start=False, stop=True).then_inc(sums, 1)
            nc.tensor.matmul(ps[7][0:NS, 0:HQ], K("negsuf", NS, NS), sp_[0:NS, new], start=True, stop=True).then_inc(sums, 1)
            pe.wait_ge(exp_ok, 2)
            pe.wait_ge(att_ok, 1)
            pe.wait_ge(v_in, 16 * NPAGES)
            att = z[:, 0:N2].rearrange("p (g h b q) -> p g h b q", g=NPG, h=HEADS, b=DB)
            an = z[:, new].rearrange("p (h q) -> p h q", h=HEADS)
            for pair in range(2):
                hh = slice(2 * pair, 2 * pair + 2)
                out = ps[0][:, pair * 64:(pair + 1) * 64]
                nc.tensor.matmul(out, vtok[0:NS, NT, pair * P:(pair + 1) * P], an[0:NS, hh, :].rearrange("p h q -> p (h q)"),
                                 start=(pair == 0), stop=False, skip_group_check=True)
                ov = out.rearrange("p (h b q) -> p h b q", h=2, b=DB)
                for g in range(NPAGES):
                    last = nc.tensor.matmul(ov[:, :, g // NPG, :], Vp[:, g, pair * P:(pair + 1) * P],
                                            att[:, g % NPG, hh, g // NPG, :], start=False, stop=(g == NPAGES - 1),
                                            skip_group_check=True)
            last.then_inc(pv, 1)

        @block.scalar
        def _(act):
            link = Chain(act, act_chain)
            nc.scalar.preload_act_table_set(EXPLN)
            for u in range(NPAGES // 2):
                act.wait_ge(turned, u + 1)
                nc.scalar.copy(kTs[:, 2 * u:2 * u + 2, :], ps[u % 4][:, :].rearrange("p (g n) -> p g n", g=2)).then_inc(kT_ok, 1)
            act.wait_ge(zb_ok, 2)
            for r, sl in ((P, slice(0, N2)), (NS, new)):
                link(nc.scalar.activation(t[0:r, sl], z[0:r, sl], ACT.Abs))
                link(nc.scalar.activation(t[0:r, sl], t[0:r, sl], ACT.Exp, scale=-1.0))
                nc.scalar.activation(t[0:r, sl], t[0:r, sl], ACT.Ln, bias=1.0).then_inc(soft, 1)
            act.wait_ge(arg_ok, 2)
            nc.scalar.activation(z[:, 0:N2], z[:, 0:N2], ACT.Exp).then_inc(exp_ok, 1)
            nc.scalar.activation(z[0:NS, new], z[0:NS, new], ACT.Exp).then_inc(exp_ok, 1)

        @block.vector
        def _(dve):
            link = Chain(dve, dve_chain)
            nc.vector.memset(c.A("qzs"), 0.0).then_inc(q_ok, 1)
            dve.wait_ge(q_ok, 1)
            nc.vector.tensor_copy(qzs[0:DH, 0:4:2, :], qT[0:DH, :, SEQ:TOK]).then_inc(q_ok, 1)
            nc.vector.tensor_copy(qzs[DH:P, 1:4:2, :], qT[DH:P, :, SEQ:TOK]).then_inc(q_ok, 1)
            dve.wait_ge(bias_in, 16)
            bias = c.A("biasS")
            for h in range(HEADS):
                ins = nc.vector.tensor_scalar(bias[:, h * NS:(h + 1) * NS], K("ones", P, NS), c.A("sb")[:, h:h + 1], None, ALU.mult)
                link(ins)
            dve.wait_ge(score, 1)
            nc.vector.tensor_tensor(z[:, 0:N2].rearrange("p (g n) -> p g n", g=2), ps[4][:, 0:N2].rearrange("p (g n) -> p g n", g=2),
                                    bias.unsqueeze(1).to_broadcast([P, 2, HQ]), ALU.add).then_inc(zb_ok, 1)
            dve.wait_ge(score, 2)
            nc.vector.tensor_tensor(z[0:NS, new], ps[5][0:NS, 0:HQ], bias[0:NS, :], ALU.add).then_inc(zb_ok, 1)
            dve.wait_ge(zb_ok, 2)
            dve.wait_ge(soft, 1)
            nc.vector.scalar_tensor_tensor(sp_[:, 0:N2], z[:, 0:N2], 0.0, t[:, 0:N2], ALU.max, ALU.add).then_inc(sp_ok, 1)
            dve.wait_ge(soft, 2)
            nc.vector.scalar_tensor_tensor(sp_[0:NS, new], z[0:NS, new], 0.0, t[0:NS, new], ALU.max, ALU.add).then_inc(sp_ok, 1)
            dve.wait_ge(sp_ok, 2)
            mask = K("before4", NS, NS).unsqueeze(1).to_broadcast([NS, HEADS, NS])
            sn = sp_[0:NS, new].rearrange("p (h q) -> p h q", h=HEADS)
            zn = z[0:NS, new].rearrange("p (h q) -> p h q", h=HEADS)
            nc.vector.tensor_tensor(sn, sn, mask, ALU.mult).then_inc(sp_ok, 1)
            dve.wait_ge(sums, 1)
            nc.vector.tensor_tensor(z[:, 0:N2], ps[6][:, 0:N2], z[:, 0:N2], ALU.add).then_inc(arg_ok, 1)
            dve.wait_ge(sums, 2)
            nc.vector.tensor_tensor(z[0:NS, new], ps[7][0:NS, 0:HQ], z[0:NS, new], ALU.add).then_inc(arg_ok, 1)
            dve.wait_ge(exp_ok, 2)
            nc.vector.tensor_tensor(zn, zn, mask, ALU.mult).then_inc(att_ok, 1)
            dve.wait_ge(pv, 1)
            ov = ps[0][:, 0:P].rearrange("p (c h q) -> p c h q", c=2, h=2)
            for half in range(2):
                q = slice(half * DH, (half + 1) * DH)
                nc.vector.tensor_copy(oT[q, 0:2, SEQ:TOK], ov[q, :, half, :]).then_inc(out_ok, 1)


def stage_delta_inputs(c):
    nc, T, O, K = c.nc, c.T, c.O, c.K
    c.place(start=0, dnorm=1, SQ=2 * TOK)
    c.place(start=c.free_at + 6 * TOK, cs=768, cw=6 * 28, xs=6 * DB * 7, y=2 * SEQ, ys=6 * NS, stp=768, sts=768, rn=3 * GT,
            rows4=8)
    qkvT = c.qkvT
    cs, stp, sts, rn = c.A("cs"), c.A("stp"), c.A("sts"), c.A("rn")
    cw = c.A("cw").rearrange("p (c n) -> p c n", c=6)
    xs = c.A("xs").rearrange("p (c b t) -> p c b t", c=6, b=DB)
    ys = c.A("ys").rearrange("p (c b t) -> p c b t", c=6, b=DB)
    y = c.A("y").rearrange("p (s t) -> p s t", s=2)
    sq = c.A("SQ").rearrange("p (s t) -> p s t", s=2)
    NC = TILES * HEADS

    def col():
        return c.new_small(NC).rearrange("p (i h) -> p i h", i=TILES)

    c.beta, c.g, c.log_decay, c.be, c.kgf = col(), col(), col(), col(), col()
    tx, tl = col(), col()
    eps6 = c.new_small(1)
    c.eps6 = eps6
    bd, ad = c.ba[:, :, 0:HEADS], c.ba[:, :, HEADS:2 * HEADS]
    ps = c.ps
    s = c.sem
    loaded, cw_mm, cw_ok, st_mm, st_ok, stored = s("c_load"), s("c_cwmm"), s("c_cwok"), s("c_stmm"), s("c_stok"), s("c_stored")
    gd, ga, gpe, conv_ok, silu_ok, staged = s("c_gd"), s("c_ga"), s("c_gpe"), s("c_conv"), s("c_silu"), s("c_staged")
    sq_ok, ss, rn_ok, unit, dve_chain, act_chain, eps_ok = (s("c_sq"), s("c_ss"), s("c_rn"), s("c_unit"), s("c_dve"),
                                                            s("c_act"), s("c_eps"))
    rows4 = c.A("rows4")

    with nc.Block() as block:
        @block.sync
        def _(sp):
            sp.dma_start(cs[0:24, :], T['state_conv'][0].rearrange("b t n -> (b t) n")).then_inc(loaded, 16)
            sp.dma_start(cs[24:28, :], T['conv_w'][0]).then_inc(loaded, 16)
            sp.dma_start(rows4[:, 0:4], row_bc(T['dn_dt_bias'][0])).then_inc(loaded, 16)
            sp.dma_start(rows4[:, 4:8], row_bc(T['dn_a_log'][0])).then_inc(loaded, 16)
            for half in range(2):
                sp.dma_start(c.A("dnorm")[half * DH:(half + 1) * DH, :], T['dn_norm_g'][0].unsqueeze(1)).then_inc(loaded, 16)
            sp.wait_ge(st_ok, 4)
            sp.dma_start(O['conv_prompt'][0, 0], stp[0:3, :]).then_inc(stored, 16)
            for b in range(DB):
                sp.dma_start(O['conv_sample'][0, b], sts[b * DS + 1:(b + 1) * DS, :]).then_inc(stored, 16)
            sp.wait_ge(stored, 16 * (DB + 1))

        @block.tensor
        def _(pe):
            pe.wait_ge(loaded, 96)
            for n in range(6):
                last = nc.tensor.transpose(ps[0][:, n * 28:(n + 1) * 28], cs[0:28, n * P:(n + 1) * P], K("ident", 28, 28))
            last.then_inc(cw_mm, 1)
            for bank, r, t0, chunks in ((1, 3, SEQ - 3, range(4)), (2, 3, SEQ - 3, range(4, 6)),
                                        (3, NS, SEQ, range(4)), (4, NS, SEQ, range(4, 6))):
                for n in chunks:
                    last = nc.tensor.transpose(ps[bank][0:r, (n % 4) * P:(n % 4 + 1) * P], qkvT[:, n, t0:t0 + r], K("ident"))
                last.then_inc(st_mm, 1)
            pe.wait_ge(gd, 5)
            for q, (a, b) in enumerate((("cum64", "cum4"), ("blk64", "blk4"))):
                nc.tensor.matmul(ps[5][:, q * NC:q * NC + NT * HEADS], K(a), c.g[:, 0:NT, :].rearrange("p i h -> p (i h)"),
                                 start=True, stop=True)
                last = nc.tensor.matmul(ps[5][0:NS, q * NC + NT * HEADS:(q + 1) * NC], K(b, NS, NS), c.g[0:NS, NT, :],
                                        start=True, stop=True)
            last.then_inc(gpe, 1)
            for n in range(4):
                pe.wait_ge(sq_ok, n + 1)
                for g in range(GRP):
                    if n >= 1:
                        pe.wait_ge(rn_ok, GRP * (n - 1) + g + 1)
                    elif g == 0:
                        pe.wait_ge(gd, 6)
                    bank = (5, 6, 7)[g]
                    nc.tensor.matmul(ps[bank][:, 0:GT], K("blk64"), sq[:, n % 2, g * GT:(g + 1) * GT],
                                     start=True, stop=True).then_inc(ss, 1)

        @block.scalar
        def _(act):
            link = Chain(act, act_chain)
            nc.scalar.preload_act_table_set(EXPLN)
            act.wait_ge(cw_mm, 1)
            nc.scalar.copy(cw, ps[0][:, 0:168].rearrange("p (c n) -> p c n", c=6)).then_inc(cw_ok, 1)
            for n, (bank, r, dst, w) in enumerate(((1, 3, stp[0:3, 0:512], 512), (2, 3, stp[0:3, 512:768], 256),
                                                   (3, NS, sts[0:NS, 0:512], 512), (4, NS, sts[0:NS, 512:768], 256))):
                act.wait_ge(st_mm, n + 1)
                nc.scalar.copy(dst, ps[bank][0:r, 0:w]).then_inc(st_ok, 1)
            act.wait_ge(gd, 1)
            nc.scalar.activation(c.beta, bd, ACT.Exp, scale=-1.0).then_inc(ga, 1)
            nc.scalar.activation(rows4[:, 4:8], rows4[:, 4:8], ACT.Exp).then_inc(ga, 1)
            link(nc.scalar.activation(tl, tx, ACT.Abs))
            link(nc.scalar.activation(tl, tl, ACT.Exp, scale=-1.0))
            nc.scalar.activation(tl, tl, ACT.Ln, bias=1.0).then_inc(ga, 1)
            act.wait_ge(gd, 6)
            nc.scalar.activation(c.be, c.log_decay, ACT.Exp).then_inc(ga, 1)
            nc.scalar.activation(c.kgf, c.kgf, ACT.Exp).then_inc(ga, 1)
            for n in range(6):
                act.wait_ge(conv_ok, n + 1)
                nc.scalar.activation(qkvT[:, n, 0:SEQ], y[:, n % 2, :], ACT.Silu).then_inc(silu_ok, 1)
                nc.scalar.activation(qkvT[:, n, SEQ:TOK].rearrange("p (b t) -> p b t", b=DB), ys[:, n], ACT.Silu).then_inc(silu_ok, 1)
            act.wait_ge(silu_ok, 12)
            act.wait_ge(eps_ok, 1)
            for n in range(4):
                if n >= 2:
                    act.wait_ge(ss, GRP * (n - 1))
                nc.scalar.activation(sq[:, n % 2, :], qkvT[:, n, :], ACT.Square).then_inc(sq_ok, 1)
                nc.scalar.preload_act_table_set(EXPLN)
                for g in range(GRP):
                    u = GRP * n + g
                    act.wait_ge(ss, u + 1)
                    if n >= 1:
                        act.wait_ge(unit, u - 2)
                    t = rn[:, g * GT:(g + 1) * GT]
                    link(nc.scalar.activation(t, ps[(5, 6, 7)[g]][:, 0:GT], ACT.Ln, bias=eps6))
                    nc.scalar.activation(t, t, ACT.Exp, scale=-0.5).then_inc(rn_ok, 1)

        @block.vector
        def _(dve):
            link = Chain(dve, dve_chain)
            nc.vector.memset(eps6, 1e-6).then_inc(eps_ok, 1)
            nc.vector.memset(c.log_decay[:, NT, :], 0.0).then_inc(staged, 1)
            nc.vector.memset(c.kgf[:, NT, :], 0.0).then_inc(staged, 1)
            dve.wait_ge(loaded, 96)
            bc = rows4[:, 0:4].unsqueeze(1).to_broadcast([P, TILES, HEADS])
            nea = rows4[:, 4:8]
            nc.vector.tensor_tensor(tx, ad, bc, ALU.add).then_inc(gd, 1)
            dve.wait_ge(ga, 3)
            nc.vector.tensor_scalar(c.beta, c.beta, 1.0, None, ALU.add).then_inc(gd, 1)
            dve.wait_ge(gd, 2)
            nc.vector.reciprocal(c.beta, c.beta).then_inc(gd, 1)
            link(nc.vector.scalar_tensor_tensor(tx, tx, 0.0, tl, ALU.max, ALU.add))
            nc.vector.tensor_scalar(nea, nea, -1.0, None, ALU.mult).then_inc(gd, 1)
            dve.wait_ge(gd, 4)
            nc.vector.tensor_tensor(c.g, tx, nea.unsqueeze(1).to_broadcast([P, TILES, HEADS]), ALU.mult).then_inc(gd, 1)
            dve.wait_ge(gpe, 1)
            dve.wait_ge(staged, 2)
            gp = ps[5][:, 0:2 * NC].rearrange("p (q i h) -> p q i h", q=2, i=TILES)
            link(nc.vector.tensor_copy(c.log_decay[:, 0:NT, :], gp[:, 0, 0:NT, :]))
            link(nc.vector.tensor_copy(c.log_decay[0:NS, NT, :], gp[0:NS, 0, NT, :]))
            link(nc.vector.tensor_tensor(c.kgf[:, 0:NT, :], gp[:, 1, 0:NT, :], c.log_decay[:, 0:NT, :], ALU.subtract))
            nc.vector.tensor_tensor(c.kgf[0:NS, NT, :], gp[0:NS, 1, NT, :], c.log_decay[0:NS, NT, :], ALU.subtract).then_inc(gd, 1)
            dve.wait_ge(ga, 4)
            link(nc.vector.tensor_tensor(c.be, c.be, c.beta, ALU.mult))
            dve.wait_ge(cw_ok, 1)
            nc.vector.tensor_copy(xs[:, :, :, 0:3], cw[:, :, 0:24].rearrange("p c (b t) -> p c b t", b=DB)).then_inc(staged, 1)
            nc.vector.tensor_copy(xs[:, :, :, 3:7], qkvT[:, :, SEQ:TOK].rearrange("p c (b t) -> p c b t", b=DB)).then_inc(staged, 1)
            dve.wait_ge(staged, 4)
            dve.wait_ge(st_mm, 4)
            for n in range(6):
                if n >= 2:
                    dve.wait_ge(silu_ok, 2 * (n - 1))
                yy = y[:, n % 2, :]
                w = lambda i: cw[:, n, 24 + i:25 + i]
                link(nc.vector.tensor_scalar(yy, qkvT[:, n, 0:SEQ], w(3), None, ALU.mult))
                for sh in (3, 2, 1):
                    link(nc.vector.scalar_tensor_tensor(yy[:, sh:], qkvT[:, n, 0:SEQ - sh], w(3 - sh), yy[:, sh:],
                                                        ALU.mult, ALU.add))
                link(nc.vector.tensor_scalar(ys[:, n], xs[:, n, :, 3:7], w(3), None, ALU.mult))
                for sh in (3, 2, 1):
                    ins = nc.vector.scalar_tensor_tensor(ys[:, n], xs[:, n, :, 3 - sh:7 - sh], w(3 - sh), ys[:, n],
                                                         ALU.mult, ALU.add)
                    if sh > 1:
                        link(ins)
                ins.then_inc(conv_ok, 1)
            for n in range(4):
                for g in range(GRP):
                    u = GRP * n + g
                    dve.wait_ge(rn_ok, u + 1)
                    t = qkvT[:, n, g * GT:(g + 1) * GT]
                    nc.vector.scalar_tensor_tensor(t, t, DH ** -0.5 if n < 2 else 1.0, rn[:, g * GT:(g + 1) * GT],
                                                   ALU.mult, ALU.mult).then_inc(unit, 1)


def stage_delta(c):
    nc, T, O, K = c.nc, c.T, c.O, c.K
    kept = dict(u=256, wT=256, eg=256)
    c.place(start=0, dnorm=1, SQ=2 * TOK, S=2 * P, dS=2 * P, **{f"{k}{u}": n for u in range(2) for k, n in kept.items()})
    lane_sizes = dict(kvt=512, gcum=512, DL=512, DT=512, kz=512, qz=512, L=512, Lb=1024, X=512, Y=512, Pm=512,
                      vb=256, kbe=256, kg=512, qg=256, vz=512)
    sizes = {f"{k}{u}": n for u in range(2) for k, n in lane_sizes.items()}
    c.place(start=c.free_at + 6 * TOK, **sizes)
    h4 = "p (h t) -> p h t"
    B = {k: [c.A(f"{k}{u}") for u in range(2)] for k in {**lane_sizes, **kept}}

    def V(k, u, h=HEADS):
        return B[k][u].rearrange(h4, h=h)

    odT = c.A("SQ").rearrange("p (c t) -> p c t", c=2)
    S = c.A("S").rearrange("p (c n) -> p c n", c=2)
    dS = c.A("dS").rearrange("p (c n) -> p c n", c=2)
    c.place(start=c.at["kvt0"][0], rsq=2 * TOK, rrn=2 * TOK)
    c.rsq = c.A("rsq").rearrange("p (n t) -> p n t", n=2)
    c.rrn = c.A("rrn").rearrange("p (n t) -> p n t", n=2)
    a1 = c.at["kvt1"][0]
    c.place(start=a1, SS=DB * 2 * P, wSs=2 * NS, Vx=HEADS * 512, Sn=HEADS * 512)
    SS = c.A("SS").rearrange("p (b c n) -> p b c n", b=DB, c=2)
    wSs = c.A("wSs").rearrange("p (c t) -> p c t", c=2)
    Vx = c.A("Vx").rearrange("p (h b n) -> p h b n", h=HEADS, b=DB)
    Sn = c.A("Sn").rearrange("p (h b n) -> p h b n", h=HEADS, b=DB)
    qkvT, zT, oT = c.qkvT, c.zT, c.hT
    ps = c.ps
    LV = {i: ((2, 4, 8, 16, 32) if i < NT else (2,)) for i in range(TILES)}
    groups = [(0, 1), (2, 3), (4, 5), (6, 7), (8,)]
    number, n = {}, 0
    for grp in groups:
        for l in range(len(LV[grp[0]])):
            for i in grp:
                n += 1
                number[(i, l)] = n
    total_levels = n
    s = c.sem
    sx = {k: s("d_" + k) for k in ("zero", "kvt", "kvc", "gcum", "G", "dif", "ddve", "eg", "dexp", "dmask", "kz", "kk", "L",
                                   "intra", "X1", "Xt", "Y1", "Lb", "P", "Pc", "YX", "Y", "scaled", "uw", "uc", "qg",
                                   "vW", "vn", "o", "oc", "S", "dve", "act", "init", "sload", "swS", "swc", "swt",
                                   "svn", "svx", "so", "soc", "sdS", "sSn", "ost", "rs", "rss", "rrn", "rout", "zq")}
    dims = lambda i: (rows(i), (K("cum64"), K("low64")) if i < NT else (K("cum4", NS, NS), K("low4", NS, NS)))

    def bk(i, n):
        return ps[4 * (i % 2 if i < NT else 0) + n]

    def lane(i):
        return i % 2

    def v4(ap, i):
        r = rows(i)
        return ap[:, 0:4 * r].rearrange("p (h t) -> p h t", h=HEADS)

    def v2(ap, i):
        r = rows(i)
        return ap[:, 0:2 * r].rearrange("p (c t) -> p c t", c=2)

    def tok(i):
        return slice(i * P, i * P + rows(i))

    with nc.Block() as block:
        @block.gpsimd
        def _(pool):
            for nm in ("kz", "qz", "kg", "vz"):
                for u in range(2):
                    nc.gpsimd.memset(B[nm][u], 0.0).then_inc(sx["zero"], 1)
            nc.gpsimd.memset(c.A("S"), 0.0).then_inc(sx["zero"], 1)
            pool.wait_ge(sx["zero"], 9)
            for grp in groups:
                for i in grp:
                    r, (cum, low) = dims(i)
                    u = lane(i)
                    pool.wait_ge(sx["dexp"], 2 * i + 2)
                    for q, (nm, m) in enumerate((("DL", low), ("DT", cum))):
                        a = v4(B[nm][u], i)[0:r]
                        nc.gpsimd.tensor_tensor(a, a, m.unsqueeze(1).to_broadcast([r, HEADS, r]), ALU.mult).then_inc(sx["dmask"], 1)
                        pool.wait_ge(sx["dmask"], 2 * i + q + 1)
                for l in range(len(LV[grp[0]])):
                    for i in grp:
                        r = rows(i)
                        pool.wait_ge(sx["L"], i + 1)
                        m = K(f"lvl{LV[i][l]}", r, r).unsqueeze(1).to_broadcast([r, HEADS, r])
                        if l >= 2:
                            pool.wait_ge(sx["P"], number[(i, l - 2)])
                        elif i >= 2:
                            pool.wait_ge(sx["P"], number[(i - 2, len(LV[i - 2]) - 1)])
                        dst = B["Lb"][lane(i)].rearrange("p (s n) -> p s n", s=2)[:, l % 2, :]
                        nc.gpsimd.tensor_tensor(v4(dst, i)[0:r], v4(B["L"][lane(i)], i)[0:r], m, ALU.mult).then_inc(sx["Lb"], 1)
                        pool.wait_ge(sx["Lb"], number[(i, l)])

        @block.tensor
        def _(pe):
            pe.wait_ge(sx["zero"], 9)
            for gi, grp in enumerate(groups):
                for i in grp:
                    r = rows(i)
                    if gi >= 1:
                        pe.wait_ge(sx["uc"], 2 * (grp[0] - 1))
                        pe.wait_ge(sx["S"], 2 * grp[0])
                        pe.wait_ge(sx["oc"], 2 * grp[0])
                    for n in range(4):
                        last = nc.tensor.transpose(bk(i, 3)[0:r, n * P:(n + 1) * P], qkvT[:, 2 + n, tok(i)], K("ident"))
                    last.then_inc(sx["kvt"], 1)
                for i in grp:
                    r = rows(i)
                    pe.wait_ge(sx["gcum"], i + 1)
                    nc.tensor.matmul(bk(i, 0)[:, 0:4 * r], K("ones", r, P), B["gcum"][lane(i)][0:r, 0:4 * r],
                                     start=True, stop=True).then_inc(sx["G"], 1)
                for i in grp:
                    r = rows(i)
                    pe.wait_ge(sx["kz"], 4 * i + 4)
                    for n, nm in ((1, "kz"), (2, "qz")):
                        z = v4(B[nm][lane(i)], i)
                        for pair in range(2):
                            last = nc.tensor.matmul(bk(i, n)[0:r, pair * 2 * r:(pair + 1) * 2 * r], qkvT[:, 2 + pair, tok(i)],
                                                    z[:, 2 * pair:2 * pair + 2, :].rearrange("p h t -> p (h t)"),
                                                    start=True, stop=True)
                    last.then_inc(sx["kk"], 1)
                for i in grp:
                    r = rows(i)
                    pe.wait_ge(sx["X1"], i + 1)
                    pe.wait_ge(sx["eg"], 2 * i + 2)
                    X = v4(B["X"][lane(i)], i)
                    for hd in range(HEADS):
                        last = nc.tensor.transpose(bk(i, 0)[0:r, hd * r:(hd + 1) * r], X[0:r, hd, :], K("ident", r, r))
                    last.then_inc(sx["Xt"], 1)
                for l in range(len(LV[grp[0]])):
                    for i in grp:
                        r = rows(i)
                        pe.wait_ge(sx["Lb"], number[(i, l)])
                        if l == 0:
                            pe.wait_ge(sx["Y1"], i + 1)
                        else:
                            pe.wait_ge(sx["Y"], 2 * number[(i, l - 1)])
                        Lb = v4(B["Lb"][lane(i)].rearrange("p (s n) -> p s n", s=2)[:, l % 2, :], i)
                        Y = v4(B["Y"][lane(i)], i)
                        for hd in range(HEADS):
                            last = nc.tensor.matmul(bk(i, 0)[0:r, hd * r:(hd + 1) * r], Lb[0:r, hd, :], Y[0:r, hd, :],
                                                    start=True, stop=True)
                        last.then_inc(sx["P"], 1)
                    for i in grp:
                        r = rows(i)
                        pe.wait_ge(sx["Pc"], number[(i, l)])
                        X, Pm = v4(B["X"][lane(i)], i), v4(B["Pm"][lane(i)], i)
                        for hd in range(HEADS):
                            nc.tensor.matmul(bk(i, 1)[0:r, hd * r:(hd + 1) * r], X[0:r, hd, :], Pm[0:r, hd, :],
                                             start=True, stop=True)
                        for hd in range(HEADS):
                            last = nc.tensor.matmul(bk(i, 2)[0:r, hd * r:(hd + 1) * r], Pm[0:r, hd, :], X[0:r, hd, :],
                                                    start=True, stop=True)
                        last.then_inc(sx["YX"], 1)
                for i in grp:
                    r = rows(i)
                    pe.wait_ge(sx["scaled"], 4 * i + 4)
                    pe.wait_ge(sx["Y"], 2 * number[(i, len(LV[i]) - 1)])
                    Y = v4(B["Y"][lane(i)], i)
                    for hd in range(HEADS):
                        nc.tensor.matmul(bk(i, 3)[0:r, hd * DH:(hd + 1) * DH], Y[0:r, hd, :],
                                         B["vb"][lane(i)][0:r, hd * DH:(hd + 1) * DH], start=True, stop=True)
                    for hd in range(HEADS):
                        q = (hd % 2) * DH
                        last = nc.tensor.matmul(bk(i, 0)[q:q + DH, (hd // 2) * r:(hd // 2 + 1) * r],
                                                B["kbe"][lane(i)][0:r, hd * DH:(hd + 1) * DH], Y[0:r, hd, :],
                                                start=True, stop=True)
                    last.then_inc(sx["uw"], 1)
                if grp[0] < NT:
                    for i in grp:
                        u = lane(i)
                        pe.wait_ge(sx["uc"], 2 * i + 2)
                        pe.wait_ge(sx["qg"], i + 1)
                        wT, qg = v2(B["wT"][u], i), v2(B["qg"][u], i)
                        vz = V("vz", u)
                        dT = V("DT", u)
                        kg = B["kg"][u].rearrange("p (s n) -> p s n", s=2)
                        for cc in range(2):
                            e = 2 * i + cc
                            if e >= 1:
                                pe.wait_ge(sx["S"], e)
                            for pair in range(2):
                                last = nc.tensor.matmul(bk(i, 0)[:, pair * P:(pair + 1) * P], wT[:, pair, :], S[:, pair, :],
                                                        start=True, stop=True)
                            last.then_inc(sx["vW"], 1)
                            t = slice(cc * CH, (cc + 1) * CH)
                            if e >= 1:
                                pe.wait_ge(sx["oc"], e)
                            pe.wait_ge(sx["vn"], e + 1)
                            for pair in range(2):
                                out = bk(i, 1)[:, pair * CH:(pair + 1) * CH]
                                nc.tensor.matmul(out, S[:, pair, :], qg[:, pair, t], start=True, stop=False)
                                for hh in range(2):
                                    hd = 2 * pair + hh
                                    last = nc.tensor.matmul(out, vz[:, hd, :], dT[:, hd, t], start=False, stop=(hh == 1))
                            last.then_inc(sx["o"], 1)
                            for pair in range(2):
                                vp = B["vz"][u][:, pair * 256:(pair + 1) * 256].rearrange("p (h n) -> p h n", h=2)
                                for hh in range(2):
                                    last = nc.tensor.matmul(bk(i, 2)[:, pair * P + hh * DH:pair * P + (hh + 1) * DH],
                                                            kg[:, cc, pair * P:(pair + 1) * P], vp[:, hh, hh * DH:(hh + 1) * DH],
                                                            start=True, stop=True)
                            last.then_inc(sx["vW"], 1)
                else:
                    i = NT
                    pe.wait_ge(sx["uc"], 2 * i + 2)
                    pe.wait_ge(sx["qg"], i + 1)
                    pe.wait_ge(sx["sload"], 16 * DB * HEADS)
                    wT, qg = v2(B["wT"][0], i), v2(B["qg"][0], i)
                    for pair in range(2):
                        for b in range(DB):
                            t = slice(b * DS, (b + 1) * DS)
                            last = nc.tensor.matmul(ps[4][:, pair * NS + b * DS:pair * NS + (b + 1) * DS], SS[:, b, pair, :],
                                                    wT[:, pair, t], start=True, stop=True)
                    last.then_inc(sx["swS"], 1)
                    pe.wait_ge(sx["swc"], 1)
                    for pair in range(2):
                        last = nc.tensor.transpose(ps[5][0:NS, pair * P:(pair + 1) * P], wSs[:, pair, :], K("ident"))
                    last.then_inc(sx["swt"], 1)
                    pe.wait_ge(sx["svn"], 1)
                    vz, dT = V("vz", 0), v4(B["DT"][0], i)
                    for pair in range(2):
                        for hh in range(2):
                            hd = 2 * pair + hh
                            nc.tensor.matmul(ps[6][:, pair * NS:(pair + 1) * NS], vz[0:NS, hd, :], dT[0:NS, hd, :],
                                             start=(pair == 0 and hh == 0), stop=False, skip_group_check=True)
                        for b in range(DB):
                            t = slice(b * DS, (b + 1) * DS)
                            last = nc.tensor.matmul(ps[6][:, pair * NS + b * DS:pair * NS + (b + 1) * DS], SS[:, b, pair, :],
                                                    qg[:, pair, t], start=False, stop=(b == DB - 1), skip_group_check=True)
                    last.then_inc(sx["so"], 1)
                    for hd in range(HEADS):
                        bank = (7, 1, 2, 5)[hd]
                        pe.wait_ge(sx["svx"], hd + 1)
                        nc.tensor.matmul(ps[bank][:, :], B["kg"][0][0:NS, (hd // 2) * P:(hd // 2 + 1) * P],
                                         Vx[0:NS, hd].rearrange("p b n -> p (b n)"), start=True, stop=True).then_inc(sx["sdS"], 1)
            for n in range(2):
                pe.wait_ge(sx["rs"], n + 1)
                for g in range(GRP):
                    bank = ps[(0, 3, 4)[g]]
                    if n:
                        pe.wait_ge(sx["rrn"], g + 1)
                    nc.tensor.matmul(bank[:, 0:GT], K("blk64"), c.rsq[:, n, g * GT:(g + 1) * GT], start=True,
                                     stop=True).then_inc(sx["rss"], 1)

        @block.scalar
        def _(act):
            link = Chain(act, sx["act"])
            nc.scalar.preload_act_table_set(EXPLN)
            for gi, grp in enumerate(groups):
                for i in grp:
                    r = rows(i)
                    act.wait_ge(sx["kvt"], i + 1)
                    nc.scalar.copy(B["kvt"][lane(i)][0:r, :], bk(i, 3)[0:r, :]).then_inc(sx["kvc"], 1)
                for i in grp:
                    r, _ = dims(i)
                    act.wait_ge(sx["ddve"], 2 * i + 2)
                    G = v4(bk(i, 0), i)
                    eg = v2(B["eg"][lane(i)], i)
                    for half in range(2):
                        q = slice(half * DH, (half + 1) * DH)
                        nc.scalar.activation(eg[q], G[q, half:4:2, :], ACT.Exp).then_inc(sx["eg"], 1)
                    for nm, sc in (("DL", -1.0), ("DT", 1.0)):
                        a = v4(B[nm][lane(i)], i)[0:r]
                        nc.scalar.activation(a, a, ACT.Exp, scale=sc).then_inc(sx["dexp"], 1)
                for i in grp:
                    r = rows(i)
                    act.wait_ge(sx["Xt"], i + 1)
                    nc.scalar.copy(B["Y"][lane(i)][0:r, 0:4 * r], bk(i, 0)[0:r, 0:4 * r]).then_inc(sx["Y1"], 1)
                for l in range(len(LV[grp[0]])):
                    for i in grp:
                        r = rows(i)
                        act.wait_ge(sx["P"], number[(i, l)])
                        nc.scalar.copy(B["Pm"][lane(i)][0:r, 0:4 * r], bk(i, 0)[0:r, 0:4 * r]).then_inc(sx["Pc"], 1)
                for i in grp:
                    r = rows(i)
                    act.wait_ge(sx["uw"], i + 1)
                    nc.scalar.copy(B["u"][lane(i)][0:r, :], bk(i, 3)[0:r, 0:256]).then_inc(sx["uc"], 1)
                    nc.scalar.copy(B["wT"][lane(i)][:, 0:2 * r], bk(i, 0)[:, 0:2 * r]).then_inc(sx["uc"], 1)
                if grp[0] < NT:
                    for i in grp:
                        for cc in range(2):
                            act.wait_ge(sx["o"], 2 * i + cc + 1)
                            nc.scalar.copy(odT[:, :, i * P + cc * CH:i * P + (cc + 1) * CH],
                                           bk(i, 1)[:, 0:P].rearrange("p (c t) -> p c t", c=2)).then_inc(sx["oc"], 1)
                else:
                    act.wait_ge(sx["swS"], 1)
                    nc.scalar.copy(wSs, ps[4][:, 0:2 * NS].rearrange("p (c t) -> p c t", c=2)).then_inc(sx["swc"], 1)
                    act.wait_ge(sx["so"], 1)
                    nc.scalar.copy(odT[:, :, SEQ:TOK], ps[6][:, 0:2 * NS].rearrange("p (c t) -> p c t", c=2)).then_inc(sx["oc"], 1)
            act.wait_ge(sx["oc"], 2 * NT + 1)
            for n in range(2):
                nc.scalar.activation(c.rsq[:, n, :], odT[:, n, :], ACT.Square).then_inc(sx["rs"], 1)
            for n in range(2):
                for g in range(GRP):
                    act.wait_ge(sx["rss"], GRP * n + g + 1)
                    t = c.rrn[:, n, g * GT:(g + 1) * GT]
                    link(nc.scalar.activation(t, ps[(0, 3, 4)[g]][:, 0:GT], ACT.Ln, bias=c.eps6, scale=1.0 / DH))
                    nc.scalar.activation(t, t, ACT.Exp, scale=-0.5).then_inc(sx["rrn"], 1)

        @block.vector
        def _(dve):
            link = Chain(dve, sx["dve"])
            dve.wait_ge(sx["zero"], 9)
            for gi, grp in enumerate(groups):
                for i in grp:
                    r, (cum, low) = dims(i)
                    u = lane(i)
                    if gi >= 1:
                        dve.wait_ge(sx["vW"], 4 * grp[0])
                    gb = c.g[0:r, i, :].unsqueeze(2).to_broadcast([r, HEADS, r])
                    nc.vector.tensor_tensor(v4(B["gcum"][u], i)[0:r], cum.unsqueeze(1).to_broadcast([r, HEADS, r]), gb,
                                            ALU.mult).then_inc(sx["gcum"], 1)
                    if i == NT:
                        for nm in ("kz", "qz"):
                            nc.vector.memset(B[nm][0], 0.0).then_inc(sx["zq"], 1)
                        dve.wait_ge(sx["zq"], 2)
                    for nm, ch in (("kz", 2), ("qz", 0)):
                        z = v4(B[nm][u], i)
                        for half in range(2):
                            q = slice(half * DH, (half + 1) * DH)
                            nc.vector.tensor_copy(z[q, half:4:2, :], qkvT[q, ch:ch + 2, tok(i)]).then_inc(sx["kz"], 1)
                for i in grp:
                    r = rows(i)
                    u = lane(i)
                    dve.wait_ge(sx["G"], i + 1)
                    gcb = c.log_decay[0:r, i, :].unsqueeze(2).to_broadcast([r, HEADS, r])
                    d = v4(B["gcum"][u], i)[0:r]
                    nc.vector.tensor_tensor(d, v4(bk(i, 0), i)[0:r], gcb, ALU.subtract).then_inc(sx["dif"], 1)
                    dve.wait_ge(sx["dif"], i + 1)
                    nc.vector.tensor_scalar(v4(B["DL"][u], i)[0:r], d, 0.0, None, ALU.max).then_inc(sx["ddve"], 1)
                    nc.vector.tensor_scalar(v4(B["DT"][u], i)[0:r], d, 0.0, None, ALU.min).then_inc(sx["ddve"], 1)
                for i in grp:
                    r = rows(i)
                    u = lane(i)
                    dve.wait_ge(sx["kvc"], i + 1)
                    kv = B["kvt"][u].rearrange("p (q h d) -> p q h d", q=2, h=HEADS)

                    def by(col):
                        return col[0:r, i, :].unsqueeze(2).to_broadcast([r, HEADS, DH])

                    hd_view = lambda ap: ap.rearrange("p (h d) -> p h d", h=HEADS)
                    nc.vector.tensor_tensor(hd_view(B["vb"][u])[0:r], kv[0:r, 1], by(c.beta), ALU.mult).then_inc(sx["scaled"], 1)
                    nc.vector.tensor_tensor(hd_view(B["kbe"][u])[0:r], kv[0:r, 0], by(c.be), ALU.mult).then_inc(sx["scaled"], 1)
                    kg = B["kg"][u].rearrange("p (s h d) -> p s h d", s=2, h=HEADS)
                    if i < NT:
                        for cc in range(2):
                            q = slice(cc * CH, (cc + 1) * CH)
                            nc.vector.tensor_tensor(kg[q, cc], kv[q, 0], c.kgf[q, i, :].unsqueeze(2).to_broadcast([CH, HEADS, DH]),
                                                    ALU.mult).then_inc(sx["scaled"], 1)
                    else:
                        nc.vector.tensor_tensor(kg[0:r, 0], kv[0:r, 0], by(c.kgf), ALU.mult).then_inc(sx["scaled"], 2)
                    dve.wait_ge(sx["eg"], 2 * i + 2)
                    nc.vector.tensor_tensor(v2(B["qg"][u], i), qkvT[:, 0:2, tok(i)], v2(B["eg"][u], i), ALU.mult).then_inc(sx["qg"], 1)
                for i in grp:
                    r = rows(i)
                    u = lane(i)
                    dve.wait_ge(sx["kk"], i + 1)
                    dve.wait_ge(sx["dmask"], 2 * i + 2)
                    L, DL, X = (v4(B[nm][u], i)[0:r] for nm in ("L", "DL", "X"))
                    for hd in range(HEADS):
                        ins = nc.vector.scalar_tensor_tensor(L[:, hd, :], v4(bk(i, 1), i)[0:r, hd, :], c.beta[0:r, i, hd:hd + 1],
                                                             DL[:, hd, :], ALU.mult, ALU.mult)
                        link(ins) if hd < HEADS - 1 else ins.then_inc(sx["L"], 1)
                    dt = v4(B["DT"][u], i)[0:r]
                    nc.vector.tensor_tensor(dt, v4(bk(i, 2), i)[0:r], dt, ALU.mult).then_inc(sx["intra"], 1)
                    dve.wait_ge(sx["L"], i + 1)
                    link(nc.vector.tensor_tensor(X, L, K("lvl1", r, r).unsqueeze(1).to_broadcast([r, HEADS, r]), ALU.mult))
                    nc.vector.scalar_tensor_tensor(X, X, -1.0, K("ident", r, r).unsqueeze(1).to_broadcast([r, HEADS, r]),
                                                   ALU.mult, ALU.add).then_inc(sx["X1"], 1)
                for l in range(len(LV[grp[0]])):
                    for i in grp:
                        r = rows(i)
                        u = lane(i)
                        dve.wait_ge(sx["YX"], number[(i, l)])
                        Y, X = B["Y"][u][0:r, 0:4 * r], B["X"][u][0:r, 0:4 * r]
                        if l == 0:
                            dve.wait_ge(sx["Y1"], i + 1)
                            dve.wait_ge(sx["X1"], i + 1)
                        nc.vector.tensor_tensor(Y, Y, bk(i, 1)[0:r, 0:4 * r], ALU.subtract).then_inc(sx["Y"], 1)
                        nc.vector.tensor_tensor(X, X, bk(i, 2)[0:r, 0:4 * r], ALU.subtract).then_inc(sx["Y"], 1)
                        if l + 1 < len(LV[i]):
                            dve.wait_ge(sx["Y"], 2 * number[(i, l)])
                if grp[0] < NT:
                    for i in grp:
                        u = lane(i)
                        r = P
                        eg = v2(B["eg"][u], i)
                        dve.wait_ge(sx["uc"], 2 * i + 2)
                        for cc in range(2):
                            e = 2 * i + cc
                            q = slice(cc * CH, (cc + 1) * CH)
                            dve.wait_ge(sx["vW"], 2 * e + 1)
                            for pair in range(2):
                                for hh in range(2):
                                    hd = 2 * pair + hh
                                    nc.vector.tensor_tensor(V("vz", u)[q, hd, hh * DH:(hh + 1) * DH],
                                                            B["u"][u][q, hd * DH:(hd + 1) * DH],
                                                            bk(i, 0)[q, hd * DH:(hd + 1) * DH], ALU.subtract)\
                                        .then_inc(sx["vn"] if hd == 3 else sx["init"], 1)
                            dve.wait_ge(sx["vW"], 2 * e + 2)
                            link(nc.vector.tensor_tensor(dS, bk(i, 2)[:, 0:256].rearrange("p (c n) -> p c n", c=2),
                                                         K("blk64").unsqueeze(1).to_broadcast([P, 2, P]), ALU.mult))
                            for pair in range(2):
                                ins = nc.vector.scalar_tensor_tensor(S[:, pair, :], S[:, pair, :],
                                                                     eg[:, pair, cc * CH + CH - 1:cc * CH + CH], dS[:, pair, :],
                                                                     ALU.mult, ALU.add)
                                link(ins) if pair == 0 else ins.then_inc(sx["S"], 1)
                            dve.wait_ge(sx["S"], e + 1)
                    if grp[0] == NT - 2:
                        nc.vector.memset(c.A("SS"), 0.0).then_inc(sx["sSn"], 1)
                else:
                    i = NT
                    dve.wait_ge(sx["swt"], 1)
                    dve.wait_ge(sx["uc"], 2 * i + 2)
                    for hd in range(HEADS):
                        hh = hd % 2
                        ins = nc.vector.tensor_tensor(V("vz", 0)[0:NS, hd, hh * DH:(hh + 1) * DH],
                                                      B["u"][0][0:NS, hd * DH:(hd + 1) * DH],
                                                      ps[5][0:NS, hd * DH:(hd + 1) * DH], ALU.subtract)
                        link(ins) if hd < 3 else ins.then_inc(sx["svn"], 1)
                    dve.wait_ge(sx["svn"], 1)
                    sel = K("blk4", NS, NS)[:, 0:NS:DS]
                    for hd in range(HEADS):
                        hh = hd % 2
                        vn = V("vz", 0)[0:NS, hd, hh * DH:(hh + 1) * DH].unsqueeze(1).to_broadcast([NS, DB, DH])
                        nc.vector.tensor_tensor(Vx[0:NS, hd], vn, sel.unsqueeze(2).to_broadcast([NS, DB, DH]),
                                                ALU.mult).then_inc(sx["svx"], 1)
                    eg = v2(B["eg"][0], i)
                    for hd in range(HEADS):
                        pair, hh = hd // 2, hd % 2
                        q = slice(hh * DH, (hh + 1) * DH)
                        gl = eg[q, pair, DS - 1:NS:DS].unsqueeze(2).to_broadcast([DH, DB, DH])
                        link(nc.vector.tensor_tensor(Sn[q, hd], SS[q, :, pair, q], gl, ALU.mult))
                        dve.wait_ge(sx["sdS"], hd + 1)
                        bank = (7, 1, 2, 5)[hd]
                        nc.vector.tensor_tensor(Sn[q, hd], ps[bank][q, :].rearrange("p (b n) -> p b n", b=DB), Sn[q, hd],
                                                ALU.add).then_inc(sx["ost"], 1)
            for n in range(2):
                for g in range(GRP):
                    t = slice(g * GT, (g + 1) * GT)
                    dve.wait_ge(sx["rrn"], GRP * n + g + 1)
                    link(nc.vector.scalar_tensor_tensor(odT[:, n, t], odT[:, n, t], c.A("dnorm")[:, 0:1], c.rrn[:, n, t],
                                                        ALU.mult, ALU.mult))
                    nc.vector.tensor_tensor(oT[:, 6 + n, t], odT[:, n, t], zT[:, n, t], ALU.mult).then_inc(sx["rout"], 1)

        @block.sync
        def _(sp):
            sp.wait_ge(sx["sSn"], 1)
            for hd in range(HEADS):
                q = slice((hd % 2) * DH, (hd % 2 + 1) * DH)
                for b in range(DB):
                    sp.dma_start(SS[q, b, hd // 2, q], T['state_delta'][0, b, hd]).then_inc(sx["sload"], 16)
            for hd in range(HEADS):
                q = slice((hd % 2) * DH, (hd % 2 + 1) * DH)
                sp.dma_start(O['delta_prompt'][0, 0, hd], S[q, hd // 2, q]).then_inc(sx["soc"], 16)
            for hd in range(HEADS):
                q = slice((hd % 2) * DH, (hd % 2 + 1) * DH)
                sp.wait_ge(sx["ost"], hd + 1)
                sp.dma_start(O['delta_sample'][0, :, hd].rearrange("b k v -> k b v"), Sn[q, hd]).then_inc(sx["soc"], 16)
            sp.wait_ge(sx["soc"], 16 * 2 * HEADS)


def stage_residual(c, tag, src, weight, gain, shift, turn):
    nc, T, O, K = c.nc, c.T, c.O, c.K
    c.place(start=c.res_at, rw=KC * D, rg=D, rb=D)
    w = c.A("rw").rearrange("p (k n) -> p k n", k=KC)
    g, b = c.A("rg"), c.A("rb")
    h, hT, ps = c.h, c.hT, c.ps
    s = lambda n: c.sem(f"{tag}_{n}")
    w_in = [s(f"w{n}") for n in range(2)]
    ln_in, prod, added, stats, rstd_ok, normed, turned, hT_ok = (s("ln"), s("prod"), s("added"), s("stats"), s("rstd"),
                                                                 s("normed"), s("turned"), s("hT"))
    dve_chain, act_chain = s("dve"), s("act")
    wv = T[weight][0].rearrange("(k p) n -> p k n", p=P)

    with nc.Block() as block:
        @block.sync
        def _(sp):
            for q in range(2):
                sp.dma_start(w[:, :, q * 512:(q + 1) * 512], wv[:, :, q * 512:(q + 1) * 512]).then_inc(w_in[q], 16)
            sp.dma_start(g, row_bc(T[gain][0])).then_inc(ln_in, 16)
            sp.dma_start(b, row_bc(T[shift][0])).then_inc(ln_in, 16)

        @block.tensor
        def _(pe):
            def product(i):
                r = rows(i)
                for q in range(2):
                    if i == 0:
                        pe.wait_ge(w_in[q], 16)
                    if i >= 2:
                        pe.wait_ge(added, 2 * (i - 2) + q + 1)
                    for k in range(KC):
                        last = nc.tensor.matmul(ps[2 * (i % 2) + q][0:r, :], src[:, k, i * P:i * P + r],
                                                w[:, k, q * 512:(q + 1) * 512], start=(k == 0), stop=(k == KC - 1))
                    last.then_inc(prod, 1)

            def transposes(i):
                r = rows(i)
                pe.wait_ge(normed, i + 1)
                for q in range(2):
                    if i >= 1:
                        pe.wait_ge(hT_ok, 2 * (i - 1) + q + 1)
                    for k in range(4):
                        last = nc.tensor.transpose(ps[4 + q][:, k * r:(k + 1) * r],
                                                   h[0:r, i, (4 * q + k) * P:(4 * q + k + 1) * P], K("ident", r, r))
                    last.then_inc(turned, 1)

            for i in range(TILES + 1):
                if i < TILES:
                    product(i)
                if turn and i >= 1:
                    transposes(i - 1)

        @block.vector
        def _(dve):
            link = Chain(dve, dve_chain)

            def add(i):
                r = rows(i)
                for q in range(2):
                    dve.wait_ge(prod, 2 * i + q + 1)
                    x = h[0:r, i, q * 512:(q + 1) * 512]
                    nc.vector.scalar_tensor_tensor(x, x, ALPHA, ps[2 * (i % 2) + q][0:r, :], ALU.mult, ALU.add).then_inc(added, 1)
                dve.wait_ge(added, 2 * i + 2)
                if i >= 2:
                    dve.wait_ge(rstd_ok, i - 1)
                ln_stats(nc, link, h, i, c.st[:, i % 2, :], c.mv[:, i % 2, :]).then_inc(stats, 1)
                dve.wait_ge(stats, i + 1)

            def apply(i):
                dve.wait_ge(rstd_ok, i + 1)
                ln_apply(nc, link, h, i, c.mv[:, i % 2, :], c.rstd[:, i % 2, :], g, b).then_inc(normed, 1)

            dve.wait_ge(ln_in, 32)
            for i in range(TILES):
                add(i)
                apply(i)

        @block.scalar
        def _(act):
            link = Chain(act, act_chain)
            nc.scalar.preload_act_table_set(EXPLN)
            for i in range(TILES + 1):
                if i < TILES:
                    act.wait_ge(stats, i + 1)
                    if i >= 2:
                        act.wait_ge(normed, i - 1)
                    ln_rstd(nc, link, i, c.mv[:, i % 2, :], c.rstd[:, i % 2, :], c.eps).then_inc(rstd_ok, 1)
                if turn and i >= 1:
                    r = rows(i - 1)
                    for q in range(2):
                        act.wait_ge(turned, 2 * (i - 1) + q + 1)
                        act.wait_ge(prod, 2 * i)
                        nc.scalar.copy(hT[:, 4 * q:4 * q + 4, (i - 1) * P:(i - 1) * P + r],
                                       ps[4 + q][:, 0:4 * r].rearrange("p (k t) -> p k t", k=4)).then_inc(hT_ok, 1)


def stage_memory(c):
    nc, T, O, K = c.nc, c.T, c.O, c.K
    c.place(start=0, KT=KC * NMEM, Vm=2 * D, qXT=KC * TOK)
    c.place(start=4096, Km=2 * D, mem=2 * D, memT=KC * NMEM, wk=KC * D, wv=KC * D)
    KT = c.A("KT").rearrange("p (k m) -> p k m", k=KC)
    Vm, Km, mem = (c.A(n).rearrange("p (m n) -> p m n", m=2) for n in ("Vm", "Km", "mem"))
    memT = c.A("memT").rearrange("p (k m) -> p k m", k=KC)
    w = {n: c.A(n).rearrange("p (k n) -> p k n", k=KC) for n in ("wk", "wv")}
    c.KT, c.Vm = KT, Vm
    ps = c.ps
    s = lambda n: c.sem(f"m_{n}")
    mem_in, wk_in, wv_in, turned, mT_ok, prod, out_ok, kturned, kT_ok, stored = (
        s("mem"), s("wk"), s("wv"), s("turned"), s("mT"), s("prod"), s("out"), s("kturned"), s("kT"), s("stored"))

    with nc.Block() as block:
        @block.sync
        def _(sp):
            sp.dma_start(mem, T['mem_prompt'][0].rearrange("(m p) n -> p m n", p=P)).then_inc(mem_in, 16)
            sp.dma_start(w["wk"], T['xa_wk'][0].rearrange("(k p) n -> p k n", p=P)).then_inc(wk_in, 16)
            sp.dma_start(w["wv"], T['xa_wv'][0].rearrange("(k p) n -> p k n", p=P)).then_inc(wv_in, 16)
            for n, (name, t) in enumerate((('mem_k_prompt', Km), ('mem_v_prompt', Vm))):
                sp.wait_ge(out_ok, 4 * (n + 1))
                sp.dma_start(O[name][0, 0].rearrange("(m p) h d -> p m (h d)", p=P), t).then_inc(stored, 16)
            sp.wait_ge(stored, 32)

        @block.tensor
        def _(pe):
            def turns(src, f, base, sem_t, freed):
                for k in (2 * f, 2 * f + 1):
                    for m in range(2):
                        last = nc.tensor.transpose(ps[base + f % 4][:, (k % 2) * NMEM + m * P:(k % 2) * NMEM + (m + 1) * P],
                                                   src[:, m, k * P:(k + 1) * P], K("ident"))
                last.then_inc(sem_t, 1)

            pe.wait_ge(mem_in, 16)
            for f in range(4):
                turns(mem, f, 0, turned, None)
            pe.wait_ge(mT_ok, 4)
            u = 0
            for name, arrived in (("wk", wk_in), ("wv", wv_in)):
                pe.wait_ge(arrived, 16)
                for m in range(2):
                    for q in range(2):
                        if u >= 4:
                            pe.wait_ge(out_ok, u - 3)
                        for k in range(KC):
                            last = nc.tensor.matmul(ps[4 + u % 4][:, :], memT[:, k, m * P:(m + 1) * P],
                                                    w[name][:, k, q * 512:(q + 1) * 512], start=(k == 0), stop=(k == KC - 1))
                        last.then_inc(prod, 1)
                        u += 1
                if name == "wk":
                    pe.wait_ge(out_ok, 4)
                    for f in range(4):
                        turns(Km, f, 0, kturned, None)

        @block.scalar
        def _(act):
            for f in range(4):
                act.wait_ge(turned, f + 1)
                nc.scalar.copy(memT[:, 2 * f:2 * f + 2, :], ps[f][:, :].rearrange("p (k m) -> p k m", k=2)).then_inc(mT_ok, 1)
            for f in range(4):
                act.wait_ge(kturned, f + 1)
                nc.scalar.copy(KT[:, 2 * f:2 * f + 2, :], ps[f][:, :].rearrange("p (k m) -> p k m", k=2)).then_inc(kT_ok, 1)

        @block.vector
        def _(dve):
            for u in range(8):
                dst = (Km, Vm)[u // 4][:, (u // 2) % 2, (u % 2) * 512:(u % 2 + 1) * 512]
                dve.wait_ge(prod, u + 1)
                nc.vector.tensor_copy(dst, ps[4 + u % 4][:, :]).then_inc(out_ok, 1)


def stage_queries(c):
    nc, T = c.nc, c.T
    c.place(start=4096 + KC * TOK, qring=4 * KC * P)
    ring = c.A("qring").rearrange("p (s k n) -> p s k n", s=4, k=KC)
    qXT = c.A("qXT").rearrange("p (k t) -> p k t", k=KC)
    c.qXT = qXT
    ps, hT = c.ps, c.hT
    s = lambda n: c.sem(f"q_{n}")
    w_in, prod, evac = [s(f"w{n}") for n in range(4)], s("prod"), s("evac")
    wv = T['xa_wq'][0].rearrange("(k p) n -> p k n", p=P)
    with nc.Block() as block:
        @block.sync
        def _(sp):
            for n in range(KC):
                if n >= 4:
                    sp.wait_ge(prod, GRP * (n - 3))
                sp.dma_start(ring[:, n % 4], wv[:, :, n * P:(n + 1) * P]).then_inc(w_in[n % 4], 16)

        @block.tensor
        def _(pe):
            for n in range(KC):
                pe.wait_ge(w_in[n % 4], 16 * (n // 4 + 1))
                for g in range(GRP):
                    u = GRP * n + g
                    if u >= 8:
                        pe.wait_ge(evac, u - 7)
                    for k in range(KC):
                        last = nc.tensor.matmul(ps[u % 8][:, 0:GT], ring[:, n % 4, k, :], hT[:, k, g * GT:(g + 1) * GT],
                                                start=(k == 0), stop=(k == KC - 1))
                    last.then_inc(prod, 1)

        @block.scalar
        def _(act):
            for u in range(GRP * KC):
                act.wait_ge(prod, u + 1)
                nc.scalar.copy(qXT[:, u // GRP, (u % GRP) * GT:(u % GRP + 1) * GT], ps[u % 8][:, 0:GT]).then_inc(evac, 1)


def stage_cross(c):
    nc, T, O, K = c.nc, c.T, c.O, c.K
    c.place(start=4096 + KC * TOK, xp=2 * D, xpT=D, Kb=2 * 2 * D, KTb=2 * D, Vb=3 * 2 * D, sS=256, xps=256, xpTs=256)
    KT, Vm, qXT = c.KT, c.Vm, c.qXT
    xp = c.A("xp").rearrange("p (s h m) -> p s h m", s=2, h=HEADS)
    xpT = c.A("xpT").rearrange("p (m h q) -> p m h q", m=2, h=HEADS)
    Kb = c.A("Kb").rearrange("p (s m n) -> p s m n", s=2, m=2)
    Vb = c.A("Vb").rearrange("p (s m n) -> p s m n", s=3, m=2)
    KTb = c.A("KTb").rearrange("p (k m) -> p k m", k=KC)
    sS, xps, xpTs = c.A("sS"), c.A("xps"), c.A("xpTs")
    mx = c.new_small(2 * HEADS).rearrange("p (s h) -> p s h", s=2)
    sm = c.new_small(2 * HEADS).rearrange("p (s h) -> p s h", s=2)
    mxs, sms = c.new_small(1), c.new_small(1)
    ps = c.ps
    s = lambda n: c.sem(f"x_{n}")
    k_in, v_in = [s("k0"), s("k1")], [s(f"v{n}") for n in range(3)]
    score, neg, exp_ok, p_ok, pturned, pT_ok, val, val_ok = (s("score"), s("neg"), s("exp"), s("p"), s("pturned"),
                                                             s("pT"), s("val"), s("valok"))
    kturned, kT_ok, sscore, s_ok, s_back, s_neg, s_exp, s_p, s_pt, s_pT, v_done, x_ok = (
        s("kturned"), s("kT"), s("sscore"), s("sok"), s("sback"), s("sneg"), s("sexp"), s("sp"), s("spt"), s("spT"),
        s("vdone"), s("xok"))
    dve_chain, act_chain = s("dve"), s("act")
    SC = XDH ** -0.5

    with nc.Block() as block:
        @block.sync
        def _(sp):
            def load(name, dst, b, done):
                sp.dma_start(dst, T[name][0, b].rearrange("(m p) h d -> p m (h d)", p=P)).then_inc(done, 16)

            for b in range(DB):
                if b >= 2:
                    sp.wait_ge(kturned, 4 * (b - 1))
                load('cache_mem_k', Kb[:, b % 2], b, k_in[b % 2])
            for b in range(DB):
                if b >= 3:
                    sp.wait_ge(v_done, b - 2)
                load('cache_mem_v', Vb[:, b % 3], b, v_in[b % 3])

        @block.tensor
        def _(pe):
            def turn_keys(b, f):
                if f == 0:
                    pe.wait_ge(k_in[b % 2], 16 * (b // 2 + 1))
                if 4 * b + f >= 1:
                    pe.wait_ge(kT_ok, 4 * b + f)
                for k in (2 * f, 2 * f + 1):
                    for m in range(2):
                        last = nc.tensor.transpose(ps[6][:, (k % 2) * NMEM + m * P:(k % 2) * NMEM + (m + 1) * P],
                                                   Kb[:, b % 2, m, k * P:(k + 1) * P], K("ident"))
                last.then_inc(kturned, 1)

            def sample_scores(b):
                pe.wait_ge(kT_ok, 4 * b + 4)
                for m in range(2):
                    for hd in range(HEADS):
                        at = m * P + b * HEADS * DS + hd * DS
                        for dc in range(2):
                            last = nc.tensor.matmul(ps[7][:, at:at + DS], KTb[:, 2 * hd + dc, m * P:(m + 1) * P],
                                                    qXT[:, 2 * hd + dc, SEQ + b * DS:SEQ + (b + 1) * DS],
                                                    start=(dc == 0), stop=(dc == 1))
                last.then_inc(sscore, 1)

            def scores(i):
                if i >= 1:
                    pe.wait_ge(exp_ok, HEADS * i)
                    pe.wait_ge(neg, i)
                for hd in range(HEADS):
                    for dc in range(2):
                        last = nc.tensor.matmul(ps[hd // 2][:, (hd % 2) * NMEM:(hd % 2 + 1) * NMEM],
                                                qXT[:, 2 * hd + dc, i * P:(i + 1) * P], KT[:, 2 * hd + dc, :],
                                                start=(dc == 0), stop=(dc == 1))
                last.then_inc(score, 1)

            def turn_p(i):
                pe.wait_ge(p_ok, i + 1)
                if i >= 1:
                    pe.wait_ge(pT_ok, 2 * i)
                for m in range(2):
                    for hd in range(HEADS):
                        last = nc.tensor.transpose(ps[2 + m][:, hd * P:(hd + 1) * P], xp[:, i % 2, hd, m * P:(m + 1) * P],
                                                   K("ident"))
                    last.then_inc(pturned, 1)

            def values(i):
                pe.wait_ge(pT_ok, 2 * i + 2)
                if i >= 1:
                    pe.wait_ge(val_ok, 2 * i)
                for k in range(KC):
                    for m in range(2):
                        last = nc.tensor.matmul(ps[4 + k // 4][:, (k % 4) * P:(k % 4 + 1) * P], Vm[:, m, k * P:(k + 1) * P],
                                                xpT[:, m, k // 2, :], start=(m == 0), stop=(m == 1))
                    if k % 4 == 3:
                        last.then_inc(val, 1)

            for i in range(NT + 1):
                if i < NT:
                    turn_keys(i, 0)
                    scores(i)
                    turn_keys(i, 1)
                if i >= 1:
                    turn_p(i - 1)
                if i < NT:
                    turn_keys(i, 2)
                if i >= 1:
                    values(i - 1)
                if i < NT:
                    turn_keys(i, 3)
                    sample_scores(i)
            pe.wait_ge(s_ok, 1)
            pe.wait_ge(exp_ok, HEADS * NT)
            for m in range(2):
                last = nc.tensor.transpose(ps[0][:, m * P:(m + 1) * P], sS[:, m * P:(m + 1) * P], K("ident"))
            last.then_inc(s_back, 1)
            pe.wait_ge(s_p, 1)
            for m in range(2):
                last = nc.tensor.transpose(ps[1][:, m * P:(m + 1) * P], xps[:, m * P:(m + 1) * P], K("ident"))
            last.then_inc(s_pt, 1)
            pe.wait_ge(s_pT, 1)
            for b in range(DB):
                pe.wait_ge(v_in[b % 3], 16 * (b // 3 + 1))
                for k in range(KC):
                    at = b * HEADS * DS + (k // 2) * DS
                    for m in range(2):
                        last = nc.tensor.matmul(ps[6][:, k * NS + b * DS:k * NS + (b + 1) * DS],
                                                Vb[:, b % 3, m, k * P:(k + 1) * P], xpTs[:, m * P + at:m * P + at + DS],
                                                start=(m == 0), stop=(m == 1))
                last.then_inc(v_done, 1)

        @block.scalar
        def _(act):
            link = Chain(act, act_chain)
            nc.scalar.preload_act_table_set(EXPLN)

            def exps(i):
                act.wait_ge(neg, i + 1)
                if i >= 2:
                    act.wait_ge(pturned, 2 * (i - 1))
                for hd in range(HEADS):
                    nc.scalar.activation(xp[:, i % 2, hd, :], ps[hd // 2][:, (hd % 2) * NMEM:(hd % 2 + 1) * NMEM], ACT.Exp,
                                         bias=mx[:, i % 2, hd:hd + 1], scale=SC,
                                         accum_out=sm[:, i % 2, hd:hd + 1]).then_inc(exp_ok, 1)

            def pT(i):
                for m in range(2):
                    act.wait_ge(pturned, 2 * i + m + 1)
                    if i >= 1:
                        act.wait_ge(val, 2 * i)
                    nc.scalar.copy(xpT[:, m], ps[2 + m][:, :].rearrange("p (h q) -> p h q", h=HEADS)).then_inc(pT_ok, 1)

            def keyT(b, f):
                act.wait_ge(kturned, 4 * b + f + 1)
                if b >= 1 and f == 0:
                    act.wait_ge(sscore, b)
                nc.scalar.copy(KTb[:, 2 * f:2 * f + 2, :], ps[6][:, :].rearrange("p (k m) -> p k m", k=2)).then_inc(kT_ok, 1)

            for i in range(NT + 1):
                if i < NT:
                    keyT(i, 0)
                    keyT(i, 1)
                if i >= 1:
                    pT(i - 1)
                if i < NT:
                    keyT(i, 2)
                    exps(i)
                    keyT(i, 3)
            act.wait_ge(s_neg, 1)
            nc.scalar.activation(xps, ps[0][:, 0:256], ACT.Exp, bias=mxs, scale=SC, accum_out=sms).then_inc(s_exp, 1)

        @block.vector
        def _(dve):
            link = Chain(dve, dve_chain)

            def maxima(i):
                dve.wait_ge(score, i + 1)
                if i >= 2:
                    dve.wait_ge(exp_ok, HEADS * (i - 1))
                m = mx[:, i % 2, :]
                for q in range(2):
                    link(nc.vector.tensor_reduce(m[:, 2 * q:2 * q + 2], ps[q][:, :].rearrange("p (h m) -> p h m", h=2), AX, ALU.max))
                nc.vector.tensor_scalar(m, m, -SC, None, ALU.mult).then_inc(neg, 1)

            def normalise(i):
                dve.wait_ge(exp_ok, HEADS * (i + 1))
                link(nc.vector.reciprocal(sm[:, i % 2, :], sm[:, i % 2, :]))
                p = xp[:, i % 2]
                nc.vector.tensor_tensor(p, p, sm[:, i % 2, :].unsqueeze(2).to_broadcast([P, HEADS, NMEM]), ALU.mult)\
                    .then_inc(p_ok, 1)

            def outs(i):
                for q in range(2):
                    dve.wait_ge(val, 2 * i + q + 1)
                    nc.vector.tensor_copy(qXT[:, 4 * q:4 * q + 4, i * P:(i + 1) * P],
                                          ps[4 + q][:, :].rearrange("p (k t) -> p k t", k=4)).then_inc(val_ok, 1)

            for i in range(NT + 1):
                if i < NT:
                    maxima(i)
                if i >= 1:
                    outs(i - 1)
                if i < NT:
                    normalise(i)
            dve.wait_ge(sscore, DB)
            nc.vector.tensor_copy(sS, ps[7][:, 0:256]).then_inc(s_ok, 1)
            dve.wait_ge(s_back, 1)
            link(nc.vector.tensor_reduce(mxs, ps[0][:, 0:256], AX, ALU.max))
            nc.vector.tensor_scalar(mxs, mxs, -SC, None, ALU.mult).then_inc(s_neg, 1)
            dve.wait_ge(s_exp, 1)
            link(nc.vector.reciprocal(sms, sms))
            nc.vector.tensor_scalar(xps, xps, sms, None, ALU.mult).then_inc(s_p, 1)
            dve.wait_ge(s_pt, 1)
            nc.vector.tensor_copy(xpTs, ps[1][:, 0:256]).then_inc(s_pT, 1)
            dve.wait_ge(v_done, DB)
            nc.vector.tensor_copy(qXT[:, :, SEQ:TOK], ps[6][:, 0:KC * NS].rearrange("p (k t) -> p k t", k=KC)).then_inc(x_ok, 1)


def stage_route(c):
    nc, T, K = c.nc, c.T, c.K
    G4 = 4
    TE = TILES * NE
    c.place(start=0, wr=KC * NE, rbias=NE, tab=NROUTE, sel=TE, sc=TE, cmpa=TE * 4, cmpb=TE * 4,
            rank=TE, mask=TE, mask0=TE, masked=TE, pre=TE, gs=TILES * G4, grank=TILES * G4, den=TILES,
            tiles_cmp=NE * 9, tiles_of=NE, base_cmp=NE * NE, base=NE, ends=NE, exp_cmp=MOE_TILES * NE, exp_f=MOE_TILES,
            rk=2 * TILES, bs=2 * TILES, flo_cmp=2 * TILES * NT, flo=2 * TILES, lo=2 * TILES, hi=2 * TILES,
            slot_f=2 * TILES, one_lo=2 * TILES * P, one_hi=2 * TILES * MOE_TILES, work=TE)
    wr = c.A("wr").rearrange("p (k e) -> p k e", k=KC)
    sc, sel = c.A("sc"), c.A("sel")
    rank, gs, grank, den = c.A("rank"), c.A("gs"), c.A("grank"), c.A("den")
    ca, cb = c.A("cmpa"), c.A("cmpb")
    tab = lambda k, w: c.A("tab")[:, ROUTE_AT[k]:ROUTE_AT[k] + w]
    e3 = lambda x: x.rearrange("p (i e) -> p i e", e=NE)
    one_lo = c.A("one_lo").rearrange("p (n f) -> p n f", f=P)
    one_hi = c.A("one_hi").rearrange("p (n f) -> p n f", f=MOE_TILES)
    ps, hT, h = c.ps, c.hT, c.h
    s = lambda n: c.sem(f"r_{n}")
    loaded, logit, e_ok, chain, masks, counted, onehots, rows_ok, zeroed, h_out = (
        s("load"), s("logit"), s("e"), s("dve"), s("masks"), s("counted"), s("onehots"), s("rows"), s("zero"), s("h"))
    M = TILES * G4

    with nc.Block() as block:
        @block.sync
        def _(sp):
            sp.dma_start(wr, T['w_router'].rearrange("(k p) e -> p k e", p=P)).then_inc(loaded, 16)
            sp.dma_start(c.A("rbias"), row_bc(T['router_bias'])).then_inc(loaded, 16)
            sp.dma_start(c.A("tab"), T['route_table']).then_inc(loaded, 16)
            sp.dma_start(c.tokens_dram[0:SEQ, :].rearrange("(i p) d -> p i d", p=P), h[:, 0:NT, :]).then_inc(h_out, 16)
            sp.dma_start(c.tokens_dram[SEQ:TOK, :], h[0:NS, NT, :]).then_inc(h_out, 16)
            sp.wait_ge(h_out, 32)

        @block.tensor
        def _(pe):
            pe.wait_ge(loaded, 48)
            for i in range(TILES):
                r = rows(i)
                for k in range(KC):
                    last = nc.tensor.matmul(ps[0][0:r, i * NE:(i + 1) * NE], hT[:, k, i * P:i * P + r], wr[:, k, :],
                                            start=(k == 0), stop=(k == KC - 1))
            last.then_inc(logit, 1)
            pe.wait_ge(masks, 1)
            nc.tensor.matmul(ps[1][:, 0:TE], K("before"), c.A("mask"), start=True, stop=False)
            nc.tensor.matmul(ps[1][:, 0:TE], K("ones"), c.A("pre"), start=False, stop=True)
            nc.tensor.matmul(ps[2][:, 0:NE], K("ones"), c.A("pre")[:, TE - NE:TE], start=True, stop=False)
            nc.tensor.matmul(ps[2][:, 0:NE], K("ones"), c.A("mask")[:, TE - NE:TE], start=False, stop=True).then_inc(counted, 1)
            pe.wait_ge(onehots, 1)
            for n in range(2 * TILES):
                last = nc.tensor.matmul(ps[3][:, 0:MOE_TILES], one_lo[:, n, :], one_hi[:, n, :],
                                        start=(n == 0), stop=(n == 2 * TILES - 1))
            last.then_inc(rows_ok, 1)

        @block.scalar
        def _(act):
            act.wait_ge(zeroed, 1)
            act.wait_ge(logit, 1)
            nc.scalar.preload_act_table_set(EXPLN)
            nc.scalar.activation(sc[:, 0:NT * NE], ps[0][:, 0:NT * NE], ACT.Exp, scale=-1.0).then_inc(e_ok, 1)
            nc.scalar.activation(sc[0:NS, NT * NE:], ps[0][0:NS, NT * NE:TILES * NE], ACT.Exp, scale=-1.0).then_inc(e_ok, 1)

        @block.vector
        def _(dve):
            link = Chain(dve, chain)
            vt = nc.vector
            vt.memset(sc, 0.0).then_inc(zeroed, 1)
            dve.wait_ge(e_ok, 2)
            dve.wait_ge(loaded, 48)
            link(vt.tensor_scalar(sc, sc, 1.0, None, ALU.add))
            link(vt.reciprocal(sc, sc))
            link(vt.tensor_tensor(e3(sel), e3(sc), c.A("rbias").unsqueeze(1).to_broadcast([P, TILES, NE]), ALU.add))

            def ranks(x, m, out):
                xi = x.rearrange("p (m i) -> p m i", i=4).unsqueeze(2).to_broadcast([P, m, 4, 4])
                xj = x.rearrange("p (m j) -> p m j", j=4).unsqueeze(3).to_broadcast([P, m, 4, 4])
                a = ca[:, 0:16 * m].rearrange("p (m j i) -> p m j i", j=4, i=4)
                b = cb[:, 0:16 * m].rearrange("p (m j i) -> p m j i", j=4, i=4)
                tri = tab("tie", 16).rearrange("p (j i) -> p j i", j=4).unsqueeze(1).to_broadcast([P, m, 4, 4])
                link(vt.tensor_tensor(a, xi, xj, ALU.is_equal))
                link(vt.tensor_tensor(a, a, tri, ALU.mult))
                link(vt.tensor_tensor(b, xi, xj, ALU.is_gt))
                link(vt.tensor_tensor(a, a, b, ALU.add))
                link(vt.tensor_reduce(out.rearrange("p (m j) -> p m j", j=4), a, AX, ALU.add))

            mask, mask0, work = c.A("mask"), c.A("mask0"), c.A("work")
            ranks(sel, M, rank)
            link(vt.tensor_scalar(mask, rank, 1.5, None, ALU.is_lt))
            link(vt.tensor_tensor(work, mask, sel, ALU.mult))
            link(vt.tensor_reduce(gs, work.rearrange("p (m e) -> p m e", e=4), AX, ALU.add))
            ranks(gs, TILES, grank)
            link(vt.tensor_scalar(grank, grank, 0.5, None, ALU.is_lt))
            g4 = lambda x: x.rearrange("p (m e) -> p m e", e=4)
            link(vt.tensor_tensor(g4(mask), g4(mask), grank.unsqueeze(2).to_broadcast([P, M, 4]), ALU.mult))
            link(vt.tensor_tensor(e3(mask), e3(mask), tab("valid", TILES).unsqueeze(2).to_broadcast([P, TILES, NE]), ALU.mult))
            link(vt.tensor_scalar(mask0, rank, 0.5, None, ALU.is_lt))
            link(vt.tensor_tensor(mask0, mask0, mask, ALU.mult))
            pre = c.A("pre")
            link(vt.memset(pre[:, 0:NE], 0.0))
            for i in range(1, TILES):
                ins = vt.tensor_tensor(pre[:, i * NE:(i + 1) * NE], pre[:, (i - 1) * NE:i * NE], mask[:, (i - 1) * NE:i * NE], ALU.add)
                if i < TILES - 1:
                    link(ins)
            ins.then_inc(masks, 1)
            dve.wait_ge(masks, 1)

            def pick(m, x, out):
                link(vt.tensor_tensor(e3(work), e3(m), x, ALU.mult))
                link(vt.tensor_reduce(out, e3(work), AX, ALU.add))

            pick(mask, e3(sc), den)
            link(vt.tensor_scalar(den, den, 1e-38, None, ALU.max))
            link(vt.reciprocal(den, den))
            mask1 = c.A("masked")
            link(vt.tensor_tensor(mask1, mask, mask0, ALU.subtract))
            for q, m in enumerate((mask0, mask1)):
                pick(m, e3(sc), c.gate[:, q * TILES:(q + 1) * TILES])
                link(vt.tensor_tensor(c.gate[:, q * TILES:(q + 1) * TILES], c.gate[:, q * TILES:(q + 1) * TILES], den, ALU.mult))

            dve.wait_ge(counted, 1)
            cmp9 = c.A("tiles_cmp").rearrange("p (e j) -> p e j", j=9)
            link(vt.tensor_copy(work[:, 0:NE], ps[2][:, 0:NE]))
            link(vt.tensor_tensor(cmp9, work[:, 0:NE].unsqueeze(2).to_broadcast([P, NE, 9]),
                                  tab("thr9", 9).unsqueeze(1).to_broadcast([P, NE, 9]), ALU.is_gt))
            tiles_of, base, ends = c.A("tiles_of"), c.A("base"), c.A("ends")
            link(vt.tensor_reduce(tiles_of, cmp9, AX, ALU.add))
            bc = c.A("base_cmp").rearrange("p (e f) -> p e f", f=NE)
            link(vt.tensor_tensor(bc, tiles_of.unsqueeze(1).to_broadcast([P, NE, NE]),
                                  tab("tri16", NE * NE).rearrange("p (e f) -> p e f", f=NE), ALU.mult))
            link(vt.tensor_reduce(base, bc, AX, ALU.add))
            link(vt.tensor_tensor(ends, base, tiles_of, ALU.add))
            ec = c.A("exp_cmp").rearrange("p (s e) -> p s e", e=NE)
            link(vt.tensor_tensor(ec, tab("iota32", MOE_TILES).unsqueeze(2).to_broadcast([P, MOE_TILES, NE]),
                                  ends.unsqueeze(1).to_broadcast([P, MOE_TILES, NE]), ALU.is_ge))
            exp_f = c.A("exp_f")
            link(vt.tensor_reduce(exp_f, ec, AX, ALU.add))
            link(vt.tensor_scalar(exp_f, exp_f, float(NE - 1), None, ALU.min))
            link(vt.tensor_copy(c.tile_expert[:], exp_f[0:1, :]))

            rk, bs, flo, lo, hi = c.A("rk"), c.A("bs"), c.A("flo"), c.A("lo"), c.A("hi")
            ranked = cb[:, 0:TE]
            link(vt.tensor_copy(ranked, ps[1][:, 0:TE]))
            for q, m in enumerate((mask0, mask1)):
                pick(m, e3(ranked), rk[:, q * TILES:(q + 1) * TILES])
                pick(m, base.unsqueeze(1).to_broadcast([P, TILES, NE]), bs[:, q * TILES:(q + 1) * TILES])
            N2 = 2 * TILES
            fc = c.A("flo_cmp").rearrange("p (n j) -> p n j", j=NT)
            link(vt.tensor_tensor(fc, rk.unsqueeze(2).to_broadcast([P, N2, NT]),
                                  tab("thr9", 9)[:, 1:9].unsqueeze(1).to_broadcast([P, N2, NT]), ALU.is_ge))
            link(vt.tensor_reduce(flo, fc, AX, ALU.add))
            link(vt.scalar_tensor_tensor(lo, flo, -float(P), rk, ALU.mult, ALU.add))
            link(vt.tensor_tensor(hi, bs, flo, ALU.add))
            link(vt.scalar_tensor_tensor(c.A("slot_f"), hi, float(P), lo, ALU.mult, ALU.add))
            link(vt.tensor_copy(c.slot[:], c.A("slot_f")))
            link(vt.tensor_tensor(one_lo, lo.unsqueeze(2).to_broadcast([P, N2, P]),
                                  tab("iota128", P).unsqueeze(1).to_broadcast([P, N2, P]), ALU.is_equal))
            link(vt.tensor_tensor(one_hi, hi.unsqueeze(2).to_broadcast([P, N2, MOE_TILES]),
                                  tab("iota32", MOE_TILES).unsqueeze(1).to_broadcast([P, N2, MOE_TILES]), ALU.is_equal))
            for q in range(2):
                x = one_hi[:, q * TILES:(q + 1) * TILES, :]
                ins = vt.tensor_tensor(x, x, tab("token", TILES).unsqueeze(2).to_broadcast([P, TILES, MOE_TILES]), ALU.mult)
                if q == 0:
                    link(ins)
            ins.then_inc(onehots, 1)
            dve.wait_ge(rows_ok, 1)
            link(vt.tensor_copy(c.row_token[:], ps[3][:, 0:MOE_TILES]))


def stage_experts(c):
    nc, T, K = c.nc, c.T, c.K
    EW = KC * DE
    c.place(start=0, xw=4 * 3 * EW)
    xw = c.A("xw").rearrange("p (s n) -> p s n", s=4)
    guv = [xw[:, u, 0:2 * EW].rearrange("p (g k f) -> p g k f", g=2, k=KC) for u in range(4)]
    wdv = [xw[:, u, 2 * EW:].rearrange("p (j n) -> p j n", j=2) for u in range(4)]
    free = c.hT.rearrange("p k t -> p (k t)")
    x = free[:, 0:2 * D].rearrange("p (s d) -> p s d", s=2)
    xT = free[:, 2 * D:4 * D].rearrange("p (s k t) -> p s k t", s=2, k=KC)
    y = free[:, 4 * D:6 * D].rearrange("p (s d) -> p s d", s=2)
    sg = free[:, 6 * D:6 * D + 2 * DE].rearrange("p (s f) -> p s f", s=2)
    hid = free[:, 6 * D + 2 * DE:6 * D + 4 * DE].rearrange("p (s f) -> p s f", s=2)
    hidT = free[:, 6 * D + 4 * DE:6 * D + 6 * DE].rearrange("p (s j t) -> p s j t", s=2, j=2)
    ps, h = c.ps, c.h
    s = lambda n: c.sem(f"x{n}")
    w_in = [s(f"w{u}") for u in range(4)]
    x_in = [s(f"x{u}") for u in range(2)]
    y_out = [s(f"y{u}") for u in range(2)]
    xT_ok = [s(f"xT{q}") for q in range(2)]
    y_ok = [s(f"yok{q}") for q in range(2)]
    x_turned, up, sig, hid_ok, hid_turned, hidT_ok, down, scaled = (
        s("xturned"), s("up"), s("sig"), s("hid"), s("hturned"), s("hidT"), s("down"), s("scaled"))
    U = 4
    J = MOE_TILES // U
    XT, UPB, HT, DNB = (0, 1), (2, 3), 4, (6, 7)

    with nc.Block() as block:
        @block.gpsimd
        def _(gp):
            for t in range(MOE_TILES):
                if t >= 2:
                    gp.wait_ge(x_turned, 2 * t - 2)
                gp.indirect_dma_start(x[:, t % 2, :], None, c.tokens_dram,
                                      bass.IndirectOffsetOnAxis(ap=c.row_token[:, t:t + 1], axis=0)).then_inc(x_in[t % 2], 16)

        @block.tensor
        def _(pe):
            def turn_x(j, u):
                t = j * U + u
                pe.wait_ge(x_in[u % 2], 16 * (j * 2 + u // 2 + 1))
                for q in range(2):
                    if not (isinstance(j, int) and t < 1):
                        pe.wait_ge(xT_ok[q], t)
                    for k in range(4):
                        last = nc.tensor.transpose(ps[XT[q]][:, k * P:(k + 1) * P], x[:, u % 2, slice(4 * q + k, D, KC)],
                                                   K("ident"))
                    last.then_inc(x_turned, 1)

            def gate_up(j, u, half):
                t = j * U + u
                if half == 0:
                    pe.wait_ge(w_in[u], 48 * (j + 1))
                    pe.wait_ge(xT_ok[0], t + 1)
                    pe.wait_ge(xT_ok[1], t + 1)
                    if not (isinstance(j, int) and t < 2):
                        pe.wait_ge(hid_ok, t - 1)
                for k in range(4 * half, 4 * half + 4):
                    last = nc.tensor.matmul(ps[UPB[u % 2]][:, :], xT[:, u % 2, k, :], guv[u][:, :, k, :], start=(k == 0), stop=(k == KC - 1))
                if half == 1:
                    last.then_inc(up, 1)

            def turn_hid(j, u):
                t = j * U + u
                pe.wait_ge(hid_ok, t + 1)
                if not (isinstance(j, int) and t < 1):
                    pe.wait_ge(hidT_ok, t)
                for f in range(2):
                    last = nc.tensor.transpose(ps[HT][:, f * P:(f + 1) * P], hid[:, u % 2, slice(f, DE, 2)], K("ident"))
                last.then_inc(hid_turned, 1)

            def product_down(j, u):
                t = j * U + u
                pe.wait_ge(hidT_ok, t + 1)
                for q in range(2):
                    if not (isinstance(j, int) and t < 1):
                        pe.wait_ge(y_ok[q], t)
                    for f in range(2):
                        last = nc.tensor.matmul(ps[DNB[q]][:, :], hidT[:, u % 2, f, :], wdv[u][:, f, q * 512:(q + 1) * 512],
                                                start=(f == 0), stop=(f == 1))
                    last.then_inc(down, 1)

            def step(j, u, first, last):
                prev = (j, u - 1) if u else (j - 1, U - 1)
                gate_up(j, u, 0)
                if not first:
                    turn_hid(*prev)
                gate_up(j, u, 1)
                if not last:
                    turn_x(*((j, u + 1) if u < U - 1 else (j + 1, 0)))
                if not first:
                    product_down(*prev)

            turn_x(0, 0)
            for u in range(U):
                step(0, u, u == 0, False)
            with pe.Fori(1, J - 1) as j:
                for u in range(U):
                    step(j, u, False, False)
            for u in range(U):
                step(J - 1, u, False, u == U - 1)
            turn_hid(J - 1, U - 1)
            product_down(J - 1, U - 1)

        @block.scalar
        def _(act):
            def load(j, u):
                t = j * U + u
                e = act.value_load(c.tile_expert[0:1, bass.ds(t, 1)], min_val=0, max_val=NE - 1)
                for wname, dst in (('ex_wg', xw[:, u, 0:EW]), ('ex_wu', xw[:, u, EW:2 * EW]), ('ex_wd', xw[:, u, 2 * EW:])):
                    act.dma_start(dst, T[wname][0][bass.ds(e, 1)].rearrange("a (p k) f -> p (a k f)", p=P)).then_inc(w_in[u], 16)

            def turned_x(t, u):
                act.wait_ge(x_turned, 2 * t + 1)
                nc.scalar.copy(xT[:, u % 2, 0:4, :], ps[XT[0]][:, :].rearrange("p (k t) -> p k t", k=4)).then_inc(xT_ok[0], 1)

            def turned_hid(t, u):
                act.wait_ge(hid_turned, t + 1)
                nc.scalar.copy(hidT[:, u % 2], ps[HT][:, 0:DE].rearrange("p (f t) -> p f t", f=2)).then_inc(hidT_ok, 1)

            def silu(t, u, first):
                act.wait_ge(up, t + 1)
                if not first:
                    act.wait_ge(hid_ok, t - 1)
                nc.scalar.activation(sg[:, u % 2, :], ps[UPB[u % 2]][:, 0:DE], ACT.Silu).then_inc(sig, 1)

            def finish(t, j2, u, first):
                act.wait_ge(down, 2 * t + 1)
                if not first:
                    act.wait_ge(y_out[u % 2], 16 * j2)
                nc.scalar.copy(y[:, u % 2, 0:512], ps[DNB[0]][:, :]).then_inc(y_ok[0], 1)
                act.wait_ge(y_ok[0], t + 1)
                act.wait_ge(y_ok[1], t + 1)
                act.dma_start(c.rows_dram[bass.ds(t, 1)].rearrange("a p d -> (a p) d"), y[:, u % 2, :]).then_inc(y_out[u % 2], 16)

            def step(j, u, first, last):
                t = j * U + u
                if not (first and u == 0):
                    turned_hid(j * U + u - 1, (u - 1) % U)
                silu(t, u, first and u < 2)
                if not (last and u == U - 1):
                    turned_x(j * U + u + 1, (u + 1) % U)
                if not (first and u == 0):
                    finish(j * U + u - 1, j * 2 + (u - 1) // 2, (u - 1) % U, first and u < 3)
                    if not (last and u > 0):
                        load(*((j + 1, u - 1) if u else (j, U - 1)))

            for u in range(U):
                load(0, u)
            turned_x(0, 0)
            for u in range(U):
                step(0, u, True, False)
            with act.Fori(1, J - 1) as j:
                for u in range(U):
                    step(j, u, False, False)
            for u in range(U):
                step(J - 1, u, False, True)
            turned_hid(MOE_TILES - 1, U - 1)
            finish(MOE_TILES - 1, (MOE_TILES - 1) // 2, U - 1, False)
            for u in range(2):
                act.wait_ge(y_out[u], 16 * MOE_TILES // 2)

        @block.vector
        def _(dve):
            def hidden(t, u):
                dve.wait_ge(sig, t + 1)
                nc.vector.tensor_tensor(hid[:, u % 2, :], ps[UPB[u % 2]][:, DE:2 * DE], sg[:, u % 2, :], ALU.mult).then_inc(hid_ok, 1)

            def turned_x(t, u):
                dve.wait_ge(x_turned, 2 * t + 2)
                nc.vector.tensor_copy(xT[:, u % 2, 4:8, :], ps[XT[1]][:, :].rearrange("p (k t) -> p k t", k=4)).then_inc(xT_ok[1], 1)

            def finish(t, j2, u, first):
                dve.wait_ge(down, 2 * t + 2)
                if not first:
                    dve.wait_ge(y_out[u % 2], 16 * j2)
                nc.vector.tensor_copy(y[:, u % 2, 512:D], ps[DNB[1]][:, :]).then_inc(y_ok[1], 1)

            def step(j, u, first, last):
                hidden(j * U + u, u)
                if not (last and u == U - 1):
                    turned_x(j * U + u + 1, (u + 1) % U)
                if not (first and u == 0):
                    finish(j * U + u - 1, j * 2 + (u - 1) // 2, (u - 1) % U, first and u < 3)

            turned_x(0, 0)
            nc.vector.tensor_scalar(h[:, 0:NT, :], h[:, 0:NT, :], ALPHA, None, ALU.mult).then_inc(scaled, 1)
            nc.vector.tensor_scalar(h[0:NS, NT, :], h[0:NS, NT, :], ALPHA, None, ALU.mult).then_inc(scaled, 1)
            for u in range(U):
                step(0, u, True, False)
            with dve.Fori(1, J - 1) as j:
                for u in range(U):
                    step(j, u, False, False)
            for u in range(U):
                step(J - 1, u, False, True)
            finish(MOE_TILES - 1, (MOE_TILES - 1) // 2, U - 1, False)


def stage_combine(c):
    nc, T, O = c.nc, c.T, c.O
    S = 6
    c.place(start=0, z=S * D, cg=D, cb=D)
    z = c.A("z").rearrange("p (s d) -> p s d", s=S)
    g, b = c.A("cg"), c.A("cb")
    h = c.h
    s = lambda n: c.sem(f"c_{n}")
    z_in = [s(f"z{n}") for n in range(S)]
    ln_in, summed, stats, scaled, gained, normed, stored, dve_chain, act_chain = (
        s("ln"), s("summed"), s("stats"), s("scaled"), s("gained"), s("normed"), s("stored"), s("dve"), s("act"))

    with nc.Block() as block:
        @block.sync
        def _(sp):
            sp.dma_start(g, row_bc(T['ln3_g'][0])).then_inc(ln_in, 16)
            sp.dma_start(b, row_bc(T['ln3_b'][0])).then_inc(ln_in, 16)
            for i in range(TILES):
                sp.wait_ge(normed, i + 1)
                dst = O['y_prompt'][0, i * P:(i + 1) * P, :] if i < NT else O['y_sample'].rearrange("b t d -> (b t) d")
                sp.dma_start(dst, h[0:rows(i), i, :]).then_inc(stored, 16)
            sp.wait_ge(stored, 16 * TILES)

        @block.gpsimd
        def _(gp):
            def gather(n):
                i, q = n // 2, n % 2
                if n >= S:
                    gp.wait_ge(summed, n - S + 1)
                r = rows(i)
                gp.indirect_dma_start(z[0:r, n % S, :], None, c.rows_dram.rearrange("s p d -> (s p) d"),
                                      bass.IndirectOffsetOnAxis(ap=c.slot[0:r, q * TILES + i:q * TILES + i + 1], axis=0))\
                    .then_inc(z_in[n % S], 16)

            for n in range(S):
                gather(n)
            gp.wait_ge(ln_in, 32)
            for i in range(TILES):
                for n in (S + 2 * i, S + 2 * i + 1):
                    if n < 2 * TILES:
                        gather(n)
                r = rows(i)
                gp.wait_ge(gained, i + 1)
                nc.gpsimd.tensor_tensor(h[0:r, i, :], h[0:r, i, :], b[0:r, :], ALU.add).then_inc(normed, 1)

        @block.vector
        def _(dve):
            link = Chain(dve, dve_chain)

            def sum_up(i):
                r = rows(i)
                for q in range(2):
                    n = 2 * i + q
                    dve.wait_ge(z_in[n % S], 16 * (n // S + 1))
                    if q == 1:
                        dve.wait_ge(summed, n)
                    nc.vector.scalar_tensor_tensor(h[0:r, i, :], z[0:r, n % S, :], c.gate[0:r, q * TILES + i:q * TILES + i + 1],
                                                   h[0:r, i, :], ALU.mult, ALU.add).then_inc(summed, 1)
                dve.wait_ge(summed, 2 * i + 2)
                if i >= 2:
                    dve.wait_ge(scaled, i - 1)
                ln_stats(nc, link, h, i, c.st[:, i % 2, :], c.mv[:, i % 2, :]).then_inc(stats, 1)

            def gain(i):
                r = rows(i)
                dve.wait_ge(scaled, i + 1)
                nc.vector.tensor_tensor(h[0:r, i, :], h[0:r, i, :], g[0:r, :], ALU.mult).then_inc(gained, 1)

            for i in range(TILES):
                sum_up(i)
                if i == 0:
                    dve.wait_ge(ln_in, 32)
                if i >= 1:
                    gain(i - 1)
            gain(TILES - 1)

        @block.scalar
        def _(act):
            link = Chain(act, act_chain)
            nc.scalar.preload_act_table_set(EXPLN)
            for i in range(TILES):
                r = rows(i)
                act.wait_ge(stats, i + 1)
                mv, rstd, off = c.mv[:, i % 2, :], c.rstd[:, i % 2, :], c.off[:, i % 2:i % 2 + 1]
                link(ln_rstd(nc, link, i, mv, rstd, c.eps))
                link(nc.scalar.activation(off[0:r, :], mv[0:r, 0:1], ACT.Copy, scale=rstd[0:r, :]))
                link(nc.scalar.activation(off[0:r, :], off[0:r, :], ACT.Copy, scale=-1.0))
                nc.scalar.activation(h[0:r, i, :], h[0:r, i, :], ACT.Identity, bias=off[0:r, :], scale=rstd[0:r, :]).then_inc(scaled, 1)


def build(nc, T, O):
    with ExitStack() as ctx:
        c = setup(nc, ctx, T, O)
        c.tokens_dram = nc.dram_tensor("tokens", (TOK, D), F32, kind="Internal").ap()
        c.rows_dram = nc.dram_tensor("expert_rows", (MOE_TILES, P, D), F32, kind="Internal").ap()
        stage_entry(c)
        stage_features(c)
        stage_gate_and_pool(c)
        stage_stick_prompt(c)
        stage_stick_sample(c)
        stage_delta_inputs(c)
        stage_delta(c)
        c.renew_semaphores()
        c.res_at = 0
        stage_residual(c, "o", c.hT, 'w_out', 'ln1_g', 'ln1_b', True)
        stage_memory(c)
        stage_queries(c)
        stage_cross(c)
        c.res_at = 4096 + KC * TOK
        stage_residual(c, "w", c.qXT, 'xa_wo', 'ln2_g', 'ln2_b', True)
        stage_route(c)
        stage_experts(c)
        stage_combine(c)


def kernel(**inputs):
    import numpy as _np
    import concourse.bacc as _bacc
    from concourse import mybir as _mybir
    from concourse.bass_utils import run_bass_kernel_spmd as _run

    nc = _bacc.Bacc("TRN2", target_bir_lowering=False, num_devices=1)
    arrays, T, O = {}, {}, {}
    for name in _INS:
        a = _np.ascontiguousarray(inputs[name])
        arrays[f"in_{name}_dram"] = a
        T[name] = nc.dram_tensor(f"in_{name}_dram", a.shape, _mybir.dt.from_np(a.dtype), kind="ExternalInput").ap()
    for key, blocks in (('const_tables', CONSTS), ('pool_tables', POOL_CONSTS), ('route_table', ROUTE_CONSTS)):
        table = _np.concatenate(list(blocks.values()), axis=1)
        arrays[f"{key}_dram"] = table
        T[key] = nc.dram_tensor(f"{key}_dram", table.shape, F32, kind="ExternalInput").ap()
    for name, shape in _OUTS:
        O[name] = nc.dram_tensor(f"out_{name}_dram", shape, F32, kind="ExternalOutput").ap()
    build(nc, T, O)
    r = _run(nc, [arrays], core_ids=[0])
    return tuple(r.results[0][f"out_{name}_dram"] for name, _ in _OUTS)
```

```python
from contextlib import ExitStack

import numpy as np
import concourse.bass as bass
from concourse import mybir

F32 = mybir.dt.float32
I32 = mybir.dt.int32
R32 = mybir.dt.float32r
ALU = mybir.AluOpType
ACT = mybir.ActivationFunctionType
AX = mybir.AxisListType.X

P = 128
D = 1024
KC = D // P
SEQ = 1024
NT = SEQ // P
DB, DS = 8, 4
NS = DB * DS
TOK = SEQ + NS
TILES = NT + 1
GRP = 3
GT = TOK // GRP
PAGE = 128
NPG = 2
HEADS = 4
DH = 64
CH = 64
POOLB = 15
WINDOWS = (2, 4, 8, 16)
NMEM = 256
XDH = 256
NE = 16
DE = 256
MOE_TILES = (2 * TOK - NE) // P + NE
ALPHA = float(2 ** 0.25)
LN_EPS = 1e-5
QA, KA, VA, UB, VB, XC, QKV, ZG, BD = 0, 256, 512, 768, 1024, 1280, 1536, 2304, 2560

EXPLN = "natural_log_exp_and_others"


def rows(i):
    return P if i < NT else NS


def const_blocks():
    p = np.arange(P)[:, None]
    f = np.arange(P)[None, :]
    one = np.ones((P, P))
    chunk = p // CH == f // CH
    blk4 = p // DS == f // DS
    c = {
        "ident": p == f,
        "ones": one,
        "cum64": (p <= f) & chunk,
        "low64": (p > f) & chunk,
        "blk64": chunk,
        "negsuf": -1.0 * (p >= f),
        "negone": -one,
        "before": p < f,
        "upto": p <= f,
        "cum4": (p <= f) & blk4,
        "low4": (p > f) & blk4,
        "blk4": blk4,
        "before4": (p < f) & blk4,
        "rep4": np.where((p < DS) & (f % DS == p), 1.0, 0.0),
        "up1": (f % 2 == 1) & (p == f - 1),
    }
    for b in (1, 2, 4, 8, 16, 32):
        c[f"lvl{b}"] = (p // (2 * b) == f // (2 * b)) & ((p // b) % 2 == 1) & ((f // b) % 2 == 0)
    return {k: np.asarray(v, np.float32) for k, v in c.items()}


def pool_blocks():
    p = np.arange(P)[:, None]
    f = np.arange(P)[None, :]
    blk4 = p // DS == f // DS
    c = {}
    for g, w in enumerate(WINDOWS):
        c[f"band{g}"] = ((p <= f) & (p > f - w)) / w - 1.0 * (p == f)
        c[f"bandprev{g}"] = (p > f - w + P) / w
        c[f"bandfirst{g}"] = ((p <= f) & (p > f - w)) / np.minimum(f + 1, w) - 1.0 * (p == f)
        b_, q_ = p // POOLB, p % POOLB
        c[f"spool{g}"] = ((b_ == f // DS) & (q_ >= POOLB + 1 + f % DS - w) & (p < DB * POOLB) & (f < NS)) / w
        c[f"scur{g}"] = (blk4 & (p <= f) & (p > f - w)) / w - 1.0 * (p == f)
    return {k: np.asarray(v, np.float32) for k, v in c.items()}


CONSTS = const_blocks()
POOL_CONSTS = pool_blocks()
CONST_AT = {k: n * P for n, k in enumerate(CONSTS)}
POOL_AT = {k: n * P for n, k in enumerate(POOL_CONSTS)}
NCONST = len(CONSTS) * P


def route_blocks():
    p = np.arange(P)[:, None]
    row = lambda x: np.tile(np.asarray(x).reshape(1, -1), (P, 1))
    token = p + P * np.arange(TILES)[None, :]
    c = {
        "tie": row(np.arange(4)[None, :] < np.arange(4)[:, None]),
        "iota128": row(np.arange(P)),
        "iota32": row(np.arange(MOE_TILES)),
        "thr9": row(P * np.arange(9)),
        "tri16": row(np.arange(NE)[None, :] < np.arange(NE)[:, None]),
        "token": np.where(token < TOK, token, 0),
        "valid": token < TOK,
    }
    return {k: np.asarray(v, np.float32) for k, v in c.items()}


ROUTE_CONSTS = route_blocks()
ROUTE_AT, NROUTE = {}, 0
for _name, _block in ROUTE_CONSTS.items():
    ROUTE_AT[_name] = NROUTE
    NROUTE += _block.shape[1]

_INS = ['x_prompt', 'x_sample', 'cache_sb_k', 'cache_sb_v', 'state_pool', 'state_conv', 'state_delta',
        'cache_mem_k', 'cache_mem_v', 'page_table', 'mem_prompt', 'ln0_g', 'ln0_b', 'w_in', 'sb_bias',
        'gmlp_ln_g', 'gmlp_ln_b', 'gmlp_ws', 'gmlp_bs', 'pool_w', 'pool_gamma', 'conv_w', 'dn_a_log',
        'dn_dt_bias', 'dn_norm_g', 'w_out', 'ln1_g', 'ln1_b', 'xa_wq', 'xa_wk', 'xa_wv', 'xa_wo', 'ln2_g',
        'ln2_b', 'w_router', 'router_bias', 'ex_wg', 'ex_wu', 'ex_wd', 'ln3_g', 'ln3_b']
_OUTS = [('y_prompt', (1, SEQ, D)), ('y_sample', (DB, DS, D)),
         ('sb_k_prompt', (1, 1, SEQ, HEADS, DH)), ('sb_v_prompt', (1, 1, SEQ, HEADS, DH)),
         ('sb_k_sample', (1, DB, DS, HEADS, DH)), ('sb_v_sample', (1, DB, DS, HEADS, DH)),
         ('gmlp_v_sample', (1, DB, DS, 256)),
         ('pool_prompt', (1, 1, POOLB, 256)), ('pool_sample', (1, DB, POOLB, 256)),
         ('conv_prompt', (1, 1, 3, 768)), ('conv_sample', (1, DB, 3, 768)),
         ('delta_prompt', (1, 1, HEADS, DH, DH)), ('delta_sample', (1, DB, HEADS, DH, DH)),
         ('mem_k_prompt', (1, 1, NMEM, HEADS, XDH)), ('mem_v_prompt', (1, 1, NMEM, HEADS, XDH))]


class Chain:

    def __init__(self, eng, sem):
        self.eng, self.sem, self.n = eng, sem, 0

    def __call__(self, ins):
        self.n += 1
        ins.then_inc(self.sem, 1)
        self.eng.wait_ge(self.sem, self.n)


class Ctx:
    pass


def setup(nc, ctx, T, O):
    c = Ctx()
    c.nc, c.T, c.O = nc, T, O

    held, stack = [], [ctx.enter_context(ExitStack())]

    def sem(name):
        held.append(stack[0].enter_context(nc.semaphore(name)))
        return held[-1]

    def renew_semaphores():
        with nc.Block() as block:
            @block.sync
            def _(sp):
                for x in held:
                    sp.sem_clear(x)
        held.clear()
        stack[0].close()
        stack[0] = ctx.enter_context(ExitStack())

    c.sem, c.renew_semaphores = sem, renew_semaphores
    c.ps = [ctx.enter_context(nc.psum_tensor(f"bank{b}", [P, 512], F32)) for b in range(8)]
    c.const = ctx.enter_context(nc.sbuf_tensor("const", [P, NCONST], F32))
    c.h = ctx.enter_context(nc.sbuf_tensor("h", [P, TILES, D], F32))
    c.hT = ctx.enter_context(nc.sbuf_tensor("hT", [P, KC, TOK], F32))
    c.small = ctx.enter_context(nc.sbuf_tensor("small", [P, 1024], F32))
    hT_at = nc.sbuf_base - 4 * KC * TOK - 4 * 1024
    AR = 31600
    arena_at = nc.sbuf_base
    c.arena = ctx.enter_context(nc.sbuf_tensor("arena", [P, AR], F32))
    assert nc.sbuf_base == arena_at + 4 * AR, (nc.sbuf_base, arena_at)
    c.at = {}
    c.small_used = 0

    def K(name, r=P, w=P):
        a = CONST_AT[name]
        return c.const[0:r, a:a + w]

    c.K = K

    def place(**sizes):
        at = sizes.pop("start", 0)
        for k, n in sizes.items():
            assert at + n <= AR, (k, at, n)
            c.at[k] = (at, n)
            at += n
        return at

    def A(k):
        a, n = c.at[k]
        return c.arena[:, a:a + n]

    def rounded(name, key):
        a, n = c.at[key]
        return nc.alloc_sbuf_tensor_at(name, [P, n], R32, offset=arena_at + 4 * a)[:, :]

    c.place, c.A, c.rounded = place, A, rounded
    h_at = hT_at - 4 * TILES * D

    def rounded_in_h(name, at, n):
        return nc.alloc_sbuf_tensor_at(name, [P, n], R32, offset=h_at + 4 * at)[:, :]

    c.rounded_in_h = rounded_in_h
    c.hT_rest = nc.alloc_sbuf_tensor_at("hT_rest", [P, KC * TOK], R32, offset=hT_at)[:, :].rearrange("p (k t) -> p k t", k=KC)
    c.hT_high = nc.alloc_sbuf_tensor_at("hT_high", [P, KC * TOK], R32, offset=hT_at)[:, :].rearrange("p (k t) -> p k t", k=KC)

    def small(n):
        a = c.small_used
        c.small_used += n
        assert c.small_used <= 1024
        return c.small[:, a:a + n]

    c.new_small = small
    c.slot = ctx.enter_context(nc.sbuf_tensor("slot", [P, 2 * TILES], I32))
    c.row_token = ctx.enter_context(nc.sbuf_tensor("row_token", [P, MOE_TILES], I32))
    c.tile_expert = ctx.enter_context(nc.sbuf_tensor("tile_expert", [1, MOE_TILES], I32))
    c.expert_end = ctx.enter_context(nc.sbuf_tensor("expert_end", [1, NE], I32))
    c.gate, c.off = small(2 * TILES), small(2)
    c.ids = ctx.enter_context(nc.sbuf_tensor("page_ids", [1, DB * NPG], I32))
    return c


def row_bc(ap, n=P):
    return ap.partition_broadcast(n)


def x_tile(T, i):
    if i < NT:
        return T['x_prompt'][0, i * P:(i + 1) * P, :]
    return T['x_sample'].rearrange("b t d -> (b t) d")


def ln_stats(nc, link, h, i, st, mv):
    r = rows(i)
    nc.vector.bn_stats(st[0:r, 0:6], h[0:r, i, 0:512])
    link(nc.vector.bn_stats(st[0:r, 6:12], h[0:r, i, 512:1024]))
    return nc.vector.bn_aggr(mv[0:r, :], st[0:r, :])


def ln_rstd(nc, link, i, mv, rstd, eps):
    r = rows(i)
    link(nc.scalar.activation(rstd[0:r, :], mv[0:r, 1:2], ACT.Ln, bias=eps[0:r, :]))
    return nc.scalar.activation(rstd[0:r, :], rstd[0:r, :], ACT.Exp, scale=-0.5)


def ln_apply(nc, link, h, i, mv, rstd, g, b):
    r = rows(i)
    link(nc.vector.tensor_scalar(h[0:r, i, :], h[0:r, i, :], mv[0:r, 0:1], rstd[0:r, :],
                                 ALU.subtract, ALU.mult))
    link(nc.vector.tensor_tensor(h[0:r, i, :], h[0:r, i, :], g[0:r, :], ALU.mult))
    return nc.vector.tensor_tensor(h[0:r, i, :], h[0:r, i, :], b[0:r, :], ALU.add)


def stage_entry(c):
    nc, T, O, K = c.nc, c.T, c.O, c.K
    c.free_at = c.place(kT=2 * TOK, vtok=TILES * 256, zT=2 * TOK)
    c.after_q = c.place(start=c.free_at, qkvT=6 * TOK, qT=2 * TOK)
    at = c.place(start=c.after_q, vg=TILES * 256, xc=TILES * 256, uT=2 * TOK)
    c.place(start=c.free_at, wtok=KC * 1032)
    c.place(start=at, ring=2 * KC * P, lng=D, lnb=D, ktok=2 * 256)
    c.f_w_in = [c.sem(f"f_w{n}") for n in range(2)]
    c.scratch = at
    kT = c.A("kT").rearrange("p (c t) -> p c t", c=2)
    vtok = c.A("vtok").rearrange("p (i n) -> p i n", i=TILES)
    vg = c.A("vg").rearrange("p (i n) -> p i n", i=TILES)
    xc = c.A("xc").rearrange("p (i n) -> p i n", i=TILES)
    wt = c.A("wtok").rearrange("p (k n) -> p k n", k=KC)
    ktok = c.A("ktok").rearrange("p (s n) -> p s n", s=2)
    g, b = c.A("lng"), c.A("lnb")
    c.kT, c.vtok, c.vg, c.xc = kT, vtok, vg, xc
    c.ba = c.new_small(TILES * 8).rearrange("p (i n) -> p i n", i=TILES)
    c.st = c.new_small(2 * 12).rearrange("p (s n) -> p s n", s=2)
    c.mv = c.new_small(2 * 2).rearrange("p (s n) -> p s n", s=2)
    c.rstd = c.new_small(2).rearrange("p (s n) -> p s n", s=2)
    c.eps = c.new_small(1)
    h, hT, ps = c.h, c.hT, c.ps

    s = c.sem
    x_in = [s(f"e_x{n}") for n in range(3)]
    h_out = s("e_h")
    w_in, const_in, ln_in = s("e_w"), s("e_const"), s("e_ln")
    eps_set, stats, rstd_ok, normed = s("e_eps"), s("e_stats"), s("e_rstd"), s("e_normed")
    turned, hT_ok, proj_kv, proj_vx, proj_ba = s("e_turned"), s("e_hT"), s("e_kv"), s("e_vx"), s("e_ba")
    kv_out, vx_out, ba_out, k_turned, kT_ok = s("e_kvo"), s("e_vxo"), s("e_bao"), s("e_kt"), s("e_kTo")
    stored = [s("e_stored0"), s("e_stored1")]
    dve_chain, act_chain, zeroed = s("e_dve"), s("e_act"), s("e_zero")
    w_view = T['w_in'][0].rearrange("(k p) n -> p k n", p=P)

    with nc.Block() as block:
        @block.sync
        def _(sp):
            for i in range(TILES):
                sp.dma_start(h[0:rows(i), i, :], x_tile(T, i)).then_inc(x_in[min(i // 2, 2)], 16)
                if i == 0:
                    sp.dma_start(g, row_bc(T['ln0_g'])).then_inc(ln_in, 16)
                    sp.dma_start(b, row_bc(T['ln0_b'])).then_inc(ln_in, 16)
                if i == 1:
                    sp.dma_start(wt[:, :, 0:512], w_view[:, :, KA:KA + 512]).then_inc(w_in, 16)
                    sp.dma_start(wt[:, :, 512:1024], w_view[:, :, VB:VB + 512]).then_inc(w_in, 16)
                    sp.dma_start(wt[:, :, 1024:1032], w_view[:, :, BD:BD + 8]).then_inc(w_in, 16)
            for n in range(2):
                sp.dma_start(c.A("ring").rearrange("p (s k n) -> p s k n", s=2, k=KC)[:, n],
                             w_view[:, :, QKV + P * n:QKV + P * (n + 1)]).then_inc(c.f_w_in[n], 16)
            for i in range(TILES):
                sp.wait_ge(normed, i + 1)
                sp.dma_start(c.tokens_dram[i * P:i * P + rows(i), :], h[0:rows(i), i, :]).then_inc(h_out, 16)
                sp.wait_ge(kv_out, 2 * i + 2)
                if i < NT:
                    ko = O['sb_k_prompt'][0, 0, i * P:(i + 1) * P].rearrange("t h d -> t (h d)")
                    vo = O['sb_v_prompt'][0, 0, i * P:(i + 1) * P].rearrange("t h d -> t (h d)")
                else:
                    ko = O['sb_k_sample'][0].rearrange("b t h d -> (b t) (h d)")
                    vo = O['sb_v_sample'][0].rearrange("b t h d -> (b t) (h d)")
                sp.dma_start(ko, ktok[0:rows(i), i % 2, :]).then_inc(stored[i % 2], 16)
                sp.dma_start(vo, vtok[0:rows(i), i, :]).then_inc(stored[i % 2], 16)
            sp.wait_ge(stored[0], 32 * 5)
            sp.wait_ge(stored[1], 32 * 4)
            sp.wait_ge(h_out, 16 * TILES)

        @block.vector
        def _(dve):
            link = Chain(dve, dve_chain)
            nc.vector.memset(c.eps, LN_EPS).then_inc(eps_set, 1)
            nc.vector.memset(vg[:, NT, :], 0.0).then_inc(zeroed, 1)
            nc.vector.memset(c.ba[:, NT, :], 0.0).then_inc(zeroed, 1)
            dve.wait_ge(zeroed, 2)

            def evac_ba(i):
                dve.wait_ge(proj_ba, i + 1)
                nc.vector.tensor_copy(c.ba[0:rows(i), i, :], ps[4][0:rows(i), 0:8]).then_inc(ba_out, 1)

            for i in range(TILES):
                dve.wait_ge(x_in[min(i // 2, 2)], 32 if i < 4 else 16 * (TILES - 4))
                if i >= 2:
                    dve.wait_ge(rstd_ok, i - 1)
                ln_stats(nc, link, h, i, c.st[:, i % 2, :], c.mv[:, i % 2, :]).then_inc(stats, 1)
                if i == 0:
                    dve.wait_ge(ln_in, 32)
                dve.wait_ge(stats, i + 1)
                dve.wait_ge(rstd_ok, i + 1)
                ln_apply(nc, link, h, i, c.mv[:, i % 2, :], c.rstd[:, i % 2, :], g, b).then_inc(normed, 1)
                if i >= 2:
                    evac_ba(i - 2)
            evac_ba(TILES - 2)
            evac_ba(TILES - 1)

        @block.scalar
        def _(act):
            link = Chain(act, act_chain)
            act.dma_start(c.const[:, :], T['const_tables']).then_inc(const_in, 16)
            nc.scalar.preload_act_table_set(EXPLN)
            act.wait_ge(eps_set, 1)
            act.wait_ge(zeroed, 2)

            def evac(i):
                r = rows(i)
                act.wait_ge(proj_kv, i + 1)
                if i >= 2:
                    act.wait_ge(k_turned, i - 1)
                    act.wait_ge(stored[i % 2], 32 * (i // 2))
                nc.scalar.copy(ktok[0:r, i % 2, :], ps[2 + 4 * (i % 2)][0:r, 0:256]).then_inc(kv_out, 1)
                nc.scalar.copy(vtok[0:r, i, :], ps[2 + 4 * (i % 2)][0:r, 256:512]).then_inc(kv_out, 1)
                act.wait_ge(proj_vx, i + 1)
                nc.scalar.copy(vg[0:r, i, :], ps[3 + 4 * (i % 2)][0:r, 0:256]).then_inc(vx_out, 1)
                nc.scalar.copy(xc[0:r, i, :], ps[3 + 4 * (i % 2)][0:r, 256:512]).then_inc(vx_out, 1)

            def evac_kT(i):
                r = rows(i)
                act.wait_ge(k_turned, i + 1)
                nc.scalar.copy(kT[:, :, i * P:i * P + r],
                               ps[5][:, 0:2 * r].rearrange("p (c t) -> p c t", c=2)).then_inc(kT_ok, 1)

            def deviation(i):
                act.wait_ge(stats, i + 1)
                if i >= 2:
                    act.wait_ge(normed, i - 1)
                ln_rstd(nc, link, i, c.mv[:, i % 2, :], c.rstd[:, i % 2, :], c.eps).then_inc(rstd_ok, 1)

            deviation(0)
            for i in range(TILES + 2):
                if i < TILES:
                    r = rows(i)
                    if i + 1 < TILES:
                        deviation(i + 1)
                    for q in range(2):
                        act.wait_ge(turned, 2 * i + q + 1)
                        nc.scalar.copy(hT[:, 4 * q:4 * q + 4, i * P:i * P + r],
                                       ps[q][:, 0:4 * r].rearrange("p (k t) -> p k t", k=4)).then_inc(hT_ok, 1)
                if 1 <= i <= TILES:
                    evac(i - 1)
                if i >= 2:
                    evac_kT(i - 2)

        @block.tensor
        def _(pe):
            pe.wait_ge(const_in, 16)

            def turn(i):
                r = rows(i)
                pe.wait_ge(normed, i + 1)
                for q in range(2):
                    if i >= 1:
                        pe.wait_ge(hT_ok, 2 * (i - 1) + q + 1)
                    for k in range(4):
                        last = nc.tensor.transpose(ps[q][:, k * r:(k + 1) * r],
                                                   h[0:r, i, (4 * q + k) * P:(4 * q + k + 1) * P], K("ident", r, r))
                    last.then_inc(turned, 1)

            def project(i):
                r = rows(i)
                pe.wait_ge(hT_ok, 2 * i + 2)
                for bank, col, n, out_sem, free in ((2 + 4 * (i % 2), 0, 512, proj_kv, kv_out),
                                                    (3 + 4 * (i % 2), 512, 512, proj_vx, vx_out),
                                                    (4, 1024, 8, proj_ba, ba_out)):
                    if bank == 4:
                        if i >= 1:
                            pe.wait_ge(free, i)
                    elif i >= 2:
                        pe.wait_ge(free, 2 * (i - 1))
                    for k in range(KC):
                        last = nc.tensor.matmul(ps[bank][0:r, 0:n], hT[:, k, i * P:i * P + r],
                                                wt[:, k, col:col + n], start=(k == 0), stop=(k == KC - 1))
                    last.then_inc(out_sem, 1)

            def turn_k(i):
                r = rows(i)
                pe.wait_ge(kv_out, 2 * i + 1)
                if i >= 1:
                    pe.wait_ge(kT_ok, i)
                for q in range(2):
                    last = nc.tensor.transpose(ps[5][:, q * r:(q + 1) * r], ktok[0:r, i % 2, q * P:(q + 1) * P],
                                               K("ident", r, r))
                last.then_inc(k_turned, 1)

            turn(0)
            pe.wait_ge(w_in, 48)
            for i in range(TILES):
                if i + 1 < TILES:
                    turn(i + 1)
                project(i)
                if i >= 1:
                    turn_k(i - 1)
            turn_k(TILES - 1)


def stage_features(c):
    nc, T, O, K = c.nc, c.T, c.O, c.K
    KA_ = 5
    c.place(start=c.scratch, ring=2 * KC * P, rhigh=2 * KC * P, glng=256, glnb=256, hTh=KA_ * TOK)
    rview = lambda x: x.rearrange("p (s k n) -> p s k n", s=2, k=KC)
    ring, wlow, whigh = rview(c.A("ring")), rview(c.rounded("f_w_low", "ring")), rview(c.rounded("f_w_high", "rhigh"))
    part = [(c.rounded("f_h_high_a", "hTh").rearrange("p (k t) -> p k t", k=KA_), slice(0, KA_)),
            (c.rounded_in_h("f_h_high_b", 4096, (KC - KA_) * TOK).rearrange("p (k t) -> p k t", k=KC - KA_), slice(KA_, KC))]
    hlow = c.hT_rest
    hhigh = lambda k, t: part[0][0][:, k, t] if k < KA_ else part[1][0][:, k - KA_, t]
    qT = c.A("qT").rearrange("p (c t) -> p c t", c=2)
    uT = c.A("uT").rearrange("p (c t) -> p c t", c=2)
    zT = c.A("zT").rearrange("p (c t) -> p c t", c=2)
    qkvT = c.A("qkvT").rearrange("p (c t) -> p c t", c=6)
    c.qT, c.uT, c.zT, c.qkvT = qT, uT, zT, qkvT
    hT, ps = c.hT, c.ps
    plan = ([(QKV + P * n, qkvT[:, n], "copy") for n in range(6)] + [(ZG + P * n, zT[:, n], "silu") for n in range(2)]
            + [(UB + P * n, uT[:, n], "gelu") for n in range(2)] + [(QA + P * n, qT[:, n], "scale") for n in range(2)])
    spare = c.h.rearrange("p i d -> p (i d)")
    c.xs = spare[:, 0:336].rearrange("p (c b t) -> p c b t", c=6, b=DB)
    c.tail = spare[:, 714:714 + 6 * (3 + NS)].rearrange("p (c t) -> p c t", c=6)
    c.pages = spare[:, 1024:9216].rearrange("p (s g n) -> p s g n", s=2, n=256)
    cw = spare[:, 354:522].rearrange("p (c n) -> p c n", c=6)
    ys = spare[:, 522:714].rearrange("p (c b t) -> p c b t", c=6, b=DB)
    cs = spare[:, 1024:1792]
    y = spare[:, 2048:4096].rearrange("p (s t) -> p s t", s=2)
    xs, tail = c.xs, c.tail
    G0 = 4096 + (KC - KA_) * TOK
    c.ws = spare[:, G0:G0 + 512].rearrange("p (g s) -> p g s", g=HEADS)
    c.bs, c.prev, c.gam = spare[:, G0 + 512:G0 + 1024], spare[:, G0 + 1024:G0 + 1280], spare[:, G0 + 1280:G0 + 1282]
    c.pw = spare[:, G0 + 1282:G0 + 1538].rearrange("p (c s) -> p c s", c=2)
    s = c.sem
    w_in = c.f_w_in
    hh_ok, hl_ok, wh_ok, wl_ok, gelu_ok = s("f_hh"), s("f_hl"), s("f_wh"), s("f_wl"), s("f_gelu")
    ln_in, product, evacuated = s("f_ln"), s("f_prod"), s("f_evac")
    stats, rstd_ok, normed, stored = s("f_stats"), s("f_rstd"), s("f_normed"), s("f_stored")
    c.gp_in, pw_zero = s("g_load"), s("g_zero")
    cs_in, cw_mm, cw_ok, staged, conv_ok, silu_ok = (s("f_cs"), s("f_cwmm"), s("f_cwok"), s("f_staged"),
                                                            s("f_conv"), s("f_silu"))
    dve_chain, act_chain = s("f_dve"), s("f_act")
    w_view = T['w_in'][0].rearrange("(k p) n -> p k n", p=P)
    vg = c.vg.rearrange("p i (g d) -> p (i g) d", g=HEADS)
    vsq = spare[:, 1792:4096].rearrange("p (m d) -> p m d", d=DH)
    mom = c.new_small(2 * TILES * HEADS).rearrange("p (s n) -> p s n", s=2)
    NG = TILES * HEADS

    with nc.Block() as block:
        @block.sync
        def _(sp):
            for n, (col, _, _) in enumerate(plan):
                if n >= 2:
                    sp.wait_ge(product, GRP * (n - 1))
                    sp.dma_start(ring[:, n % 2], w_view[:, :, col:col + P]).then_inc(w_in[n % 2], 16)
                if n == 1:
                    sp.dma_start(cs[0:24, :], T['state_conv'][0].rearrange("b t n -> (b t) n")).then_inc(cs_in, 16)
                    sp.dma_start(cs[24:28, :], T['conv_w'][0]).then_inc(cs_in, 16)
                if n == 5:
                    sp.dma_start(c.ws, T['gmlp_ws'][0].rearrange("g t s -> t g s")).then_inc(c.gp_in, 16)
                    sp.dma_start(c.bs[0:1, :], T['gmlp_bs'].rearrange("a g s -> a (g s)")).then_inc(c.gp_in, 16)
                    sp.dma_start(c.prev[0:DB * POOLB, :], T['state_pool'][0].rearrange("b q n -> (b q) n")).then_inc(c.gp_in, 16)
                    for m in range(2):
                        sp.dma_start(c.gam[:, m:m + 1], T['pool_gamma'][0, m * P:(m + 1) * P].unsqueeze(1)).then_inc(c.gp_in, 16)
                    sp.wait_ge(pw_zero, 1)
                    for g in range(HEADS):
                        q = (g % 2) * DH
                        sp.dma_start(c.pw[q:q + DH, g // 2, q:q + DH], T['pool_w'][0, g]).then_inc(c.gp_in, 16)
                if n == 0:
                    sp.dma_start(c.A("glng"), row_bc(T['gmlp_ln_g'][0].rearrange("g d -> (g d)"))).then_inc(ln_in, 16)
                    sp.dma_start(c.A("glnb"), row_bc(T['gmlp_ln_b'][0].rearrange("g d -> (g d)"))).then_inc(ln_in, 16)
            sp.wait_ge(normed, 1)
            sp.dma_start(O['gmlp_v_sample'][0].rearrange("b t n -> (b t) n"), c.vg[0:NS, NT, :]).then_inc(stored, 16)
            sp.wait_ge(stored, 16)

        @block.gpsimd
        def _(pool):
            nc.gpsimd.memset(c.pw, 0.0).then_inc(pw_zero, 1)

        @block.tensor
        def _(pe):
            for n in range(len(plan)):
                pe.wait_ge(wl_ok, n + 1)
                if n == 2:
                    pe.wait_ge(cs_in, 32)
                for g in range(GRP):
                    u = GRP * n + g
                    b = u % 7
                    if u >= 7:
                        pe.wait_ge(evacuated, u - 6)
                    if n == 0:
                        pe.wait_ge(hl_ok, 2 * g + 2)
                    t = slice(g * GT, (g + 1) * GT)
                    for k in range(KC):
                        last = three_passes(nc, ps[b][:, 0:GT], whigh[:, n % 2, k, :], wlow[:, n % 2, k, :],
                                            hhigh(k, t), hlow[:, k, t], k == 0, k == KC - 1)
                    last.then_inc(product, 1)
                if n == 2:
                    for m in range(6):
                        last = nc.tensor.transpose(ps[7][:, m * 28:(m + 1) * 28], cs[0:28, m * P:(m + 1) * P],
                                                   K("ident", 28, 28))
                    last.then_inc(cw_mm, 1)

        @block.scalar
        def _(act):
            link = Chain(act, act_chain)

            def conv_silu(n):
                act.wait_ge(conv_ok, n + 1)
                nc.scalar.activation(qkvT[:, n, 0:SEQ], y[:, n % 2, :], ACT.Silu).then_inc(silu_ok, 1)
                nc.scalar.activation(qkvT[:, n, SEQ:TOK].rearrange("p (b t) -> p b t", b=DB), ys[:, n], ACT.Silu).then_inc(silu_ok, 1)

            def round_h(g):
                t = slice(g * GT, (g + 1) * GT)
                for dst, ks in part:
                    nc.scalar.copy(dst[:, :, t], hT[:, ks, t]).then_inc(hh_ok, 1)

            def round_w(n):
                act.wait_ge(w_in[n % 2], 16 * (n // 2 + 1))
                nc.scalar.copy(whigh[:, n % 2], ring[:, n % 2]).then_inc(wh_ok, 1)

            round_h(0)
            round_w(0)
            round_h(1)
            round_h(2)
            round_w(1)
            nc.scalar.activation(c.vg, c.vg, ACT.Gelu_apprx_tanh).then_inc(gelu_ok, 1)
            for n, (_, dst, how) in enumerate(plan):
                if 2 <= n + 1 < len(plan):
                    round_w(n + 1)
                for g in range(GRP):
                    u = GRP * n + g
                    act.wait_ge(product, u + 1)
                    o, i = dst[:, g * GT:(g + 1) * GT], ps[u % 7][:, 0:GT]
                    if how == "gelu":
                        ins = nc.scalar.activation(o, i, ACT.Gelu_apprx_tanh)
                    elif how == "silu":
                        ins = nc.scalar.activation(o, i, ACT.Silu)
                    elif how == "scale":
                        ins = nc.scalar.mul(o, i, DH ** -0.5)
                    else:
                        ins = nc.scalar.copy(o, i)
                    ins.then_inc(evacuated, 1)
                if n == 2:
                    act.wait_ge(cw_mm, 1)
                    nc.scalar.copy(cw, ps[7][:, 0:168].rearrange("p (c n) -> p c n", c=6)).then_inc(cw_ok, 1)
                if n >= 4:
                    if n - 4 < 6:
                        conv_silu(n - 4)
            nc.scalar.preload_act_table_set(EXPLN)
            act.wait_ge(stats, 1)
            link(nc.scalar.activation(mom[:, 1, :], mom[:, 1, :], ACT.Ln, bias=c.eps, scale=1.0 / DH))
            nc.scalar.activation(mom[:, 1, :], mom[:, 1, :], ACT.Exp, scale=-0.5).then_inc(rstd_ok, 1)

        @block.vector
        def _(dve):
            link = Chain(dve, dve_chain)

            def bc(row):
                return row.unsqueeze(2).to_broadcast([P, NG, DH])

            def low_h(g):
                t = slice(g * GT, (g + 1) * GT)
                for m, (high, ks) in enumerate(part):
                    dve.wait_ge(hh_ok, 2 * g + m + 1)
                    nc.vector.tensor_tensor(hlow[:, ks, t], hT[:, ks, t], high[:, :, t].bitcast(F32), ALU.subtract).then_inc(hl_ok, 1)

            def low_w(n):
                dve.wait_ge(wh_ok, n + 1)
                nc.vector.tensor_tensor(wlow[:, n % 2], ring[:, n % 2], whigh[:, n % 2].bitcast(F32), ALU.subtract).then_inc(wl_ok, 1)

            low_h(0)
            low_w(0)
            low_h(1)
            low_h(2)
            low_w(1)
            dve.wait_ge(gelu_ok, 1)
            link(nc.vector.tensor_reduce(mom[:, 0, :], vg, AX, ALU.add))
            link(nc.vector.tensor_scalar(mom[:, 0, :], mom[:, 0, :], 1.0 / DH, None, ALU.mult))
            link(nc.vector.tensor_tensor(vg, vg, bc(mom[:, 0, :]), ALU.subtract))
            link(nc.vector.tensor_tensor(vsq, vg, vg, ALU.mult))
            nc.vector.tensor_reduce(mom[:, 1, :], vsq, AX, ALU.add).then_inc(stats, 1)
            low_w(2)
            low_w(3)
            dve.wait_ge(cw_ok, 1)
            nc.vector.tensor_copy(xs[:, :, :, 0:3], cw[:, :, 0:24].rearrange("p c (b t) -> p c b t", b=DB)).then_inc(staged, 1)
            dve.wait_ge(staged, 1)
            for n in range(6):
                if n + 4 < len(plan):
                    low_w(n + 4)
                dve.wait_ge(evacuated, GRP * (n + 1))
                if n >= 2:
                    dve.wait_ge(silu_ok, 2 * (n - 1))
                nc.vector.tensor_copy(xs[:, n, :, 3:7], qkvT[:, n, SEQ:TOK].rearrange("p (b t) -> p b t", b=DB)).then_inc(staged, 1)
                nc.vector.tensor_copy(tail[:, n, :], qkvT[:, n, SEQ - 3:TOK]).then_inc(staged, 1)
                yy = y[:, n % 2, :]
                w = lambda i: cw[:, n, 24 + i:25 + i]
                link(nc.vector.tensor_scalar(yy, qkvT[:, n, 0:SEQ], w(3), None, ALU.mult))
                for sh in (3, 2, 1):
                    link(nc.vector.scalar_tensor_tensor(yy[:, sh:], qkvT[:, n, 0:SEQ - sh], w(3 - sh), yy[:, sh:],
                                                        ALU.mult, ALU.add))
                dve.wait_ge(staged, 2 * n + 3)
                link(nc.vector.tensor_scalar(ys[:, n], xs[:, n, :, 3:7], w(3), None, ALU.mult))
                for sh in (3, 2, 1):
                    ins = nc.vector.scalar_tensor_tensor(ys[:, n], xs[:, n, :, 3 - sh:7 - sh], w(3 - sh), ys[:, n],
                                                         ALU.mult, ALU.add)
                    if sh > 1:
                        link(ins)
                ins.then_inc(conv_ok, 1)
            for n in range(10, len(plan)):
                low_w(n)
            dve.wait_ge(rstd_ok, 1)
            link(nc.vector.tensor_tensor(vg, vg, bc(mom[:, 1, :]), ALU.mult))
            dve.wait_ge(ln_in, 32)
            link(nc.vector.tensor_tensor(c.vg, c.vg, c.A("glng").unsqueeze(1).to_broadcast([P, TILES, 256]), ALU.mult))
            nc.vector.tensor_tensor(c.vg, c.vg, c.A("glnb").unsqueeze(1).to_broadcast([P, TILES, 256]),
                                    ALU.add).then_inc(normed, 1)


def stage_gate_and_pool(c):
    nc, T, O, K = c.nc, c.T, c.O, c.K
    c.place(start=c.scratch, wsT=HEADS * P, wsS=HEADS * NS, bsb=2 * P, bsbS=2 * NS, dT=2 * 256, mix=256, ws4=128)
    ws, bs = c.ws, c.bs
    wsT = c.A("wsT").rearrange("p (g s) -> p g s", g=HEADS)
    wsS = c.A("wsS").rearrange("p (g s) -> p g s", g=HEADS)
    ws4 = c.A("ws4").rearrange("p (g s) -> p g s", g=HEADS)
    bsb = c.A("bsb").rearrange("p (c s) -> p c s", c=2)
    bsbS = c.A("bsbS").rearrange("p (c s) -> p c s", c=2)
    dT = c.A("dT").rearrange("p (s n) -> p s n", s=2)
    mix = c.A("mix")
    c.place(start=c.at["ws4"][0] + 128, bands=len(POOL_CONSTS) * P)
    bands, prev, gam, pw = c.A("bands"), c.prev, c.gam, c.pw
    ps, oT, xc, vg, uT = c.ps, c.hT, c.xc, c.vg, c.uT

    def band(name, r=P, w=P):
        return bands[0:r, POOL_AT[name]:POOL_AT[name] + w]

    s = c.sem
    loaded, stored, bands_in = c.gp_in, s("g_stored"), s("g_bands")
    small_mm, small_ev, mixed, mixed_used = s("g_smm"), s("g_sev"), s("g_mixed"), s("g_mixused")
    diff, diff_ok, pooled, pooled_used, dve_chain = s("g_diff"), s("g_diffok"), s("g_pooled"), s("g_poolused"), s("g_dve")
    with nc.Block() as block:
        @block.sync
        def _(sp):
            sp.dma_start(bands, T['pool_tables']).then_inc(bands_in, 16)
            sp.dma_start(O['pool_prompt'][0, 0], xc[P - POOLB:P, NT - 1, :]).then_inc(stored, 16)
            sp.dma_start(O['pool_sample'][0, :, 0:POOLB - DS, :], T['state_pool'][0, :, DS:POOLB, :]).then_inc(stored, 16)
            for b in range(DB):
                sp.dma_start(O['pool_sample'][0, b, POOLB - DS:POOLB, :], xc[b * DS:(b + 1) * DS, NT, :]).then_inc(stored, 16)
            sp.wait_ge(stored, 16 * (2 + DB))

        @block.tensor
        def _(pe):
            pe.wait_ge(loaded, 16 * 9)
            for g in range(HEADS):
                last = nc.tensor.transpose(ps[0][:, g * P:(g + 1) * P], ws[:, g, :], K("ident"))
            last.then_inc(small_mm, 1)
            for g in range(HEADS):
                q = (g % 2) * DH
                last = nc.tensor.matmul(ps[1][q:q + DH, (g // 2) * P:(g // 2 + 1) * P], K("ones", 1, DH),
                                        bs[0:1, g * P:(g + 1) * P], start=True, stop=True)
            last.then_inc(small_mm, 1)
            for g in range(HEADS):
                last = nc.tensor.matmul(ps[2][0:DS, g * NS:(g + 1) * NS], ws[0:DS, g, 0:DS], K("rep4", DS, NS),
                                        start=True, stop=True)
            last.then_inc(small_mm, 1)
            pe.wait_ge(small_ev, 3)
            last = nc.tensor.matmul(ps[3][0:NS, 0:4 * NS], K("rep4", DS, NS), ws4[0:DS].rearrange("p g s -> p (g s)"),
                                    start=True, stop=True)
            last.then_inc(small_mm, 1)
            pe.wait_ge(small_ev, 5)

            def mixes(i):
                r = rows(i)
                if i >= 2:
                    pe.wait_ge(mixed_used, i - 1)
                for g in range(HEADS):
                    q = (g % 2) * DH
                    w = wsT[:, g, :] if i < NT else wsS[0:NS, g, :]
                    last = nc.tensor.matmul(ps[4 + i % 2][q:q + DH, (g // 2) * P:(g // 2) * P + r],
                                            vg[0:r, i, g * DH:(g + 1) * DH], w, start=True, stop=True)
                last.then_inc(mixed, 1)

            def diffs(i):
                r = rows(i)
                if i >= 1:
                    pe.wait_ge(diff_ok, i)
                for g in range(HEADS):
                    q = (g % 2) * DH
                    out = ps[6][q:q + DH, (g // 2) * P:(g // 2) * P + r]
                    x = xc[0:r, i, g * DH:(g + 1) * DH]
                    if i == 0:
                        last = nc.tensor.matmul(out, x, band(f"bandfirst{g}"), start=True, stop=True)
                    elif i < NT:
                        nc.tensor.matmul(out, x, band(f"band{g}"), start=True, stop=False)
                        last = nc.tensor.matmul(out, xc[:, i - 1, g * DH:(g + 1) * DH], band(f"bandprev{g}"),
                                                start=False, stop=True)
                    else:
                        nc.tensor.matmul(out, x, band(f"scur{g}", NS, NS), start=True, stop=False)
                        n = DB * POOLB
                        last = nc.tensor.matmul(out, prev[0:n, g * DH:(g + 1) * DH], band(f"spool{g}", n, NS),
                                                start=False, stop=True)
                last.then_inc(diff, 1)

            def pools(i):
                r = rows(i)
                pe.wait_ge(diff_ok, i + 1)
                if i >= 1:
                    pe.wait_ge(pooled_used, i)
                for n in range(2):
                    last = nc.tensor.matmul(ps[7][:, n * P:n * P + r], pw[:, n, :], dT[:, i % 2, n * P:n * P + r],
                                            start=True, stop=True)
                last.then_inc(pooled, 1)

            for i in range(TILES + 1):
                if i < TILES:
                    mixes(i)
                    if i == 0:
                        pe.wait_ge(bands_in, 16)
                    diffs(i)
                if i >= 1:
                    pools(i - 1)

        @block.vector
        def _(dve):
            link = Chain(dve, dve_chain)
            dve.wait_ge(small_mm, 1)
            nc.vector.tensor_tensor(wsT, ps[0][:, :].rearrange("p (g s) -> p g s", g=HEADS),
                                    K("upto").unsqueeze(1).to_broadcast([P, HEADS, P]), ALU.mult).then_inc(small_ev, 1)
            dve.wait_ge(small_mm, 2)
            nc.vector.tensor_copy(bsb, ps[1][:, 0:2 * P].rearrange("p (c s) -> p c s", c=2)).then_inc(small_ev, 1)
            dve.wait_ge(small_mm, 3)
            nc.vector.tensor_copy(ws4[0:DS], ps[2][0:DS, 0:4 * NS].rearrange("p (g s) -> p g s", g=HEADS)).then_inc(small_ev, 1)
            dve.wait_ge(small_mm, 4)
            nc.vector.tensor_tensor(wsS[0:NS], ps[3][0:NS, 0:4 * NS].rearrange("p (g s) -> p g s", g=HEADS),
                                    K("cum4", NS, NS).unsqueeze(1).to_broadcast([NS, HEADS, NS]), ALU.mult).then_inc(small_ev, 1)
            for n in range(2):
                last = nc.vector.tensor_copy(bsbS[:, n, :].rearrange("p (b t) -> p b t", b=DB),
                                             bsb[:, n, 0:DS].unsqueeze(1).to_broadcast([P, DB, DS]))
                if n == 0:
                    link(last)
            last.then_inc(small_ev, 1)
            dve.wait_ge(small_ev, 5)
            for i in range(TILES):
                r = rows(i)
                dve.wait_ge(mixed, i + 1)
                m = mix.rearrange("p (c s) -> p c s", c=2)[:, :, 0:r]
                p = ps[4 + i % 2][:, 0:2 * P].rearrange("p (c s) -> p c s", c=2)[:, :, 0:r]
                if i >= 1:
                    dve.wait_ge(mixed_used, i)
                link(nc.vector.tensor_tensor(m, p, bsb if i < NT else bsbS, ALU.add))
                nc.vector.tensor_tensor(oT[:, 2:4, i * P:i * P + r], m, uT[:, :, i * P:i * P + r],
                                        ALU.mult).then_inc(mixed_used, 1)

        @block.scalar
        def _(act):
            act.wait_ge(loaded, 16 * 9)

            def outputs(i):
                r = rows(i)
                act.wait_ge(pooled, i + 1)
                for n in range(2):
                    last = nc.scalar.activation(oT[:, 4 + n, i * P:i * P + r], ps[7][:, n * P:n * P + r], ACT.Copy,
                                                scale=gam[:, n:n + 1])
                last.then_inc(pooled_used, 1)

            for i in range(TILES):
                r = rows(i)
                act.wait_ge(diff, i + 1)
                if i >= 2:
                    act.wait_ge(pooled, i - 1)
                nc.scalar.copy(dT[:, i % 2, :].rearrange("p (c s) -> p c s", c=2)[:, :, 0:r],
                               ps[6][:, 0:2 * P].rearrange("p (c s) -> p c s", c=2)[:, :, 0:r]).then_inc(diff_ok, 1)
                if i >= 1:
                    outputs(i - 1)
            outputs(TILES - 1)


def stage_stick_prompt(c):
    nc, K = c.nc, c.K
    c.place(start=c.after_q, qz=2 * 512, bias=512, zb=3 * 512, tmp=2 * 512, sp=3 * 512, att=2 * 512, ssum=3 * 512,
            sb=HEADS)

    def ring(name, n):
        return c.A(name).rearrange("p (s h q) -> p s h q", s=n, h=HEADS)

    qz, zb, tmp, sp_, att, ssum = ring("qz", 2), ring("zb", 3), ring("tmp", 2), ring("sp", 3), ring("att", 2), ring("ssum", 3)
    bias = c.A("bias").rearrange("p (h q) -> p h q", h=HEADS)
    c.bias = bias
    ps, oT, qT, kT, vtok = c.ps, c.hT, c.qT, c.kT, c.vtok
    steps = [(qb, kb) for qb in range(NT) for kb in range(qb, -1, -1)]
    N = len(steps)
    s = c.sem
    c.k_pages_in, c.v_pages_in, ids_in = s("a_kpages"), s("a_vpages"), s("a_ids")
    zeroed, q_ready, bias_in, bias_ok = s("a_zero"), s("a_q"), s("a_bin"), s("a_bias")
    score, zb_ok, soft, sp_ok, sum_ok, sums = s("a_score"), s("a_zb"), s("a_soft"), s("a_sp"), s("a_sumok"), s("a_sums")
    arg_ok, exp_ok, att_ok, pv, out_ok = s("a_arg"), s("a_exp"), s("a_att"), s("a_pv"), s("a_out")
    dve_chain, act_chain = s("a_dve"), s("a_act")
    last_of = [max(n for n, x in enumerate(steps) if x[0] == qb) for qb in range(NT)]

    def head4(bank):
        return ps[bank][:, :].rearrange("p (h q) -> p h q", h=HEADS)

    with nc.Block() as block:
        @block.sync
        def _(sp):
            sp.dma_start(c.A("sb"), row_bc(c.T['sb_bias'][0])).then_inc(bias_in, 16)
            ids, T = c.ids, c.T
            sp.dma_start(ids[0:1, :], T['page_table'].rearrange("b g -> (b g)").unsqueeze(0)).then_inc(ids_in, 16)
            sp.wait_ge(ids_in, 16)
            n_phys = T['cache_sb_k'].shape[1]
            for g in range(DB * NPG):
                page = sp.value_load(ids[0:1, g:g + 1], min_val=0, max_val=n_phys - 1)
                for q, (src, done) in enumerate((('cache_sb_k', c.k_pages_in), ('cache_sb_v', c.v_pages_in))):
                    pages = T[src][0].rearrange("n t h d -> n t (h d)")
                    sp.dma_start(c.pages[:, q, g, :], pages[bass.ds(page, 1)].rearrange("a t n -> (a t) n")).then_inc(done, 16)

        @block.gpsimd
        def _(pool):
            nc.gpsimd.memset(c.A("qz"), 0.0).then_inc(zeroed, 1)
            pool.wait_ge(zeroed, 1)
            n = 0

            def stage_queries(qb):
                if qb >= 2:
                    pool.wait_ge(score, last_of[qb - 2] + 1)
                t = slice(qb * P, (qb + 1) * P)
                nc.gpsimd.tensor_copy(qz[0:DH, qb % 2, 0:4:2, :], qT[0:DH, :, t]).then_inc(q_ready, 1)
                pool.wait_ge(q_ready, 2 * qb + 1)
                nc.gpsimd.tensor_copy(qz[DH:P, qb % 2, 1:4:2, :], qT[DH:P, :, t]).then_inc(q_ready, 1)
                pool.wait_ge(q_ready, 2 * qb + 2)

            stage_queries(0)
            for qb in range(NT):
                if qb + 1 < NT:
                    stage_queries(qb + 1)
                for j in range(qb + 1):
                    pool.wait_ge(sp_ok, n + 1)
                    if n >= 2:
                        pool.wait_ge(sums, n - 1)
                    if j == 0:
                        nc.gpsimd.tensor_copy(ssum[:, n % 3], sp_[:, n % 3]).then_inc(sum_ok, 1)
                    else:
                        nc.gpsimd.tensor_tensor(ssum[:, n % 3], ssum[:, (n - 1) % 3], sp_[:, n % 3],
                                                ALU.add).then_inc(sum_ok, 1)
                    n += 1
                    pool.wait_ge(sum_ok, n)

        @block.tensor
        def _(pe):
            def scores(n):
                qb, kb = steps[n]
                pe.wait_ge(q_ready, 2 * qb + 2)
                if n >= 2:
                    pe.wait_ge(zb_ok, n - 1)
                for pair in range(2):
                    last = nc.tensor.matmul(ps[n % 2][:, pair * 256:(pair + 1) * 256], kT[:, pair, kb * P:(kb + 1) * P],
                                            qz[:, qb % 2, 2 * pair:2 * pair + 2, :].rearrange("p h q -> p (h q)"),
                                            start=True, stop=True)
                last.then_inc(score, 1)

            def suffix(n):
                qb, kb = steps[n]
                pe.wait_ge(sp_ok, n + 1)
                if n >= 2:
                    pe.wait_ge(arg_ok, n - 1)
                flat = "p h q -> p (h q)"
                last = nc.tensor.matmul(ps[2 + n % 2][:, :], K("negsuf"), sp_[:, n % 3].rearrange(flat),
                                        start=True, stop=(kb == qb))
                if kb < qb:
                    pe.wait_ge(sum_ok, n)
                    last = nc.tensor.matmul(ps[2 + n % 2][:, :], K("negone"), ssum[:, (n - 1) % 3].rearrange(flat),
                                            start=False, stop=True)
                last.then_inc(sums, 1)

            def values(n):
                qb, kb = steps[n]
                if kb == qb:
                    pe.wait_ge(att_ok, qb + 1)
                else:
                    pe.wait_ge(exp_ok, n + 1)
                if kb == qb and qb >= 2:
                    pe.wait_ge(out_ok, 2 * (qb - 1))
                for pair in range(2):
                    last = nc.tensor.matmul(ps[4 + qb % 2][:, pair * 256:(pair + 1) * 256],
                                            vtok[:, kb, pair * P:(pair + 1) * P],
                                            att[:, n % 2, 2 * pair:2 * pair + 2, :].rearrange("p h q -> p (h q)"),
                                            start=(kb == qb and pair == 0), stop=(kb == 0), skip_group_check=True)
                last.then_inc(pv, 1)

            for n in range(N + 2):
                if n < N:
                    scores(n)
                if 1 <= n <= N:
                    suffix(n - 1)
                if n >= 2:
                    values(n - 2)

        @block.scalar
        def _(act):
            link = Chain(act, act_chain)
            nc.scalar.preload_act_table_set(EXPLN)

            def softplus(n):
                act.wait_ge(zb_ok, n + 1)
                if n >= 2:
                    act.wait_ge(sp_ok, n - 1)
                t = tmp[:, n % 2]
                link(nc.scalar.activation(t, zb[:, n % 3], ACT.Abs))
                link(nc.scalar.activation(t, t, ACT.Exp, scale=-1.0))
                nc.scalar.activation(t, t, ACT.Ln, bias=1.0).then_inc(soft, 1)

            def weights(n):
                act.wait_ge(arg_ok, n + 1)
                if n >= 2:
                    act.wait_ge(pv, n - 1)
                nc.scalar.activation(att[:, n % 2], zb[:, n % 3], ACT.Exp).then_inc(exp_ok, 1)

            for n in range(N + 2):
                if n >= 2:
                    weights(n - 2)
                if n < N:
                    softplus(n)

        @block.vector
        def _(dve):
            link = Chain(dve, dve_chain)
            dve.wait_ge(bias_in, 16)
            for h in range(HEADS):
                ins = nc.vector.tensor_scalar(bias[:, h, :], K("ones"), c.A("sb")[:, h:h + 1], None, ALU.mult)
                ins.then_inc(bias_ok, 1)
            dve.wait_ge(bias_ok, HEADS)
            mask = K("before").unsqueeze(1).to_broadcast([P, HEADS, P])

            def add_bias(n):
                dve.wait_ge(score, n + 1)
                if n >= 3:
                    dve.wait_ge(exp_ok, n - 2)
                nc.vector.tensor_tensor(zb[:, n % 3], head4(n % 2), bias, ALU.add).then_inc(zb_ok, 1)

            def soft_sum(n):
                qb, kb = steps[n]
                dve.wait_ge(soft, n + 1)
                if n >= 3:
                    dve.wait_ge(sums, n - 2)
                    dve.wait_ge(sum_ok, n - 2)
                ins = nc.vector.scalar_tensor_tensor(sp_[:, n % 3], zb[:, n % 3], 0.0, tmp[:, n % 2], ALU.max, ALU.add)
                if kb == qb:
                    link(ins)
                    ins = nc.vector.tensor_tensor(sp_[:, n % 3], sp_[:, n % 3], mask, ALU.mult)
                ins.then_inc(sp_ok, 1)

            def argument(n):
                dve.wait_ge(sums, n + 1)
                dve.wait_ge(sp_ok, n + 1)
                nc.vector.tensor_tensor(zb[:, n % 3], head4(2 + n % 2), zb[:, n % 3], ALU.add).then_inc(arg_ok, 1)

            def mask_weights(n):
                dve.wait_ge(exp_ok, n + 1)
                a = att[:, n % 2]
                nc.vector.tensor_tensor(a, a, mask, ALU.mult).then_inc(att_ok, 1)

            def outputs(qb):
                dve.wait_ge(pv, last_of[qb] + 1)
                for half in range(2):
                    q = slice(half * DH, (half + 1) * DH)
                    nc.vector.tensor_copy(oT[q, 0:2, qb * P:(qb + 1) * P],
                                          head4(4 + qb % 2)[q, half:4:2, :]).then_inc(out_ok, 1)

            for n in range(N + 3):
                if n >= 3 and steps[n - 3][0] == steps[n - 3][1]:
                    mask_weights(n - 3)
                if 2 <= n <= N + 1:
                    argument(n - 2)
                if 1 <= n <= N:
                    soft_sum(n - 1)
                if n < N:
                    add_bias(n)
                if n >= 3 and n - 3 in last_of:
                    outputs(last_of.index(n - 3))


def stage_stick_sample(c):
    nc, T, K = c.nc, c.T, c.K
    HQ = HEADS * NS
    c.place(start=c.after_q, kTs=DB * NPG * 256, qzs=HQ, biasS=HQ, sb=HEADS,
            zS=3 * HQ, tS=3 * HQ, spS=3 * HQ)
    Kp, Vp = c.pages[:, 0], c.pages[:, 1]
    kTs = c.A("kTs").rearrange("p (g n) -> p g n", n=256)
    qzs = c.A("qzs").rearrange("p (h q) -> p h q", h=HEADS)
    z, t, sp_ = c.A("zS"), c.A("tS"), c.A("spS")
    ps, oT, qT, kT, vtok = c.ps, c.hT, c.qT, c.kT, c.vtok
    NPAGES = DB * NPG
    s = c.sem
    bias_in = s("s_bias")
    q_ok, turned, kT_ok, score, zb_ok = s("s_q"), s("s_turned"), s("s_kT"), s("s_score"), s("s_zb")
    soft, sp_ok, sums, arg_ok, exp_ok, att_ok, pv = (s("s_soft"), s("s_sp"), s("s_sums"), s("s_arg"), s("s_exp"),
                                                     s("s_att"), s("s_pv"))
    out_ok, dve_chain, act_chain = s("s_out"), s("s_dve"), s("s_act")
    N2, N3 = 2 * HQ, 3 * HQ
    new = slice(N2, N3)

    with nc.Block() as block:
        @block.sync
        def _(sp):
            sp.dma_start(c.A("sb"), row_bc(T['sb_bias'][0])).then_inc(bias_in, 16)

        @block.tensor
        def _(pe):
            def turn(g):
                pe.wait_ge(c.k_pages_in, 16 * NPAGES)
                u = g // 2
                if u >= 4 and g % 2 == 0:
                    pe.wait_ge(kT_ok, u - 3)
                for pair in range(2):
                    last = nc.tensor.transpose(ps[u % 4][:, (g % 2) * 256 + pair * P:(g % 2) * 256 + (pair + 1) * P],
                                               Kp[:, g, pair * P:(pair + 1) * P], K("ident"))
                if g % 2 == 1:
                    last.then_inc(turned, 1)

            for g in range(NPAGES):
                turn(g)
            pe.wait_ge(q_ok, 3)
            pages = ps[4][:, 0:N2].rearrange("p (g h b q) -> p g h b q", g=NPG, h=HEADS, b=DB)
            qv = qzs.rearrange("p h (b q) -> p h b q", b=DB)
            for g in range(NPAGES):
                b, page = g // NPG, g % NPG
                pe.wait_ge(kT_ok, g // 2 + 1)
                for pair in range(2):
                    hh = slice(2 * pair, 2 * pair + 2)
                    last = nc.tensor.matmul(pages[:, page, hh, b, :], kTs[:, g, pair * P:(pair + 1) * P], qv[:, hh, b, :],
                                            start=True, stop=True)
            last.then_inc(score, 1)
            for pair in range(2):
                last = nc.tensor.matmul(ps[5][0:NS, pair * 64:(pair + 1) * 64], kT[:, pair, SEQ:TOK],
                                        qzs[:, 2 * pair:2 * pair + 2, :].rearrange("p h q -> p (h q)"), start=True, stop=True)
            last.then_inc(score, 1)
            pe.wait_ge(sp_ok, 3)
            nc.tensor.matmul(ps[6][:, HQ:N2], K("negsuf"), sp_[:, HQ:N2], start=True, stop=False)
            nc.tensor.matmul(ps[6][:, HQ:N2], K("negone", NS), sp_[0:NS, new], start=False, stop=True)
            nc.tensor.matmul(ps[6][:, 0:HQ], K("negsuf"), sp_[:, 0:HQ], start=True, stop=False)
            nc.tensor.matmul(ps[6][:, 0:HQ], K("negone"), sp_[:, HQ:N2], start=False, stop=False)
            nc.tensor.matmul(ps[6][:, 0:HQ], K("negone", NS), sp_[0:NS, new], start=False, stop=True).then_inc(sums, 1)
            nc.tensor.matmul(ps[7][0:NS, 0:HQ], K("negsuf", NS, NS), sp_[0:NS, new], start=True, stop=True).then_inc(sums, 1)
            pe.wait_ge(exp_ok, 2)
            pe.wait_ge(att_ok, 1)
            pe.wait_ge(c.v_pages_in, 16 * NPAGES)
            att = z[:, 0:N2].rearrange("p (g h b q) -> p g h b q", g=NPG, h=HEADS, b=DB)
            an = z[:, new].rearrange("p (h q) -> p h q", h=HEADS)
            for pair in range(2):
                hh = slice(2 * pair, 2 * pair + 2)
                out = ps[0][:, pair * 64:(pair + 1) * 64]
                nc.tensor.matmul(out, vtok[0:NS, NT, pair * P:(pair + 1) * P], an[0:NS, hh, :].rearrange("p h q -> p (h q)"),
                                 start=(pair == 0), stop=False, skip_group_check=True)
                ov = out.rearrange("p (h b q) -> p h b q", h=2, b=DB)
                for g in range(NPAGES):
                    last = nc.tensor.matmul(ov[:, :, g // NPG, :], Vp[:, g, pair * P:(pair + 1) * P],
                                            att[:, g % NPG, hh, g // NPG, :], start=False, stop=(g == NPAGES - 1),
                                            skip_group_check=True)
            last.then_inc(pv, 1)

        @block.scalar
        def _(act):
            link = Chain(act, act_chain)
            nc.scalar.preload_act_table_set(EXPLN)
            for u in range(NPAGES // 2):
                act.wait_ge(turned, u + 1)
                nc.scalar.copy(kTs[:, 2 * u:2 * u + 2, :], ps[u % 4][:, :].rearrange("p (g n) -> p g n", g=2)).then_inc(kT_ok, 1)
            act.wait_ge(zb_ok, 2)
            for r, sl in ((P, slice(0, N2)), (NS, new)):
                link(nc.scalar.activation(t[0:r, sl], z[0:r, sl], ACT.Abs))
                link(nc.scalar.activation(t[0:r, sl], t[0:r, sl], ACT.Exp, scale=-1.0))
                nc.scalar.activation(t[0:r, sl], t[0:r, sl], ACT.Ln, bias=1.0).then_inc(soft, 1)
            act.wait_ge(arg_ok, 2)
            nc.scalar.activation(z[:, 0:N2], z[:, 0:N2], ACT.Exp).then_inc(exp_ok, 1)
            nc.scalar.activation(z[0:NS, new], z[0:NS, new], ACT.Exp).then_inc(exp_ok, 1)

        @block.vector
        def _(dve):
            link = Chain(dve, dve_chain)
            nc.vector.memset(c.A("qzs"), 0.0).then_inc(q_ok, 1)
            dve.wait_ge(q_ok, 1)
            nc.vector.tensor_copy(qzs[0:DH, 0:4:2, :], qT[0:DH, :, SEQ:TOK]).then_inc(q_ok, 1)
            nc.vector.tensor_copy(qzs[DH:P, 1:4:2, :], qT[DH:P, :, SEQ:TOK]).then_inc(q_ok, 1)
            dve.wait_ge(bias_in, 16)
            bias = c.A("biasS")
            for h in range(HEADS):
                ins = nc.vector.tensor_scalar(bias[:, h * NS:(h + 1) * NS], K("ones", P, NS), c.A("sb")[:, h:h + 1], None, ALU.mult)
                link(ins)
            dve.wait_ge(score, 1)
            nc.vector.tensor_tensor(z[:, 0:N2].rearrange("p (g n) -> p g n", g=2), ps[4][:, 0:N2].rearrange("p (g n) -> p g n", g=2),
                                    bias.unsqueeze(1).to_broadcast([P, 2, HQ]), ALU.add).then_inc(zb_ok, 1)
            dve.wait_ge(score, 2)
            nc.vector.tensor_tensor(z[0:NS, new], ps[5][0:NS, 0:HQ], bias[0:NS, :], ALU.add).then_inc(zb_ok, 1)
            dve.wait_ge(zb_ok, 2)
            dve.wait_ge(soft, 1)
            nc.vector.scalar_tensor_tensor(sp_[:, 0:N2], z[:, 0:N2], 0.0, t[:, 0:N2], ALU.max, ALU.add).then_inc(sp_ok, 1)
            dve.wait_ge(soft, 2)
            nc.vector.scalar_tensor_tensor(sp_[0:NS, new], z[0:NS, new], 0.0, t[0:NS, new], ALU.max, ALU.add).then_inc(sp_ok, 1)
            dve.wait_ge(sp_ok, 2)
            mask = K("before4", NS, NS).unsqueeze(1).to_broadcast([NS, HEADS, NS])
            sn = sp_[0:NS, new].rearrange("p (h q) -> p h q", h=HEADS)
            zn = z[0:NS, new].rearrange("p (h q) -> p h q", h=HEADS)
            nc.vector.tensor_tensor(sn, sn, mask, ALU.mult).then_inc(sp_ok, 1)
            dve.wait_ge(sums, 1)
            nc.vector.tensor_tensor(z[:, 0:N2], ps[6][:, 0:N2], z[:, 0:N2], ALU.add).then_inc(arg_ok, 1)
            dve.wait_ge(sums, 2)
            nc.vector.tensor_tensor(z[0:NS, new], ps[7][0:NS, 0:HQ], z[0:NS, new], ALU.add).then_inc(arg_ok, 1)
            dve.wait_ge(exp_ok, 2)
            nc.vector.tensor_tensor(zn, zn, mask, ALU.mult).then_inc(att_ok, 1)
            dve.wait_ge(pv, 1)
            ov = ps[0][:, 0:P].rearrange("p (c h q) -> p c h q", c=2, h=2)
            for half in range(2):
                q = slice(half * DH, (half + 1) * DH)
                nc.vector.tensor_copy(oT[q, 0:2, SEQ:TOK], ov[q, :, half, :]).then_inc(out_ok, 1)


def stage_delta_inputs(c):
    nc, T, O, K = c.nc, c.T, c.O, c.K
    c.place(start=0, dnorm=1, SQ=2 * TOK)
    c.place(start=c.free_at + 6 * TOK, stp=768, sts=768, rn=3 * GT, rows4=8)
    qkvT = c.qkvT
    stp, sts, rn = c.A("stp"), c.A("sts"), c.A("rn")
    sq = c.A("SQ").rearrange("p (s t) -> p s t", s=2)
    NC = TILES * HEADS

    def col():
        return c.new_small(NC).rearrange("p (i h) -> p i h", i=TILES)

    c.beta, c.g, c.log_decay, c.be, c.kgf = col(), col(), col(), col(), col()
    tx, tl = col(), col()
    eps6 = c.new_small(1)
    c.eps6 = eps6
    bd, ad = c.ba[:, :, 0:HEADS], c.ba[:, :, HEADS:2 * HEADS]
    ps = c.ps
    s = c.sem
    loaded, st_mm, st_ok, stored = s("c_load"), s("c_stmm"), s("c_stok"), s("c_stored")
    gd, ga, gpe, staged = s("c_gd"), s("c_ga"), s("c_gpe"), s("c_staged")
    sq_ok, ss, rn_ok, unit, dve_chain, act_chain, eps_ok = (s("c_sq"), s("c_ss"), s("c_rn"), s("c_unit"), s("c_dve"),
                                                            s("c_act"), s("c_eps"))
    rows4 = c.A("rows4")

    with nc.Block() as block:
        @block.sync
        def _(sp):
            sp.dma_start(rows4[:, 0:4], row_bc(T['dn_dt_bias'][0])).then_inc(loaded, 16)
            sp.dma_start(rows4[:, 4:8], row_bc(T['dn_a_log'][0])).then_inc(loaded, 16)
            for half in range(2):
                sp.dma_start(c.A("dnorm")[half * DH:(half + 1) * DH, :], T['dn_norm_g'][0].unsqueeze(1)).then_inc(loaded, 16)
            sp.wait_ge(st_ok, 4)
            sp.dma_start(O['conv_prompt'][0, 0], stp[0:3, :]).then_inc(stored, 16)
            for b in range(DB):
                sp.dma_start(O['conv_sample'][0, b], sts[b * DS + 1:(b + 1) * DS, :]).then_inc(stored, 16)
            sp.wait_ge(stored, 16 * (DB + 1))

        @block.tensor
        def _(pe):
            for bank, r, t0, chunks in ((1, 3, 0, range(4)), (2, 3, 0, range(4, 6)), (3, NS, 3, range(4)), (4, NS, 3, range(4, 6))):
                for n in chunks:
                    last = nc.tensor.transpose(ps[bank][0:r, (n % 4) * P:(n % 4 + 1) * P], c.tail[:, n, t0:t0 + r], K("ident"))
                last.then_inc(st_mm, 1)
            pe.wait_ge(gd, 5)
            for q, (a, b) in enumerate((("cum64", "cum4"), ("blk64", "blk4"))):
                nc.tensor.matmul(ps[5][:, q * NC:q * NC + NT * HEADS], K(a), c.g[:, 0:NT, :].rearrange("p i h -> p (i h)"),
                                 start=True, stop=True)
                last = nc.tensor.matmul(ps[5][0:NS, q * NC + NT * HEADS:(q + 1) * NC], K(b, NS, NS), c.g[0:NS, NT, :],
                                        start=True, stop=True)
            last.then_inc(gpe, 1)
            for n in range(4):
                pe.wait_ge(sq_ok, n + 1)
                for g in range(GRP):
                    if n >= 1:
                        pe.wait_ge(rn_ok, GRP * (n - 1) + g + 1)
                    elif g == 0:
                        pe.wait_ge(gd, 6)
                    bank = (5, 6, 7)[g]
                    nc.tensor.matmul(ps[bank][:, 0:GT], K("blk64"), sq[:, n % 2, g * GT:(g + 1) * GT],
                                     start=True, stop=True).then_inc(ss, 1)

        @block.scalar
        def _(act):
            link = Chain(act, act_chain)
            nc.scalar.preload_act_table_set(EXPLN)
            for n, (bank, r, dst, w) in enumerate(((1, 3, stp[0:3, 0:512], 512), (2, 3, stp[0:3, 512:768], 256),
                                                   (3, NS, sts[0:NS, 0:512], 512), (4, NS, sts[0:NS, 512:768], 256))):
                act.wait_ge(st_mm, n + 1)
                nc.scalar.copy(dst, ps[bank][0:r, 0:w]).then_inc(st_ok, 1)
            act.wait_ge(gd, 1)
            nc.scalar.activation(c.beta, bd, ACT.Exp, scale=-1.0).then_inc(ga, 1)
            nc.scalar.activation(rows4[:, 4:8], rows4[:, 4:8], ACT.Exp).then_inc(ga, 1)
            link(nc.scalar.activation(tl, tx, ACT.Abs))
            link(nc.scalar.activation(tl, tl, ACT.Exp, scale=-1.0))
            nc.scalar.activation(tl, tl, ACT.Ln, bias=1.0).then_inc(ga, 1)
            act.wait_ge(gd, 6)
            nc.scalar.activation(c.be, c.log_decay, ACT.Exp).then_inc(ga, 1)
            nc.scalar.activation(c.kgf, c.kgf, ACT.Exp).then_inc(ga, 1)
            act.wait_ge(eps_ok, 1)
            for n in range(4):
                if n >= 2:
                    act.wait_ge(ss, GRP * (n - 1))
                nc.scalar.activation(sq[:, n % 2, :], qkvT[:, n, :], ACT.Square).then_inc(sq_ok, 1)
                nc.scalar.preload_act_table_set(EXPLN)
                for g in range(GRP):
                    u = GRP * n + g
                    act.wait_ge(ss, u + 1)
                    if n >= 1:
                        act.wait_ge(unit, u - 2)
                    t = rn[:, g * GT:(g + 1) * GT]
                    link(nc.scalar.activation(t, ps[(5, 6, 7)[g]][:, 0:GT], ACT.Ln, bias=eps6))
                    nc.scalar.activation(t, t, ACT.Exp, scale=-0.5).then_inc(rn_ok, 1)

        @block.vector
        def _(dve):
            link = Chain(dve, dve_chain)
            nc.vector.memset(eps6, 1e-6).then_inc(eps_ok, 1)
            nc.vector.memset(c.log_decay[:, NT, :], 0.0).then_inc(staged, 1)
            nc.vector.memset(c.kgf[:, NT, :], 0.0).then_inc(staged, 1)
            dve.wait_ge(loaded, 64)
            bc = rows4[:, 0:4].unsqueeze(1).to_broadcast([P, TILES, HEADS])
            nea = rows4[:, 4:8]
            nc.vector.tensor_tensor(tx, ad, bc, ALU.add).then_inc(gd, 1)
            dve.wait_ge(ga, 3)
            nc.vector.tensor_scalar(c.beta, c.beta, 1.0, None, ALU.add).then_inc(gd, 1)
            dve.wait_ge(gd, 2)
            nc.vector.reciprocal(c.beta, c.beta).then_inc(gd, 1)
            link(nc.vector.scalar_tensor_tensor(tx, tx, 0.0, tl, ALU.max, ALU.add))
            nc.vector.tensor_scalar(nea, nea, -1.0, None, ALU.mult).then_inc(gd, 1)
            dve.wait_ge(gd, 4)
            nc.vector.tensor_tensor(c.g, tx, nea.unsqueeze(1).to_broadcast([P, TILES, HEADS]), ALU.mult).then_inc(gd, 1)
            dve.wait_ge(gpe, 1)
            dve.wait_ge(staged, 2)
            gp = ps[5][:, 0:2 * NC].rearrange("p (q i h) -> p q i h", q=2, i=TILES)
            link(nc.vector.tensor_copy(c.log_decay[:, 0:NT, :], gp[:, 0, 0:NT, :]))
            link(nc.vector.tensor_copy(c.log_decay[0:NS, NT, :], gp[0:NS, 0, NT, :]))
            link(nc.vector.tensor_tensor(c.kgf[:, 0:NT, :], gp[:, 1, 0:NT, :], c.log_decay[:, 0:NT, :], ALU.subtract))
            nc.vector.tensor_tensor(c.kgf[0:NS, NT, :], gp[0:NS, 1, NT, :], c.log_decay[0:NS, NT, :], ALU.subtract).then_inc(gd, 1)
            dve.wait_ge(ga, 4)
            link(nc.vector.tensor_tensor(c.be, c.be, c.beta, ALU.mult))
            for n in range(4):
                for g in range(GRP):
                    u = GRP * n + g
                    dve.wait_ge(rn_ok, u + 1)
                    t = qkvT[:, n, g * GT:(g + 1) * GT]
                    nc.vector.scalar_tensor_tensor(t, t, DH ** -0.5 if n < 2 else 1.0, rn[:, g * GT:(g + 1) * GT],
                                                   ALU.mult, ALU.mult).then_inc(unit, 1)


def stage_delta(c):
    nc, T, O, K = c.nc, c.T, c.O, c.K
    kept = dict(u=256, wT=256, eg=256)
    c.place(start=0, dnorm=1, SQ=2 * TOK, S=2 * P, dS=2 * P, **{f"{k}{u}": n for u in range(2) for k, n in kept.items()})
    lane_sizes = dict(kvt=512, gcum=512, DL=512, DT=512, kz=512, qz=512, L=512, Lb=1024, X=512, Y=512, Pm=512,
                      vb=256, kbe=256, kg=512, qg=256, vz=512)
    sizes = {f"{k}{u}": n for u in range(2) for k, n in lane_sizes.items()}
    lanes_end = c.place(start=c.free_at + 6 * TOK, **sizes)
    h4 = "p (h t) -> p h t"
    B = {k: [c.A(f"{k}{u}") for u in range(2)] for k in {**lane_sizes, **kept}}

    def V(k, u, h=HEADS):
        return B[k][u].rearrange(h4, h=h)

    odT = c.A("SQ").rearrange("p (c t) -> p c t", c=2)
    S = c.A("S").rearrange("p (c n) -> p c n", c=2)
    dS = c.A("dS").rearrange("p (c n) -> p c n", c=2)
    c.place(start=c.at["kvt0"][0], rsq=2 * TOK, rrn=2 * TOK)
    c.rsq = c.A("rsq").rearrange("p (n t) -> p n t", n=2)
    c.rrn = c.A("rrn").rearrange("p (n t) -> p n t", n=2)
    a1 = c.at["kvt1"][0]
    c.place(start=lanes_end, SS=DB * 2 * P)
    c.place(start=a1, wSs=2 * NS, Vx=HEADS * 512, Sn=HEADS * 512)
    SS = c.A("SS").rearrange("p (b c n) -> p b c n", b=DB, c=2)
    wSs = c.A("wSs").rearrange("p (c t) -> p c t", c=2)
    Vx = c.A("Vx").rearrange("p (h b n) -> p h b n", h=HEADS, b=DB)
    Sn = c.A("Sn").rearrange("p (h b n) -> p h b n", h=HEADS, b=DB)
    qkvT, zT, oT = c.qkvT, c.zT, c.hT
    ps = c.ps
    LV = {i: ((2, 4, 8, 16, 32) if i < NT else (2,)) for i in range(TILES)}
    groups = [(0, 1), (2, 3), (4, 5), (6, 7), (8,)]
    number, n = {}, 0
    for grp in groups:
        for l in range(len(LV[grp[0]])):
            for i in grp:
                n += 1
                number[(i, l)] = n
    total_levels = n
    s = c.sem
    sx = {k: s("d_" + k) for k in ("zero", "kvt", "kvc", "gcum", "G", "dif", "ddve", "eg", "dexp", "dmask", "kz", "kk", "L",
                                   "intra", "X1", "Xt", "Y1", "Lb", "P", "Pc", "YX", "Y", "scaled", "uw", "uc", "qg",
                                   "vW", "vn", "o", "oc", "S", "dve", "act", "init", "sload", "swS", "swc", "swt",
                                   "svn", "svx", "so", "soc", "sdS", "sSn", "ost", "rs", "rss", "rrn", "rout", "zq", "hin")}
    dims = lambda i: (rows(i), (K("cum64"), K("low64")) if i < NT else (K("cum4", NS, NS), K("low4", NS, NS)))

    def bk(i, n):
        return ps[4 * (i % 2 if i < NT else 0) + n]

    def lane(i):
        return i % 2

    def v4(ap, i):
        r = rows(i)
        return ap[:, 0:4 * r].rearrange("p (h t) -> p h t", h=HEADS)

    def v2(ap, i):
        r = rows(i)
        return ap[:, 0:2 * r].rearrange("p (c t) -> p c t", c=2)

    def tok(i):
        return slice(i * P, i * P + rows(i))

    with nc.Block() as block:
        @block.gpsimd
        def _(pool):
            for nm in ("kz", "qz", "kg", "vz"):
                for u in range(2):
                    nc.gpsimd.memset(B[nm][u], 0.0).then_inc(sx["zero"], 1)
            nc.gpsimd.memset(c.A("S"), 0.0).then_inc(sx["zero"], 1)
            pool.wait_ge(sx["zero"], 9)
            nc.gpsimd.memset(c.A("SS"), 0.0).then_inc(sx["sSn"], 1)
            pool.wait_ge(sx["sSn"], 1)
            for grp in groups:
                for i in grp:
                    r, (cum, low) = dims(i)
                    u = lane(i)
                    pool.wait_ge(sx["dexp"], 2 * i + 2)
                    for q, (nm, m) in enumerate((("DL", low), ("DT", cum))):
                        a = v4(B[nm][u], i)[0:r]
                        nc.gpsimd.tensor_tensor(a, a, m.unsqueeze(1).to_broadcast([r, HEADS, r]), ALU.mult).then_inc(sx["dmask"], 1)
                        pool.wait_ge(sx["dmask"], 2 * i + q + 1)
                for l in range(len(LV[grp[0]])):
                    for i in grp:
                        r = rows(i)
                        pool.wait_ge(sx["L"], i + 1)
                        m = K(f"lvl{LV[i][l]}", r, r).unsqueeze(1).to_broadcast([r, HEADS, r])
                        if l >= 2:
                            pool.wait_ge(sx["P"], number[(i, l - 2)])
                        elif i >= 2:
                            pool.wait_ge(sx["P"], number[(i - 2, len(LV[i - 2]) - 1)])
                        dst = B["Lb"][lane(i)].rearrange("p (s n) -> p s n", s=2)[:, l % 2, :]
                        nc.gpsimd.tensor_tensor(v4(dst, i)[0:r], v4(B["L"][lane(i)], i)[0:r], m, ALU.mult).then_inc(sx["Lb"], 1)
                        pool.wait_ge(sx["Lb"], number[(i, l)])

        @block.tensor
        def _(pe):
            pe.wait_ge(sx["zero"], 9)

            def turn_kv(grp):
                for i in grp:
                    r = rows(i)
                    for n in range(4):
                        last = nc.tensor.transpose(bk(i, 3)[0:r, n * P:(n + 1) * P], qkvT[:, 2 + n, tok(i)], K("ident"))
                    last.then_inc(sx["kvt"], 1)

            turn_kv(groups[0])
            for gi, grp in enumerate(groups):
                if gi >= 1:
                    pe.wait_ge(sx["S"], 2 * grp[0])
                    pe.wait_ge(sx["oc"], 2 * grp[0])
                for i in grp:
                    r = rows(i)
                    pe.wait_ge(sx["gcum"], i + 1)
                    nc.tensor.matmul(bk(i, 0)[:, 0:4 * r], K("ones", r, P), B["gcum"][lane(i)][0:r, 0:4 * r],
                                     start=True, stop=True).then_inc(sx["G"], 1)
                for i in grp:
                    r = rows(i)
                    pe.wait_ge(sx["kz"], 4 * i + 4)
                    for n, nm in ((1, "kz"), (2, "qz")):
                        z = v4(B[nm][lane(i)], i)
                        for pair in range(2):
                            last = nc.tensor.matmul(bk(i, n)[0:r, pair * 2 * r:(pair + 1) * 2 * r], qkvT[:, 2 + pair, tok(i)],
                                                    z[:, 2 * pair:2 * pair + 2, :].rearrange("p h t -> p (h t)"),
                                                    start=True, stop=True)
                    last.then_inc(sx["kk"], 1)
                for i in grp:
                    r = rows(i)
                    pe.wait_ge(sx["X1"], i + 1)
                    pe.wait_ge(sx["eg"], 2 * i + 2)
                    X = v4(B["X"][lane(i)], i)
                    for hd in range(HEADS):
                        last = nc.tensor.transpose(bk(i, 0)[0:r, hd * r:(hd + 1) * r], X[0:r, hd, :], K("ident", r, r))
                    last.then_inc(sx["Xt"], 1)
                for l in range(len(LV[grp[0]])):
                    for i in grp:
                        r = rows(i)
                        pe.wait_ge(sx["Lb"], number[(i, l)])
                        if l == 0:
                            pe.wait_ge(sx["Y1"], i + 1)
                        else:
                            pe.wait_ge(sx["Y"], 2 * number[(i, l - 1)])
                        Lb = v4(B["Lb"][lane(i)].rearrange("p (s n) -> p s n", s=2)[:, l % 2, :], i)
                        Y = v4(B["Y"][lane(i)], i)
                        for hd in range(HEADS):
                            last = nc.tensor.matmul(bk(i, 0)[0:r, hd * r:(hd + 1) * r], Lb[0:r, hd, :], Y[0:r, hd, :],
                                                    start=True, stop=True)
                        last.then_inc(sx["P"], 1)
                    for i in grp:
                        r = rows(i)
                        pe.wait_ge(sx["Pc"], number[(i, l)])
                        X, Pm = v4(B["X"][lane(i)], i), v4(B["Pm"][lane(i)], i)
                        for hd in range(HEADS):
                            nc.tensor.matmul(bk(i, 1)[0:r, hd * r:(hd + 1) * r], X[0:r, hd, :], Pm[0:r, hd, :],
                                             start=True, stop=True)
                        for hd in range(HEADS):
                            last = nc.tensor.matmul(bk(i, 2)[0:r, hd * r:(hd + 1) * r], Pm[0:r, hd, :], X[0:r, hd, :],
                                                    start=True, stop=True)
                        last.then_inc(sx["YX"], 1)
                for i in grp:
                    r = rows(i)
                    pe.wait_ge(sx["scaled"], 4 * i + 4)
                    pe.wait_ge(sx["Y"], 2 * number[(i, len(LV[i]) - 1)])
                    Y = v4(B["Y"][lane(i)], i)
                    for hd in range(HEADS):
                        nc.tensor.matmul(bk(i, 3)[0:r, hd * DH:(hd + 1) * DH], Y[0:r, hd, :],
                                         B["vb"][lane(i)][0:r, hd * DH:(hd + 1) * DH], start=True, stop=True)
                    for hd in range(HEADS):
                        q = (hd % 2) * DH
                        last = nc.tensor.matmul(bk(i, 0)[q:q + DH, (hd // 2) * r:(hd // 2 + 1) * r],
                                                B["kbe"][lane(i)][0:r, hd * DH:(hd + 1) * DH], Y[0:r, hd, :],
                                                start=True, stop=True)
                    last.then_inc(sx["uw"], 1)
                if grp[0] < NT:
                    pe.wait_ge(sx["uc"], 2 * grp[0] + 4)
                    turn_kv(groups[gi + 1])
                    for i in grp:
                        u = lane(i)
                        pe.wait_ge(sx["uc"], 2 * i + 2)
                        pe.wait_ge(sx["qg"], i + 1)
                        wT, qg = v2(B["wT"][u], i), v2(B["qg"][u], i)
                        vz = V("vz", u)
                        dT = V("DT", u)
                        kg = B["kg"][u].rearrange("p (s n) -> p s n", s=2)
                        for cc in range(2):
                            e = 2 * i + cc
                            if e >= 1:
                                pe.wait_ge(sx["S"], e)
                            for pair in range(2):
                                last = nc.tensor.matmul(bk(i, 0)[:, pair * P:(pair + 1) * P], wT[:, pair, :], S[:, pair, :],
                                                        start=True, stop=True)
                            last.then_inc(sx["vW"], 1)
                            t = slice(cc * CH, (cc + 1) * CH)
                            if e >= 1:
                                pe.wait_ge(sx["oc"], e)
                            out = lambda pair: bk(i, 1)[:, pair * CH:(pair + 1) * CH]
                            for pair in range(2):
                                nc.tensor.matmul(out(pair), S[:, pair, :], qg[:, pair, t], start=(pair == 0), stop=False,
                                                 skip_group_check=True)
                            pe.wait_ge(sx["vn"], e + 1)
                            for pair in range(2):
                                vp = B["vz"][u][:, pair * 256:(pair + 1) * 256].rearrange("p (h n) -> p h n", h=2)
                                for hh in range(2):
                                    last = nc.tensor.matmul(bk(i, 2)[:, pair * P + hh * DH:pair * P + (hh + 1) * DH],
                                                            kg[:, cc, pair * P:(pair + 1) * P], vp[:, hh, hh * DH:(hh + 1) * DH],
                                                            start=True, stop=True)
                            last.then_inc(sx["vW"], 1)
                            for pair in range(2):
                                for hh in range(2):
                                    hd = 2 * pair + hh
                                    last = nc.tensor.matmul(out(pair), vz[:, hd, :], dT[:, hd, t], start=False, stop=(hh == 1),
                                                            skip_group_check=True)
                            last.then_inc(sx["o"], 1)
                else:
                    i = NT
                    pe.wait_ge(sx["uc"], 2 * i + 2)
                    pe.wait_ge(sx["qg"], i + 1)
                    pe.wait_ge(sx["sload"], 16 * DB * HEADS)
                    wT, qg = v2(B["wT"][0], i), v2(B["qg"][0], i)
                    for pair in range(2):
                        for b in range(DB):
                            t = slice(b * DS, (b + 1) * DS)
                            last = nc.tensor.matmul(ps[4][:, pair * NS + b * DS:pair * NS + (b + 1) * DS], SS[:, b, pair, :],
                                                    wT[:, pair, t], start=True, stop=True)
                    last.then_inc(sx["swS"], 1)
                    pe.wait_ge(sx["swc"], 1)
                    for pair in range(2):
                        last = nc.tensor.transpose(ps[5][0:NS, pair * P:(pair + 1) * P], wSs[:, pair, :], K("ident"))
                    last.then_inc(sx["swt"], 1)
                    pe.wait_ge(sx["svn"], 1)
                    vz, dT = V("vz", 0), v4(B["DT"][0], i)
                    for pair in range(2):
                        for hh in range(2):
                            hd = 2 * pair + hh
                            nc.tensor.matmul(ps[6][:, pair * NS:(pair + 1) * NS], vz[0:NS, hd, :], dT[0:NS, hd, :],
                                             start=(pair == 0 and hh == 0), stop=False, skip_group_check=True)
                        for b in range(DB):
                            t = slice(b * DS, (b + 1) * DS)
                            last = nc.tensor.matmul(ps[6][:, pair * NS + b * DS:pair * NS + (b + 1) * DS], SS[:, b, pair, :],
                                                    qg[:, pair, t], start=False, stop=(b == DB - 1), skip_group_check=True)
                    last.then_inc(sx["so"], 1)
                    for hd in range(HEADS):
                        bank = (7, 1, 2, 5)[hd]
                        pe.wait_ge(sx["svx"], hd + 1)
                        nc.tensor.matmul(ps[bank][:, :], B["kg"][0][0:NS, (hd // 2) * P:(hd // 2 + 1) * P],
                                         Vx[0:NS, hd].rearrange("p b n -> p (b n)"), start=True, stop=True).then_inc(sx["sdS"], 1)
            for n in range(2):
                pe.wait_ge(sx["rs"], n + 1)
                for g in range(GRP):
                    bank = ps[(0, 3, 4)[g]]
                    if n:
                        pe.wait_ge(sx["rrn"], g + 1)
                    nc.tensor.matmul(bank[:, 0:GT], K("blk64"), c.rsq[:, n, g * GT:(g + 1) * GT], start=True,
                                     stop=True).then_inc(sx["rss"], 1)

        @block.scalar
        def _(act):
            link = Chain(act, sx["act"])
            nc.scalar.preload_act_table_set(EXPLN)

            def copy_kv(grp):
                for i in grp:
                    r = rows(i)
                    act.wait_ge(sx["kvt"], i + 1)
                    if i >= 2:
                        act.wait_ge(sx["scaled"], 4 * (i - 1))
                    nc.scalar.copy(B["kvt"][lane(i)][0:r, :], bk(i, 3)[0:r, :]).then_inc(sx["kvc"], 1)

            copy_kv(groups[0])
            for gi, grp in enumerate(groups):
                for i in grp:
                    r, _ = dims(i)
                    act.wait_ge(sx["ddve"], 2 * i + 2)
                    G = v4(bk(i, 0), i)
                    eg = v2(B["eg"][lane(i)], i)
                    for half in range(2):
                        q = slice(half * DH, (half + 1) * DH)
                        nc.scalar.activation(eg[q], G[q, half:4:2, :], ACT.Exp).then_inc(sx["eg"], 1)
                    for nm, sc in (("DL", -1.0), ("DT", 1.0)):
                        a = v4(B[nm][lane(i)], i)[0:r]
                        nc.scalar.activation(a, a, ACT.Exp, scale=sc).then_inc(sx["dexp"], 1)
                for i in grp:
                    r = rows(i)
                    act.wait_ge(sx["Xt"], i + 1)
                    nc.scalar.copy(B["Y"][lane(i)][0:r, 0:4 * r], bk(i, 0)[0:r, 0:4 * r]).then_inc(sx["Y1"], 1)
                for l in range(len(LV[grp[0]])):
                    for i in grp:
                        r = rows(i)
                        act.wait_ge(sx["P"], number[(i, l)])
                        nc.scalar.copy(B["Pm"][lane(i)][0:r, 0:4 * r], bk(i, 0)[0:r, 0:4 * r]).then_inc(sx["Pc"], 1)
                for i in grp:
                    r = rows(i)
                    act.wait_ge(sx["uw"], i + 1)
                    nc.scalar.copy(B["u"][lane(i)][0:r, :], bk(i, 3)[0:r, 0:256]).then_inc(sx["uc"], 1)
                    nc.scalar.copy(B["wT"][lane(i)][:, 0:2 * r], bk(i, 0)[:, 0:2 * r]).then_inc(sx["uc"], 1)
                if grp[0] < NT:
                    copy_kv(groups[gi + 1])
                    for i in grp:
                        for cc in range(2):
                            act.wait_ge(sx["o"], 2 * i + cc + 1)
                            nc.scalar.copy(odT[:, :, i * P + cc * CH:i * P + (cc + 1) * CH],
                                           bk(i, 1)[:, 0:P].rearrange("p (c t) -> p c t", c=2)).then_inc(sx["oc"], 1)
                else:
                    act.wait_ge(sx["swS"], 1)
                    nc.scalar.copy(wSs, ps[4][:, 0:2 * NS].rearrange("p (c t) -> p c t", c=2)).then_inc(sx["swc"], 1)
                    act.wait_ge(sx["so"], 1)
                    nc.scalar.copy(odT[:, :, SEQ:TOK], ps[6][:, 0:2 * NS].rearrange("p (c t) -> p c t", c=2)).then_inc(sx["oc"], 1)
            act.wait_ge(sx["oc"], 2 * NT + 1)
            for n in range(2):
                nc.scalar.activation(c.rsq[:, n, :], odT[:, n, :], ACT.Square).then_inc(sx["rs"], 1)
            for n in range(2):
                for g in range(GRP):
                    act.wait_ge(sx["rss"], GRP * n + g + 1)
                    t = c.rrn[:, n, g * GT:(g + 1) * GT]
                    link(nc.scalar.activation(t, ps[(0, 3, 4)[g]][:, 0:GT], ACT.Ln, bias=c.eps6, scale=1.0 / DH))
                    nc.scalar.activation(t, t, ACT.Exp, scale=-0.5).then_inc(sx["rrn"], 1)

        @block.vector
        def _(dve):
            link = Chain(dve, sx["dve"])
            dve.wait_ge(sx["zero"], 9)

            def prepare(grp):
                for i in grp:
                    r, (cum, low) = dims(i)
                    u = lane(i)
                    gb = c.g[0:r, i, :].unsqueeze(2).to_broadcast([r, HEADS, r])
                    nc.vector.tensor_tensor(v4(B["gcum"][u], i)[0:r], cum.unsqueeze(1).to_broadcast([r, HEADS, r]), gb,
                                            ALU.mult).then_inc(sx["gcum"], 1)
                    if i == NT:
                        for nm in ("kz", "qz"):
                            nc.vector.memset(B[nm][0], 0.0).then_inc(sx["zq"], 1)
                        dve.wait_ge(sx["zq"], 2)
                    for nm, ch in (("kz", 2), ("qz", 0)):
                        z = v4(B[nm][u], i)
                        for half in range(2):
                            q = slice(half * DH, (half + 1) * DH)
                            nc.vector.tensor_copy(z[q, half:4:2, :], qkvT[q, ch:ch + 2, tok(i)]).then_inc(sx["kz"], 1)

            prepare(groups[0])
            for gi, grp in enumerate(groups):
                if gi >= 1:
                    dve.wait_ge(sx["o"], 2 * grp[0])
                for i in grp:
                    r = rows(i)
                    u = lane(i)
                    dve.wait_ge(sx["G"], i + 1)
                    gcb = c.log_decay[0:r, i, :].unsqueeze(2).to_broadcast([r, HEADS, r])
                    d = v4(B["gcum"][u], i)[0:r]
                    nc.vector.tensor_tensor(d, v4(bk(i, 0), i)[0:r], gcb, ALU.subtract).then_inc(sx["dif"], 1)
                    dve.wait_ge(sx["dif"], i + 1)
                    nc.vector.tensor_scalar(v4(B["DL"][u], i)[0:r], d, 0.0, None, ALU.max).then_inc(sx["ddve"], 1)
                    nc.vector.tensor_scalar(v4(B["DT"][u], i)[0:r], d, 0.0, None, ALU.min).then_inc(sx["ddve"], 1)
                for i in grp:
                    r = rows(i)
                    u = lane(i)
                    dve.wait_ge(sx["kvc"], i + 1)
                    kv = B["kvt"][u].rearrange("p (q h d) -> p q h d", q=2, h=HEADS)

                    def by(col):
                        return col[0:r, i, :].unsqueeze(2).to_broadcast([r, HEADS, DH])

                    hd_view = lambda ap: ap.rearrange("p (h d) -> p h d", h=HEADS)
                    nc.vector.tensor_tensor(hd_view(B["vb"][u])[0:r], kv[0:r, 1], by(c.beta), ALU.mult).then_inc(sx["scaled"], 1)
                    nc.vector.tensor_tensor(hd_view(B["kbe"][u])[0:r], kv[0:r, 0], by(c.be), ALU.mult).then_inc(sx["scaled"], 1)
                    kg = B["kg"][u].rearrange("p (s h d) -> p s h d", s=2, h=HEADS)
                    if i < NT:
                        for cc in range(2):
                            q = slice(cc * CH, (cc + 1) * CH)
                            nc.vector.tensor_tensor(kg[q, cc], kv[q, 0], c.kgf[q, i, :].unsqueeze(2).to_broadcast([CH, HEADS, DH]),
                                                    ALU.mult).then_inc(sx["scaled"], 1)
                    else:
                        nc.vector.tensor_tensor(kg[0:r, 0], kv[0:r, 0], by(c.kgf), ALU.mult).then_inc(sx["scaled"], 2)
                    dve.wait_ge(sx["eg"], 2 * i + 2)
                    nc.vector.tensor_tensor(v2(B["qg"][u], i), qkvT[:, 0:2, tok(i)], v2(B["eg"][u], i), ALU.mult).then_inc(sx["qg"], 1)
                for i in grp:
                    r = rows(i)
                    u = lane(i)
                    dve.wait_ge(sx["kk"], i + 1)
                    dve.wait_ge(sx["dmask"], 2 * i + 2)
                    L, DL, X = (v4(B[nm][u], i)[0:r] for nm in ("L", "DL", "X"))
                    for hd in range(HEADS):
                        ins = nc.vector.scalar_tensor_tensor(L[:, hd, :], v4(bk(i, 1), i)[0:r, hd, :], c.beta[0:r, i, hd:hd + 1],
                                                             DL[:, hd, :], ALU.mult, ALU.mult)
                        link(ins) if hd < HEADS - 1 else ins.then_inc(sx["L"], 1)
                    dt = v4(B["DT"][u], i)[0:r]
                    nc.vector.tensor_tensor(dt, v4(bk(i, 2), i)[0:r], dt, ALU.mult).then_inc(sx["intra"], 1)
                    dve.wait_ge(sx["L"], i + 1)
                    link(nc.vector.tensor_tensor(X, L, K("lvl1", r, r).unsqueeze(1).to_broadcast([r, HEADS, r]), ALU.mult))
                    nc.vector.scalar_tensor_tensor(X, X, -1.0, K("ident", r, r).unsqueeze(1).to_broadcast([r, HEADS, r]),
                                                   ALU.mult, ALU.add).then_inc(sx["X1"], 1)
                for l in range(len(LV[grp[0]])):
                    for i in grp:
                        r = rows(i)
                        u = lane(i)
                        dve.wait_ge(sx["YX"], number[(i, l)])
                        Y, X = B["Y"][u][0:r, 0:4 * r], B["X"][u][0:r, 0:4 * r]
                        if l == 0:
                            dve.wait_ge(sx["Y1"], i + 1)
                            dve.wait_ge(sx["X1"], i + 1)
                        nc.vector.tensor_tensor(Y, Y, bk(i, 1)[0:r, 0:4 * r], ALU.subtract).then_inc(sx["Y"], 1)
                        nc.vector.tensor_tensor(X, X, bk(i, 2)[0:r, 0:4 * r], ALU.subtract).then_inc(sx["Y"], 1)
                        if l + 1 < len(LV[i]):
                            dve.wait_ge(sx["Y"], 2 * number[(i, l)])
                if grp[0] < NT:
                    prepare(groups[gi + 1])
                    for i in grp:
                        u = lane(i)
                        r = P
                        eg = v2(B["eg"][u], i)
                        dve.wait_ge(sx["uc"], 2 * i + 2)
                        for cc in range(2):
                            e = 2 * i + cc
                            q = slice(cc * CH, (cc + 1) * CH)
                            dve.wait_ge(sx["vW"], 2 * e + 1)
                            for pair in range(2):
                                for hh in range(2):
                                    hd = 2 * pair + hh
                                    nc.vector.tensor_tensor(V("vz", u)[q, hd, hh * DH:(hh + 1) * DH],
                                                            B["u"][u][q, hd * DH:(hd + 1) * DH],
                                                            bk(i, 0)[q, hd * DH:(hd + 1) * DH], ALU.subtract)\
                                        .then_inc(sx["vn"] if hd == 3 else sx["init"], 1)
                            dve.wait_ge(sx["vW"], 2 * e + 2)
                            link(nc.vector.tensor_tensor(dS, bk(i, 2)[:, 0:256].rearrange("p (c n) -> p c n", c=2),
                                                         K("blk64").unsqueeze(1).to_broadcast([P, 2, P]), ALU.mult))
                            for pair in range(2):
                                ins = nc.vector.scalar_tensor_tensor(S[:, pair, :], S[:, pair, :],
                                                                     eg[:, pair, cc * CH + CH - 1:cc * CH + CH], dS[:, pair, :],
                                                                     ALU.mult, ALU.add)
                                link(ins) if pair == 0 else ins.then_inc(sx["S"], 1)
                            dve.wait_ge(sx["S"], e + 1)
                else:
                    i = NT
                    dve.wait_ge(sx["swt"], 1)
                    dve.wait_ge(sx["uc"], 2 * i + 2)
                    for hd in range(HEADS):
                        hh = hd % 2
                        ins = nc.vector.tensor_tensor(V("vz", 0)[0:NS, hd, hh * DH:(hh + 1) * DH],
                                                      B["u"][0][0:NS, hd * DH:(hd + 1) * DH],
                                                      ps[5][0:NS, hd * DH:(hd + 1) * DH], ALU.subtract)
                        link(ins) if hd < 3 else ins.then_inc(sx["svn"], 1)
                    dve.wait_ge(sx["svn"], 1)
                    sel = K("blk4", NS, NS)[:, 0:NS:DS]
                    for hd in range(HEADS):
                        hh = hd % 2
                        vn = V("vz", 0)[0:NS, hd, hh * DH:(hh + 1) * DH].unsqueeze(1).to_broadcast([NS, DB, DH])
                        nc.vector.tensor_tensor(Vx[0:NS, hd], vn, sel.unsqueeze(2).to_broadcast([NS, DB, DH]),
                                                ALU.mult).then_inc(sx["svx"], 1)
                    eg = v2(B["eg"][0], i)
                    for hd in range(HEADS):
                        pair, hh = hd // 2, hd % 2
                        q = slice(hh * DH, (hh + 1) * DH)
                        gl = eg[q, pair, DS - 1:NS:DS].unsqueeze(2).to_broadcast([DH, DB, DH])
                        link(nc.vector.tensor_tensor(Sn[q, hd], SS[q, :, pair, q], gl, ALU.mult))
                        dve.wait_ge(sx["sdS"], hd + 1)
                        bank = (7, 1, 2, 5)[hd]
                        nc.vector.tensor_tensor(Sn[q, hd], ps[bank][q, :].rearrange("p (b n) -> p b n", b=DB), Sn[q, hd],
                                                ALU.add).then_inc(sx["ost"], 1)
            for n in range(2):
                for g in range(GRP):
                    t = slice(g * GT, (g + 1) * GT)
                    dve.wait_ge(sx["rrn"], GRP * n + g + 1)
                    link(nc.vector.scalar_tensor_tensor(odT[:, n, t], odT[:, n, t], c.A("dnorm")[:, 0:1], c.rrn[:, n, t],
                                                        ALU.mult, ALU.mult))
                    nc.vector.tensor_tensor(oT[:, 6 + n, t], odT[:, n, t], zT[:, n, t], ALU.mult).then_inc(sx["rout"], 1)

        @block.sync
        def _(sp):
            sp.dma_start(c.h[:, 0:NT, :], c.tokens_dram[0:SEQ, :].rearrange("(i p) d -> p i d", p=P)).then_inc(sx["hin"], 16)
            sp.dma_start(c.h[0:NS, NT, :], c.tokens_dram[SEQ:TOK, :]).then_inc(sx["hin"], 16)
            sp.wait_ge(sx["sSn"], 1)
            for hd in range(HEADS):
                q = slice((hd % 2) * DH, (hd % 2 + 1) * DH)
                for b in range(DB):
                    sp.dma_start(SS[q, b, hd // 2, q], T['state_delta'][0, b, hd]).then_inc(sx["sload"], 16)
            sp.wait_ge(sx["S"], 2 * NT)
            for hd in range(HEADS):
                q = slice((hd % 2) * DH, (hd % 2 + 1) * DH)
                sp.dma_start(O['delta_prompt'][0, 0, hd], S[q, hd // 2, q]).then_inc(sx["soc"], 16)
            for hd in range(HEADS):
                q = slice((hd % 2) * DH, (hd % 2 + 1) * DH)
                sp.wait_ge(sx["ost"], hd + 1)
                sp.dma_start(O['delta_sample'][0, :, hd].rearrange("b k v -> k b v"), Sn[q, hd]).then_inc(sx["soc"], 16)
            sp.wait_ge(sx["soc"], 16 * 2 * HEADS)
            sp.wait_ge(sx["hin"], 32)


def three_passes(nc, out, high, low, w_high, w_low, start, stop):
    nc.tensor.matmul(out, high, w_high, start=start, stop=False)
    nc.tensor.matmul(out, high, w_low, start=False, stop=False)
    return nc.tensor.matmul(out, low, w_high, start=False, stop=stop)


def stage_residual(c, tag, src, weight, gain, shift, split):
    nc, T, O, K = c.nc, c.T, c.O, c.K
    c.place(start=c.res_at, rw=KC * D, rwh=KC * D, rg=D, rb=D)
    c.place(start=c.split_at, sh=2 * D, sl=2 * D)
    wview = lambda x: x.rearrange("p (k n) -> p k n", k=KC)
    w, wh, wl = wview(c.A("rw")), wview(c.rounded(f"{tag}_w_high", "rwh")), wview(c.rounded(f"{tag}_w_low", "rw"))
    sview = lambda x: x.rearrange("p (s k t) -> p s k t", s=2, k=KC)
    sh, sl = sview(c.rounded(f"{tag}_s_high", "sh")), sview(c.rounded(f"{tag}_s_low", "sl"))
    g, b = c.A("rg"), c.A("rb")
    h, hT, ps = c.h, c.hT, c.ps
    s = lambda n: c.sem(f"{tag}_{n}")
    w_in = [s(f"w{n}") for n in range(4)]
    ln_in, prod, added, stats, rstd_ok, normed, turned, hT_ok, low_ok = (
        s("ln"), s("prod"), s("added"), s("stats"), s("rstd"), s("normed"), s("turned"), s("hT"), s("low"))
    wh_ok, wl_ok, sh_ok, sl_ok = s("wh"), s("wl"), s("sh"), s("sl")
    dve_chain, act_chain = s("dve"), s("act")
    wv = T[weight][0].rearrange("(k p) n -> p k n", p=P)

    def piece(x, n):
        q, kh = n // 2, n % 2
        return x[:, 4 * kh:4 * kh + 4, q * 512:(q + 1) * 512]

    def tile(i):
        return slice(i * P, i * P + rows(i))

    def bank4(q, r):
        return ps[4 + q][:, 0:4 * r].rearrange("p (k t) -> p k t", k=4)

    with nc.Block() as block:
        @block.sync
        def _(sp):
            for n in range(4):
                sp.dma_start(piece(w, n), piece(wv, n)).then_inc(w_in[n], 16)
            sp.dma_start(g, row_bc(T[gain][0])).then_inc(ln_in, 16)
            sp.dma_start(b, row_bc(T[shift][0])).then_inc(ln_in, 16)
            if not split:
                sp.dma_start(c.A("wr").rearrange("p (k e) -> p k e", k=KC), T['w_router'].rearrange("(k p) e -> p k e", p=P))\
                    .then_inc(c.route_in, 16)
                sp.dma_start(c.A("rbias"), row_bc(T['router_bias'])).then_inc(c.route_in, 16)
                sp.dma_start(c.A("tab"), T['route_table']).then_inc(c.route_in, 16)

        @block.tensor
        def _(pe):
            def product(i):
                r = rows(i)
                pe.wait_ge(sl_ok, i + 1)
                for q in range(2):
                    if i >= 2:
                        pe.wait_ge(added, 2 * (i - 2) + q + 1)
                    n = slice(q * 512, (q + 1) * 512)
                    for k in range(KC):
                        if i == 0 and k % 4 == 0:
                            pe.wait_ge(wl_ok, 2 * q + k // 4 + 1)
                        last = three_passes(nc, ps[2 * (i % 2) + q][0:r, :], sh[:, i % 2, k, 0:r], sl[:, i % 2, k, 0:r],
                                            wh[:, k, n], wl[:, k, n], k == 0, k == KC - 1)
                    last.then_inc(prod, 1)

            def transposes(i):
                r = rows(i)
                pe.wait_ge(normed, i + 1)
                for q in range(2):
                    if i >= 1:
                        pe.wait_ge(hT_ok, 2 * (i - 1) + q + 1)
                        if split:
                            pe.wait_ge(low_ok, 2 * (i - 1) + q + 1)
                    for k in range(4):
                        last = nc.tensor.transpose(ps[4 + q][:, k * r:(k + 1) * r],
                                                   h[0:r, i, (4 * q + k) * P:(4 * q + k + 1) * P], K("ident", r, r))
                    last.then_inc(turned, 1)

            for i in range(TILES + 1):
                if i < TILES:
                    product(i)
                if i >= 1:
                    transposes(i - 1)

        @block.vector
        def _(dve):
            link = Chain(dve, dve_chain)

            def src_low(i):
                dve.wait_ge(sh_ok, i + 1)
                r = rows(i)
                nc.vector.tensor_tensor(sl[:, i % 2, :, 0:r], src[:, :, tile(i)], sh[:, i % 2, :, 0:r].bitcast(F32),
                                        ALU.subtract).then_inc(sl_ok, 1)

            def add(i):
                r = rows(i)
                for q in range(2):
                    dve.wait_ge(prod, 2 * i + q + 1)
                    x = h[0:r, i, q * 512:(q + 1) * 512]
                    nc.vector.scalar_tensor_tensor(x, x, ALPHA, ps[2 * (i % 2) + q][0:r, :], ALU.mult, ALU.add).then_inc(added, 1)
                dve.wait_ge(added, 2 * i + 2)
                if i >= 2:
                    dve.wait_ge(rstd_ok, i - 1)
                ln_stats(nc, link, h, i, c.st[:, i % 2, :], c.mv[:, i % 2, :]).then_inc(stats, 1)

            def apply(i):
                dve.wait_ge(stats, i + 1)
                dve.wait_ge(rstd_ok, i + 1)
                ln_apply(nc, link, h, i, c.mv[:, i % 2, :], c.rstd[:, i % 2, :], g, b).then_inc(normed, 1)

            def hT_low(i):
                for q in range(2):
                    dve.wait_ge(hT_ok, 2 * i + q + 1)
                    nc.vector.tensor_tensor(c.hT_low[:, 4 * q:4 * q + 4, tile(i)], bank4(q, rows(i)),
                                            c.hT_high[:, 4 * q:4 * q + 4, tile(i)].bitcast(F32), ALU.subtract).then_inc(low_ok, 1)

            src_low(0)
            for n in range(4):
                dve.wait_ge(wh_ok, n + 1)
                nc.vector.tensor_tensor(piece(wl, n), piece(w, n), piece(wh, n).bitcast(F32), ALU.subtract).then_inc(wl_ok, 1)
            src_low(1)
            dve.wait_ge(ln_in, 32)
            for i in range(TILES + 1):
                if i < TILES:
                    add(i)
                if i + 2 < TILES:
                    src_low(i + 2)
                if i < TILES:
                    apply(i)
                if split and i >= 1:
                    hT_low(i - 1)

        @block.scalar
        def _(act):
            link = Chain(act, act_chain)
            nc.scalar.preload_act_table_set(EXPLN)

            def src_high(i):
                if i >= 2:
                    act.wait_ge(prod, 2 * i - 2)
                r = rows(i)
                nc.scalar.copy(sh[:, i % 2, :, 0:r], src[:, :, tile(i)]).then_inc(sh_ok, 1)

            src_high(0)
            for n in range(4):
                act.wait_ge(w_in[n], 16)
                nc.scalar.copy(piece(wh, n), piece(w, n)).then_inc(wh_ok, 1)
            src_high(1)
            for i in range(TILES + 1):
                if i + 2 < TILES:
                    src_high(i + 2)
                if i < TILES:
                    act.wait_ge(stats, i + 1)
                    if i >= 2:
                        act.wait_ge(normed, i - 1)
                    ln_rstd(nc, link, i, c.mv[:, i % 2, :], c.rstd[:, i % 2, :], c.eps).then_inc(rstd_ok, 1)
                if i >= 1:
                    for q in range(2):
                        act.wait_ge(turned, 2 * (i - 1) + q + 1)
                        act.wait_ge(sl_ok, i)
                        dst = c.hT_high if split else hT
                        nc.scalar.copy(dst[:, 4 * q:4 * q + 4, tile(i - 1)], bank4(q, rows(i - 1))).then_inc(hT_ok, 1)


def load_query_chunk(c, sp, n):
    ring = c.A("qring").rearrange("p (s k n) -> p s k n", s=4, k=KC)
    wv = c.T['xa_wq'][0].rearrange("(k p) n -> p k n", p=P)
    sp.dma_start(ring[:, n % 4], wv[:, :, n * P:(n + 1) * P]).then_inc(c.q_in[n % 4], 16)


def stage_memory(c):
    nc, T, O, K = c.nc, c.T, c.O, c.K
    c.place(start=0, KT=KC * NMEM, Vm=2 * D, qXT=KC * TOK)
    c.place(start=4096, Km=2 * D, mem=2 * D, memT=KC * NMEM, halves=3 * KC * 512)
    KT = c.A("KT").rearrange("p (k m) -> p k m", k=KC)
    Vm, Km, mem = (c.A(n).rearrange("p (m n) -> p m n", m=2) for n in ("Vm", "Km", "mem"))
    memT = c.A("memT").rearrange("p (k m) -> p k m", k=KC)
    w = c.A("halves").rearrange("p (s k n) -> p s k n", s=3, k=KC)
    c.KT, c.Vm = KT, Vm
    ps = c.ps
    s = lambda n: c.sem(f"m_{n}")
    w_in = [s(f"w{n}") for n in range(3)]
    c.place(start=c.at["halves"][0] + 4096, qring=4 * KC * P, qhigh=4 * KC * P)
    c.q_in = [s(f"q{n}") for n in range(4)]
    mem_in, turned, mT_ok, prod, out_ok, kturned, kT_ok, stored = (
        s("mem"), s("turned"), s("mT"), s("prod"), s("out"), s("kturned"), s("kT"), s("stored"))

    with nc.Block() as block:
        @block.sync
        def _(sp):
            sp.dma_start(mem, T['mem_prompt'][0].rearrange("(m p) n -> p m n", p=P)).then_inc(mem_in, 16)
            for n in range(4):
                if n == 3:
                    sp.wait_ge(prod, 2)
                src = T[('xa_wk', 'xa_wv')[n // 2]][0].rearrange("(k p) n -> p k n", p=P)
                sp.dma_start(w[:, n % 3], src[:, :, (n % 2) * 512:(n % 2 + 1) * 512]).then_inc(w_in[n % 3], 16)
            sp.wait_ge(prod, 4)
            for n in range(4):
                load_query_chunk(c, sp, n)
            for n, (name, t) in enumerate((('mem_k_prompt', Km), ('mem_v_prompt', Vm))):
                sp.wait_ge(out_ok, 4 * (n + 1))
                sp.dma_start(O[name][0, 0].rearrange("(m p) h d -> p m (h d)", p=P), t).then_inc(stored, 16)
            sp.wait_ge(stored, 32)

        @block.tensor
        def _(pe):
            def turns(src, f, base, sem_t, freed):
                for k in (2 * f, 2 * f + 1):
                    for m in range(2):
                        last = nc.tensor.transpose(ps[base + f % 4][:, (k % 2) * NMEM + m * P:(k % 2) * NMEM + (m + 1) * P],
                                                   src[:, m, k * P:(k + 1) * P], K("ident"))
                last.then_inc(sem_t, 1)

            pe.wait_ge(mem_in, 16)
            for f in range(4):
                turns(mem, f, 0, turned, None)
            pe.wait_ge(mT_ok, 4)
            for u in range(8):
                half, m = u // 2, u % 2
                pe.wait_ge(w_in[half % 3], 16 * (half // 3 + 1))
                if u >= 4:
                    pe.wait_ge(out_ok, u - 3)
                for k in range(KC):
                    last = nc.tensor.matmul(ps[4 + u % 4][:, :], memT[:, k, m * P:(m + 1) * P], w[:, half % 3, k, :],
                                            start=(k == 0), stop=(k == KC - 1))
                last.then_inc(prod, 1)
                if u == 3:
                    pe.wait_ge(out_ok, 4)
                    for f in range(4):
                        turns(Km, f, 0, kturned, None)

        @block.scalar
        def _(act):
            for f in range(4):
                act.wait_ge(turned, f + 1)
                nc.scalar.copy(memT[:, 2 * f:2 * f + 2, :], ps[f][:, :].rearrange("p (k m) -> p k m", k=2)).then_inc(mT_ok, 1)
            for f in range(4):
                act.wait_ge(kturned, f + 1)
                nc.scalar.copy(KT[:, 2 * f:2 * f + 2, :], ps[f][:, :].rearrange("p (k m) -> p k m", k=2)).then_inc(kT_ok, 1)

        @block.vector
        def _(dve):
            for u in range(8):
                dst = (Km, Vm)[u // 4][:, u % 2, (u // 2 % 2) * 512:(u // 2 % 2 + 1) * 512]
                dve.wait_ge(prod, u + 1)
                nc.vector.tensor_copy(dst, ps[4 + u % 4][:, :]).then_inc(out_ok, 1)


def stage_queries(c):
    nc, T = c.nc, c.T
    rview = lambda x: x.rearrange("p (s k n) -> p s k n", s=4, k=KC)
    ring, low, high = rview(c.A("qring")), rview(c.rounded("q_w_low", "qring")), rview(c.rounded("q_w_high", "qhigh"))
    qXT = c.A("qXT").rearrange("p (k t) -> p k t", k=KC)
    c.qXT = qXT
    ps = c.ps
    s = lambda n: c.sem(f"q_{n}")
    w_in, prod, evac, high_ok, low_ok = c.q_in, s("prod"), s("evac"), s("high"), s("low")
    with nc.Block() as block:
        @block.sync
        def _(sp):
            for n in range(4, KC):
                sp.wait_ge(prod, GRP * (n - 3))
                load_query_chunk(c, sp, n)

        @block.tensor
        def _(pe):
            for n in range(KC):
                pe.wait_ge(low_ok, n + 1)
                for g in range(GRP):
                    u = GRP * n + g
                    if u >= 8:
                        pe.wait_ge(evac, u - 7)
                    t = slice(g * GT, (g + 1) * GT)
                    for k in range(KC):
                        last = three_passes(nc, ps[u % 8][:, 0:GT], high[:, n % 4, k, :], low[:, n % 4, k, :],
                                            c.hT_high[:, k, t], c.hT_low[:, k, t], k == 0, k == KC - 1)
                    last.then_inc(prod, 1)

        @block.vector
        def _(dve):
            for n in range(KC):
                dve.wait_ge(high_ok, n + 1)
                nc.vector.tensor_tensor(low[:, n % 4], ring[:, n % 4], high[:, n % 4].bitcast(F32), ALU.subtract).then_inc(low_ok, 1)

        @block.scalar
        def _(act):
            def round_chunk(n):
                act.wait_ge(w_in[n % 4], 16 * (n // 4 + 1))
                nc.scalar.copy(high[:, n % 4], ring[:, n % 4]).then_inc(high_ok, 1)

            for n in range(3):
                round_chunk(n)
            for n in range(KC):
                for u in range(GRP * n, GRP * (n + 1)):
                    act.wait_ge(prod, u + 1)
                    nc.scalar.copy(qXT[:, n, (u % GRP) * GT:(u % GRP + 1) * GT], ps[u % 8][:, 0:GT]).then_inc(evac, 1)
                if n + 3 < KC:
                    round_chunk(n + 3)


def stage_cross(c):
    nc, T, O, K = c.nc, c.T, c.O, c.K
    c.place(start=4096 + KC * TOK, xp=2 * D, xpT=D, Kb=2 * 2 * D, KTb=2 * 2 * D, Vb=2 * 2 * D, sS=256, xps=256, xpTs=256)
    KT, Vm, qXT = c.KT, c.Vm, c.qXT
    xp = c.A("xp").rearrange("p (s h m) -> p s h m", s=2, h=HEADS)
    xpT = c.A("xpT").rearrange("p (m h q) -> p m h q", m=2, h=HEADS)
    Kb = c.A("Kb").rearrange("p (s m n) -> p s m n", s=2, m=2)
    Va = c.A("Vb").rearrange("p (s m n) -> p s m n", s=2, m=2)
    Vh = c.hT.rearrange("p k t -> p (k t)")[:, 0:8 * D].rearrange("p (s m n) -> p s m n", s=4, m=2)
    Vb = [Va[:, 0], Va[:, 1]] + [Vh[:, n] for n in range(4)]
    VS = len(Vb)
    KTb = c.A("KTb").rearrange("p (s k m) -> p s k m", s=2, k=KC)
    sS, xps, xpTs = c.A("sS"), c.A("xps"), c.A("xpTs")
    mx = c.new_small(2 * HEADS).rearrange("p (s h) -> p s h", s=2)
    sm = c.new_small(2 * HEADS).rearrange("p (s h) -> p s h", s=2)
    mxs, sms = c.new_small(1), c.new_small(1)
    ps = c.ps
    s = lambda n: c.sem(f"x_{n}")
    k_in, v_in = [s("k0"), s("k1")], [s(f"v{n}") for n in range(VS)]
    score, neg, exp_ok, p_ok, pturned, pT_ok, val, val_ok = (s("score"), s("neg"), s("exp"), s("p"), s("pturned"),
                                                             s("pT"), s("val"), s("valok"))
    kturned, kT_ok, sscore, s_ok, s_back, s_neg, s_exp, s_p, s_pt, s_pT, v_done, x_ok = (
        s("kturned"), s("kT"), s("sscore"), s("sok"), s("sback"), s("sneg"), s("sexp"), s("sp"), s("spt"), s("spT"),
        s("vdone"), s("xok"))
    dve_chain, act_chain = s("dve"), s("act")
    SC = XDH ** -0.5

    with nc.Block() as block:
        @block.sync
        def _(sp):
            def load(name, dst, b, done):
                sp.dma_start(dst, T[name][0, b].rearrange("(m p) h d -> p m (h d)", p=P)).then_inc(done, 16)

            for b in range(DB):
                if b >= 2:
                    sp.wait_ge(kturned, 4 * (b - 1))
                load('cache_mem_k', Kb[:, b % 2], b, k_in[b % 2])
                if b >= 2:
                    load('cache_mem_v', Vb[b - 2], b - 2, v_in[b - 2])
            for b in range(VS, DB):
                sp.wait_ge(v_done, b - VS + 1)
                load('cache_mem_v', Vb[b % VS], b, v_in[b % VS])

        @block.tensor
        def _(pe):
            def turn_keys(b, f):
                if f == 0:
                    pe.wait_ge(k_in[b % 2], 16 * (b // 2 + 1))
                if 4 * b + f >= 1:
                    pe.wait_ge(kT_ok, 4 * b + f)
                for k in (2 * f, 2 * f + 1):
                    for m in range(2):
                        last = nc.tensor.transpose(ps[6][:, (k % 2) * NMEM + m * P:(k % 2) * NMEM + (m + 1) * P],
                                                   Kb[:, b % 2, m, k * P:(k + 1) * P], K("ident"))
                last.then_inc(kturned, 1)

            def sample_scores(b):
                pe.wait_ge(kT_ok, 4 * b + 4)
                for m in range(2):
                    for hd in range(HEADS):
                        at = m * P + b * HEADS * DS + hd * DS
                        for dc in range(2):
                            last = nc.tensor.matmul(ps[7][:, at:at + DS], KTb[:, b % 2, 2 * hd + dc, m * P:(m + 1) * P],
                                                    qXT[:, 2 * hd + dc, SEQ + b * DS:SEQ + (b + 1) * DS],
                                                    start=(dc == 0), stop=(dc == 1))
                last.then_inc(sscore, 1)

            def scores(i):
                if i >= 1:
                    pe.wait_ge(exp_ok, HEADS * i)
                    pe.wait_ge(neg, i)
                for hd in range(HEADS):
                    for dc in range(2):
                        last = nc.tensor.matmul(ps[hd // 2][:, (hd % 2) * NMEM:(hd % 2 + 1) * NMEM],
                                                qXT[:, 2 * hd + dc, i * P:(i + 1) * P], KT[:, 2 * hd + dc, :],
                                                start=(dc == 0), stop=(dc == 1))
                last.then_inc(score, 1)

            def turn_p(i):
                pe.wait_ge(p_ok, i + 1)
                if i >= 1:
                    pe.wait_ge(pT_ok, 2 * i)
                for m in range(2):
                    for hd in range(HEADS):
                        last = nc.tensor.transpose(ps[2 + m][:, hd * P:(hd + 1) * P], xp[:, i % 2, hd, m * P:(m + 1) * P],
                                                   K("ident"))
                    last.then_inc(pturned, 1)

            def values(i):
                pe.wait_ge(pT_ok, 2 * i + 2)
                if i >= 1:
                    pe.wait_ge(val_ok, 2 * i)
                for k in range(KC):
                    for m in range(2):
                        last = nc.tensor.matmul(ps[4 + k // 4][:, (k % 4) * P:(k % 4 + 1) * P], Vm[:, m, k * P:(k + 1) * P],
                                                xpT[:, m, k // 2, :], start=(m == 0), stop=(m == 1))
                    if k % 4 == 3:
                        last.then_inc(val, 1)

            for i in range(NT + 1):
                if i == 0:
                    scores(i)
                    turn_keys(i, 0)
                    turn_keys(i, 1)
                elif i < NT:
                    turn_keys(i, 0)
                    scores(i)
                    turn_keys(i, 1)
                if i >= 1:
                    sample_scores(i - 1)
                if i >= 1:
                    turn_p(i - 1)
                if i < NT:
                    turn_keys(i, 2)
                if i >= 1:
                    values(i - 1)
                if i < NT:
                    turn_keys(i, 3)
            pe.wait_ge(s_ok, 1)
            pe.wait_ge(exp_ok, HEADS * NT)
            for m in range(2):
                last = nc.tensor.transpose(ps[0][:, m * P:(m + 1) * P], sS[:, m * P:(m + 1) * P], K("ident"))
            last.then_inc(s_back, 1)
            pe.wait_ge(s_p, 1)
            for m in range(2):
                last = nc.tensor.transpose(ps[1][:, m * P:(m + 1) * P], xps[:, m * P:(m + 1) * P], K("ident"))
            last.then_inc(s_pt, 1)
            pe.wait_ge(s_pT, 1)
            for b in range(DB):
                pe.wait_ge(v_in[b % VS], 16 * (b // VS + 1))
                for k in range(KC):
                    at = b * HEADS * DS + (k // 2) * DS
                    for m in range(2):
                        last = nc.tensor.matmul(ps[6][:, k * NS + b * DS:k * NS + (b + 1) * DS],
                                                Vb[b % VS][:, m, k * P:(k + 1) * P], xpTs[:, m * P + at:m * P + at + DS],
                                                start=(m == 0), stop=(m == 1))
                last.then_inc(v_done, 1)

        @block.scalar
        def _(act):
            link = Chain(act, act_chain)
            nc.scalar.preload_act_table_set(EXPLN)

            def exps(i):
                act.wait_ge(neg, i + 1)
                if i >= 2:
                    act.wait_ge(pturned, 2 * (i - 1))
                for hd in range(HEADS):
                    nc.scalar.activation(xp[:, i % 2, hd, :], ps[hd // 2][:, (hd % 2) * NMEM:(hd % 2 + 1) * NMEM], ACT.Exp,
                                         bias=mx[:, i % 2, hd:hd + 1], scale=SC,
                                         accum_out=sm[:, i % 2, hd:hd + 1]).then_inc(exp_ok, 1)

            def pT(i):
                for m in range(2):
                    act.wait_ge(pturned, 2 * i + m + 1)
                    if i >= 1:
                        act.wait_ge(val, 2 * i)
                    nc.scalar.copy(xpT[:, m], ps[2 + m][:, :].rearrange("p (h q) -> p h q", h=HEADS)).then_inc(pT_ok, 1)

            def keyT(b, f):
                act.wait_ge(kturned, 4 * b + f + 1)
                if b >= 2 and f == 0:
                    act.wait_ge(sscore, b - 1)
                nc.scalar.copy(KTb[:, b % 2, 2 * f:2 * f + 2, :], ps[6][:, :].rearrange("p (k m) -> p k m", k=2)).then_inc(kT_ok, 1)

            for i in range(NT + 1):
                if i < NT:
                    keyT(i, 0)
                    keyT(i, 1)
                if i >= 1:
                    pT(i - 1)
                if i < NT:
                    keyT(i, 2)
                    exps(i)
                    keyT(i, 3)
            act.wait_ge(s_neg, 1)
            nc.scalar.activation(xps, ps[0][:, 0:256], ACT.Exp, bias=mxs, scale=SC, accum_out=sms).then_inc(s_exp, 1)

        @block.vector
        def _(dve):
            link = Chain(dve, dve_chain)

            def maxima(i):
                dve.wait_ge(score, i + 1)
                if i >= 2:
                    dve.wait_ge(exp_ok, HEADS * (i - 1))
                m = mx[:, i % 2, :]
                for q in range(2):
                    link(nc.vector.tensor_reduce(m[:, 2 * q:2 * q + 2], ps[q][:, :].rearrange("p (h m) -> p h m", h=2), AX, ALU.max))
                nc.vector.tensor_scalar(m, m, -SC, None, ALU.mult).then_inc(neg, 1)

            def normalise(i):
                dve.wait_ge(exp_ok, HEADS * (i + 1))
                link(nc.vector.reciprocal(sm[:, i % 2, :], sm[:, i % 2, :]))
                p = xp[:, i % 2]
                nc.vector.tensor_tensor(p, p, sm[:, i % 2, :].unsqueeze(2).to_broadcast([P, HEADS, NMEM]), ALU.mult)\
                    .then_inc(p_ok, 1)

            def outs(i):
                for q in range(2):
                    dve.wait_ge(val, 2 * i + q + 1)
                    nc.vector.tensor_copy(qXT[:, 4 * q:4 * q + 4, i * P:(i + 1) * P],
                                          ps[4 + q][:, :].rearrange("p (k t) -> p k t", k=4)).then_inc(val_ok, 1)

            for i in range(NT + 1):
                if i < NT:
                    maxima(i)
                if i >= 1:
                    outs(i - 1)
                if i < NT:
                    normalise(i)
            dve.wait_ge(sscore, DB)
            nc.vector.tensor_copy(sS, ps[7][:, 0:256]).then_inc(s_ok, 1)
            dve.wait_ge(s_back, 1)
            link(nc.vector.tensor_reduce(mxs, ps[0][:, 0:256], AX, ALU.max))
            nc.vector.tensor_scalar(mxs, mxs, -SC, None, ALU.mult).then_inc(s_neg, 1)
            dve.wait_ge(s_exp, 1)
            link(nc.vector.reciprocal(sms, sms))
            nc.vector.tensor_scalar(xps, xps, sms, None, ALU.mult).then_inc(s_p, 1)
            dve.wait_ge(s_pt, 1)
            nc.vector.tensor_copy(xpTs, ps[1][:, 0:256]).then_inc(s_pT, 1)
            dve.wait_ge(v_done, DB)
            nc.vector.tensor_copy(qXT[:, :, SEQ:TOK], ps[6][:, 0:KC * NS].rearrange("p (k t) -> p k t", k=KC)).then_inc(x_ok, 1)


def expert_slots(c):
    EW = KC * DE
    c.place(start=0, xw=4 * 3 * EW)
    c.xw = c.A("xw").rearrange("p (s n) -> p s n", s=4)
    c.xw_in = [c.sem(f"x_w{u}") for u in range(4)]


def load_expert(c, sp, e):
    EW = KC * DE
    for q, name in enumerate(('ex_wg', 'ex_wu', 'ex_wd')):
        sp.dma_start(c.xw[:, e % 4, q * EW:(q + 1) * EW], c.T[name][0, e].rearrange("(p k) f -> p (k f)", p=P))\
            .then_inc(c.xw_in[e % 4], 16)


def stage_route(c):
    nc, T, K = c.nc, c.T, c.K
    G4 = 4
    TE = TILES * NE
    c.place(start=3 * 3 * KC * DE, lT=TOK, sel=TE, sc=TE, cmpa=TE * 4, cmpb=TE * 4,
            rank=TE, mask=TE, mask0=TE, masked=TE, pre=TE, gs=TILES * G4, grank=TILES * G4, den=TILES,
            tiles_cmp=NE * 9, tiles_of=NE, base_cmp=NE * NE, base=NE, ends=NE, exp_cmp=MOE_TILES * NE, exp_f=MOE_TILES,
            rk=2 * TILES, bs=2 * TILES, flo_cmp=2 * TILES * NT, flo=2 * TILES, lo=2 * TILES, hi=2 * TILES,
            slot_f=2 * TILES, one_lo=2 * TILES * P, one_hi=2 * TILES * MOE_TILES, work=TE)
    wr = c.A("wr").rearrange("p (k e) -> p k e", k=KC)
    sc, sel, lT = c.A("sc"), c.A("sel"), c.A("lT")
    rank, gs, grank, den = c.A("rank"), c.A("gs"), c.A("grank"), c.A("den")
    ca, cb = c.A("cmpa"), c.A("cmpb")
    tab = lambda k, w: c.A("tab")[:, ROUTE_AT[k]:ROUTE_AT[k] + w]
    e3 = lambda x: x.rearrange("p (i e) -> p i e", e=NE)
    one_lo = c.A("one_lo").rearrange("p (n f) -> p n f", f=P)
    one_hi = c.A("one_hi").rearrange("p (n f) -> p n f", f=MOE_TILES)
    ps, hT, h = c.ps, c.hT, c.h
    s = lambda n: c.sem(f"r_{n}")
    loaded, lT_ok = c.route_in, s("lT")
    logit, e_ok, chain, masks, counted, onehots, rows_ok, zeroed, h_out = (
        s("logit"), s("e"), s("dve"), s("masks"), s("counted"), s("onehots"), s("rows"), s("zero"), s("h"))
    M = TILES * G4

    with nc.Block() as block:
        @block.sync
        def _(sp):
            for e in range(3):
                load_expert(c, sp, e)
            sp.dma_start(c.tokens_dram[0:SEQ, :].rearrange("(i p) d -> p i d", p=P), h[:, 0:NT, :]).then_inc(h_out, 16)
            sp.dma_start(c.tokens_dram[SEQ:TOK, :], h[0:NS, NT, :]).then_inc(h_out, 16)
            sp.wait_ge(h_out, 32)

        @block.tensor
        def _(pe):
            pe.wait_ge(loaded, 48)
            for n in range(GRP):
                for k in range(KC):
                    last = nc.tensor.matmul(ps[4 + n][0:NE, 0:GT], wr[:, k, :], hT[:, k, n * GT:(n + 1) * GT],
                                            start=(k == 0), stop=(k == KC - 1))
                last.then_inc(logit, 1)
            pe.wait_ge(lT_ok, GRP)
            for i in range(TILES):
                r = rows(i)
                last = nc.tensor.transpose(ps[0][0:r, i * NE:(i + 1) * NE], lT[0:NE, i * P:i * P + r], K("ident", NE, NE))
            last.then_inc(logit, 1)
            pe.wait_ge(masks, 1)
            nc.tensor.matmul(ps[1][:, 0:TE], K("before"), c.A("mask"), start=True, stop=False)
            nc.tensor.matmul(ps[1][:, 0:TE], K("ones"), c.A("pre"), start=False, stop=True)
            nc.tensor.matmul(ps[2][:, 0:NE], K("ones"), c.A("pre")[:, TE - NE:TE], start=True, stop=False)
            nc.tensor.matmul(ps[2][:, 0:NE], K("ones"), c.A("mask")[:, TE - NE:TE], start=False, stop=True).then_inc(counted, 1)
            pe.wait_ge(onehots, 1)
            for n in range(2 * TILES):
                last = nc.tensor.matmul(ps[3][:, 0:MOE_TILES], one_lo[:, n, :], one_hi[:, n, :],
                                        start=(n == 0), stop=(n == 2 * TILES - 1))
            last.then_inc(rows_ok, 1)

        @block.scalar
        def _(act):
            nc.scalar.preload_act_table_set(EXPLN)
            for n in range(GRP):
                act.wait_ge(logit, n + 1)
                nc.scalar.copy(lT[0:NE, n * GT:(n + 1) * GT], ps[4 + n][0:NE, 0:GT]).then_inc(lT_ok, 1)
            act.wait_ge(zeroed, 1)
            act.wait_ge(logit, GRP + 1)
            nc.scalar.activation(sc[:, 0:NT * NE], ps[0][:, 0:NT * NE], ACT.Exp, scale=-1.0).then_inc(e_ok, 1)
            nc.scalar.activation(sc[0:NS, NT * NE:], ps[0][0:NS, NT * NE:TILES * NE], ACT.Exp, scale=-1.0).then_inc(e_ok, 1)

        @block.vector
        def _(dve):
            link = Chain(dve, chain)
            vt = nc.vector
            vt.memset(sc, 0.0).then_inc(zeroed, 1)
            dve.wait_ge(e_ok, 2)
            dve.wait_ge(loaded, 48)
            link(vt.tensor_scalar(sc, sc, 1.0, None, ALU.add))
            link(vt.reciprocal(sc, sc))
            link(vt.tensor_tensor(e3(sel), e3(sc), c.A("rbias").unsqueeze(1).to_broadcast([P, TILES, NE]), ALU.add))

            def ranks(x, m, out):
                xi = x.rearrange("p (m i) -> p m i", i=4).unsqueeze(2).to_broadcast([P, m, 4, 4])
                xj = x.rearrange("p (m j) -> p m j", j=4).unsqueeze(3).to_broadcast([P, m, 4, 4])
                a = ca[:, 0:16 * m].rearrange("p (m j i) -> p m j i", j=4, i=4)
                b = cb[:, 0:16 * m].rearrange("p (m j i) -> p m j i", j=4, i=4)
                tri = tab("tie", 16).rearrange("p (j i) -> p j i", j=4).unsqueeze(1).to_broadcast([P, m, 4, 4])
                link(vt.tensor_tensor(a, xi, xj, ALU.is_equal))
                link(vt.tensor_tensor(a, a, tri, ALU.mult))
                link(vt.tensor_tensor(b, xi, xj, ALU.is_gt))
                link(vt.tensor_tensor(a, a, b, ALU.add))
                link(vt.tensor_reduce(out.rearrange("p (m j) -> p m j", j=4), a, AX, ALU.add))

            mask, mask0, work = c.A("mask"), c.A("mask0"), c.A("work")
            ranks(sel, M, rank)
            link(vt.tensor_scalar(mask, rank, 1.5, None, ALU.is_lt))
            link(vt.tensor_tensor(work, mask, sel, ALU.mult))
            link(vt.tensor_reduce(gs, work.rearrange("p (m e) -> p m e", e=4), AX, ALU.add))
            ranks(gs, TILES, grank)
            link(vt.tensor_scalar(grank, grank, 0.5, None, ALU.is_lt))
            g4 = lambda x: x.rearrange("p (m e) -> p m e", e=4)
            link(vt.tensor_tensor(g4(mask), g4(mask), grank.unsqueeze(2).to_broadcast([P, M, 4]), ALU.mult))
            link(vt.tensor_tensor(e3(mask), e3(mask), tab("valid", TILES).unsqueeze(2).to_broadcast([P, TILES, NE]), ALU.mult))
            link(vt.tensor_scalar(mask0, rank, 0.5, None, ALU.is_lt))
            link(vt.tensor_tensor(mask0, mask0, mask, ALU.mult))
            pre = c.A("pre")
            link(vt.memset(pre[:, 0:NE], 0.0))
            for i in range(1, TILES):
                ins = vt.tensor_tensor(pre[:, i * NE:(i + 1) * NE], pre[:, (i - 1) * NE:i * NE], mask[:, (i - 1) * NE:i * NE], ALU.add)
                if i < TILES - 1:
                    link(ins)
            ins.then_inc(masks, 1)
            dve.wait_ge(masks, 1)

            def pick(m, x, out):
                link(vt.tensor_tensor(e3(work), e3(m), x, ALU.mult))
                link(vt.tensor_reduce(out, e3(work), AX, ALU.add))

            pick(mask, e3(sc), den)
            link(vt.tensor_scalar(den, den, 1e-38, None, ALU.max))
            link(vt.reciprocal(den, den))
            mask1 = c.A("masked")
            link(vt.tensor_tensor(mask1, mask, mask0, ALU.subtract))
            for q, m in enumerate((mask0, mask1)):
                pick(m, e3(sc), c.gate[:, q * TILES:(q + 1) * TILES])
                link(vt.tensor_tensor(c.gate[:, q * TILES:(q + 1) * TILES], c.gate[:, q * TILES:(q + 1) * TILES], den, ALU.mult))

            dve.wait_ge(counted, 1)
            cmp9 = c.A("tiles_cmp").rearrange("p (e j) -> p e j", j=9)
            link(vt.tensor_copy(work[:, 0:NE], ps[2][:, 0:NE]))
            link(vt.tensor_tensor(cmp9, work[:, 0:NE].unsqueeze(2).to_broadcast([P, NE, 9]),
                                  tab("thr9", 9).unsqueeze(1).to_broadcast([P, NE, 9]), ALU.is_gt))
            tiles_of, base, ends = c.A("tiles_of"), c.A("base"), c.A("ends")
            link(vt.tensor_reduce(tiles_of, cmp9, AX, ALU.add))
            bc = c.A("base_cmp").rearrange("p (e f) -> p e f", f=NE)
            link(vt.tensor_tensor(bc, tiles_of.unsqueeze(1).to_broadcast([P, NE, NE]),
                                  tab("tri16", NE * NE).rearrange("p (e f) -> p e f", f=NE), ALU.mult))
            link(vt.tensor_reduce(base, bc, AX, ALU.add))
            link(vt.tensor_tensor(ends, base, tiles_of, ALU.add))
            ec = c.A("exp_cmp").rearrange("p (s e) -> p s e", e=NE)
            link(vt.tensor_tensor(ec, tab("iota32", MOE_TILES).unsqueeze(2).to_broadcast([P, MOE_TILES, NE]),
                                  ends.unsqueeze(1).to_broadcast([P, MOE_TILES, NE]), ALU.is_ge))
            exp_f = c.A("exp_f")
            link(vt.tensor_reduce(exp_f, ec, AX, ALU.add))
            link(vt.tensor_scalar(exp_f, exp_f, float(NE - 1), None, ALU.min))
            link(vt.tensor_copy(c.tile_expert[:], exp_f[0:1, :]))
            link(vt.tensor_scalar(ends, ends, 1.0, None, ALU.add))
            link(vt.tensor_copy(c.expert_end[:], ends[0:1, :]))

            rk, bs, flo, lo, hi = c.A("rk"), c.A("bs"), c.A("flo"), c.A("lo"), c.A("hi")
            ranked = cb[:, 0:TE]
            link(vt.tensor_copy(ranked, ps[1][:, 0:TE]))
            for q, m in enumerate((mask0, mask1)):
                pick(m, e3(ranked), rk[:, q * TILES:(q + 1) * TILES])
                pick(m, base.unsqueeze(1).to_broadcast([P, TILES, NE]), bs[:, q * TILES:(q + 1) * TILES])
            N2 = 2 * TILES
            fc = c.A("flo_cmp").rearrange("p (n j) -> p n j", j=NT)
            link(vt.tensor_tensor(fc, rk.unsqueeze(2).to_broadcast([P, N2, NT]),
                                  tab("thr9", 9)[:, 1:9].unsqueeze(1).to_broadcast([P, N2, NT]), ALU.is_ge))
            link(vt.tensor_reduce(flo, fc, AX, ALU.add))
            link(vt.scalar_tensor_tensor(lo, flo, -float(P), rk, ALU.mult, ALU.add))
            link(vt.tensor_tensor(hi, bs, flo, ALU.add))
            link(vt.scalar_tensor_tensor(c.A("slot_f"), hi, float(P), lo, ALU.mult, ALU.add))
            link(vt.tensor_copy(c.slot[:], c.A("slot_f")))
            link(vt.tensor_tensor(one_lo, lo.unsqueeze(2).to_broadcast([P, N2, P]),
                                  tab("iota128", P).unsqueeze(1).to_broadcast([P, N2, P]), ALU.is_equal))
            link(vt.tensor_tensor(one_hi, hi.unsqueeze(2).to_broadcast([P, N2, MOE_TILES]),
                                  tab("iota32", MOE_TILES).unsqueeze(1).to_broadcast([P, N2, MOE_TILES]), ALU.is_equal))
            for q in range(2):
                x = one_hi[:, q * TILES:(q + 1) * TILES, :]
                ins = vt.tensor_tensor(x, x, tab("token", TILES).unsqueeze(2).to_broadcast([P, TILES, MOE_TILES]), ALU.mult)
                if q == 0:
                    link(ins)
            ins.then_inc(onehots, 1)
            dve.wait_ge(rows_ok, 1)
            link(vt.tensor_copy(c.row_token[:], ps[3][:, 0:MOE_TILES]))


def stage_experts(c):
    nc, T, K = c.nc, c.T, c.K
    EW = KC * DE
    gate_up_of = c.xw[:, :, 0:2 * EW].rearrange("p s (g k f) -> p s g k f", g=2, k=KC)
    down_of = c.xw[:, :, 2 * EW:].rearrange("p s (j n) -> p s j n", j=2)
    free = c.hT.rearrange("p k t -> p (k t)")
    x = free[:, 0:2 * D].rearrange("p (s d) -> p s d", s=2)
    xT = free[:, 2 * D:4 * D].rearrange("p (s k t) -> p s k t", s=2, k=KC)
    y = free[:, 4 * D:6 * D].rearrange("p (s d) -> p s d", s=2)
    sg = free[:, 6 * D:6 * D + 2 * DE].rearrange("p (s f) -> p s f", s=2)
    hid = free[:, 6 * D + 2 * DE:6 * D + 4 * DE].rearrange("p (s f) -> p s f", s=2)
    hidT = free[:, 6 * D + 4 * DE:6 * D + 6 * DE].rearrange("p (s j t) -> p s j t", s=2, j=2)
    ps, h = c.ps, c.h
    s = lambda n: c.sem(f"x{n}")
    w_ok = s("wok")
    x_in = [s(f"x{u}") for u in range(2)]
    y_out = [s(f"y{u}") for u in range(2)]
    xT_ok = [s(f"xT{q}") for q in range(2)]
    y_ok = [s(f"yok{q}") for q in range(2)]
    x_turned, up, sig, hid_ok, hid_turned, hidT_ok, down, scaled = (
        s("xturned"), s("up"), s("sig"), s("hid"), s("hturned"), s("hidT"), s("down"), s("scaled"))
    U = 4
    J = MOE_TILES // U
    XT, UPB, HT, DNB = (0, 1), (2, 3), 4, (6, 7)

    with nc.Block() as block:
        @block.sync
        def _(sp):
            sp.sem_inc(y_ok[1], 1)
            for e in range(NE):
                sp.wait_ge(c.xw_in[e % 4], 48 * (e // 4 + 1))
                sp.sem_inc(w_ok, 1)
                if e == 0:
                    load_expert(c, sp, 3)
                if e >= 2 and e + 2 < NE:
                    sp.wait_ge(y_ok[1], sp.value_load(c.expert_end[0:1, e - 2:e - 1], min_val=1, max_val=MOE_TILES + 1))
                    load_expert(c, sp, e + 2)

        @block.gpsimd
        def _(gp):
            for t in range(MOE_TILES):
                if t >= 2:
                    gp.wait_ge(x_turned, 2 * t - 2)
                gp.indirect_dma_start(x[:, t % 2, :], None, c.tokens_dram,
                                      bass.IndirectOffsetOnAxis(ap=c.row_token[:, t:t + 1], axis=0)).then_inc(x_in[t % 2], 16)

        @block.tensor
        def _(pe):
            def expert(t):
                return pe.value_load(c.tile_expert[0:1, bass.ds(t, 1)], min_val=0, max_val=NE - 1)

            def turn_x(j, u):
                t = j * U + u
                pe.wait_ge(x_in[u % 2], 16 * (j * 2 + u // 2 + 1))
                for q in range(2):
                    if not (isinstance(j, int) and t < 1):
                        pe.wait_ge(xT_ok[q], t)
                    for k in range(4):
                        last = nc.tensor.transpose(ps[XT[q]][:, k * P:(k + 1) * P], x[:, u % 2, slice(4 * q + k, D, KC)],
                                                   K("ident"))
                    last.then_inc(x_turned, 1)

            def gate_up(j, u, half, e):
                t = j * U + u
                if half == 0:
                    pe.wait_ge(w_ok, e + 1)
                    pe.wait_ge(xT_ok[0], t + 1)
                    pe.wait_ge(xT_ok[1], t + 1)
                    if not (isinstance(j, int) and t < 2):
                        pe.wait_ge(hid_ok, t - 1)
                slot = e & 3
                for k in range(4 * half, 4 * half + 4):
                    last = nc.tensor.matmul(ps[UPB[u % 2]][:, :], xT[:, u % 2, k, :], gate_up_of[:, bass.ds(slot, 1), :, k, :].rearrange("p a g f -> p (a g) f"), start=(k == 0), stop=(k == KC - 1))
                if half == 1:
                    last.then_inc(up, 1)

            def turn_hid(j, u):
                t = j * U + u
                pe.wait_ge(hid_ok, t + 1)
                if not (isinstance(j, int) and t < 1):
                    pe.wait_ge(hidT_ok, t)
                for f in range(2):
                    last = nc.tensor.transpose(ps[HT][:, f * P:(f + 1) * P], hid[:, u % 2, slice(f, DE, 2)], K("ident"))
                last.then_inc(hid_turned, 1)

            def product_down(j, u, slot):
                t = j * U + u
                pe.wait_ge(hidT_ok, t + 1)
                for q in range(2):
                    if not (isinstance(j, int) and t < 1):
                        pe.wait_ge(y_ok[q], t + q)
                    for f in range(2):
                        last = nc.tensor.matmul(ps[DNB[q]][:, :], hidT[:, u % 2, f, :], down_of[:, bass.ds(slot, 1), f, q * 512:(q + 1) * 512].rearrange("p a n -> p (a n)"),
                                                start=(f == 0), stop=(f == 1))
                    last.then_inc(down, 1)

            def step(j, u, first, last):
                prev = (j, u - 1) if u else (j - 1, U - 1)
                e = expert(j * U + u)
                prev_e = None if first else expert(j * U + u - 1)
                gate_up(j, u, 0, e)
                if not first:
                    turn_hid(*prev)
                gate_up(j, u, 1, e)
                if not last:
                    turn_x(*((j, u + 1) if u < U - 1 else (j + 1, 0)))
                if not first:
                    product_down(*prev, prev_e & 3)

            turn_x(0, 0)
            for u in range(U):
                step(0, u, u == 0, False)
            with pe.Fori(1, J - 1) as j:
                for u in range(U):
                    step(j, u, False, False)
            for u in range(U):
                step(J - 1, u, False, u == U - 1)
            turn_hid(J - 1, U - 1)
            product_down(J - 1, U - 1, expert(MOE_TILES - 1) & 3)

        @block.scalar
        def _(act):
            def turned_x(t, u):
                act.wait_ge(x_turned, 2 * t + 1)
                nc.scalar.copy(xT[:, u % 2, 0:4, :], ps[XT[0]][:, :].rearrange("p (k t) -> p k t", k=4)).then_inc(xT_ok[0], 1)

            def turned_hid(t, u):
                act.wait_ge(hid_turned, t + 1)
                nc.scalar.copy(hidT[:, u % 2], ps[HT][:, 0:DE].rearrange("p (f t) -> p f t", f=2)).then_inc(hidT_ok, 1)

            def silu(t, u, first):
                act.wait_ge(up, t + 1)
                if not first:
                    act.wait_ge(hid_ok, t - 1)
                nc.scalar.activation(sg[:, u % 2, :], ps[UPB[u % 2]][:, 0:DE], ACT.Silu).then_inc(sig, 1)

            def finish(t, j2, u, first):
                act.wait_ge(down, 2 * t + 1)
                if not first:
                    act.wait_ge(y_out[u % 2], 16 * j2)
                nc.scalar.copy(y[:, u % 2, 0:512], ps[DNB[0]][:, :]).then_inc(y_ok[0], 1)
                act.wait_ge(y_ok[0], t + 1)
                act.wait_ge(y_ok[1], t + 2)
                act.dma_start(c.rows_dram[bass.ds(t, 1)].rearrange("a p d -> (a p) d"), y[:, u % 2, :]).then_inc(y_out[u % 2], 16)

            def step(j, u, first, last):
                t = j * U + u
                if not (first and u == 0):
                    turned_hid(j * U + u - 1, (u - 1) % U)
                silu(t, u, first and u < 2)
                if not (last and u == U - 1):
                    turned_x(j * U + u + 1, (u + 1) % U)
                if not (first and u == 0):
                    finish(j * U + u - 1, j * 2 + (u - 1) // 2, (u - 1) % U, first and u < 3)

            turned_x(0, 0)
            for u in range(U):
                step(0, u, True, False)
            with act.Fori(1, J - 1) as j:
                for u in range(U):
                    step(j, u, False, False)
            for u in range(U):
                step(J - 1, u, False, True)
            turned_hid(MOE_TILES - 1, U - 1)
            finish(MOE_TILES - 1, (MOE_TILES - 1) // 2, U - 1, False)
            for u in range(2):
                act.wait_ge(y_out[u], 16 * MOE_TILES // 2)

        @block.vector
        def _(dve):
            def hidden(t, u):
                dve.wait_ge(sig, t + 1)
                nc.vector.tensor_tensor(hid[:, u % 2, :], ps[UPB[u % 2]][:, DE:2 * DE], sg[:, u % 2, :], ALU.mult).then_inc(hid_ok, 1)

            def turned_x(t, u):
                dve.wait_ge(x_turned, 2 * t + 2)
                nc.vector.tensor_copy(xT[:, u % 2, 4:8, :], ps[XT[1]][:, :].rearrange("p (k t) -> p k t", k=4)).then_inc(xT_ok[1], 1)

            def finish(t, j2, u, first):
                dve.wait_ge(down, 2 * t + 2)
                if not first:
                    dve.wait_ge(y_out[u % 2], 16 * j2)
                nc.vector.tensor_copy(y[:, u % 2, 512:D], ps[DNB[1]][:, :]).then_inc(y_ok[1], 1)

            def step(j, u, first, last):
                hidden(j * U + u, u)
                if not (last and u == U - 1):
                    turned_x(j * U + u + 1, (u + 1) % U)
                if not (first and u == 0):
                    finish(j * U + u - 1, j * 2 + (u - 1) // 2, (u - 1) % U, first and u < 3)

            turned_x(0, 0)
            nc.vector.tensor_scalar(h[:, 0:NT, :], h[:, 0:NT, :], ALPHA, None, ALU.mult).then_inc(scaled, 1)
            nc.vector.tensor_scalar(h[0:NS, NT, :], h[0:NS, NT, :], ALPHA, None, ALU.mult).then_inc(scaled, 1)
            for u in range(U):
                step(0, u, True, False)
            with dve.Fori(1, J - 1) as j:
                for u in range(U):
                    step(j, u, False, False)
            for u in range(U):
                step(J - 1, u, False, True)
            finish(MOE_TILES - 1, (MOE_TILES - 1) // 2, U - 1, False)


def stage_combine(c):
    nc, T, O = c.nc, c.T, c.O
    S = 6
    c.place(start=0, z=S * D, cg=D, cb=D)
    z = c.A("z").rearrange("p (s d) -> p s d", s=S)
    g, b = c.A("cg"), c.A("cb")
    h = c.h
    s = lambda n: c.sem(f"c_{n}")
    z_in = [s(f"z{n}") for n in range(S)]
    ln_in, summed, stats, scaled, gained, normed, stored, dve_chain, act_chain = (
        s("ln"), s("summed"), s("stats"), s("scaled"), s("gained"), s("normed"), s("stored"), s("dve"), s("act"))

    with nc.Block() as block:
        @block.sync
        def _(sp):
            sp.dma_start(g, row_bc(T['ln3_g'][0])).then_inc(ln_in, 16)
            sp.dma_start(b, row_bc(T['ln3_b'][0])).then_inc(ln_in, 16)
            for i in range(TILES):
                sp.wait_ge(normed, i + 1)
                dst = O['y_prompt'][0, i * P:(i + 1) * P, :] if i < NT else O['y_sample'].rearrange("b t d -> (b t) d")
                sp.dma_start(dst, h[0:rows(i), i, :]).then_inc(stored, 16)
            sp.wait_ge(stored, 16 * TILES)

        @block.gpsimd
        def _(gp):
            def gather(n):
                i, q = n // 2, n % 2
                if n >= S:
                    gp.wait_ge(summed, n - S + 1)
                r = rows(i)
                gp.indirect_dma_start(z[0:r, n % S, :], None, c.rows_dram.rearrange("s p d -> (s p) d"),
                                      bass.IndirectOffsetOnAxis(ap=c.slot[0:r, q * TILES + i:q * TILES + i + 1], axis=0))\
                    .then_inc(z_in[n % S], 16)

            for n in range(S):
                gather(n)
            gp.wait_ge(ln_in, 32)
            for i in range(TILES):
                for n in (S + 2 * i, S + 2 * i + 1):
                    if n < 2 * TILES:
                        gather(n)
                r = rows(i)
                gp.wait_ge(gained, i + 1)
                nc.gpsimd.tensor_tensor(h[0:r, i, :], h[0:r, i, :], b[0:r, :], ALU.add).then_inc(normed, 1)

        @block.vector
        def _(dve):
            link = Chain(dve, dve_chain)

            def sum_up(i):
                r = rows(i)
                for q in range(2):
                    n = 2 * i + q
                    dve.wait_ge(z_in[n % S], 16 * (n // S + 1))
                    if q == 1:
                        dve.wait_ge(summed, n)
                    nc.vector.scalar_tensor_tensor(h[0:r, i, :], z[0:r, n % S, :], c.gate[0:r, q * TILES + i:q * TILES + i + 1],
                                                   h[0:r, i, :], ALU.mult, ALU.add).then_inc(summed, 1)
                dve.wait_ge(summed, 2 * i + 2)
                if i >= 2:
                    dve.wait_ge(scaled, i - 1)
                ln_stats(nc, link, h, i, c.st[:, i % 2, :], c.mv[:, i % 2, :]).then_inc(stats, 1)

            def gain(i):
                r = rows(i)
                dve.wait_ge(scaled, i + 1)
                nc.vector.tensor_tensor(h[0:r, i, :], h[0:r, i, :], g[0:r, :], ALU.mult).then_inc(gained, 1)

            for i in range(TILES):
                sum_up(i)
                if i == 0:
                    dve.wait_ge(ln_in, 32)
                if i >= 1:
                    gain(i - 1)
            gain(TILES - 1)

        @block.scalar
        def _(act):
            link = Chain(act, act_chain)
            nc.scalar.preload_act_table_set(EXPLN)
            for i in range(TILES):
                r = rows(i)
                act.wait_ge(stats, i + 1)
                mv, rstd, off = c.mv[:, i % 2, :], c.rstd[:, i % 2, :], c.off[:, i % 2:i % 2 + 1]
                link(ln_rstd(nc, link, i, mv, rstd, c.eps))
                link(nc.scalar.activation(off[0:r, :], mv[0:r, 0:1], ACT.Copy, scale=rstd[0:r, :]))
                link(nc.scalar.activation(off[0:r, :], off[0:r, :], ACT.Copy, scale=-1.0))
                nc.scalar.activation(h[0:r, i, :], h[0:r, i, :], ACT.Identity, bias=off[0:r, :], scale=rstd[0:r, :]).then_inc(scaled, 1)


def build(nc, T, O):
    with ExitStack() as ctx:
        c = setup(nc, ctx, T, O)
        c.tokens_dram = nc.dram_tensor("tokens", (TOK, D), F32, kind="Internal").ap()
        c.rows_dram = nc.dram_tensor("expert_rows", (MOE_TILES, P, D), F32, kind="Internal").ap()
        stage_entry(c)
        stage_features(c)
        stage_gate_and_pool(c)
        stage_stick_prompt(c)
        stage_stick_sample(c)
        c.renew_semaphores()
        stage_delta_inputs(c)
        stage_delta(c)
        c.renew_semaphores()
        c.res_at, c.split_at = 0, 2 * KC * D + 2 * D
        c.place(start=23144, hTl=KC * TOK)
        c.hT_low = c.rounded("hT_low", "hTl").rearrange("p (k t) -> p k t", k=KC)
        stage_residual(c, "o", c.hT, 'w_out', 'ln1_g', 'ln1_b', True)
        stage_memory(c)
        stage_queries(c)
        stage_cross(c)
        c.res_at, c.split_at = 4096 + KC * TOK, 0
        c.place(start=c.res_at + 2 * KC * D + 2 * D, wr=KC * NE, rbias=NE, tab=NROUTE)
        c.renew_semaphores()
        c.route_in = c.sem("route_in")
        stage_residual(c, "w", c.qXT, 'xa_wo', 'ln2_g', 'ln2_b', False)
        expert_slots(c)
        stage_route(c)
        stage_experts(c)
        stage_combine(c)


def kernel(**inputs):
    import numpy as _np
    import concourse.bacc as _bacc
    from concourse import mybir as _mybir
    from concourse.bass_utils import run_bass_kernel_spmd as _run

    nc = _bacc.Bacc("TRN2", target_bir_lowering=False, num_devices=1)
    arrays, T, O = {}, {}, {}
    for name in _INS:
        a = _np.ascontiguousarray(inputs[name])
        arrays[f"in_{name}_dram"] = a
        T[name] = nc.dram_tensor(f"in_{name}_dram", a.shape, _mybir.dt.from_np(a.dtype), kind="ExternalInput").ap()
    for key, blocks in (('const_tables', CONSTS), ('pool_tables', POOL_CONSTS), ('route_table', ROUTE_CONSTS)):
        table = _np.concatenate(list(blocks.values()), axis=1)
        arrays[f"{key}_dram"] = table
        T[key] = nc.dram_tensor(f"{key}_dram", table.shape, F32, kind="ExternalInput").ap()
    for name, shape in _OUTS:
        O[name] = nc.dram_tensor(f"out_{name}_dram", shape, F32, kind="ExternalOutput").ap()
    build(nc, T, O)
    r = _run(nc, [arrays], core_ids=[0])
    return tuple(r.results[0][f"out_{name}_dram"] for name, _ in _OUTS)
```
